# Optimizing a Trainium2 kernel written in Bass

```python
import math
import jax, jax.numpy as jnp
from jax import lax
import numpy as np

D_MODEL = 1024
BATCH = 1
SEQ = 512
DEPTH = 2
DEC_BATCH = 8
DEC_SEQ = 4
PAST_LEN = 4096
PAGE_SIZE = 128

F32 = jnp.float32

N_MIXERS = 2
N_GDN = (DEPTH + 1) // 2
N_NSA = DEPTH // 2

GDN_HEADS = 8
GDN_DK = 128
GDN_DV = 128
GDN_QK_W = GDN_HEADS * GDN_DK
GDN_V_W = GDN_HEADS * GDN_DV
GDN_CONV = 4
GDN_CONV_W = 2 * GDN_QK_W + GDN_V_W
GDN_IN = GDN_CONV_W + GDN_V_W + 2 * GDN_HEADS
GDN_CHUNK = 64

NSA_HEADS = 16
NSA_KV_HEADS = 4
NSA_GROUP = NSA_HEADS // NSA_KV_HEADS
NSA_HD = 64
NSA_Q_W = NSA_HEADS * NSA_HD
NSA_KV_W = 2 * NSA_KV_HEADS * NSA_HD
NSA_IN = NSA_Q_W + 3 * NSA_KV_W + 3 * NSA_HEADS
CMP_BLOCK = 32
SEL_BLOCK = 64
SEL_RATIO = SEL_BLOCK // CMP_BLOCK
TOP_N = 16
WINDOW = 512
Q_BLOCK = 32

N_GROUPS = 4
EXPERTS_PER_GROUP = 8
N_EXPERTS = N_GROUPS * EXPERTS_PER_GROUP
TOP_K_IN_GROUP = 2
EXPERT_FF = 256

NORM_EPS = 1e-6
NEG = -1e30
SEL_BIG = 1e6

kernel_name = 'hybrid_gdn_nsa_hmoe_step'

def rms_norm(x, gain):
    xf = x.astype(F32)
    y = xf * lax.rsqrt(jnp.mean(xf * xf, axis=-1, keepdims=True) + NORM_EPS)
    return (y * gain.astype(F32)).astype(x.dtype)

def l2_norm(x):
    xf = x.astype(F32)
    return xf * lax.rsqrt(jnp.sum(xf * xf, axis=-1, keepdims=True) + NORM_EPS)

def masked_softmax(s, mask):
    s = jnp.where(mask, s.astype(F32), NEG)
    m = jnp.max(s, axis=-1, keepdims=True)
    p = jnp.where(mask, jnp.exp(s - m), 0.0)
    return p / jnp.maximum(jnp.sum(p, axis=-1, keepdims=True), 1e-30)

def gated_delta_chunked(q, k, v, g, beta, state0):
    B, T, H, DK = q.shape
    C = min(GDN_CHUNK, T)
    pad = (-T) % C
    n = (T + pad) // C

    def prep(a):
        a = jnp.moveaxis(a.astype(F32), 2, 1)
        a = jnp.pad(a, [(0, 0), (0, 0), (0, pad)] + [(0, 0)] * (a.ndim - 3))
        return a.reshape((B, H, n, C) + a.shape[3:])

    q = prep(q) * (DK ** -0.5)
    k, v, g, beta = prep(k), prep(v), prep(g), prep(beta)
    G = jnp.cumsum(g, axis=-1)
    pos = jnp.arange(C)
    causal = pos[:, None] >= pos[None, :]
    strict = pos[:, None] > pos[None, :]
    decay = jnp.exp(jnp.where(causal, G[..., :, None] - G[..., None, :], NEG))
    kb = k * beta[..., None]
    L = jnp.where(strict, jnp.einsum('bhncd,bhnsd->bhncs', kb, k) * decay, 0.0)
    eye = jnp.eye(C, dtype=F32)
    t_inv = lax.linalg.triangular_solve(L + eye, jnp.broadcast_to(eye, L.shape),
                                        left_side=True, lower=True, unit_diagonal=True)
    u = jnp.einsum('bhncs,bhnse->bhnce', t_inv, v * beta[..., None])
    w = jnp.einsum('bhncs,bhnsd->bhncd', t_inv, kb * jnp.exp(G)[..., None])
    qk = jnp.where(causal, jnp.einsum('bhncd,bhnsd->bhncs', q, k) * decay, 0.0)
    g_last = G[..., -1]
    k_tail = k * jnp.exp(g_last[..., None] - G)[..., None]
    q_head = q * jnp.exp(G)[..., None]

    def step(S, inp):
        qh, kt, ui, wi, qki, gl = inp
        v_new = ui - jnp.einsum('bhcd,bhde->bhce', wi, S)
        o = jnp.einsum('bhcd,bhde->bhce', qh, S) + jnp.einsum('bhcs,bhse->bhce', qki, v_new)
        S = S * jnp.exp(gl)[..., None, None] + jnp.einsum('bhcd,bhce->bhde', kt, v_new)
        return S, o

    xs = tuple(jnp.moveaxis(a, 2, 0) for a in (q_head, k_tail, u, w, qk, g_last))
    S, o = lax.scan(step, state0.astype(F32), xs)
    o = jnp.moveaxis(o, 0, 2).reshape(B, H, n * C, -1)[:, :, :T]
    return jnp.moveaxis(o, 1, 2), S

def gdn_mixer(xn, conv_prev, state0, w_in, conv_w, a_log, dt_bias, o_gain, w_out):
    B, T, _ = xn.shape
    proj = xn @ w_in
    qkv = proj[..., :GDN_CONV_W]
    z = proj[..., GDN_CONV_W:GDN_CONV_W + GDN_V_W]
    a = proj[..., GDN_CONV_W + GDN_V_W:GDN_CONV_W + GDN_V_W + GDN_HEADS]
    b = proj[..., GDN_CONV_W + GDN_V_W + GDN_HEADS:]
    xc = jnp.concatenate([conv_prev.astype(qkv.dtype), qkv], axis=1)
    conv = xc[:, 0:T] * conv_w[0]
    for i in range(1, GDN_CONV):
        conv = conv + xc[:, i:i + T] * conv_w[i]
    conv = jax.nn.silu(conv)
    new_conv = xc[:, T:]
    q = l2_norm(conv[..., :GDN_QK_W].reshape(B, T, GDN_HEADS, GDN_DK))
    k = l2_norm(conv[..., GDN_QK_W:2 * GDN_QK_W].reshape(B, T, GDN_HEADS, GDN_DK))
    v = conv[..., 2 * GDN_QK_W:].reshape(B, T, GDN_HEADS, GDN_DV)
    beta = jax.nn.sigmoid(b.astype(F32))
    g = -jnp.exp(a_log.astype(F32)) * jax.nn.softplus(a.astype(F32) + dt_bias.astype(F32))
    o, S = gated_delta_chunked(q, k, v, g, beta, state0)
    o = rms_norm(o, o_gain) * jax.nn.silu(z.astype(F32).reshape(B, T, GDN_HEADS, GDN_DV))
    y = o.reshape(B, T, GDN_V_W).astype(xn.dtype) @ w_out
    return y, S, new_conv

def nsa_project(xn, w_in, q_gain, k_gain):
    B, T, _ = xn.shape
    proj = xn @ w_in
    q = rms_norm(proj[..., :NSA_Q_W].reshape(B, T, NSA_HEADS, NSA_HD), q_gain)
    kv = [proj[..., NSA_Q_W + i * NSA_KV_W:NSA_Q_W + (i + 1) * NSA_KV_W]
          .reshape(B, T, 2, NSA_KV_HEADS, NSA_HD) for i in range(3)]
    gates = jax.nn.sigmoid(proj[..., NSA_Q_W + 3 * NSA_KV_W:].astype(F32)).reshape(B, T, NSA_HEADS, 3)

    def norm_k(r):
        return jnp.stack([rms_norm(r[:, :, 0], k_gain), r[:, :, 1]], axis=2)

    return q, kv[0], norm_k(kv[1]), norm_k(kv[2]), gates

def compress(kv_rows, k_gain):
    B, L = kv_rows.shape[:2]
    m = kv_rows.astype(F32).reshape(B, L // CMP_BLOCK, CMP_BLOCK, 2, NSA_KV_HEADS, NSA_HD).mean(axis=2)
    return rms_norm(m[:, :, 0], k_gain), m[:, :, 1]

def nsa_core(q, gates, qpos, kc, vc, c_end, fetch_sel, n_sel, win_kv, win_pos):
    B, T = q.shape[:2]
    qg = q.astype(F32).reshape(B, T, NSA_KV_HEADS, NSA_GROUP, NSA_HD) * (NSA_HD ** -0.5)
    s_c = jnp.einsum('btkgd,bckd->bkgtc', qg, kc)
    p_c = masked_softmax(s_c, c_end[None, :] <= qpos[:, None])
    o_c = jnp.einsum('bkgtc,bckd->btkgd', p_c, vc)
    nc = kc.shape[1]
    imp = jnp.pad(p_c.sum(axis=2), ((0, 0), (0, 0), (0, 0), (0, n_sel * SEL_RATIO - nc)))
    imp = imp.reshape(B, NSA_KV_HEADS, T, n_sel, SEL_RATIO).sum(axis=-1)
    blk = jnp.arange(n_sel)[None, :]
    cur = (qpos // SEL_BLOCK)[:, None]
    forced = (blk == 0) | (blk == cur) | (blk == cur - 1)
    score = jnp.where(blk > cur, -SEL_BIG, jnp.where(forced, SEL_BIG, imp))
    _, idx = lax.top_k(score, min(TOP_N, n_sel))
    n = idx.shape[-1]
    kv_s = fetch_sel(idx).astype(F32)
    pos_s = idx[..., None] * SEL_BLOCK + jnp.arange(SEL_BLOCK)
    s_s = jnp.einsum('btkgd,bktnjd->bkgtnj', qg, kv_s[..., 0, :]).reshape(B, NSA_KV_HEADS, NSA_GROUP, T, n * SEL_BLOCK)
    m_s = (pos_s <= qpos[None, None, :, None, None]).reshape(B, NSA_KV_HEADS, 1, T, n * SEL_BLOCK)
    p_s = masked_softmax(s_s, m_s)
    o_s = jnp.einsum('bkgtm,bktmd->btkgd', p_s, kv_s[..., 1, :].reshape(B, NSA_KV_HEADS, T, n * SEL_BLOCK, NSA_HD))
    wkv = win_kv.astype(F32)
    s_w = jnp.einsum('btkgd,blkd->bkgtl', qg, wkv[:, :, 0])
    dpos = qpos[:, None] - win_pos[None, :]
    p_w = masked_softmax(s_w, (dpos >= 0) & (dpos < WINDOW) & (win_pos[None, :] >= 0))
    o_w = jnp.einsum('bkgtl,blkd->btkgd', p_w, wkv[:, :, 1])
    shp = (B, T, NSA_HEADS, NSA_HD)
    return (gates[..., 0:1] * o_c.reshape(shp) + gates[..., 1:2] * o_s.reshape(shp)
            + gates[..., 2:3] * o_w.reshape(shp))

def nsa_prompt(xn, w_in, q_gain, k_gain, w_out):
    B, T, _ = xn.shape
    q, cmp_kv, slc_kv, win_kv, gates = nsa_project(xn, w_in, q_gain, k_gain)
    kc, vc = compress(cmp_kv, k_gain)
    c_end = (jnp.arange(T // CMP_BLOCK) + 1) * CMP_BLOCK - 1
    n_sel = T // SEL_BLOCK
    slc_blocks = jnp.moveaxis(slc_kv.reshape(B, n_sel, SEL_BLOCK, 2, NSA_KV_HEADS, NSA_HD), 4, 1)
    bi = jnp.arange(B)[:, None, None, None]
    ki = jnp.arange(NSA_KV_HEADS)[None, :, None, None]

    def fetch(idx):
        return slc_blocks[bi, ki, idx]

    win_pad = jnp.pad(win_kv, ((0, 0), (WINDOW, 0), (0, 0), (0, 0), (0, 0)))

    def one_block(start):
        qpos = start + jnp.arange(Q_BLOCK)
        qb = lax.dynamic_slice_in_dim(q, start, Q_BLOCK, axis=1)
        gb = lax.dynamic_slice_in_dim(gates, start, Q_BLOCK, axis=1)
        wkv = lax.dynamic_slice_in_dim(win_pad, start, WINDOW + Q_BLOCK, axis=1)
        wpos = start - WINDOW + jnp.arange(WINDOW + Q_BLOCK)
        return nsa_core(qb, gb, qpos, kc, vc, c_end, fetch, n_sel, wkv, wpos)

    o = lax.map(one_block, jnp.arange(T // Q_BLOCK) * Q_BLOCK)
    o = jnp.moveaxis(o, 0, 1).reshape(B, T, NSA_Q_W)
    y = o.astype(xn.dtype) @ w_out
    win_keep = min(WINDOW, T)
    return y, cmp_kv, slc_kv, win_kv[:, T - win_keep:]

def nsa_sample(xn, cmp_pool, slc_pool, win_buf, page_table, w_in, q_gain, k_gain, w_out):
    B, T, _ = xn.shape
    q, cmp_new, slc_new, win_new, gates = nsa_project(xn, w_in, q_gain, k_gain)
    past_cmp = cmp_pool[page_table].reshape(B, PAST_LEN, 2, NSA_KV_HEADS, NSA_HD)
    n_new_c = -(-T // CMP_BLOCK)
    new_cmp = jnp.pad(cmp_new, ((0, 0), (0, n_new_c * CMP_BLOCK - T), (0, 0), (0, 0), (0, 0)))
    kc_p, vc_p = compress(past_cmp, k_gain)
    kc_n, vc_n = compress(new_cmp, k_gain)
    kc = jnp.concatenate([kc_p, kc_n], axis=1)
    vc = jnp.concatenate([vc_p, vc_n], axis=1)
    c_end = (jnp.arange(PAST_LEN // CMP_BLOCK + n_new_c) + 1) * CMP_BLOCK - 1
    n_sel = -(-(PAST_LEN + T) // SEL_BLOCK)
    bi = jnp.arange(B)[:, None, None, None, None]
    ki = jnp.arange(NSA_KV_HEADS)[None, :, None, None, None]

    def fetch(idx):
        pos = idx[..., None] * SEL_BLOCK + jnp.arange(SEL_BLOCK)
        pp = jnp.minimum(pos, PAST_LEN - 1)
        phys = page_table[bi, pp // PAGE_SIZE]
        past = slc_pool[phys, pp % PAGE_SIZE, :, ki]
        new = slc_new[bi, jnp.clip(pos - PAST_LEN, 0, T - 1), :, ki]
        return jnp.where((pos < PAST_LEN)[..., None, None], past.astype(new.dtype), new)

    win_all = jnp.concatenate([win_buf.astype(win_new.dtype), win_new], axis=1)
    win_keep = win_buf.shape[1]
    wpos = PAST_LEN - win_keep + jnp.arange(win_keep + T)
    qpos = PAST_LEN + jnp.arange(T)
    o = nsa_core(q, gates, qpos, kc, vc, c_end, fetch, n_sel, win_all, wpos)
    y = o.reshape(B, T, NSA_Q_W).astype(xn.dtype) @ w_out
    return y, cmp_new, slc_new, win_all[:, T:]

def hier_moe(xn, w_grp, b_grp, w_exp, b_exp, w_gate, w_up, w_down):
    B, T, D = xn.shape
    x2 = xn.reshape(B * T, D)
    grp_prob = jax.nn.softmax((x2 @ w_grp + b_grp).astype(F32), axis=-1)
    grp_w, grp_i = lax.top_k(grp_prob, 1)
    exp_logits = (x2 @ w_exp + b_exp).astype(F32).reshape(-1, N_GROUPS, EXPERTS_PER_GROUP)
    in_grp = jnp.sum(exp_logits * jax.nn.one_hot(grp_i[:, 0], N_GROUPS, dtype=F32)[:, :, None], axis=1)
    top_l, top_i = lax.top_k(in_grp, TOP_K_IN_GROUP)
    w = jax.nn.softmax(top_l, axis=-1) * grp_w
    eid = grp_i * EXPERTS_PER_GROUP + top_i
    combine = jnp.sum(jax.nn.one_hot(eid, N_EXPERTS, dtype=F32) * w[..., None], axis=1)
    h = jax.nn.silu(jnp.einsum('nd,edf->nef', x2, w_gate)) * jnp.einsum('nd,edf->nef', x2, w_up)
    y = jnp.einsum('nef,efd->nd', h * combine.astype(h.dtype)[..., None], w_down)
    return y.reshape(B, T, D)

def setup_inputs(seed: int = 0) -> dict:
    key = jax.random.key(seed)
    ks = iter(jax.random.split(key, 40))

    def nrm(shape, scale):
        return jax.random.normal(next(ks), shape, F32) * scale

    n_pages = PAST_LEN // PAGE_SIZE
    n_pool = (DEC_BATCH * n_pages * 5) // 4
    win_keep = min(WINDOW, PAST_LEN)
    page_table = jax.random.permutation(next(ks), n_pool)[:DEC_BATCH * n_pages]
    page_table = page_table.reshape(DEC_BATCH, n_pages).astype(jnp.int32)
    a_log = jnp.log(jax.random.uniform(next(ks), (N_GDN, GDN_HEADS), F32, minval=1.0, maxval=16.0))
    dt = jnp.exp(jax.random.uniform(next(ks), (N_GDN, GDN_HEADS), F32,
                                    minval=math.log(1e-3), maxval=math.log(1e-1)))
    dt_bias = dt + jnp.log(-jnp.expm1(-dt))
    return {
        'x_prompt': nrm((BATCH, SEQ, D_MODEL), 1.0),
        'x_sample': nrm((DEC_BATCH, DEC_SEQ, D_MODEL), 1.0),
        'state_gdn_S': nrm((N_GDN, DEC_BATCH, GDN_HEADS, GDN_DK, GDN_DV), 0.1),
        'state_gdn_conv': nrm((N_GDN, DEC_BATCH, GDN_CONV - 1, GDN_CONV_W), 1.0),
        'cache_nsa_cmp_kv': nrm((N_NSA, n_pool, PAGE_SIZE, 2, NSA_KV_HEADS, NSA_HD), 1.0),
        'cache_nsa_slc_kv': nrm((N_NSA, n_pool, PAGE_SIZE, 2, NSA_KV_HEADS, NSA_HD), 1.0),
        'cache_nsa_win_kv': nrm((N_NSA, DEC_BATCH, win_keep, 2, NSA_KV_HEADS, NSA_HD), 1.0),
        'page_table': page_table,
        'ln_mix': 1.0 + nrm((DEPTH, D_MODEL), 0.02),
        'ln_ffn': 1.0 + nrm((DEPTH, D_MODEL), 0.02),
        'gdn_w_in': nrm((N_GDN, D_MODEL, GDN_IN), D_MODEL ** -0.5),
        'gdn_conv_w': nrm((N_GDN, GDN_CONV, GDN_CONV_W), GDN_CONV ** -0.5),
        'gdn_a_log': a_log,
        'gdn_dt_bias': dt_bias,
        'gdn_o_gain': 1.0 + nrm((N_GDN, GDN_DV), 0.02),
        'gdn_w_out': nrm((N_GDN, GDN_V_W, D_MODEL), GDN_V_W ** -0.5),
        'nsa_w_in': nrm((N_NSA, D_MODEL, NSA_IN), D_MODEL ** -0.5),
        'nsa_q_gain': 1.0 + nrm((N_NSA, NSA_HD), 0.02),
        'nsa_k_gain': 1.0 + nrm((N_NSA, NSA_HD), 0.02),
        'nsa_w_out': nrm((N_NSA, NSA_Q_W, D_MODEL), NSA_Q_W ** -0.5),
        'moe_w_grp': nrm((DEPTH, D_MODEL, N_GROUPS), D_MODEL ** -0.5),
        'moe_b_grp': nrm((DEPTH, N_GROUPS), 0.01),
        'moe_w_exp': nrm((DEPTH, D_MODEL, N_EXPERTS), D_MODEL ** -0.5),
        'moe_b_exp': nrm((DEPTH, N_EXPERTS), 0.01),
        'moe_w_gate': nrm((DEPTH, N_EXPERTS, D_MODEL, EXPERT_FF), D_MODEL ** -0.5),
        'moe_w_up': nrm((DEPTH, N_EXPERTS, D_MODEL, EXPERT_FF), D_MODEL ** -0.5),
        'moe_w_down': nrm((DEPTH, N_EXPERTS, EXPERT_FF, D_MODEL), EXPERT_FF ** -0.5),
    }

def reference(x_prompt, x_sample, state_gdn_S, state_gdn_conv, cache_nsa_cmp_kv, cache_nsa_slc_kv,
              cache_nsa_win_kv, page_table, ln_mix, ln_ffn, gdn_w_in, gdn_conv_w, gdn_a_log, gdn_dt_bias,
              gdn_o_gain, gdn_w_out, nsa_w_in, nsa_q_gain, nsa_k_gain, nsa_w_out, moe_w_grp, moe_b_grp,
              moe_w_exp, moe_b_exp, moe_w_gate, moe_w_up, moe_w_down):
    xp, xs = x_prompt, x_sample
    p_S, p_conv, s_S, s_conv = [], [], [], []
    p_cmp, p_slc, p_win, s_cmp, s_slc, s_win = [], [], [], [], [], []
    for layer in range(DEPTH):
        j = layer // N_MIXERS
        hp = rms_norm(xp, ln_mix[layer])
        hs = rms_norm(xs, ln_mix[layer])
        if layer % N_MIXERS == 0:
            w = (gdn_w_in[j], gdn_conv_w[j], gdn_a_log[j], gdn_dt_bias[j], gdn_o_gain[j], gdn_w_out[j])
            bp = xp.shape[0]
            conv0 = jnp.zeros((bp, GDN_CONV - 1, GDN_CONV_W), xp.dtype)
            s0 = jnp.zeros((bp, GDN_HEADS, GDN_DK, GDN_DV), F32)
            yp, Sp, cp = gdn_mixer(hp, conv0, s0, *w)
            ys, Ss, cs = gdn_mixer(hs, state_gdn_conv[j], state_gdn_S[j], *w)
            p_S.append(Sp); p_conv.append(cp); s_S.append(Ss); s_conv.append(cs)
        else:
            w = (nsa_w_in[j], nsa_q_gain[j], nsa_k_gain[j], nsa_w_out[j])
            yp, pc, psl, pw = nsa_prompt(hp, *w)
            ys, sc, ssl, sw = nsa_sample(hs, cache_nsa_cmp_kv[j], cache_nsa_slc_kv[j], cache_nsa_win_kv[j],
                                         page_table, *w)
            p_cmp.append(pc); p_slc.append(psl); p_win.append(pw)
            s_cmp.append(sc); s_slc.append(ssl); s_win.append(sw)
        xp = xp + yp
        xs = xs + ys
        mw = (moe_w_grp[layer], moe_b_grp[layer], moe_w_exp[layer], moe_b_exp[layer],
              moe_w_gate[layer], moe_w_up[layer], moe_w_down[layer])
        xp = xp + hier_moe(rms_norm(xp, ln_ffn[layer]), *mw)
        xs = xs + hier_moe(rms_norm(xs, ln_ffn[layer]), *mw)
    return (xp, xs,
            jnp.stack(p_S), jnp.stack(p_conv), jnp.stack(p_cmp), jnp.stack(p_slc), jnp.stack(p_win),
            jnp.stack(s_S), jnp.stack(s_conv), jnp.stack(s_cmp), jnp.stack(s_slc), jnp.stack(s_win))


_drawn_inputs = setup_inputs


def setup_inputs(seed=0):
    import zlib

    import numpy as np

    out = dict(_drawn_inputs(seed))
    spreads = {}
    factors = {'nsa_q_gain': 8.0, 'nsa_k_gain': 3.999}
    for name, (base, spread) in spreads.items():
        noise = np.random.default_rng([zlib.crc32(name.encode()), seed]).standard_normal(out[name].shape)
        drawn = base * np.exp(spread * noise) if base else spread * noise
        out[name] = __import__('jax').numpy.asarray(drawn.astype(out[name].dtype))
    for name, factor in factors.items():
        out[name] = (out[name] * factor).astype(out[name].dtype)
    return out
```

```python
from contextlib import ExitStack

import concourse.bass as bass
import numpy as np
from concourse import mybir

F32 = mybir.dt.float32
I32 = mybir.dt.int32
ALU = mybir.AluOpType
ACT = mybir.ActivationFunctionType
AX_X = mybir.AxisListType.X

P = 128
D_MODEL = 1024
KT = D_MODEL // P
SEQ = 512
DEC_BATCH = 8
DEC_SEQ = 4
NEW = DEC_BATCH * DEC_SEQ
TOKENS = SEQ + NEW
HALF = TOKENS // 2
TILES = SEQ // P
PAST = 4096
PAGE = 128
N_PAGES = PAST // PAGE
N_POOL = DEC_BATCH * N_PAGES * 5 // 4
HEADS = 8
CHUNK = 64
CONV = 4
CONV_TILES = 3 * HEADS
NSA_HEADS = 16
KVH = 4
GROUP = NSA_HEADS // KVH
HD = 64
CMP = 32
SEL = 64
TOP_N = 16
WINDOW = 512
GROUPS = 4
PER_GROUP = 8
EXPERTS = 32
FF = 256
EPS = 1e-6
NEG = -1e30
SEL_BIG = 1e6

ENGINES = ("pe", "dve", "act", "pool", "sp")


class Steps:

    def __init__(self, nc, ctx, name, steps, ahead=1):
        self.sem = ctx.enter_context(nc.semaphore(name))
        self.ahead = ahead
        self.steps = steps
        self.at = 0

    def credit(self, eng):
        eng.sem_inc(self.sem, len(self.steps))

    def done(self, step):
        assert self.steps[self.at] == step, (self.steps[self.at], step)
        self.at = (self.at + 1) % len(self.steps)
        return self.sem, 1

    def past(self, step, i=0):
        return (i + self.ahead) * len(self.steps) + self.steps.index(step) + 1


def constants():
    r = np.arange(P)
    chunk = r // CHUNK
    c = {}
    c["ident"] = np.eye(P)
    c["ones"] = np.ones((P, P))
    c["head_ones"] = (r[:, None] // HD == r[None, :] // HD) * 1.0
    low = (r[:, None] <= r[None, :]) & (chunk[:, None] == chunk[None, :])
    c["tri"] = low * 1.0
    c["same"] = (chunk[:, None] == chunk[None, :]) * 1.0
    c["decay_neg"] = np.where(low, 0.0, NEG)
    c["half0"] = (chunk == 0)[:, None] * np.ones((1, P))
    c["half1"] = (chunk == 1)[:, None] * np.ones((1, P))
    for k in range(6):
        b = 1 << k
        m = (r[:, None] // (2 * b) == r[None, :] // (2 * b)) & (r[:, None] % (2 * b) < b) & (r[None, :] % (2 * b) >= b)
        c[f"level{k}"] = m * 1.0
    s = np.arange(NEW)
    own = s[:, None] // DEC_SEQ == s[None, :] // DEC_SEQ
    def rows(a):
        out = np.zeros((P, a.shape[1]))
        out[: len(a)] = a
        return out
    low4 = own & (s[:, None] <= s[None, :])
    c["tri_new"] = rows(low4 * 1.0)
    c["same_new"] = rows(own * 1.0)
    c["decay_neg_new"] = rows(np.where(low4, 0.0, NEG))
    c["batch_of"] = rows((s[:, None] // DEC_SEQ == np.arange(DEC_BATCH)[None, :]) * 1.0)
    c["first_pick"] = np.tile(float(PER_GROUP) - np.arange(PER_GROUP), (P, 1))
    c["causal_neg"] = np.where(r[None, :] <= r[:, None], 0.0, NEG)
    blocks = SEQ // CMP
    q = np.arange(SEQ).reshape(TILES, P).T
    seen = ((np.arange(blocks) + 1) * CMP - 1)[None, None, :] <= q[:, :, None]
    c["q_scale"] = np.full((P, 1), HD ** -0.5)
    c["cmp_seen"] = (seen * 1.0).reshape(P, TILES * blocks)
    c["cmp_neg"] = np.where(seen, 0.0, NEG).reshape(P, TILES * blocks)
    row = np.arange(KVH * GROUP * DEC_SEQ)
    t = row % DEC_SEQ
    kvh = row // (GROUP * DEC_SEQ)
    c["group_sum"] = rows(((kvh[:, None] == kvh[None, :]) & (t[:, None] == t[None, :])) * 1.0)
    key_t, key_b = np.arange(NEW) % DEC_SEQ, np.arange(NEW) // DEC_SEQ
    seen = (key_b[None, None, :] == np.arange(DEC_BATCH)[None, :, None]) & (key_t[None, None, :] <= t[:, None, None])
    c["new_neg"] = rows(np.where(seen, 0.0, NEG).reshape(len(row), -1))
    w = np.arange(WINDOW)
    c["win_neg"] = rows(np.where(w[None, :] > t[:, None], 0.0, NEG))
    n_sel = PAST // SEL + 1
    blk = np.arange(n_sel - 1)
    forced = (blk == 0) | (blk == n_sel - 2)
    c["forced"] = rows(np.tile(forced * SEL_BIG, (len(row), 1)))
    return {k: np.ascontiguousarray(v, dtype=np.float32) for k, v in c.items()}


CONSTANTS = constants()
CONST_AT = {}
_n = 0
for _k, _v in CONSTANTS.items():
    CONST_AT[_k] = (_n, _v.shape[1])
    _n += _v.shape[1]
CONST_W = _n


def halves(ap):
    return ap.rearrange("p (a b) -> p a b", a=2)


class Stage:

    def __init__(self, nc, name):
        self.nc, self.name, self.ctx = nc, name, ExitStack()

    def __enter__(self):
        return self

    def __exit__(self, *_):
        self.ctx.close()

    def sb(self, name, shape, dt=F32):
        return self.ctx.enter_context(self.nc.sbuf_tensor(f"{self.name}_{name}", shape, dt))

    def ps(self, name, shape=(P, 512)):
        return self.ctx.enter_context(self.nc.psum_tensor(f"{self.name}_{name}", list(shape), F32))

    def steps(self, name, steps):
        return Steps(self.nc, self.ctx, f"{self.name}_{name}", steps)

    def line(self, name, steps):
        return Steps(self.nc, self.ctx, f"{self.name}_{name}", steps, ahead=0)

    def sem(self, name):
        return self.ctx.enter_context(self.nc.semaphore(f"{self.name}_{name}"))

    def block(self):
        return self.nc.Block(no_gpsimd_drain=True)


def load_inputs(nc, g):
    with Stage(nc, "load") as st:
        loaded = st.sem("loaded")
        copied = st.sem("copied")
        with st.block() as block:
            @block.sync
            def _(sp):
                sp.dma_start(g.d["win_out"].rearrange("b p a n -> (b p) (a n)"),
                             g.d["win"].rearrange("b p a n -> (b p) (a n)")).then_inc(copied, 16)
                sp.dma_start(g.consts[:, :], g.d["consts"]).then_inc(loaded, 16)
                sp.dma_start(g.gains[:, :], g.d["gains"]).then_inc(loaded, 16)
                sp.dma_start(g.xT[:, :, :], g.d["x"]).then_inc(loaded, 16)
                sp.wait_ge(loaded, 48)
                sp.wait_ge(copied, 16)


def rms_norm_stage(nc, g, name, gain0):
    with Stage(nc, name) as st:
        sq = st.sb("sq", [P, KT, TOKENS])
        rms = st.sb("rms", [P, TOKENS])
        total = st.ps("total", (P, 2, 512))
        squares = st.sem("squares")
        summed = st.sem("summed")
        rooted = st.sem("rooted")
        inverted = st.sem("inverted")
        ones = g.const("ones")
        with st.block() as block:
            @block.scalar
            def _(act):
                for k in range(KT):
                    act.activation(sq[:, k, :], g.xT[:, k, :], ACT.Square).then_inc(squares, 1)
                act.wait_ge(summed, 1)
                act.activation(halves(rms[:, :]), total[:, :, 0:HALF], ACT.Sqrt, bias=g.eps[:, 0:1],
                               scale=1.0 / D_MODEL).then_inc(rooted, 1)

            @block.tensor
            def _(pe):
                for k in range(KT):
                    pe.wait_ge(squares, k + 1)
                    for a in range(2):
                        mm = pe.matmul(total[:, a, 0:HALF], ones, sq[:, k, a * HALF:(a + 1) * HALF],
                                       start=(k == 0), stop=(k == KT - 1))
                mm.then_inc(summed, 1)

            @block.vector
            def _(dve):
                dve.wait_ge(rooted, 1)
                dve.reciprocal(rms[:, :], rms[:, :]).then_inc(inverted, 1)
                dve.wait_ge(inverted, 1)
                for k in range(KT):
                    dve.scalar_tensor_tensor(out=g.hT[:, k, :], in0=g.xT[:, k, :],
                                             scalar=g.gains[:, gain0 + k:gain0 + k + 1], in1=rms[:, :],
                                             op0=ALU.mult, op1=ALU.mult)


def gdn_project_stage(nc, g):
    with Stage(nc, "proj") as st:
        w = [st.sb(f"w{s}", [P, KT, P]) for s in range(2)]
        xc = [st.sb(f"xc{s}", [P, CONV - 1 + SEQ]) for s in range(2)]
        xs = [st.sb(f"xs{s}", [P, DEC_BATCH, CONV - 1 + DEC_SEQ]) for s in range(2)]
        conv = [st.sb(f"conv{s}", [P, TOKENS]) for s in range(2)]
        taps = st.sb("taps", [P, CONV_TILES, CONV])
        prev = st.sb("prev", [P, CONV_TILES, DEC_BATCH, CONV - 1])
        tails = st.sb("tails", [P, CONV_TILES, (1 + DEC_BATCH) * (CONV - 1)])
        acc = [st.ps(f"acc{s}", (P, 2, 512)) for s in range(2)]
        loaded = [st.sem(f"loaded{s}") for s in range(2)]
        small = st.sem("small")
        stored = st.sem("stored")
        pe_s = [st.steps(f"pe{s}", ["product"]) for s in range(2)]
        act_s = [st.steps(f"act{s}", ["prompt out", "sample out", "silu"]) for s in range(2)]
        dve_s = [st.steps(f"dve{s}", [f"{part} tap {i}" for i in range(CONV) for part in ("prompt", "sample")])
                 for s in range(2)]
        pool_s = [st.steps(f"pool{s}", ["history", "prompt tail", "sample tail"]) for s in range(2)]
        cleared = st.sem("cleared")
        z_out = st.sem("z_out")
        rounds = CONV_TILES // 2
        z_rounds = HEADS // 2
        with st.block() as block:
            @block.sync
            def _(sp):
                sp.dma_start(taps[:, :, :], g.d["taps"]).then_inc(small, 16)
                sp.dma_start(prev[:, :, :, :], g.d["conv_prev"]).then_inc(small, 16)
                for s in range(2):
                    sp.dma_start(w[s][:, :, :], g.d["gdn_w"][s]).then_inc(loaded[s], 16)
                with sp.Fori(0, rounds + z_rounds - 1) as i:
                    for s in range(2):
                        sp.wait_ge(pe_s[s].sem, pe_s[s].past("product", i))
                        sp.dma_start(w[s][:, :, :],
                                     g.d["gdn_w"][bass.ds(2 * i + 2 + s, 1)].rearrange("t p k c -> (t p) k c")
                                     ).then_inc(loaded[s], 16)
                for s in range(2):
                    sp.wait_ge(pool_s[s].sem, pool_s[s].past("sample tail", rounds - 1))
                sp.dma_start(g.d["conv_out"], tails[:, :, :]).then_inc(stored, 16)
                sp.wait_ge(stored, 16)

            @block.tensor
            def _(pe):
                for s in range(2):
                    pe_s[s].credit(pe)

                def product(s, i):
                    pe.wait_ge(loaded[s], 16 * (i + 1))
                    for k in range(KT):
                        for a in range(2):
                            mm = pe.matmul(acc[s][:, a, 0:HALF], w[s][:, k, :], g.hT[:, k, a * HALF:(a + 1) * HALF],
                                           start=(k == 0), stop=(k == KT - 1))
                    mm.then_inc(*pe_s[s].done("product"))

                with pe.Fori(0, rounds) as i:
                    for s in range(2):
                        pe.wait_ge(act_s[s].sem, act_s[s].past("sample out", i - 1))
                        product(s, i)
                for i in range(z_rounds):
                    for s in range(2):
                        if i == 0:
                            pe.wait_ge(act_s[s].sem, act_s[s].past("sample out", rounds - 1))
                        else:
                            pe.wait_ge(z_out, 2 * (i - 1) + s + 1)
                        product(s, rounds + i)

            @block.scalar
            def _(act):
                for s in range(2):
                    act_s[s].credit(act)
                act.wait_ge(cleared, 2)
                with act.Fori(0, rounds) as i:
                    for s in range(2):
                        act.wait_ge(pe_s[s].sem, pe_s[s].past("product", i))
                        act.wait_ge(dve_s[s].sem, dve_s[s].past(f"sample tap {CONV - 1}", i - 1))
                        act.wait_ge(pool_s[s].sem, pool_s[s].past("sample tail", i - 1))
                        act.activation(xc[s][:, CONV - 1:CONV - 1 + HALF], acc[s][:, 0, 0:HALF],
                                       ACT.Copy).then_inc(*act_s[s].done("prompt out"))
                        act.activation(xc[s][:, CONV - 1 + HALF:], acc[s][:, 1, 0:SEQ - HALF], ACT.Copy)
                        act.activation(xs[s][:, :, CONV - 1:],
                                       acc[s][:, 1, SEQ - HALF:HALF].rearrange("p (b t) -> p b t", t=DEC_SEQ),
                                       ACT.Copy).then_inc(*act_s[s].done("sample out"))
                    for s in range(2):
                        act.wait_ge(dve_s[s].sem, dve_s[s].past(f"sample tap {CONV - 1}", i))
                        act.activation(g.qkv[:, bass.ds(2 * i + s, 1), :].rearrange("p a t -> p (a t)"),
                                       conv[s][:, :], ACT.Silu).then_inc(*act_s[s].done("silu"))
                for i in range(z_rounds):
                    for s in range(2):
                        act.wait_ge(pe_s[s].sem, pe_s[s].past("product", rounds + i))
                        act.activation(halves(g.zT[:, 2 * i + s, :]), acc[s][:, :, 0:HALF],
                                       ACT.Silu).then_inc(z_out, 1)

            @block.vector
            def _(dve):
                for s in range(2):
                    dve_s[s].credit(dve)
                    dve.memset(xc[s][:, 0:CONV - 1], 0.0).then_inc(cleared, 1)
                dve.wait_ge(cleared, 2)
                dve.wait_ge(small, 32)
                with dve.Fori(0, rounds) as i:
                    for s in range(2):
                        dve.wait_ge(act_s[s].sem, act_s[s].past("sample out", i))
                        dve.wait_ge(act_s[s].sem, act_s[s].past("silu", i - 1))
                        dve.wait_ge(pool_s[s].sem, pool_s[s].past("history", i))
                        prompt = conv[s][:, 0:SEQ]
                        sample = conv[s][:, SEQ:TOKENS].rearrange("p (b t) -> p b t", t=DEC_SEQ)
                        for tap in range(CONV):
                            weight = taps[:, bass.ds(2 * i + s, 1), tap:tap + 1].rearrange("p a t -> p (a t)")
                            rows, new = xc[s][:, tap:tap + SEQ], xs[s][:, :, tap:tap + DEC_SEQ]
                            if tap == 0:
                                dve.tensor_scalar(prompt, rows, weight, None, ALU.mult
                                                  ).then_inc(*dve_s[s].done("prompt tap 0"))
                                dve.tensor_scalar(sample, new, weight, None, ALU.mult
                                                  ).then_inc(*dve_s[s].done("sample tap 0"))
                                continue
                            dve.wait_ge(dve_s[s].sem, dve_s[s].past(f"prompt tap {tap - 1}", i))
                            dve.scalar_tensor_tensor(out=prompt, in0=rows, scalar=weight, in1=prompt, op0=ALU.mult,
                                                     op1=ALU.add).then_inc(*dve_s[s].done(f"prompt tap {tap}"))
                            dve.wait_ge(dve_s[s].sem, dve_s[s].past(f"sample tap {tap - 1}", i))
                            dve.scalar_tensor_tensor(out=sample, in0=new, scalar=weight, in1=sample, op0=ALU.mult,
                                                     op1=ALU.add).then_inc(*dve_s[s].done(f"sample tap {tap}"))

            @block.gpsimd
            def _(pool):
                for s in range(2):
                    pool_s[s].credit(pool)
                pool.wait_ge(small, 32)
                n = CONV - 1
                with pool.Fori(0, rounds) as i:
                    for s in range(2):
                        tile = bass.ds(2 * i + s, 1)
                        pool.wait_ge(dve_s[s].sem, dve_s[s].past(f"sample tap {CONV - 1}", i - 1))
                        pool.tensor_copy(xs[s][:, :, 0:n], prev[:, tile, :, :].rearrange("p a b t -> p (a b) t")
                                         ).then_inc(*pool_s[s].done("history"))
                        pool.wait_ge(act_s[s].sem, act_s[s].past("sample out", i))
                        pool.tensor_copy(tails[:, tile, 0:n].rearrange("p a t -> p (a t)"), xc[s][:, SEQ:SEQ + n]
                                         ).then_inc(*pool_s[s].done("prompt tail"))
                        pool.tensor_copy(
                            tails[:, tile, n:].rearrange("p a (b t) -> p (a b) t", t=n),
                            xs[s][:, :, DEC_SEQ:DEC_SEQ + n]).then_inc(*pool_s[s].done("sample tail"))


def gdn_gates_stage(nc, g):
    NT = TILES + 1
    with Stage(nc, "gates") as st:
        w = st.sb("w", [P, KT, 2 * HEADS])
        rows = st.sb("rows", [P, 2, HEADS])
        ab = st.sb("ab", [P, NT, 2 * HEADS])
        mag = st.sb("mag", [P, NT, HEADS])
        pos = st.sb("pos", [P, NT, HEADS])
        decay = st.sb("decay", [P, HEADS])
        diff = st.sb("diff", [P, NT, HEADS])
        by_batch = st.sb("by_batch", [NEW, DEC_BATCH, HEADS])
        proj, cum, whole, chunks = st.ps("proj"), st.ps("cum"), st.ps("whole"), st.ps("chunks")
        loaded = st.sem("loaded")
        pe_s = st.line("pe", ["ab", "chunk sums", "batch sums"])
        dve_s = st.line("dve", ["clear", "copy", "copy new", "bias", "magnitude", "positive", "softplus", "g",
                                "by batch", "G", "G new", "diff", "diff new"])
        act_s = st.line("act", ["rate", "exp", "log", "beta", "eG", "tail"])
        a = ab[:, :, 0:HEADS]
        rows_of = [P] * TILES + [NEW]

        def tiles(t, n):
            return t[:, 0:NT * n].rearrange("p (t n) -> p t n", n=n)

        with st.block() as block:
            @block.sync
            def _(sp):
                sp.dma_start(w[:, :, :], g.d["gdn_w_ab"]).then_inc(loaded, 16)
                sp.dma_start(rows[:, :, :], g.d["gdn_rows"]).then_inc(loaded, 16)

            @block.tensor
            def _(pe):
                pe.wait_ge(loaded, 32)
                for t, n in enumerate(rows_of):
                    for k in range(KT):
                        mm = pe.matmul(tiles(proj, 2 * HEADS)[0:n, t, :], g.hT[:, k, t * P:t * P + n], w[:, k, :],
                                       start=(k == 0), stop=(k == KT - 1))
                mm.then_inc(*pe_s.done("ab"))
                pe.wait_ge(dve_s.sem, dve_s.past("g"))
                for t, n in enumerate(rows_of):
                    tri, same = ("tri", "same") if n == P else ("tri_new", "same_new")
                    pe.matmul(tiles(cum, HEADS)[0:n, t, :], g.const(tri, n)[:, 0:n], g.gate_g[0:n, t, :],
                              start=True, stop=True)
                    pe.matmul(tiles(whole, HEADS)[0:n, t, :], g.const(same, n)[:, 0:n], g.gate_g[0:n, t, :],
                              start=True, stop=True)
                for t in range(TILES):
                    for half in range(2):
                        at = (2 * t + half) * HEADS
                        mm = pe.matmul(chunks[:, at:at + HEADS], g.const(f"half{half}"), g.gate_g[:, t, :],
                                       start=True, stop=True)
                mm.then_inc(*pe_s.done("chunk sums"))
                pe.wait_ge(dve_s.sem, dve_s.past("by batch"))
                pe.matmul(chunks[:, 128:128 + DEC_BATCH * HEADS], g.const("ones", NEW),
                          by_batch[:, :, :].rearrange("s b h -> s (b h)"), start=True, stop=True
                          ).then_inc(*pe_s.done("batch sums"))

            @block.scalar
            def _(act):
                act.wait_ge(loaded, 32)
                act.activation(decay[:, :], rows[:, 0, :], ACT.Exp).then_inc(*act_s.done("rate"))
                act.wait_ge(dve_s.sem, dve_s.past("magnitude"))
                act.activation(mag[:, :, :], mag[:, :, :], ACT.Exp, scale=-1.0).then_inc(*act_s.done("exp"))
                act.wait_ge(act_s.sem, act_s.past("exp"))
                act.activation(mag[:, :, :], mag[:, :, :], ACT.Ln, bias=1.0).then_inc(*act_s.done("log"))
                act.activation(g.beta[:, :, :], ab[:, :, HEADS:], ACT.Sigmoid).then_inc(*act_s.done("beta"))
                act.wait_ge(dve_s.sem, dve_s.past("G new"))
                act.activation(g.eG[:, :, :], g.G[:, :, :], ACT.Exp).then_inc(*act_s.done("eG"))
                act.wait_ge(dve_s.sem, dve_s.past("diff new"))
                act.activation(g.tail[:, :, :], diff[:, :, :], ACT.Exp).then_inc(*act_s.done("tail"))
                act.wait_ge(pe_s.sem, pe_s.past("batch sums"))
                act.activation(g.e_chunk[:, :, :].rearrange("p c h -> p (c h)"), chunks[:, 0:2 * TILES * HEADS],
                               ACT.Exp)
                act.activation(g.e_batch[:, :, :].rearrange("p b h -> p (b h)"),
                               chunks[:, 128:128 + DEC_BATCH * HEADS], ACT.Exp)

            @block.vector
            def _(dve):
                dve.memset(ab[:, :, :], 0.0)
                dve.memset(g.G[:, TILES, :], 0.0)
                dve.memset(diff[:, TILES, :], 0.0).then_inc(*dve_s.done("clear"))
                dve.wait_ge(dve_s.sem, dve_s.past("clear"))
                dve.wait_ge(pe_s.sem, pe_s.past("ab"))
                dve.tensor_copy(ab[:, 0:TILES, :], tiles(proj, 2 * HEADS)[:, 0:TILES, :]
                                ).then_inc(*dve_s.done("copy"))
                dve.tensor_copy(ab[0:NEW, TILES, :], tiles(proj, 2 * HEADS)[0:NEW, TILES, :]
                                ).then_inc(*dve_s.done("copy new"))
                dve.wait_ge(dve_s.sem, dve_s.past("copy new"))
                dve.wait_ge(loaded, 32)
                dve.tensor_tensor(a, a, rows[:, 1:2, :].broadcast_to([P, NT, HEADS]), ALU.add
                                  ).then_inc(*dve_s.done("bias"))
                dve.wait_ge(dve_s.sem, dve_s.past("bias"))
                dve.scalar_tensor_tensor(out=mag[:, :, :], in0=a, scalar=-1.0, in1=a, op0=ALU.mult, op1=ALU.max).then_inc(*dve_s.done("magnitude"))
                dve.tensor_scalar(pos[:, :, :], a, 0.0, None, ALU.max).then_inc(*dve_s.done("positive"))
                dve.wait_ge(act_s.sem, act_s.past("log"))
                dve.wait_ge(dve_s.sem, dve_s.past("positive"))
                dve.tensor_tensor(pos[:, :, :], pos[:, :, :], mag[:, :, :], ALU.add
                                  ).then_inc(*dve_s.done("softplus"))
                dve.wait_ge(dve_s.sem, dve_s.past("softplus"))
                dve.scalar_tensor_tensor(out=g.gate_g[:, :, :], in0=pos[:, :, :], scalar=-1.0,
                                         in1=decay[:, :].unsqueeze(1).broadcast_to([P, NT, HEADS]),
                                         op0=ALU.mult, op1=ALU.mult).then_inc(*dve_s.done("g"))
                dve.wait_ge(dve_s.sem, dve_s.past("g"))
                dve.tensor_tensor(by_batch[:, :, :],
                                  g.gate_g[0:NEW, TILES, :].unsqueeze(1).broadcast_to([NEW, DEC_BATCH, HEADS]),
                                  g.const("batch_of", NEW).unsqueeze(2).broadcast_to([NEW, DEC_BATCH, HEADS]),
                                  ALU.mult).then_inc(*dve_s.done("by batch"))
                dve.wait_ge(pe_s.sem, pe_s.past("chunk sums"))
                new = slice(0, NEW)
                dve.tensor_copy(g.G[:, 0:TILES, :], tiles(cum, HEADS)[:, 0:TILES, :]).then_inc(*dve_s.done("G"))
                dve.tensor_copy(g.G[new, TILES, :], tiles(cum, HEADS)[new, TILES, :]).then_inc(*dve_s.done("G new"))
                dve.wait_ge(dve_s.sem, dve_s.past("G new"))
                dve.tensor_tensor(diff[:, 0:TILES, :], tiles(whole, HEADS)[:, 0:TILES, :], g.G[:, 0:TILES, :],
                                  ALU.subtract).then_inc(*dve_s.done("diff"))
                dve.tensor_tensor(diff[new, TILES, :], tiles(whole, HEADS)[new, TILES, :], g.G[new, TILES, :],
                                  ALU.subtract).then_inc(*dve_s.done("diff new"))


LEVELS = 6
DOUBLINGS = range(1, LEVELS)
CHUNKS = SEQ // CHUNK
LANE_PE = (["squares", "k rows", "v rows", "kk", "qk", "G wide", "beta wide", "T 0"]
           + [x for n in DOUBLINGS for x in (f"W {n}", f"TT {n}")]
           + ["u", "w", "new u w"]
           + [x for j in range(CHUNKS) for x in (f"wS {j}", f"KV {j}", f"o {j}")]
           + ["new wS qS", "new v rows", "new o", "new KV", "o squares"])
LANE_DVE = (["gates", "k beta decay staged", "k", "q", "k beta decay", "difference", "qk", "kk", "L", "TT 0"]
            + [f"T {n}" for n in DOUBLINGS]
            + [x for j in range(CHUNKS) for x in (f"v {j}", f"S {j}")]
            + ["new v", "new v by batch", "new S decayed", "new S", "new o", "o normed", "o gated"])
LANE_ACT = (["squares", "v", "log norms", "norms", "k tail", "v beta", "eG wide", "decay", "T 0"]
            + [f"W {n}" for n in DOUBLINGS]
            + ["u", "w", "new wS qS", "new v rows", "o", "o square", "o log", "o norm"])
LANE_POOL = ["clear S", "q decayed"] + [f"level {n}" for n in range(LEVELS)]


def gdn_heads_stage(nc, g):
    with Stage(nc, "heads") as st:
        class Lane:
            pass
        lanes = []
        N = slice(0, NEW)
        for s in range(2):
            ln = Lane()
            lanes.append(ln)
            ln.s = s
            ln.sq = st.sb(f"sq{s}", [P, 2, TOKENS])
            ln.norm = st.sb(f"norm{s}", [P, 2, TOKENS])
            ln.kT = st.sb(f"kT{s}", [P, TOKENS])
            ln.qT = st.sb(f"qT{s}", [P, TOKENS])
            ln.kbe = st.sb(f"kbe{s}", [P, TILES + 1, P])
            ln.kt = st.sb(f"kt{s}", [P, TILES + 1, P])
            ln.vb = st.sb(f"vb{s}", [P, TILES + 1, P])
            ln.dec = st.sb(f"dec{s}", [P, TOKENS])
            ln.LT = st.sb(f"LT{s}", [P, TOKENS])
            ln.QK = st.sb(f"QK{s}", [P, TOKENS])
            ln.B = st.sb(f"B{s}", [P, 2, TOKENS])
            ln.T = st.sb(f"T{s}", [P, TOKENS])
            ln.TT = st.sb(f"TT{s}", [P, TOKENS])
            ln.W = st.sb(f"W{s}", [P, TOKENS])
            ln.u = st.sb(f"u{s}", [P, TILES, P])
            ln.wq = st.sb(f"wq{s}", [P, 2, TOKENS])
            ln.S = st.sb(f"S{s}", [P, P])
            ln.vn = st.sb(f"vn{s}", [P, P])
            ln.o = st.sb(f"o{s}", [P, TOKENS])
            ln.S_new = st.sb(f"S_new{s}", [P, DEC_BATCH, P])
            ln.wSqS = st.sb(f"wSqS{s}", [P, DEC_BATCH, 2, DEC_SEQ])
            ln.vT = st.sb(f"vT{s}", [P, NEW])
            ln.v_rows = st.sb(f"v_rows{s}", [NEW, P])
            ln.gates = st.sb(f"gates{s}", [P, 5, TILES + 1])
            ln.v_batch = ln.B[N, :, :].rearrange("s a t -> s (a t)")[:, 0:DEC_BATCH * P].rearrange(
                "s (b v) -> s b v", b=DEC_BATCH)
            ln.bank = [st.ps(f"bank{s}{n}") for n in range(4)]
            ln.pe = st.steps(f"pe{s}", LANE_PE)
            ln.dve = st.steps(f"dve{s}", LANE_DVE)
            ln.act = st.steps(f"act{s}", LANE_ACT)
            ln.pool = st.steps(f"pool{s}", LANE_POOL)
            ln.sp = st.steps(f"sp{s}", ["states stored"])
            ln.loaded = st.sem(f"loaded{s}")
            ln.stored = st.sem(f"stored{s}")
        rounds = HEADS // 2
        NT = slice(SEQ, TOKENS)
        G_, BETA, CUM, BETA_DECAY, TAIL = range(5)

        def tile(t):
            return slice(t * P, (t + 1) * P)

        def tiled(ap):
            return ap.rearrange("p (t c) -> p t c", c=P)

        def wide(mask):
            return g.const(mask).unsqueeze(1).broadcast_to([P, TILES, P])

        def new_const(name):
            return g.const(name, NEW)[:, 0:NEW]

        def head_of(t, ln, i):
            return t[:, bass.ds(2 * i + ln.s, 1), :].rearrange("p a t -> p (a t)")

        def alternate(rule, i):
            for _ in zip(*(rule(ln, i) for ln in lanes)):
                pass

        with st.block() as block:
            @block.sync
            def _(sp):
                for ln in lanes:
                    ln.sp.credit(sp)
                with sp.Fori(0, rounds) as i:
                    for ln in lanes:
                        h = bass.ds(2 * i + ln.s, 1)
                        sp.dma_start(ln.S_new[:, :, :], g.d["gdn_S"][h].rearrange("h k b v -> (h k) b v")
                                     ).then_inc(ln.loaded, 16)
                    for ln in lanes:
                        h = bass.ds(2 * i + ln.s, 1)
                        sp.wait_ge(ln.dve.sem, ln.dve.past(f"S {CHUNKS - 1}", i))
                        sp.dma_start(g.d["p_S"][h].rearrange("h k v -> (h k) v"), ln.S[:, :]).then_inc(ln.stored, 16)
                    for ln in lanes:
                        h = bass.ds(2 * i + ln.s, 1)
                        sp.wait_ge(ln.dve.sem, ln.dve.past("new S", i))
                        sp.dma_start(g.d["s_S"][h].rearrange("h k b v -> (h k) b v"), ln.S_new[:, :, :]
                                     ).then_inc(ln.stored, 16)
                    for ln in lanes:
                        sp.wait_ge(ln.stored, 32 * (i + 1))
                        sp.sem_inc(*ln.sp.done("states stored"))

            @block.tensor
            def _(pe):
                def rule(ln, i):
                    b0, b1, b2, b3 = ln.bank

                    def each(out, lhsT, rhs):
                        for t in range(TILES):
                            mm = pe.matmul(out[:, tile(t)], lhsT(t), rhs(t), start=True, stop=True)
                        return mm

                    def new(out, lhsT, rhs):
                        return pe.matmul(out, lhsT, rhs, start=True, stop=True)
                    ones, ident = g.const("ones"), g.const("ident")
                    pe.wait_ge(ln.act.sem, ln.act.past("squares", i))
                    pe.wait_ge(ln.dve.sem, ln.dve.past("new S", i - 1))
                    pe.wait_ge(ln.act.sem, ln.act.past("o norm", i - 1))
                    new(b0[:, :], ones, ln.sq[:, 0, 0:SEQ])
                    new(b1[:, :], ones, ln.sq[:, 1, 0:SEQ])
                    new(b2[:, 0:NEW], ones, ln.sq[:, 0, NT])
                    new(b2[:, NEW:2 * NEW], ones, ln.sq[:, 1, NT]).then_inc(*ln.pe.done("squares"))
                    yield
                    pe.wait_ge(ln.dve.sem, ln.dve.past("k", i))
                    for t in range(TILES):
                        pe.transpose(b3[:, tile(t)], ln.kT[:, tile(t)], ident)
                    pe.transpose(b2[N, 192:320], ln.QK[:, NT], ident)
                    pe.transpose(b2[N, 64:192], ln.kT[:, NT], ident).then_inc(*ln.pe.done("k rows"))
                    yield
                    for t in range(TILES):
                        mm = pe.transpose(b0[:, tile(t)], ln.QK[:, tile(t)], ident)
                    mm.then_inc(*ln.pe.done("v rows"))
                    yield
                    each(b1, lambda t: ln.kT[:, tile(t)], lambda t: ln.kT[:, tile(t)]
                         ).then_inc(*ln.pe.done("kk"))
                    yield
                    pe.wait_ge(ln.act.sem, ln.act.past("k tail", i))
                    each(b3, lambda t: ln.kT[:, tile(t)], lambda t: ln.qT[:, tile(t)]
                         ).then_inc(*ln.pe.done("qk"))
                    yield
                    pe.wait_ge(ln.act.sem, ln.act.past("v beta", i))
                    each(b0, lambda t: ln.gates[:, G_, t:t + 1].broadcast_to([P, P]), lambda t: g.const("tri"))
                    new(b2[N, 320:352], ln.kT[:, NT], ln.kT[:, NT])
                    new(b2[N, 352:384], ln.kT[:, NT], ln.qT[:, NT])
                    new(b2[:, 384:416], ln.gates[N, G_, TILES:TILES + 1].broadcast_to([NEW, P]),
                        new_const("tri_new")).then_inc(*ln.pe.done("G wide"))
                    yield
                    pe.wait_ge(ln.act.sem, ln.act.past("eG wide", i))
                    each(b0, lambda t: ln.gates[:, BETA, t:t + 1].broadcast_to([P, P]), lambda t: ident)
                    new(b2[N, 416:448], ln.gates[N, BETA, TILES:TILES + 1].broadcast_to([NEW, NEW]),
                        new_const("ident")).then_inc(*ln.pe.done("beta wide"))
                    yield
                    pe.wait_ge(ln.dve.sem, ln.dve.past("TT 0", i))
                    for t in range(TILES):
                        pe.transpose(b1[:, tile(t)], ln.TT[:, tile(t)], ident)
                    pe.transpose(b2[N, 0:32], ln.TT[N, NT], new_const("ident")).then_inc(*ln.pe.done("T 0"))
                    yield
                    for n in DOUBLINGS:
                        pe.wait_ge(ln.pool.sem, ln.pool.past(f"level {n}", i))
                        if n == 1:
                            pe.wait_ge(ln.act.sem, ln.act.past("T 0", i))
                        else:
                            pe.wait_ge(ln.dve.sem, ln.dve.past(f"T {n - 1}", i))
                        mm = each(b1, lambda t: ln.B[:, n % 2, tile(t)], lambda t: ln.T[:, tile(t)])
                        if n == 1:
                            mm = new(b2[N, 32:64], ln.B[N, 1, NT], ln.T[N, NT])
                        mm.then_inc(*ln.pe.done(f"W {n}"))
                        yield
                        pe.wait_ge(ln.act.sem, ln.act.past(f"W {n}", i))
                        if n < LEVELS - 1:
                            each(b3, lambda t: ln.TT[:, tile(t)], lambda t: ln.W[:, tile(t)])
                        mm = each(b0, lambda t: ln.W[:, tile(t)], lambda t: ln.TT[:, tile(t)])
                        if n == 1:
                            mm = new(b2[N, 64:96], ln.W[N, NT], ln.TT[N, NT])
                        mm.then_inc(*ln.pe.done(f"TT {n}"))
                        yield
                    pe.wait_ge(ln.dve.sem, ln.dve.past(f"T {LEVELS - 1}", i))
                    each(b1, lambda t: ln.TT[:, tile(t)], lambda t: ln.vb[:, t, :]).then_inc(*ln.pe.done("u"))
                    each(b3, lambda t: ln.kbe[:, t, :], lambda t: ln.TT[:, tile(t)]).then_inc(*ln.pe.done("w"))
                    new(b2[:, 96:128], ln.vb[N, TILES, :], ln.TT[N, NT])
                    new(b2[:, 128:160], ln.kbe[N, TILES, :], ln.TT[N, NT]).then_inc(*ln.pe.done("new u w"))
                    yield
                    pe.wait_ge(ln.pool.sem, ln.pool.past("q decayed", i))
                    pe.wait_ge(ln.act.sem, ln.act.past("w", i))
                    for j in range(CHUNKS):
                        t, R, C = j // 2, slice(CHUNK * (j % 2), CHUNK * (j % 2 + 1)), slice(j * CHUNK, (j + 1) * CHUNK)
                        if j:
                            pe.wait_ge(ln.dve.sem, ln.dve.past(f"S {j - 1}", i))
                        new(b1[R, 0:P], ln.wq[:, 0, C], ln.S[:, :]).then_inc(*ln.pe.done(f"wS {j}"))
                        pe.matmul(b0[:, C], ln.S[:, :], ln.wq[:, 1, C], start=True, stop=False)
                        yield
                        pe.wait_ge(ln.dve.sem, ln.dve.past(f"v {j}", i))
                        new(b3[:, 0:P], ln.kt[R, t, :], ln.vn[R, :]).then_inc(*ln.pe.done(f"KV {j}"))
                        pe.matmul(b0[:, C], ln.vn[R, :], ln.QK[R, C], start=False, stop=True
                                  ).then_inc(*ln.pe.done(f"o {j}"))
                        yield
                    pe.wait_ge(ln.loaded, 16 * (i + 1))
                    for b in range(DEC_BATCH):
                        at = 160 + 2 * DEC_SEQ * b
                        mm = new(b2[:, at:at + 2 * DEC_SEQ].rearrange("p (w t) -> p w t", w=2), ln.S_new[:, b, :],
                                 ln.wq[:, :, SEQ + DEC_SEQ * b:SEQ + DEC_SEQ * (b + 1)])
                    mm.then_inc(*ln.pe.done("new wS qS"))
                    yield
                    pe.wait_ge(ln.dve.sem, ln.dve.past("new v", i))
                    pe.transpose(b2[N, 224:352], ln.vT[:, :], ident).then_inc(*ln.pe.done("new v rows"))
                    yield
                    pe.wait_ge(ln.act.sem, ln.act.past("new v rows", i))
                    new(b2[:, 352:384], ln.v_rows[:, :], ln.QK[N, NT]).then_inc(*ln.pe.done("new o"))
                    pe.wait_ge(ln.dve.sem, ln.dve.past("new v by batch", i))
                    for a, bank in enumerate((b1, b3)):
                        mm = new(bank[:, :], ln.kt[N, TILES, :],
                                 ln.v_batch[:, 4 * a:4 * a + 4, :].rearrange("s b v -> s (b v)"))
                    mm.then_inc(*ln.pe.done("new KV"))
                    yield
                    pe.wait_ge(ln.act.sem, ln.act.past("o square", i))
                    new(b0[:, :], ones, ln.sq[:, 1, 0:SEQ])
                    new(b2[:, 384:416], ones, ln.sq[:, 1, NT]).then_inc(*ln.pe.done("o squares"))
                    yield

                for ln in lanes:
                    ln.pe.credit(pe)
                with pe.Fori(0, rounds) as i:
                    alternate(rule, i)

            @block.scalar
            def _(act):
                def rule(ln, i):
                    b0, b1, b2, b3 = ln.bank
                    q, k, v = (g.qkv[:, bass.ds(2 * i + ln.s + HEADS * n, 1), :].rearrange("p a t -> p (a t)")
                               for n in range(3))
                    act.wait_ge(ln.pe.sem, ln.pe.past("o squares", i - 1))
                    act.wait_ge(ln.pool.sem, ln.pool.past("q decayed", i - 1))
                    act.activation(ln.sq[:, 0, :], q, ACT.Square)
                    act.activation(ln.sq[:, 1, :], k, ACT.Square).then_inc(*ln.act.done("squares"))
                    act.activation(ln.QK[:, :], v, ACT.Copy).then_inc(*ln.act.done("v"))
                    yield
                    act.wait_ge(ln.pe.sem, ln.pe.past("squares", i))
                    act.wait_ge(ln.dve.sem, ln.dve.past("o normed", i - 1))
                    for n, bank in enumerate((b0, b1)):
                        act.activation(ln.norm[:, n, 0:SEQ], bank[:, :], ACT.Ln, bias=g.eps[:, 0:1])
                    act.activation(ln.norm[:, :, NT], b2[:, 0:2 * NEW].rearrange("p (n t) -> p n t", n=2), ACT.Ln,
                                   bias=g.eps[:, 0:1]).then_inc(*ln.act.done("log norms"))
                    act.wait_ge(ln.act.sem, ln.act.past("log norms", i))
                    act.activation(ln.norm[:, :, :], ln.norm[:, :, :], ACT.Exp, scale=-0.5
                                   ).then_inc(*ln.act.done("norms"))
                    yield
                    act.wait_ge(ln.dve.sem, ln.dve.past("k beta decay", i))
                    for t in range(TILES):
                        act.activation(ln.kt[:, t, :], b3[:, tile(t)], ACT.Copy, scale=ln.gates[:, TAIL, t:t + 1])
                    act.activation(ln.kt[N, TILES, :], b2[N, 64:192], ACT.Copy,
                                   scale=ln.gates[N, TAIL, TILES:TILES + 1]).then_inc(*ln.act.done("k tail"))
                    act.wait_ge(ln.pe.sem, ln.pe.past("v rows", i))
                    for t in range(TILES):
                        act.activation(ln.vb[:, t, :], b0[:, tile(t)], ACT.Copy, scale=ln.gates[:, BETA, t:t + 1])
                    act.activation(ln.vb[N, TILES, :], b2[N, 192:320], ACT.Copy,
                                   scale=ln.gates[N, BETA, TILES:TILES + 1]).then_inc(*ln.act.done("v beta"))
                    yield
                    act.wait_ge(ln.dve.sem, ln.dve.past("difference", i))
                    act.activation(ln.sq[:, 0, 0:SEQ], b0[:, :], ACT.Exp)
                    act.activation(ln.sq[:, 0, NT], b2[:, 384:416], ACT.Exp).then_inc(*ln.act.done("eG wide"))
                    act.activation(ln.dec[:, 0:SEQ], ln.dec[:, 0:SEQ], ACT.Exp)
                    act.activation(ln.dec[N, NT], ln.dec[N, NT], ACT.Exp).then_inc(*ln.act.done("decay"))
                    yield
                    act.wait_ge(ln.pe.sem, ln.pe.past("T 0", i))
                    act.activation(ln.T[:, 0:SEQ], b1[:, :], ACT.Copy)
                    act.activation(ln.T[N, NT], b2[N, 0:32], ACT.Copy).then_inc(*ln.act.done("T 0"))
                    yield
                    for n in DOUBLINGS:
                        act.wait_ge(ln.pe.sem, ln.pe.past(f"W {n}", i))
                        if n == 1:
                            act.activation(ln.W[N, NT], b2[N, 32:64], ACT.Copy)
                        act.activation(ln.W[:, 0:SEQ], b1[:, :], ACT.Copy).then_inc(*ln.act.done(f"W {n}"))
                        yield
                    act.wait_ge(ln.pe.sem, ln.pe.past("u", i))
                    act.activation(ln.u[:, :, :].rearrange("p t v -> p (t v)"), b1[:, :], ACT.Copy
                                   ).then_inc(*ln.act.done("u"))
                    act.wait_ge(ln.pe.sem, ln.pe.past("new u w", i))
                    act.activation(ln.wq[:, 0, 0:SEQ], b3[:, :], ACT.Copy)
                    act.activation(ln.wq[:, 0, NT], b2[:, 128:160], ACT.Copy).then_inc(*ln.act.done("w"))
                    yield
                    act.wait_ge(ln.pe.sem, ln.pe.past("new wS qS", i))
                    act.activation(ln.wSqS[:, :, :, :].rearrange("p b w t -> p (b w t)"), b2[:, 160:224], ACT.Copy
                                   ).then_inc(*ln.act.done("new wS qS"))
                    yield
                    act.wait_ge(ln.pe.sem, ln.pe.past("new v rows", i))
                    act.activation(ln.v_rows[:, :], b2[N, 224:352], ACT.Copy).then_inc(*ln.act.done("new v rows"))
                    yield
                    act.wait_ge(ln.dve.sem, ln.dve.past("o gated", i - 1))
                    act.activation(ln.o[:, 0:SEQ], b0[:, :], ACT.Copy).then_inc(*ln.act.done("o"))
                    act.wait_ge(ln.act.sem, ln.act.past("o", i))
                    act.wait_ge(ln.dve.sem, ln.dve.past("new o", i))
                    act.activation(ln.sq[:, 1, :], ln.o[:, :], ACT.Square).then_inc(*ln.act.done("o square"))
                    yield
                    act.wait_ge(ln.pe.sem, ln.pe.past("o squares", i))
                    act.activation(ln.norm[:, 0, 0:SEQ], b0[:, :], ACT.Ln, scale=1.0 / P, bias=g.eps[:, 0:1])
                    act.activation(ln.norm[:, 0, NT], b2[:, 384:416], ACT.Ln, scale=1.0 / P, bias=g.eps[:, 0:1]
                                   ).then_inc(*ln.act.done("o log"))
                    act.wait_ge(ln.act.sem, ln.act.past("o log", i))
                    act.activation(ln.norm[:, 0, :], ln.norm[:, 0, :], ACT.Exp, scale=-0.5
                                   ).then_inc(*ln.act.done("o norm"))
                    yield

                for ln in lanes:
                    ln.act.credit(act)
                with act.Fori(0, rounds) as i:
                    alternate(rule, i)

            @block.vector
            def _(dve):
                def rule(ln, i):
                    b0, b1, b2, b3 = ln.bank
                    h = bass.ds(2 * i + ln.s, 1)
                    q, k = (g.qkv[:, bass.ds(2 * i + ln.s + HEADS * n, 1), :].rearrange("p a t -> p (a t)")
                            for n in range(2))
                    dve.wait_ge(ln.pe.sem, ln.pe.past("beta wide", i - 1))
                    dve.wait_ge(ln.act.sem, ln.act.past("v beta", i - 1))
                    for n, gate in ((G_, g.gate_g), (BETA, g.beta), (CUM, g.G), (TAIL, g.tail)):
                        dve.tensor_copy(ln.gates[:, n, :], gate[:, :, h].rearrange("p t a -> p (t a)"))
                    dve.tensor_copy(ln.gates[:, BETA_DECAY, :], g.eG[:, :, h].rearrange("p t a -> p (t a)")
                                    ).then_inc(*ln.dve.done("gates"))
                    dve.wait_ge(ln.dve.sem, ln.dve.past("gates", i))
                    dve.tensor_tensor(ln.gates[:, BETA_DECAY, :], ln.gates[:, BETA_DECAY, :], ln.gates[:, BETA, :],
                                      ALU.mult).then_inc(*ln.dve.done("k beta decay staged"))
                    yield
                    dve.wait_ge(ln.act.sem, ln.act.past("norms", i))
                    dve.tensor_tensor(ln.kT[:, :], k, ln.norm[:, 1, :], ALU.mult).then_inc(*ln.dve.done("k"))
                    dve.scalar_tensor_tensor(out=ln.qT[:, :], in0=q, scalar=float(P) ** -0.5, in1=ln.norm[:, 0, :],
                                             op0=ALU.mult, op1=ALU.mult).then_inc(*ln.dve.done("q"))
                    yield
                    dve.wait_ge(ln.pe.sem, ln.pe.past("k rows", i))
                    dve.wait_ge(ln.dve.sem, ln.dve.past("k beta decay staged", i))
                    for t in range(TILES):
                        dve.tensor_scalar(ln.kbe[:, t, :], b3[:, tile(t)], ln.gates[:, BETA_DECAY, t:t + 1], None,
                                          ALU.mult)
                    dve.tensor_scalar(ln.kbe[N, TILES, :], b2[N, 64:192], ln.gates[N, BETA_DECAY, TILES:TILES + 1],
                                      None, ALU.mult).then_inc(*ln.dve.done("k beta decay"))
                    yield
                    dve.wait_ge(ln.pe.sem, ln.pe.past("G wide", i))
                    for t in range(TILES):
                        dve.scalar_tensor_tensor(out=ln.dec[:, tile(t)], in0=b0[:, tile(t)],
                                                 scalar=ln.gates[:, CUM, t:t + 1], in1=g.const("decay_neg"),
                                                 op0=ALU.subtract, op1=ALU.add)
                    dve.scalar_tensor_tensor(out=ln.dec[N, NT], in0=b2[N, 384:416],
                                             scalar=ln.gates[N, CUM, TILES:TILES + 1],
                                             in1=new_const("decay_neg_new"), op0=ALU.subtract, op1=ALU.add
                                             ).then_inc(*ln.dve.done("difference"))
                    yield
                    dve.wait_ge(ln.act.sem, ln.act.past("decay", i))
                    dve.wait_ge(ln.pe.sem, ln.pe.past("beta wide", i))
                    dve.tensor_tensor(ln.QK[:, 0:SEQ], b3[:, :], ln.dec[:, 0:SEQ], ALU.mult)
                    dve.tensor_tensor(ln.QK[N, NT], b2[N, 352:384], ln.dec[N, NT], ALU.mult
                                      ).then_inc(*ln.dve.done("qk"))
                    dve.tensor_tensor(ln.LT[:, 0:SEQ], b1[:, :], ln.dec[:, 0:SEQ], ALU.mult)
                    dve.tensor_tensor(ln.LT[N, NT], b2[N, 320:352], ln.dec[N, NT], ALU.mult
                                      ).then_inc(*ln.dve.done("kk"))
                    dve.wait_ge(ln.dve.sem, ln.dve.past("kk", i))
                    dve.tensor_tensor(ln.LT[:, 0:SEQ], ln.LT[:, 0:SEQ], b0[:, :], ALU.mult)
                    dve.tensor_tensor(ln.LT[N, NT], ln.LT[N, NT], b2[N, 416:448], ALU.mult
                                      ).then_inc(*ln.dve.done("L"))
                    yield
                    dve.wait_ge(ln.pool.sem, ln.pool.past("level 0", i))
                    dve.scalar_tensor_tensor(out=tiled(ln.TT[:, 0:SEQ]), in0=tiled(ln.B[:, 0, 0:SEQ]), scalar=-1.0,
                                             in1=wide("ident"), op0=ALU.mult, op1=ALU.add)
                    dve.scalar_tensor_tensor(out=ln.TT[N, NT], in0=ln.B[N, 0, NT], scalar=-1.0,
                                             in1=new_const("ident"), op0=ALU.mult, op1=ALU.add
                                             ).then_inc(*ln.dve.done("TT 0"))
                    yield
                    for n in DOUBLINGS:
                        dve.wait_ge(ln.pe.sem, ln.pe.past(f"TT {n}", i))
                        if n == 1:
                            dve.tensor_tensor(ln.TT[N, NT], ln.TT[N, NT], b2[N, 64:96], ALU.subtract)
                        if n < LEVELS - 1:
                            dve.tensor_tensor(ln.T[:, 0:SEQ], ln.T[:, 0:SEQ], b3[:, :], ALU.subtract)
                        dve.tensor_tensor(ln.TT[:, 0:SEQ], ln.TT[:, 0:SEQ], b0[:, :], ALU.subtract
                                          ).then_inc(*ln.dve.done(f"T {n}"))
                        yield
                    dve.wait_ge(ln.act.sem, ln.act.past("u", i))
                    dve.wait_ge(ln.pool.sem, ln.pool.past("clear S", i))
                    for j in range(CHUNKS):
                        t, R = j // 2, slice(CHUNK * (j % 2), CHUNK * (j % 2 + 1))
                        dve.wait_ge(ln.pe.sem, ln.pe.past(f"wS {j}", i))
                        dve.tensor_tensor(ln.vn[R, :], ln.u[R, t, :], b1[R, 0:P], ALU.subtract
                                          ).then_inc(*ln.dve.done(f"v {j}"))
                        yield
                        dve.wait_ge(ln.pe.sem, ln.pe.past(f"KV {j}", i))
                        if j:
                            dve.wait_ge(ln.dve.sem, ln.dve.past(f"S {j - 1}", i))
                        dve.scalar_tensor_tensor(out=ln.S[:, :], in0=ln.S[:, :],
                                                 scalar=g.e_chunk[:, j:j + 1, h].rearrange("p a b -> p (a b)"),
                                                 in1=b3[:, 0:P], op0=ALU.mult, op1=ALU.add
                                                 ).then_inc(*ln.dve.done(f"S {j}"))
                        yield
                    dve.wait_ge(ln.act.sem, ln.act.past("new wS qS", i))
                    dve.tensor_tensor(ln.vT[:, :].rearrange("p (b t) -> p b t", t=DEC_SEQ),
                                      b2[:, 96:128].rearrange("p (b t) -> p b t", t=DEC_SEQ),
                                      ln.wSqS[:, :, 0, :], ALU.subtract).then_inc(*ln.dve.done("new v"))
                    yield
                    dve.wait_ge(ln.act.sem, ln.act.past("new v rows", i))
                    dve.tensor_tensor(ln.v_batch[:, :, :],
                                      ln.v_rows[:, :].unsqueeze(1).broadcast_to([NEW, DEC_BATCH, P]),
                                      g.const("batch_of", NEW).unsqueeze(2).broadcast_to([NEW, DEC_BATCH, P]),
                                      ALU.mult).then_inc(*ln.dve.done("new v by batch"))
                    dve.tensor_tensor(ln.S_new[:, :, :], ln.S_new[:, :, :],
                                      g.e_batch[:, :, h].broadcast_to([P, DEC_BATCH, P]), ALU.mult
                                      ).then_inc(*ln.dve.done("new S decayed"))
                    yield
                    dve.wait_ge(ln.pe.sem, ln.pe.past("new KV", i))
                    dve.wait_ge(ln.dve.sem, ln.dve.past("new S decayed", i))
                    for a, bank in enumerate((b1, b3)):
                        part = ln.S_new[:, 4 * a:4 * a + 4, :].rearrange("p b v -> p (b v)")
                        ins = dve.tensor_tensor(part, part, bank[:, :], ALU.add)
                    ins.then_inc(*ln.dve.done("new S"))
                    dve.wait_ge(ln.dve.sem, ln.dve.past("o gated", i - 1))
                    dve.tensor_tensor(ln.o[:, NT].rearrange("p (b t) -> p b t", t=DEC_SEQ),
                                      b2[:, 352:384].rearrange("p (b t) -> p b t", t=DEC_SEQ),
                                      ln.wSqS[:, :, 1, :], ALU.add).then_inc(*ln.dve.done("new o"))
                    yield
                    dve.wait_ge(ln.act.sem, ln.act.past("o norm", i))
                    dve.scalar_tensor_tensor(out=ln.o[:, :], in0=ln.o[:, :], scalar=g.gains[:, O_GAIN:O_GAIN + 1],
                                             in1=ln.norm[:, 0, :], op0=ALU.mult, op1=ALU.mult
                                             ).then_inc(*ln.dve.done("o normed"))
                    dve.wait_ge(ln.dve.sem, ln.dve.past("o normed", i))
                    z = head_of(g.zT, ln, i)
                    dve.tensor_tensor(z, z, ln.o[:, :], ALU.mult).then_inc(*ln.dve.done("o gated"))
                    yield

                for ln in lanes:
                    ln.dve.credit(dve)
                with dve.Fori(0, rounds) as i:
                    alternate(rule, i)

            @block.gpsimd
            def _(pool):
                def rule(ln, i):
                    pool.wait_ge(ln.sp.sem, ln.sp.past("states stored", i - 1))
                    pool.tensor_tensor(ln.S[:, :], g.const("ident"), g.const("ident"), ALU.subtract).then_inc(*ln.pool.done("clear S"))
                    pool.wait_ge(ln.act.sem, ln.act.past("eG wide", i))
                    pool.wait_ge(ln.dve.sem, ln.dve.past("q", i))
                    pool.wait_ge(ln.pe.sem, ln.pe.past("new wS qS", i - 1))
                    pool.tensor_tensor(ln.wq[:, 1, :], ln.qT[:, :], ln.sq[:, 0, :], ALU.mult
                                       ).then_inc(*ln.pool.done("q decayed"))
                    yield
                    pool.wait_ge(ln.dve.sem, ln.dve.past("L", i))
                    for n in range(LEVELS):
                        if n == 2:
                            pool.wait_ge(ln.dve.sem, ln.dve.past("TT 0", i))
                        if n > 2:
                            pool.wait_ge(ln.pe.sem, ln.pe.past(f"W {n - 2}", i))
                        if n < 2:
                            pool.tensor_tensor(ln.B[N, n, NT], ln.LT[N, NT], new_const(f"level{n}"), ALU.mult)
                        pool.tensor_tensor(tiled(ln.B[:, n % 2, 0:SEQ]), tiled(ln.LT[:, 0:SEQ]), wide(f"level{n}"),
                                           ALU.mult).then_inc(*ln.pool.done(f"level {n}"))
                        yield

                for ln in lanes:
                    ln.pool.credit(pool)
                with pool.Fori(0, rounds) as i:
                    alternate(rule, i)


def out_project_stage(nc, g, name, w_d, src):
    with Stage(nc, name) as st:
        w = [st.sb(f"w{s}", [P, KT, P]) for s in range(2)]
        acc = [st.ps(f"acc{s}", (P, 2, 512)) for s in range(2)]
        loaded = [st.sem(f"loaded{s}") for s in range(2)]
        multiplied, added = st.sem("multiplied"), st.sem("added")
        with st.block() as block:
            @block.sync
            def _(sp):
                for m in range(KT):
                    if m >= 2:
                        sp.wait_ge(multiplied, m - 1)
                    sp.dma_start(w[m % 2][:, :, :], w_d[m]).then_inc(loaded[m % 2], 16)

            @block.tensor
            def _(pe):
                for m in range(KT):
                    pe.wait_ge(loaded[m % 2], 16 * (m // 2 + 1))
                    if m >= 2:
                        pe.wait_ge(added, m - 1)
                    for k in range(KT):
                        for a in range(2):
                            mm = pe.matmul(acc[m % 2][:, a, 0:HALF], w[m % 2][:, k, :],
                                           src[:, k, a * HALF:(a + 1) * HALF], start=(k == 0), stop=(k == KT - 1))
                    mm.then_inc(multiplied, 1)

            @block.vector
            def _(dve):
                for m in range(KT):
                    dve.wait_ge(multiplied, m + 1)
                    dve.tensor_tensor(halves(g.xT[:, m, :]), acc[m % 2][:, :, 0:HALF], halves(g.xT[:, m, :]),
                                      ALU.add).then_inc(added, 1)


def router_stage(nc, g, name, layer):
    NT = TILES + 1
    n_log = GROUPS + EXPERTS
    with Stage(nc, name) as st:
        w = st.sb("w", [P, KT, n_log])
        bias = st.sb("bias", [P, n_log])
        logits = st.sb("logits", [P, NT, n_log])
        top = {x: st.sb(x, [P, NT, 1]) for x in ("grp_max", "grp_sum", "grp_pick", "m1", "m2", "p1", "p2",
                                                 "e2", "den", "w1", "w2")}
        e_grp = st.sb("e_grp", [P, NT, GROUPS])
        grp = st.sb("grp", [P, NT, GROUPS])
        inside = st.sb("inside", [P, NT, PER_GROUP])
        part = st.sb("part", [P, NT, PER_GROUP])
        first = st.sb("first", [P, NT, PER_GROUP])
        second = st.sb("second", [P, NT, PER_GROUP])
        rest = st.sb("rest", [P, NT, PER_GROUP])
        comb = st.sb("comb", [P, NT, EXPERTS])
        proj = st.ps("proj")
        turned = st.ps("turned", (P, 2, 512))
        loaded = st.sem("loaded")
        pe_done, dve_step, act_done = st.sem("pe_done"), st.sem("dve_step"), st.sem("act_done")
        rows_of = [P] * TILES + [NEW]
        pr = proj[:, 0:NT * n_log].rearrange("p (t n) -> p t n", n=n_log)
        exp_wait = {}

        with st.block() as block:
            @block.sync
            def _(sp):
                sp.dma_start(w[:, :, :], g.d["router_w"][layer]).then_inc(loaded, 16)
                sp.dma_start(bias[:, :], g.d["router_b"][layer]).then_inc(loaded, 16)

            @block.vector
            def _(dve):
                taken = [0]

                def step(ins):
                    ins.then_inc(dve_step, 1)
                    taken[0] += 1
                    dve.wait_ge(dve_step, taken[0])

                def wide(t, n):
                    return t[:, :, :].broadcast_to([P, NT, n])

                def first_of(out, pick, like, top_value, n):
                    step(dve.tensor_tensor(out, like, wide(top_value, n), ALU.is_equal))
                    order = g.const("first_pick")[:, 0:n].unsqueeze(1).broadcast_to([P, NT, n])
                    step(dve.tensor_tensor(out, out, order, ALU.mult))
                    step(dve.tensor_reduce(pick[:, :, :], out, AX_X, ALU.max))
                    step(dve.tensor_tensor(out, out, wide(pick, n), ALU.is_equal))

                step(dve.memset(logits[:, :, :], 0.0))
                dve.wait_ge(loaded, 32)
                dve.wait_ge(pe_done, 1)
                b = bias[:, :].unsqueeze(1)
                step(dve.tensor_tensor(logits[:, 0:TILES, :], pr[:, 0:TILES, :], b.broadcast_to([P, TILES, n_log]),
                                       ALU.add))
                step(dve.tensor_tensor(logits[0:NEW, TILES:NT, :], pr[0:NEW, TILES:NT, :],
                                       bias[0:NEW, :].unsqueeze(1), ALU.add))
                lg = logits[:, :, 0:GROUPS]
                step(dve.tensor_reduce(top["grp_max"][:, :, :], lg, AX_X, ALU.max))
                step(dve.tensor_tensor(e_grp[:, :, :], lg, wide(top["grp_max"], GROUPS), ALU.subtract))
                exp_wait["grp"] = taken[0]
                first_of(grp[:, :, :], top["grp_pick"], lg, top["grp_max"], GROUPS)
                for k in range(GROUPS):
                    le = logits[:, :, GROUPS + k * PER_GROUP:GROUPS + (k + 1) * PER_GROUP]
                    own = grp[:, :, k:k + 1].broadcast_to([P, NT, PER_GROUP])
                    if k == 0:
                        step(dve.tensor_tensor(inside[:, :, :], le, own, ALU.mult))
                    else:
                        step(dve.tensor_tensor(part[:, :, :], le, own, ALU.mult))
                        step(dve.tensor_tensor(inside[:, :, :], inside[:, :, :], part[:, :, :], ALU.add))
                step(dve.tensor_reduce(top["m1"][:, :, :], inside[:, :, :], AX_X, ALU.max))
                first_of(first[:, :, :], top["p1"], inside[:, :, :], top["m1"], PER_GROUP)
                step(dve.scalar_tensor_tensor(out=rest[:, :, :], in0=first[:, :, :], scalar=NEG,
                                              in1=inside[:, :, :], op0=ALU.mult, op1=ALU.add))
                step(dve.tensor_reduce(top["m2"][:, :, :], rest[:, :, :], AX_X, ALU.max))
                step(dve.tensor_tensor(top["e2"][:, :, :], top["m2"][:, :, :], top["m1"][:, :, :], ALU.subtract))
                exp_wait["pair"] = taken[0]
                first_of(second[:, :, :], top["p2"], rest[:, :, :], top["m2"], PER_GROUP)
                dve.wait_ge(act_done, 2)
                step(dve.tensor_reduce(top["grp_sum"][:, :, :], e_grp[:, :, :], AX_X, ALU.add))
                step(dve.scalar_tensor_tensor(out=top["den"][:, :, :], in0=top["e2"][:, :, :], scalar=1.0,
                                              in1=top["grp_sum"][:, :, :], op0=ALU.add, op1=ALU.mult))
                step(dve.reciprocal(top["w1"][:, :, :], top["den"][:, :, :]))
                step(dve.tensor_tensor(top["w2"][:, :, :], top["w1"][:, :, :], top["e2"][:, :, :], ALU.mult))
                step(dve.tensor_tensor(first[:, :, :], first[:, :, :], wide(top["w1"], PER_GROUP), ALU.mult))
                step(dve.tensor_tensor(second[:, :, :], second[:, :, :], wide(top["w2"], PER_GROUP), ALU.mult))
                step(dve.tensor_tensor(first[:, :, :], first[:, :, :], second[:, :, :], ALU.add))
                for k in range(GROUPS):
                    step(dve.tensor_tensor(comb[:, :, k * PER_GROUP:(k + 1) * PER_GROUP], first[:, :, :],
                                           grp[:, :, k:k + 1].broadcast_to([P, NT, PER_GROUP]), ALU.mult))
                exp_wait["comb"] = taken[0]
                dve.wait_ge(pe_done, 2)
                dve.tensor_copy(g.combT[:, 0:SEQ], turned[0:EXPERTS, 0, :])
                dve.tensor_copy(g.combT[:, SEQ:TOKENS], turned[0:EXPERTS, 1, 0:NEW])

            @block.scalar
            def _(act):
                act.wait_ge(dve_step, exp_wait["grp"])
                act.activation(e_grp[:, :, :], e_grp[:, :, :], ACT.Exp).then_inc(act_done, 1)
                act.wait_ge(dve_step, exp_wait["pair"])
                act.activation(top["e2"][:, :, :], top["e2"][:, :, :], ACT.Exp).then_inc(act_done, 1)

            @block.tensor
            def _(pe):
                pe.wait_ge(loaded, 32)
                for t, n in enumerate(rows_of):
                    for k in range(KT):
                        mm = pe.matmul(pr[0:n, t, :], g.hT[:, k, t * P:t * P + n], w[:, k, :],
                                       start=(k == 0), stop=(k == KT - 1))
                mm.then_inc(pe_done, 1)
                pe.wait_ge(dve_step, exp_wait["comb"])
                for t in range(TILES):
                    pe.transpose(turned[0:EXPERTS, 0, t * P:(t + 1) * P], comb[:, t, :], g.const("ident"))
                pe.transpose(turned[0:EXPERTS, 1, 0:NEW], comb[0:NEW, TILES, :], g.const("ident", NEW)[:, 0:NEW]
                             ).then_inc(pe_done, 1)


def experts_stage(nc, g, name, layer):
    pe_steps = ["weight row", "gate 0", "up 0", "gate 1", "up 1"] + [f"down {m}" for m in range(KT)]
    with Stage(nc, name) as st:
        w_gate = [st.sb(f"w_gate{s}", [P, KT, FF]) for s in range(2)]
        w_up = [st.sb(f"w_up{s}", [P, KT, FF]) for s in range(2)]
        w_down = [st.sb(f"w_down{s}", [P, FF // P, D_MODEL]) for s in range(2)]
        pick = [st.sb(f"pick{s}", [EXPERTS, P]) for s in range(2)]
        weight = [st.sb(f"weight{s}", [P, TOKENS]) for s in range(2)]
        act_gate = [st.sb(f"act_gate{m}", [P, TOKENS]) for m in range(2)]
        hidden = [st.sb(f"hidden{s}", [P, 2, TOKENS]) for s in range(2)]
        pair = [st.ps(f"pair{n}", (P, 2, 512)) for n in range(4)]
        loaded = [[st.sem(f"loaded{s}_{x}") for x in ("gate", "up", "down")] for s in range(2)]
        pe_s = [st.steps(f"pe{s}", pe_steps) for s in range(2)]
        act_s = [st.steps(f"act{s}", ["weight row", "silu 0", "silu 1"]) for s in range(2)]
        dve_s = [st.steps(f"dve{s}", ["pick", "up 0", "h 0", "up 1", "h 1"] + [f"add {m}" for m in range(KT)])
                 for s in range(2)]
        rounds = EXPERTS // 2
        with st.block() as block:
            @block.sync
            def _(sp):
                def load(s, e):
                    for n, (buf, src) in enumerate(((w_gate[s], "w_gate"), (w_up[s], "w_up"), (w_down[s], "w_down"))):
                        d = g.d[src][layer]
                        sp.dma_start(buf[:, :, :], d[e] if isinstance(e, int) else
                                     d[bass.ds(e, 1)].rearrange("e p k f -> (e p) k f")
                                     ).then_inc(loaded[s][n], 16)
                for s in range(2):
                    load(s, s)
                with sp.Fori(0, rounds - 1) as i:
                    for s in range(2):
                        sp.wait_ge(pe_s[s].sem, pe_s[s].past(f"down {KT - 1}", i))
                        load(s, 2 * i + 2 + s)

            @block.tensor
            def _(pe):
                for s in range(2):
                    pe_s[s].credit(pe)
                with pe.Fori(0, rounds) as i:
                    for s in range(2):
                        last = (s - 1) % 2
                        li = i if s else i - 1
                        pe.wait_ge(dve_s[s].sem, dve_s[s].past("pick", i))
                        pe.wait_ge(dve_s[last].sem, dve_s[last].past(f"add {KT - 1}", li))
                        for a in range(2):
                            mm = pe.matmul(pair[3][:, a, 0:HALF], pick[s][:, :], g.combT[:, a * HALF:(a + 1) * HALF],
                                           start=True, stop=True)
                        mm.then_inc(*pe_s[s].done("weight row"))
                        for m in range(2):
                            for x, w in ((0, w_gate[s]), (1, w_up[s])):
                                if m == 0:
                                    pe.wait_ge(loaded[s][x], 16 * (i + 1))
                                if m == 1 and x == 1:
                                    pe.wait_ge(act_s[s].sem, act_s[s].past("weight row", i))
                                for k in range(KT):
                                    for a in range(2):
                                        mm = pe.matmul(pair[2 * m + x][:, a, 0:HALF], w[:, k, m * P:(m + 1) * P],
                                                       g.hT[:, k, a * HALF:(a + 1) * HALF],
                                                       start=(k == 0), stop=(k == KT - 1))
                                mm.then_inc(*pe_s[s].done(("gate", "up")[x] + f" {m}"))
                        pe.wait_ge(loaded[s][2], 16 * (i + 1))
                        for m in range(KT):
                            if m == 0:
                                pe.wait_ge(dve_s[s].sem, dve_s[s].past("h 1", i))
                            if m >= 4:
                                pe.wait_ge(dve_s[s].sem, dve_s[s].past(f"add {m - 4}", i))
                            for k in range(2):
                                for a in range(2):
                                    mm = pe.matmul(pair[m % 4][:, a, 0:HALF], w_down[s][:, k, m * P:(m + 1) * P],
                                                   hidden[s][:, k, a * HALF:(a + 1) * HALF],
                                                   start=(k == 0), stop=(k == 1))
                            mm.then_inc(*pe_s[s].done(f"down {m}"))

            @block.scalar
            def _(act):
                for s in range(2):
                    act_s[s].credit(act)
                with act.Fori(0, rounds) as i:
                    for s in range(2):
                        act.wait_ge(pe_s[s].sem, pe_s[s].past("weight row", i))
                        act.wait_ge(dve_s[s].sem, dve_s[s].past("h 1", i - 1))
                        act.activation(halves(weight[s][:, :]), pair[3][:, :, 0:HALF], ACT.Copy
                                       ).then_inc(*act_s[s].done("weight row"))
                        for m in range(2):
                            act.wait_ge(pe_s[s].sem, pe_s[s].past(f"gate {m}", i))
                            last, li = (s - 1) % 2, (i if s else i - 1)
                            act.wait_ge(dve_s[last].sem, dve_s[last].past(f"h {m}", li))
                            act.activation(halves(act_gate[m][:, :]), pair[2 * m][:, :, 0:HALF], ACT.Silu
                                           ).then_inc(*act_s[s].done(f"silu {m}"))

            @block.vector
            def _(dve):
                for s in range(2):
                    dve_s[s].credit(dve)
                ident = g.const("ident", EXPERTS)
                with dve.Fori(0, rounds) as i:
                    for s in range(2):
                        dve.wait_ge(pe_s[s].sem, pe_s[s].past("weight row", i - 1))
                        dve.tensor_tensor(pick[s][:, :], ident[:, bass.ds(2 * i + s, 1)].broadcast_to([EXPERTS, P]),
                                          g.const("ones", EXPERTS), ALU.mult).then_inc(*dve_s[s].done("pick"))
                        for m in range(2):
                            dve.wait_ge(act_s[s].sem, act_s[s].past(f"weight row", i))
                            dve.wait_ge(pe_s[s].sem, pe_s[s].past(f"up {m}", i))
                            h = halves(hidden[s][:, m, :])
                            dve.tensor_tensor(h, pair[2 * m + 1][:, :, 0:HALF], halves(weight[s][:, :]), ALU.mult
                                              ).then_inc(*dve_s[s].done(f"up {m}"))
                            dve.wait_ge(act_s[s].sem, act_s[s].past(f"silu {m}", i))
                            dve.wait_ge(dve_s[s].sem, dve_s[s].past(f"up {m}", i))
                            dve.tensor_tensor(hidden[s][:, m, :], hidden[s][:, m, :], act_gate[m][:, :], ALU.mult
                                              ).then_inc(*dve_s[s].done(f"h {m}"))
                        for m in range(KT):
                            dve.wait_ge(pe_s[s].sem, pe_s[s].past(f"down {m}", i))
                            x = halves(g.xT[:, m, :])
                            dve.tensor_tensor(x, pair[m % 4][:, :, 0:HALF], x, ALU.add
                                              ).then_inc(*dve_s[s].done(f"add {m}"))


def moe(nc, g, name, layer, gain0):
    with ExitStack() as ctx:
        g.combT = ctx.enter_context(nc.sbuf_tensor(name + "_combT", [EXPERTS, TOKENS], F32))
        g.hT = ctx.enter_context(nc.sbuf_tensor(name + "_h", [P, KT, TOKENS], F32))
        rms_norm_stage(nc, g, name + "_norm", gain0)
        router_stage(nc, g, name + "_router", layer)
        experts_stage(nc, g, name + "_experts", layer)


Q_TILES = NSA_HEADS // 2
CMP_K, CMP_V, SLC_K, SLC_V, WIN_K, WIN_V = (Q_TILES + 2 * n for n in range(6))
NSA_TILES = Q_TILES + 12
ROWS = NSA_HEADS * DEC_SEQ
BLOCKS = PAST // CMP
P_BLOCKS = SEQ // CMP


def nsa_project_stage(nc, g):
    with Stage(nc, "nproj") as st:
        w = [st.sb(f"w{s}", [P, KT, P]) for s in range(2)]
        wg = st.sb("wg", [P, KT, 3 * NSA_HEADS])
        new_gates = st.sb("new_gates", [NEW, 3 * NSA_HEADS])
        acc = [st.ps(f"acc{s}", (P, 2, 512)) for s in range(2)]
        gate_acc = st.ps("gate_acc")
        loaded = [st.sem(f"loaded{s}") for s in range(2)]
        gates_loaded, gates_done, new_gates_done = st.sem("gates_loaded"), st.sem("gates_done"), st.sem("new_gates_done")
        spread = st.sem("spread")
        pe_s = [st.steps(f"pe{s}", ["product"]) for s in range(2)]
        act_s = [st.steps(f"act{s}", ["copied"]) for s in range(2)]
        rounds = NSA_TILES // 2
        NG = 3 * NSA_HEADS
        with st.block() as block:
            @block.sync
            def _(sp):
                sp.dma_start(wg[:, :, :], g.d["nsa_w_gates"]).then_inc(gates_loaded, 16)
                for s in range(2):
                    sp.dma_start(w[s][:, :, :], g.d["nsa_w"][s]).then_inc(loaded[s], 16)
                with sp.Fori(0, rounds - 1) as i:
                    for s in range(2):
                        sp.wait_ge(pe_s[s].sem, pe_s[s].past("product", i))
                        sp.dma_start(w[s][:, :, :],
                                     g.d["nsa_w"][bass.ds(2 * i + 2 + s, 1)].rearrange("t p k c -> (t p) k c")
                                     ).then_inc(loaded[s], 16)
                sp.wait_ge(new_gates_done, 1)
                sp.dma_start(g.d["gate_scratch"], new_gates[:, :]).then_inc(spread, 16)
                sp.wait_ge(spread, 16)
                for t in range(DEC_SEQ):
                    src = g.d["gate_scratch"].rearrange("(b t) (h r) -> t h b r", t=DEC_SEQ, r=3)
                    sp.dma_start(g.row_gates[t:ROWS:DEC_SEQ, :, :], src[t]).then_inc(spread, 16)
                sp.wait_ge(spread, 16 * (1 + DEC_SEQ))

            @block.tensor
            def _(pe):
                for s in range(2):
                    pe_s[s].credit(pe)
                pe.wait_ge(gates_loaded, 16)
                for t in range(TILES + 1):
                    n = P if t < TILES else NEW
                    for k in range(KT):
                        mm = pe.matmul(gate_acc[0:n, t * NG:(t + 1) * NG], g.hT[:, k, t * P:t * P + n], wg[:, k, :],
                                       start=(k == 0), stop=(k == KT - 1))
                mm.then_inc(gates_done, 1)
                with pe.Fori(0, rounds) as i:
                    for s in range(2):
                        pe.wait_ge(loaded[s], 16 * (i + 1))
                        pe.wait_ge(act_s[s].sem, act_s[s].past("copied", i - 1))
                        for k in range(KT):
                            for a in range(2):
                                mm = pe.matmul(acc[s][:, a, 0:HALF], w[s][:, k, :],
                                               g.hT[:, k, a * HALF:(a + 1) * HALF], start=(k == 0), stop=(k == KT - 1))
                        mm.then_inc(*pe_s[s].done("product"))

            @block.scalar
            def _(act):
                for s in range(2):
                    act_s[s].credit(act)
                act.wait_ge(gates_done, 1)
                act.activation(new_gates[:, :], gate_acc[0:NEW, TILES * NG:(TILES + 1) * NG], ACT.Sigmoid
                               ).then_inc(new_gates_done, 1)
                act.activation(g.gates[:, :, :, :].rearrange("p t h r -> p (t h r)"), gate_acc[:, 0:TILES * NG],
                               ACT.Sigmoid)
                with act.Fori(0, rounds) as i:
                    for s in range(2):
                        act.wait_ge(pe_s[s].sem, pe_s[s].past("product", i))
                        act.activation(halves(g.proj[:, bass.ds(2 * i + s, 1), :].rearrange("p a t -> p (a t)")),
                                       acc[s][:, :, 0:HALF], ACT.Copy).then_inc(*act_s[s].done("copied"))


def nsa_norm_stage(nc, g):
    normed = list(range(Q_TILES)) + [SLC_K, SLC_K + 1, WIN_K, WIN_K + 1]
    n_norm = len(normed) + 1
    with Stage(nc, "nnorm") as st:
        sq = [st.sb(f"sq{s}", [P, TOKENS]) for s in range(2)]
        root = [st.sb(f"root{s}", [P, TOKENS]) for s in range(2)]
        means = st.sb("means", [P, 4, P_BLOCKS])
        total = [st.ps(f"total{s}", (P, 2, 512)) for s in range(2)]
        turn = [st.ps(f"turn{s}") for s in range(2)]
        squared, summed, rooted = st.sem("squared"), st.sem("summed"), st.sem("rooted")
        logged, normalised = st.sem("logged"), st.sem("normalised")
        turned, turn_out = st.sem("turned"), st.sem("turn_out")
        averaged, cleared = st.sem("averaged"), st.sem("cleared")
        stored = st.sem("stored")
        ident = g.const("ident")
        turns = []
        for n, V in enumerate((SLC_V, WIN_V)):
            for pair in range(2):
                for t in range(TILES):
                    turns.append((g.proj[:, V + pair, t * P:(t + 1) * P], g.v_rows[:, n, t, pair * P:(pair + 1) * P]))
                turns.append((g.proj[:, V + pair, SEQ:TOKENS], g.v_new[:, n, pair * P:(pair + 1) * P]))
        for pair in range(2):
            turns.append((means[:, 2 + pair, :], g.vc[:, pair * P:(pair + 1) * P]))
        with st.block() as block:
            @block.sync
            def _(sp):
                sp.wait_ge(normalised, n_norm)
                sp.dma_start(g.d["kv_out"], g.proj[:, Q_TILES:, :]).then_inc(stored, 16)
                sp.wait_ge(stored, 16)

            @block.scalar
            def _(act):
                def rest(n):
                    w = TOKENS if n < len(normed) else 2 * P_BLOCKS
                    act.wait_ge(summed, n + 1)
                    out, tot = root[n % 2][:, 0:w], total[n % 2]
                    if n >= 2:
                        act.wait_ge(normalised, n - 1)
                    src = tot[:, :, 0:HALF] if w == TOKENS else tot[:, 0, 0:w]
                    act.activation(halves(out) if w == TOKENS else out, src, ACT.Ln, scale=1.0 / HD,
                                   bias=g.eps[:, 0:1]).then_inc(logged, 1)
                    act.wait_ge(logged, n + 1)
                    act.activation(out, out, ACT.Exp, scale=-0.5).then_inc(rooted, 1)

                for n in range(n_norm):
                    if n >= 2:
                        act.wait_ge(summed, n - 1)
                    if n < len(normed):
                        act.activation(sq[n % 2][:, :], g.proj[:, normed[n], :], ACT.Square).then_inc(squared, 1)
                    else:
                        act.wait_ge(averaged, 2)
                        act.activation(sq[n % 2][:, 0:2 * P_BLOCKS], means[:, 0:2, :].rearrange("p a c -> p (a c)"),
                                       ACT.Square).then_inc(squared, 1)
                    if n:
                        rest(n - 1)
                rest(n_norm - 1)

            @block.tensor
            def _(pe):
                for n in range(n_norm):
                    pe.wait_ge(squared, n + 1)
                    if n >= 2:
                        pe.wait_ge(logged, n - 1)
                    if n < len(normed):
                        for a in range(2):
                            mm = pe.matmul(total[n % 2][:, a, 0:HALF], g.const("head_ones"),
                                           sq[n % 2][:, a * HALF:(a + 1) * HALF], start=True, stop=True)
                    else:
                        mm = pe.matmul(total[n % 2][:, 0, 0:2 * P_BLOCKS], g.const("head_ones"),
                                       sq[n % 2][:, 0:2 * P_BLOCKS], start=True, stop=True)
                    mm.then_inc(summed, 1)
                pe.wait_ge(averaged, 2)
                for n, (src, dst) in enumerate(turns):
                    if n >= 2:
                        pe.wait_ge(turn_out, n - 1)
                    pe.transpose(turn[n % 2][0:dst.shape[0], 0:P], src, ident).then_inc(turned, 1)

            @block.vector
            def _(dve):
                dve.tensor_reduce(means[:, :, :], g.proj[:, CMP_K:CMP_K + 4, 0:SEQ].rearrange(
                    "p a (c t) -> p a c t", t=CMP), AX_X, ALU.add).then_inc(averaged, 1)
                dve.wait_ge(averaged, 1)
                dve.tensor_scalar(means[:, :, :], means[:, :, :], 1.0 / CMP, None, ALU.mult).then_inc(averaged, 1)
                dve.memset(g.qb[:, :, :, :], 0.0).then_inc(cleared, 1)
                for n in range(n_norm):
                    dve.wait_ge(rooted, n + 1)
                    if n < len(normed):
                        x = g.proj[:, normed[n], :]
                        gain = Q_GAIN if normed[n] < Q_TILES else K_GAIN
                        dve.scalar_tensor_tensor(out=x, in0=x, scalar=g.gains[:, gain:gain + 1],
                                                 in1=root[n % 2][:, :], op0=ALU.mult, op1=ALU.mult
                                                 ).then_inc(normalised, 1)
                    else:
                        dve.wait_ge(averaged, 2)
                        dve.scalar_tensor_tensor(out=g.kc[:, :, :].rearrange("p a c -> p (a c)"),
                                                 in0=means[:, 0:2, :].rearrange("p a c -> p (a c)"),
                                                 scalar=g.gains[:, K_GAIN:K_GAIN + 1],
                                                 in1=root[n % 2][:, 0:2 * P_BLOCKS],
                                                 op0=ALU.mult, op1=ALU.mult).then_inc(normalised, 1)
                dve.wait_ge(normalised, Q_TILES)
                dve.wait_ge(cleared, 1)
                for pair in range(2):
                    for half in range(2):
                        R = slice(HD * half, HD * (half + 1))
                        for j in range(GROUP):
                            at = 16 * half + DEC_SEQ * j
                            dve.tensor_scalar(
                                g.qb[R, pair, :, at:at + DEC_SEQ],
                                g.proj[R, pair * GROUP + j, SEQ:TOKENS].rearrange("p (b t) -> p b t", t=DEC_SEQ),
                                HD ** -0.5, None, ALU.mult)
                dve.wait_ge(normalised, len(normed))
                for n, K in enumerate((SLC_K, WIN_K)):
                    dve.tensor_copy(g.k_new[:, n, :, :], g.proj[:, K:K + 2, SEQ:TOKENS])
                for n, (src, dst) in enumerate(turns):
                    dve.wait_ge(turned, n + 1)
                    dve.tensor_copy(dst, turn[n % 2][0:dst.shape[0], 0:P]).then_inc(turn_out, 1)


UNIT_PE = ["scores", "turn slc", "turn win", "out"]
UNIT_DVE = ["mask", "mask cmp", "max", "max cmp", "seen", "cmp sum", "floor", "inverse", "gate", "scale", "cmp turned"]
UNIT_ACT = ["exp", "slc turned", "win turned", "out"]


def prompt_attention_stage(nc, g):
    assert SEQ // SEL <= TOP_N and SEQ <= WINDOW
    with Stage(nc, "patt") as st:
        class Lane:
            pass
        lanes = []
        for s in range(2):
            ln = Lane()
            lanes.append(ln)
            ln.s, ln.R = s, slice(HD * s, HD * (s + 1))
            ln.p = st.sb(f"p{s}", [P, 2, SEQ])
            ln.pT = st.sb(f"pT{s}", [P, 2, SEQ])
            ln.sc = st.sb(f"sc{s}", [P, P_BLOCKS])
            ln.pcT = st.sb(f"pcT{s}", [P_BLOCKS, P])
            ln.neg_max = st.sb(f"neg_max{s}", [P, 3])
            ln.sums = st.sb(f"sums{s}", [P, 3])
            ln.scores = st.ps(f"scores{s}", (P, 2, 512))
            ln.turn = st.ps(f"turn{s}")
            ln.out = st.ps(f"out{s}")
            def unit_steps(engine, names, s=s):
                return st.steps(f"{engine}{s}", [f"{n} {t}" for t in range(TILES) for n in names])
            ln.pe, ln.dve, ln.act = (unit_steps("pe", UNIT_PE), unit_steps("dve", UNIT_DVE),
                                     unit_steps("act", UNIT_ACT))
        q = st.sb("q", [P, SEQ])
        q_staged = st.steps("q_staged", ["q"])
        ident = g.const("ident")

        def alternate(rule, i, pair):
            for _ in zip(*(rule(ln, i, pair) for ln in lanes)):
                pass

        def before(steps, name, t, i):
            return steps.past(f"{name} {t - 1}", i) if t else steps.past(f"{name} {TILES - 1}", i - 1)

        with st.block() as block:
            @block.gpsimd
            def _(pool):
                q_staged.credit(pool)
                for pair in range(2):
                    with pool.Fori(pair * GROUP, (pair + 1) * GROUP) as i:
                        for ln in lanes:
                            pool.wait_ge(ln.pe.sem, ln.pe.past(f"scores {TILES - 1}", i - 1))
                        pool.tensor_tensor(q[:, :], g.proj[:, bass.ds(i, 1), 0:SEQ].rearrange("p a t -> p (a t)"),
                                           g.const("q_scale").broadcast_to([P, SEQ]), ALU.mult).then_inc(*q_staged.done("q"))

            @block.tensor
            def _(pe):
                def rule(ln, i, pair):
                    kvh = 2 * pair + ln.s
                    V = slice(kvh * HD, (kvh + 1) * HD)
                    for t in range(TILES):
                        n = (t + 1) * P
                        q_t = q[ln.R, t * P:(t + 1) * P]
                        if t == 0:
                            pe.wait_ge(q_staged.sem, q_staged.past("q", i))
                        pe.wait_ge(ln.act.sem, before(ln.act, "out", t, i))
                        for a, K in enumerate((SLC_K, WIN_K)):
                            pe.matmul(ln.scores[:, a, 0:n], q_t, g.proj[ln.R, K + pair, 0:n], start=True, stop=True)
                        pe.matmul(ln.out[:, 128:128 + P_BLOCKS], q_t, g.kc[ln.R, pair, :], start=True, stop=True
                                  ).then_inc(*ln.pe.done(f"scores {t}"))
                        yield
                        pe.wait_ge(ln.dve.sem, ln.dve.past(f"scale {t}", i))
                        for a, name in enumerate(("slc", "win")):
                            if a:
                                pe.wait_ge(ln.act.sem, ln.act.past(f"slc turned {t}", i))
                            for b in range(t + 1):
                                mm = pe.transpose(ln.turn[:, b * P:(b + 1) * P], ln.p[:, a, b * P:(b + 1) * P], ident)
                            if a == 0:
                                mm = pe.transpose(ln.out[0:P_BLOCKS, 256:384], ln.sc[:, :], ident)
                            mm.then_inc(*ln.pe.done(f"turn {name} {t}"))
                            yield
                        pe.wait_ge(ln.act.sem, ln.act.past(f"win turned {t}", i))
                        pe.wait_ge(ln.dve.sem, ln.dve.past(f"cmp turned {t}", i))
                        out = ln.out[ln.R, 0:P]
                        pe.matmul(out, g.vc[:, V], ln.pcT[:, :], start=True, stop=False)
                        for a in range(2):
                            for b in range(t + 1):
                                mm = pe.matmul(out, g.v_rows[:, a, b, V], ln.pT[:, a, b * P:(b + 1) * P],
                                               start=False, stop=(a == 1 and b == t))
                        mm.then_inc(*ln.pe.done(f"out {t}"))
                        yield

                for ln in lanes:
                    ln.pe.credit(pe)
                for pair in range(2):
                    with pe.Fori(pair * GROUP, (pair + 1) * GROUP) as i:
                        alternate(rule, i, pair)

            @block.vector
            def _(dve):
                def rule(ln, i, pair):
                    for t in range(TILES):
                        n = (t + 1) * P
                        blocks = slice(t * P_BLOCKS, (t + 1) * P_BLOCKS)
                        d = ln.dve

                        def after(name):
                            dve.wait_ge(d.sem, d.past(f"{name} {t}", i))
                        dve.wait_ge(ln.pe.sem, ln.pe.past(f"scores {t}", i))
                        own = ln.scores[:, :, t * P:n]
                        dve.tensor_tensor(own, own, g.const("causal_neg").unsqueeze(1).broadcast_to([P, 2, P]),
                                          ALU.add).then_inc(*d.done(f"mask {t}"))
                        dve.tensor_tensor(ln.sc[:, :], ln.out[:, 128:128 + P_BLOCKS], g.const("cmp_neg")[:, blocks],
                                          ALU.add).then_inc(*d.done(f"mask cmp {t}"))
                        after("mask")
                        dve.tensor_reduce(ln.neg_max[:, 1:3], ln.scores[:, :, 0:n], AX_X, ALU.max, negate=True
                                          ).then_inc(*d.done(f"max {t}"))
                        after("mask cmp")
                        dve.tensor_reduce(ln.neg_max[:, 0:1], ln.sc[:, :], AX_X, ALU.max, negate=True
                                          ).then_inc(*d.done(f"max cmp {t}"))
                        yield
                        dve.wait_ge(ln.act.sem, ln.act.past(f"exp {t}", i))
                        dve.tensor_tensor(ln.sc[:, :], ln.sc[:, :], g.const("cmp_seen")[:, blocks], ALU.mult
                                          ).then_inc(*d.done(f"seen {t}"))
                        after("seen")
                        dve.tensor_reduce(ln.sums[:, 0:1], ln.sc[:, :], AX_X, ALU.add).then_inc(*d.done(f"cmp sum {t}"))
                        after("cmp sum")
                        dve.tensor_scalar(ln.sums[:, :], ln.sums[:, :], 1e-30, None, ALU.max
                                          ).then_inc(*d.done(f"floor {t}"))
                        after("floor")
                        dve.reciprocal(ln.sums[:, :], ln.sums[:, :]).then_inc(*d.done(f"inverse {t}"))
                        after("inverse")
                        head = bass.ds(i + GROUP * (pair + ln.s), 1)
                        dve.tensor_tensor(ln.sums[:, :], ln.sums[:, :],
                                          g.gates[:, t, head, :].rearrange("p a r -> p (a r)"), ALU.mult
                                          ).then_inc(*d.done(f"gate {t}"))
                        after("gate")
                        for a in range(2):
                            dve.tensor_scalar(ln.p[:, a, 0:n], ln.p[:, a, 0:n], ln.sums[:, a + 1:a + 2], None, ALU.mult)
                        dve.tensor_scalar(ln.sc[:, :], ln.sc[:, :], ln.sums[:, 0:1], None, ALU.mult
                                          ).then_inc(*d.done(f"scale {t}"))
                        yield
                        dve.wait_ge(ln.pe.sem, ln.pe.past(f"turn slc {t}", i))
                        dve.tensor_copy(ln.pcT[:, :], ln.out[0:P_BLOCKS, 256:384]
                                        ).then_inc(*d.done(f"cmp turned {t}"))
                        yield

                for ln in lanes:
                    ln.dve.credit(dve)
                for pair in range(2):
                    with dve.Fori(pair * GROUP, (pair + 1) * GROUP) as i:
                        alternate(rule, i, pair)

            @block.scalar
            def _(act):
                def rule(ln, i, pair):
                    for t in range(TILES):
                        n = (t + 1) * P
                        a_ = ln.act
                        act.wait_ge(ln.dve.sem, ln.dve.past(f"max cmp {t}", i))
                        act.wait_ge(ln.pe.sem, before(ln.pe, "turn win", t, i))
                        for a in range(2):
                            act.activation(ln.p[:, a, 0:n], ln.scores[:, a, 0:n], ACT.Exp,
                                           bias=ln.neg_max[:, a + 1:a + 2], accum_out=ln.sums[:, a + 1:a + 2])
                        act.activation(ln.sc[:, :], ln.sc[:, :], ACT.Exp, bias=ln.neg_max[:, 0:1]
                                       ).then_inc(*a_.done(f"exp {t}"))
                        yield
                        for a, name in enumerate(("slc", "win")):
                            act.wait_ge(ln.pe.sem, ln.pe.past(f"turn {name} {t}", i))
                            act.activation(ln.pT[:, a, 0:n], ln.turn[:, 0:n], ACT.Copy
                                           ).then_inc(*a_.done(f"{name} turned {t}"))
                            yield
                        act.wait_ge(ln.pe.sem, ln.pe.past(f"out {t}", i))
                        act.activation(g.attT[ln.R, bass.ds(i, 1), t * P:n].rearrange("p a t -> p (a t)"),
                                       ln.out[ln.R, 0:P], ACT.Copy).then_inc(*a_.done(f"out {t}"))
                        yield

                for ln in lanes:
                    ln.act.credit(act)
                for pair in range(2):
                    with act.Fori(pair * GROUP, (pair + 1) * GROUP) as i:
                        alternate(rule, i, pair)


def compress_stage(nc, g):
    per = 8
    with Stage(nc, "cmp") as st:
        raw = [st.sb(f"raw{s}", [P, per, 4 * PAGE]) for s in range(2)]
        table = st.sb("table", [1, DEC_BATCH * N_PAGES], I32)
        loaded = [st.sem(f"loaded{s}") for s in range(2)]
        table_in = st.sem("table_in")
        dve_s = [st.steps(f"dve{s}", ["summed"]) for s in range(2)]
        rounds = DEC_BATCH * N_PAGES // per // 2
        with st.block() as block:
            @block.sync
            def _(sp):
                sp.dma_start(table[:, :], g.d["page_table"]).then_inc(table_in, 16)
                sp.wait_ge(table_in, 16)
                with sp.Fori(0, rounds) as i:
                    for s in range(2):
                        sp.wait_ge(dve_s[s].sem, dve_s[s].past("summed", i - 1))
                        for n in range(per):
                            page = sp.value_load(table[0:1, bass.ds((2 * i + s) * per + n, 1)], min_val=0,
                                                 max_val=N_POOL - 1)
                            sp.dma_start(raw[s][:, n, :],
                                         g.d["cmp_pool"][bass.ds(page, 1)].rearrange("g p n -> (g p) n")
                                         ).then_inc(loaded[s], 16)

            @block.vector
            def _(dve):
                for s in range(2):
                    dve_s[s].credit(dve)
                with dve.Fori(0, rounds) as i:
                    for s in range(2):
                        dve.wait_ge(loaded[s], 16 * per * (i + 1))
                        at = bass.ds((2 * i + s) * per, per)
                        dve.tensor_reduce(g.past_c[:, at, :].rearrange("p g c -> p (g c)"),
                                          raw[s][:, :, :].rearrange("p g (c t) -> p (g c) t", t=CMP), AX_X, ALU.add
                                          ).then_inc(*dve_s[s].done("summed"))


def compress_norm_stage(nc, g):
    with Stage(nc, "cnorm") as st:
        sq = st.sb("sq", [P, 4, 512])
        root = st.sb("root", [P, 4, 512])
        v = st.sb("v", [P, 2, DEC_BATCH * BLOCKS])
        total = st.ps("total", (P, 4, 512))
        turn = [st.ps(f"turn{s}") for s in range(2)]
        squared, summed, logged, rooted = st.sem("squared"), st.sem("summed"), st.sem("logged"), st.sem("rooted")
        averaged, turned, turn_out = st.sem("averaged"), st.sem("turned"), st.sem("turn_out")
        src = g.past_c[:, :, :].rearrange("p g (a c) -> p g a c", a=4)
        per = 64 * 8
        with st.block() as block:
            @block.vector
            def _(dve):
                for pair in range(2):
                    dve.tensor_scalar(src[:, :, pair, :], src[:, :, pair, :], 1.0 / CMP, None, ALU.mult)
                    ins = dve.tensor_scalar(v[:, pair, :].rearrange("p (g c) -> p g c", c=4), src[:, :, 2 + pair, :],
                                            1.0 / CMP, None, ALU.mult)
                ins.then_inc(averaged, 1)
                for n in range(4):
                    dve.wait_ge(rooted, n + 1)
                    dve.wait_ge(averaged, 1)
                    part = src[:, 64 * n:64 * (n + 1), 0:2, :]
                    for pair in range(2):
                        dve.scalar_tensor_tensor(
                            out=part[:, :, pair, :], in0=part[:, :, pair, :], scalar=g.gains[:, K_GAIN:K_GAIN + 1],
                            in1=root[:, n, :].rearrange("p (g a c) -> p g a c", a=2, c=4)[:, :, pair, :],
                            op0=ALU.mult, op1=ALU.mult)
                for b in range(DEC_BATCH):
                    for pair in range(2):
                        n = 2 * b + pair
                        dve.wait_ge(turned, n + 1)
                        dve.tensor_copy(g.vc_past[:, b, pair * P:(pair + 1) * P], turn[n % 2][:, 0:P]
                                        ).then_inc(turn_out, 1)

            @block.scalar
            def _(act):
                act.wait_ge(averaged, 1)
                for n in range(4):
                    act.activation(sq[:, n, :].rearrange("p (g a c) -> p g (a c)", a=2, c=4),
                                   src[:, 64 * n:64 * (n + 1), 0:2, :].rearrange("p g a c -> p g (a c)"), ACT.Square
                                   ).then_inc(squared, 1)
                for n in range(4):
                    act.wait_ge(summed, n + 1)
                    act.activation(root[:, n, :], total[:, n, :], ACT.Ln, scale=1.0 / HD, bias=g.eps[:, 0:1]
                                   ).then_inc(logged, 1)
                    act.wait_ge(logged, n + 1)
                    act.activation(root[:, n, :], root[:, n, :], ACT.Exp, scale=-0.5).then_inc(rooted, 1)

            @block.tensor
            def _(pe):
                for n in range(4):
                    pe.wait_ge(squared, n + 1)
                    pe.matmul(total[:, n, :], g.const("head_ones"), sq[:, n, :], start=True, stop=True
                              ).then_inc(summed, 1)
                pe.wait_ge(averaged, 1)
                for b in range(DEC_BATCH):
                    for pair in range(2):
                        n = 2 * b + pair
                        if n >= 2:
                            pe.wait_ge(turn_out, n - 1)
                        pe.transpose(turn[n % 2][:, 0:P],
                                     v[:, pair, b * BLOCKS:(b + 1) * BLOCKS], g.const("ident")
                                     ).then_inc(turned, 1)


CHUNKS_KV = 8
PAGES_C = N_PAGES // CHUNKS_KV
KEYS_C = PAGES_C * PAGE
SLC_END = PAST + NEW
WIN_END = SLC_END + WINDOW
KEYS = WIN_END + NEW
SMP_GROUPS = 4
PAGES_G = N_PAGES // SMP_GROUPS


def sample_attention_stage(nc, g):
    n_sel = PAST // SEL + 1
    assert TOP_N == 16
    with Stage(nc, "satt") as st:
        kv = st.sb("kv", [P, CHUNKS_KV, PAGES_C, 4 * P])
        win = st.sb("win", [P, 4, 4 * P])
        qb = st.sb("qb", [P, 2, NEW])
        kc = st.sb("kc", [P, 2, BLOCKS])
        vc = st.sb("vc", [P, KVH * HD])
        s_all = st.sb("s_all", [ROWS, KEYS])
        pc = st.sb("pc", [ROWS, BLOCKS])
        pT = st.sb("pT", [P, N_PAGES + 7, ROWS])
        table = st.sb("table", [1, DEC_BATCH * N_PAGES], I32)
        score = [st.sb(f"score{n}", [ROWS, n_sel]) for n in range(3)]
        best = [st.sb(f"best{n}", [ROWS, 8]) for n in range(2)]
        unselected = st.sb("unselected", [ROWS, n_sel])
        neg_max = st.sb("neg_max", [ROWS, 3])
        sums = st.sb("sums", [ROWS, 3])
        out = st.sb("out", [ROWS, KVH * HD])
        ps = [st.ps(f"scores{n}") for n in range(2)]
        ps_cmp, ps_new = st.ps("cmp"), st.ps("new")
        ps_turn = [st.ps(f"turn{n}") for n in range(2)]
        ps_out, ps_end = st.ps("out_acc"), st.ps("end")
        kv_in = [st.sem(f"kv_in{c}") for c in range(CHUNKS_KV)]
        win_in, table_in, cleared = st.sem("win_in"), st.sem("table_in"), st.sem("cleared")
        groups = range(SMP_GROUPS + 1)
        pe_s = st.steps("pe", ["cmp scores", "scores 0", "scores 1", "importance"]
                        + [f"scores {c}" for c in range(2, CHUNKS_KV)] + ["new scores", "win scores"]
                        + [f"{x} {n}" for n in groups for x in ("turn", "out")] + ["end"])
        dve_s = st.steps("dve", ["cmp max", "cmp floor", "cmp inverse", "cmp p", "imp", "score", "top a", "out a",
                                 "top b", "out b", "unselected"]
                         + [f"masked {c}" for c in range(CHUNKS_KV)]
                         + ["new masked", "win masked", "slc max", "win max", "floor", "inverse", "gate",
                            "cmp scaled", "slc scaled", "win scaled"] + ["placed"])
        act_s = st.steps("act", ["cmp exp", "slc exp", "win exp"] + [f"turned {n}" for n in groups] + ["out"])
        pool_s = st.steps("pool", ["staged"])
        NEW_SLC, NEW_WIN = N_PAGES + 5, N_PAGES + 6
        CMP_AT = N_PAGES + 4
        ident = g.const("ident")

        with st.block() as block:
            @block.sync
            def _(sp):
                sp.dma_start(table[:, :], g.d["page_table"]).then_inc(table_in, 16)
                sp.wait_ge(table_in, 16)
                with sp.Fori(0, DEC_BATCH) as i:
                    for c in range(CHUNKS_KV):
                        sp.wait_ge(pe_s.sem, pe_s.past(f"out {c * PAGES_C // PAGES_G}", i - 1))
                        for n in range(PAGES_C):
                            page = sp.value_load(table[0:1, bass.ds(i * N_PAGES + c * PAGES_C + n, 1)], min_val=0,
                                                 max_val=N_POOL - 1)
                            sp.dma_start(kv[:, c, n, :], g.d["slc_pool"][bass.ds(page, 1)].rearrange("g p n -> (g p) n")
                                         ).then_inc(kv_in[c], 16)
                    sp.wait_ge(pe_s.sem, pe_s.past(f"out {SMP_GROUPS}", i - 1))
                    sp.dma_start(win[:, :, :], g.d["win"][bass.ds(i, 1)].rearrange("b p a n -> (b p) a n")
                                 ).then_inc(win_in, 16)

            @block.gpsimd
            def _(pool):
                pool_s.credit(pool)
                with pool.Fori(0, DEC_BATCH) as i:
                    pool.wait_ge(pe_s.sem, pe_s.past(f"out {SMP_GROUPS}", i - 1))
                    pool.tensor_copy(qb[:, :, :], g.qb[:, :, bass.ds(i, 1), :].rearrange("p a b n -> p a (b n)"))
                    pages = g.past_c[:, bass.ds(i * N_PAGES, N_PAGES), :]
                    for pair in range(2):
                        pool.tensor_copy(kc[:, pair, :].rearrange("p (g c) -> p g c", c=PAGE // CMP),
                                         pages[:, :, 4 * pair:4 * pair + 4])
                    pool.tensor_copy(vc[:, :], g.vc_past[:, bass.ds(i, 1), :].rearrange("p a n -> p (a n)")
                                     ).then_inc(*pool_s.done("staged"))

            @block.tensor
            def _(pe):
                def by_pair(out_, rhs):
                    for pair in range(2):
                        mm = pe.matmul(out_[NEW * pair:NEW * (pair + 1), :], qb[:, pair, :], rhs(pair),
                                       start=True, stop=True)
                    return mm

                def chunk_scores(c, i):
                    pe.wait_ge(kv_in[c], 16 * PAGES_C * (i + 1))
                    if c >= 2:
                        pe.wait_ge(dve_s.sem, dve_s.past(f"masked {c - 2}", i))
                    by_pair(ps[c % 2][0:ROWS, :], lambda pair: kv[:, c, :, pair * P:(pair + 1) * P]
                            ).then_inc(*pe_s.done(f"scores {c}"))

                pe_s.credit(pe)
                with pe.Fori(0, DEC_BATCH) as i:
                    pe.wait_ge(pool_s.sem, pool_s.past("staged", i))
                    by_pair(ps_cmp[0:ROWS, 0:BLOCKS], lambda pair: kc[:, pair, :]).then_inc(*pe_s.done("cmp scores"))
                    pe.wait_ge(dve_s.sem, dve_s.past("win masked", i - 1))
                    chunk_scores(0, i)
                    chunk_scores(1, i)
                    pe.wait_ge(dve_s.sem, dve_s.past("cmp p", i))
                    pe.nop(nofuse=True)
                    pe.matmul(ps_cmp[0:ROWS, BLOCKS:2 * BLOCKS], g.const("group_sum", ROWS)[:, 0:ROWS], pc[:, :],
                              start=True, stop=True).then_inc(*pe_s.done("importance"))
                    for c in range(2, CHUNKS_KV):
                        chunk_scores(c, i)
                    by_pair(ps_new[0:ROWS, 0:NEW], lambda pair: g.k_new[:, 0, pair, :])
                    by_pair(ps_new[0:ROWS, NEW:2 * NEW], lambda pair: g.k_new[:, 1, pair, :]
                            ).then_inc(*pe_s.done("new scores"))
                    pe.wait_ge(win_in, 16 * (i + 1))
                    pe.wait_ge(dve_s.sem, dve_s.past(f"masked {CHUNKS_KV - 2}", i))
                    by_pair(ps[0][0:ROWS, :], lambda pair: win[:, pair, :]).then_inc(*pe_s.done("win scores"))
                    small = g.const("ident", ROWS)[:, 0:ROWS]
                    for n in groups:
                        pe.wait_ge(dve_s.sem, dve_s.past("win scaled" if n == SMP_GROUPS else "slc scaled", i))
                        if n >= 2:
                            pe.wait_ge(act_s.sem, act_s.past(f"turned {n - 2}", i))
                        pe.nop(nofuse=True)
                        turn = ps_turn[n % 2]

                        def turned(slot, keys, src):
                            return pe.transpose(turn[0:keys, slot * ROWS:(slot + 1) * ROWS], src, small)
                        if n < SMP_GROUPS:
                            for m in range(PAGES_G):
                                at = (n * PAGES_G + m) * PAGE
                                mm = turned(m, P, s_all[:, at:at + PAGE])
                        else:
                            for m in range(WINDOW // P):
                                at = SLC_END + m * P
                                turned(m, P, s_all[:, at:at + P])
                            turned(4, P, pc[:, :])
                            turned(5, NEW, s_all[:, PAST:SLC_END])
                            mm = turned(6, NEW, s_all[:, WIN_END:KEYS])
                        mm.then_inc(*pe_s.done(f"turn {n}"))
                        pe.wait_ge(act_s.sem, act_s.past(f"turned {n}", i))
                        acc = ps_out[0:ROWS, 0:KVH * HD]
                        if n < SMP_GROUPS:
                            for m in range(PAGES_G):
                                page = n * PAGES_G + m
                                mm = pe.matmul(acc, pT[:, page, :], kv[:, page // PAGES_C, page % PAGES_C, 2 * P:4 * P],
                                               start=(page == 0), stop=False)
                        else:
                            for m in range(WINDOW // P):
                                pe.matmul(acc, pT[:, N_PAGES + m, :],
                                          win[:, 2 + m // 2, (m % 2) * 256:(m % 2 + 1) * 256], start=False, stop=False)
                            pe.matmul(acc, pT[:, CMP_AT, :], vc[:, :], start=False, stop=False)
                            pe.matmul(acc, pT[0:NEW, NEW_SLC, :], g.v_new[:, 0, :], start=False, stop=False)
                            mm = pe.matmul(acc, pT[0:NEW, NEW_WIN, :], g.v_new[:, 1, :], start=False, stop=True)
                        mm.then_inc(*pe_s.done(f"out {n}"))
                    pe.wait_ge(act_s.sem, act_s.past("out", i))
                    pe.nop(nofuse=True)
                    for pair in range(2):
                        mm = pe.transpose(ps_end[:, pair * ROWS:(pair + 1) * ROWS], out[:, pair * P:(pair + 1) * P], small)
                    mm.then_inc(*pe_s.done("end"))

            @block.scalar
            def _(act):
                act_s.credit(act)
                with act.Fori(0, DEC_BATCH) as i:
                    act.wait_ge(dve_s.sem, dve_s.past("cmp max", i))
                    act.wait_ge(pe_s.sem, pe_s.past(f"turn {SMP_GROUPS}", i - 1))
                    act.activation(pc[:, :], ps_cmp[0:ROWS, 0:BLOCKS], ACT.Exp, bias=neg_max[:, 0:1],
                                   accum_out=sums[:, 0:1]).then_inc(*act_s.done("cmp exp"))
                    act.wait_ge(dve_s.sem, dve_s.past("slc max", i))
                    x = s_all[:, 0:SLC_END]
                    act.activation(x, x, ACT.Exp, bias=neg_max[:, 1:2], accum_out=sums[:, 1:2]
                                   ).then_inc(*act_s.done("slc exp"))
                    act.wait_ge(dve_s.sem, dve_s.past("win max", i))
                    x = s_all[:, SLC_END:KEYS]
                    act.activation(x, x, ACT.Exp, bias=neg_max[:, 2:3], accum_out=sums[:, 2:3]
                                   ).then_inc(*act_s.done("win exp"))
                    for n in groups:
                        act.wait_ge(pe_s.sem, pe_s.past(f"turn {n}", i))
                        at = n * PAGES_G
                        if n < SMP_GROUPS:
                            act.activation(pT[:, at:at + PAGES_G, :].rearrange("p g r -> p (g r)"), ps_turn[n % 2][:, :],
                                           ACT.Copy).then_inc(*act_s.done(f"turned {n}"))
                        else:
                            act.activation(pT[:, at:at + 5, :].rearrange("p g r -> p (g r)"),
                                           ps_turn[n % 2][:, 0:5 * ROWS], ACT.Copy)
                            act.activation(pT[0:NEW, at + 5:at + 7, :].rearrange("p g r -> p (g r)"),
                                           ps_turn[n % 2][0:NEW, 5 * ROWS:7 * ROWS], ACT.Copy
                                           ).then_inc(*act_s.done(f"turned {n}"))
                    act.wait_ge(pe_s.sem, pe_s.past(f"out {SMP_GROUPS}", i))
                    act.activation(out[:, :], ps_out[0:ROWS, 0:KVH * HD], ACT.Copy).then_inc(*act_s.done("out"))

            @block.vector
            def _(dve):
                def own(name, i):
                    dve.wait_ge(dve_s.sem, dve_s.past(name, i))
                rows = g.const("group_sum", ROWS)
                dve_s.credit(dve)
                dve.memset(score[0][:, n_sel - 1:n_sel], SEL_BIG).then_inc(cleared, 1)
                dve.wait_ge(cleared, 1)
                with dve.Fori(0, DEC_BATCH) as i:
                    dve.wait_ge(pe_s.sem, pe_s.past("cmp scores", i))
                    dve.tensor_reduce(neg_max[:, 0:1], ps_cmp[0:ROWS, 0:BLOCKS], AX_X, ALU.max, negate=True
                                      ).then_inc(*dve_s.done("cmp max"))
                    dve.wait_ge(act_s.sem, act_s.past("cmp exp", i))
                    dve.tensor_scalar(sums[:, 0:1], sums[:, 0:1], 1e-30, None, ALU.max
                                      ).then_inc(*dve_s.done("cmp floor"))
                    own("cmp floor", i)
                    dve.reciprocal(sums[:, 0:1], sums[:, 0:1]).then_inc(*dve_s.done("cmp inverse"))
                    own("cmp inverse", i)
                    dve.tensor_scalar(pc[:, :], pc[:, :], sums[:, 0:1], None, ALU.mult
                                      ).then_inc(*dve_s.done("cmp p"))
                    dve.wait_ge(pe_s.sem, pe_s.past("importance", i))
                    past = slice(0, n_sel - 1)
                    dve.tensor_reduce(score[1][:, past], ps_cmp[0:ROWS, BLOCKS:2 * BLOCKS].rearrange(
                        "r (s c) -> r s c", c=SEL // CMP), AX_X, ALU.add).then_inc(*dve_s.done("imp"))
                    own("imp", i)
                    dve.tensor_tensor(score[0][:, past], score[1][:, past], g.const("forced", ROWS), ALU.max
                                      ).then_inc(*dve_s.done("score"))
                    for n, name in enumerate(("a", "b")):
                        own("score" if n == 0 else "out a", i)
                        dve.nop(nofuse=True)
                        dve.max(best[n][:, :], score[n][:, :]).then_inc(*dve_s.done(f"top {name}"))
                        own(f"top {name}", i)
                        dve.nop(nofuse=True)
                        dve.match_replace(score[n + 1][:, :], best[n][:, :], score[n][:, :], NEG
                                          ).then_inc(*dve_s.done(f"out {name}"))
                    own("out b", i)
                    dve.tensor_scalar(unselected[:, :], score[2][:, :], NEG / 10, NEG, ALU.is_gt, ALU.mult
                                      ).then_inc(*dve_s.done("unselected"))
                    own("unselected", i)
                    per = KEYS_C // SEL
                    for c in range(CHUNKS_KV):
                        dve.wait_ge(pe_s.sem, pe_s.past(f"scores {c}", i))
                        dve.tensor_tensor(
                            s_all[:, c * KEYS_C:(c + 1) * KEYS_C].rearrange("r (s k) -> r s k", k=SEL),
                            ps[c % 2][0:ROWS, :].rearrange("r (s k) -> r s k", k=SEL),
                            unselected[:, c * per:(c + 1) * per].unsqueeze(2).broadcast_to([ROWS, per, SEL]), ALU.add
                        ).then_inc(*dve_s.done(f"masked {c}"))
                    dve.wait_ge(pe_s.sem, pe_s.past("new scores", i))
                    new_neg = g.const("new_neg", ROWS).rearrange("r (b k) -> r b k", b=DEC_BATCH)
                    new_neg = new_neg[:, bass.ds(i, 1), :].rearrange("r b k -> r (b k)")
                    dve.tensor_tensor(s_all[:, PAST:SLC_END], ps_new[0:ROWS, 0:NEW], new_neg, ALU.add)
                    dve.tensor_tensor(s_all[:, WIN_END:KEYS], ps_new[0:ROWS, NEW:2 * NEW], new_neg, ALU.add
                                      ).then_inc(*dve_s.done("new masked"))
                    dve.wait_ge(pe_s.sem, pe_s.past("win scores", i))
                    dve.tensor_tensor(s_all[:, SLC_END:WIN_END], ps[0][0:ROWS, :], g.const("win_neg", ROWS), ALU.add
                                      ).then_inc(*dve_s.done("win masked"))
                    own("new masked", i)
                    dve.tensor_reduce(neg_max[:, 1:2], s_all[:, 0:SLC_END], AX_X, ALU.max, negate=True
                                      ).then_inc(*dve_s.done("slc max"))
                    own("win masked", i)
                    dve.tensor_reduce(neg_max[:, 2:3], s_all[:, SLC_END:KEYS], AX_X, ALU.max, negate=True
                                      ).then_inc(*dve_s.done("win max"))
                    dve.wait_ge(act_s.sem, act_s.past("win exp", i))
                    dve.tensor_scalar(sums[:, 1:3], sums[:, 1:3], 1e-30, None, ALU.max).then_inc(*dve_s.done("floor"))
                    own("floor", i)
                    dve.reciprocal(sums[:, 1:3], sums[:, 1:3]).then_inc(*dve_s.done("inverse"))
                    gate = g.row_gates[:, bass.ds(i, 1), :].rearrange("r b n -> r (b n)")
                    own("inverse", i)
                    dve.tensor_tensor(sums[:, 1:3], sums[:, 1:3], gate[:, 1:3], ALU.mult
                                      ).then_inc(*dve_s.done("gate"))
                    dve.tensor_scalar(pc[:, :], pc[:, :], gate[:, 0:1], None, ALU.mult
                                      ).then_inc(*dve_s.done("cmp scaled"))
                    own("gate", i)
                    dve.tensor_scalar(s_all[:, 0:SLC_END], s_all[:, 0:SLC_END], sums[:, 1:2], None, ALU.mult
                                      ).then_inc(*dve_s.done("slc scaled"))
                    dve.tensor_scalar(s_all[:, SLC_END:KEYS], s_all[:, SLC_END:KEYS], sums[:, 2:3], None, ALU.mult
                                      ).then_inc(*dve_s.done("win scaled"))
                    dve.wait_ge(pe_s.sem, pe_s.past("end", i))
                    for pair in range(2):
                        for half in range(2):
                            R = slice(HD * half, HD * (half + 1))
                            at = pair * ROWS + 16 * (2 * pair + half)
                            ins = dve.tensor_copy(
                                g.attT[R, pair * GROUP:(pair + 1) * GROUP, bass.ds(i * DEC_SEQ + SEQ, DEC_SEQ)],
                                ps_end[R, at:at + 16].rearrange("p (j t) -> p j t", t=DEC_SEQ))
                    ins.then_inc(*dve_s.done("placed"))


def nsa(nc, g):
    with ExitStack() as ctx:
        def sb(stack, name, shape):
            return stack.enter_context(nc.sbuf_tensor("nsa_" + name, shape, F32))
        g.attT = sb(ctx, "attT", [P, KT, TOKENS])
        with ExitStack() as smp:
            g.past_c = sb(smp, "past_c", [P, DEC_BATCH * N_PAGES, 4 * PAGE // CMP])
            g.vc_past = sb(smp, "vc_past", [P, DEC_BATCH, KVH * HD])
            g.row_gates = sb(smp, "row_gates", [ROWS, DEC_BATCH, 3])
            g.qb = sb(smp, "qb", [P, 2, DEC_BATCH, NEW])
            g.k_new = sb(smp, "k_new", [P, 2, 2, NEW])
            g.v_new = sb(smp, "v_new", [NEW, 2, KVH * HD])
            compress_stage(nc, g)
            compress_norm_stage(nc, g)
            with ExitStack() as prompt:
                g.proj = sb(prompt, "proj", [P, NSA_TILES, TOKENS])
                g.gates = sb(prompt, "gates", [P, TILES, NSA_HEADS, 3])
                g.v_rows = sb(prompt, "v_rows", [P, 2, TILES, KVH * HD])
                g.kc = sb(prompt, "kc", [P, 2, P_BLOCKS])
                g.vc = sb(prompt, "vc", [P_BLOCKS, KVH * HD])
                with nc.sbuf_tensor("nsa_h", [P, KT, TOKENS], F32) as g.hT:
                    rms_norm_stage(nc, g, "norm1", LN_MIX + KT)
                    nsa_project_stage(nc, g)
                nsa_norm_stage(nc, g)
                prompt_attention_stage(nc, g)
            sample_attention_stage(nc, g)
        out_project_stage(nc, g, "nsa_out", g.d["nsa_wo"], g.attT)


def store_stage(nc, g):
    with Stage(nc, "store") as st:
        stored = st.sem("stored")
        with st.block() as block:
            @block.sync
            def _(sp):
                sp.dma_start(g.d["y"], g.xT[:, :, :]).then_inc(stored, 16)
                sp.wait_ge(stored, 16)


class Globals:

    def const(self, name, rows=P):
        at, n = CONST_AT[name]
        return self.consts[0:rows, at:at + n]


LN_MIX, LN_FFN, O_GAIN, Q_GAIN, K_GAIN, GAINS = 0, 16, 32, 33, 34, 35


def decoder(nc, d, stop=99):
    g = Globals()
    g.d = d
    with ExitStack() as ctx:
        def sb(name, shape, dt=F32):
            return ctx.enter_context(nc.sbuf_tensor(name, shape, dt))

        g.consts = sb("consts", [P, CONST_W])
        g.gains = sb("gains_sb", [P, GAINS])
        g.eps = sb("eps", [P, 1])
        g.xT = sb("xT", [P, KT, TOKENS])
        eps_set = ctx.enter_context(nc.semaphore("eps_set"))
        with nc.Block(no_gpsimd_drain=True) as block:
            @block.vector
            def _(dve):
                dve.memset(g.eps[:, :], EPS).then_inc(eps_set, 1)
                dve.wait_ge(eps_set, 1)
        load_inputs(nc, g)
        with ExitStack() as gdn:
            g.zT = gdn.enter_context(nc.sbuf_tensor("zT", [P, HEADS, TOKENS], F32))
            with ExitStack() as mixer:
                g.qkv = mixer.enter_context(nc.sbuf_tensor("qkv", [P, CONV_TILES, TOKENS], F32))
                def gate(name, shape):
                    return mixer.enter_context(nc.sbuf_tensor("gate_" + name, shape, F32))
                g.gate_g, g.beta, g.G, g.eG, g.tail = (
                    gate(n, [P, TILES + 1, HEADS]) for n in ("g", "beta", "G", "eG", "tail"))
                g.e_chunk = gate("e_chunk", [P, 2 * TILES, HEADS])
                g.e_batch = gate("e_batch", [P, DEC_BATCH, HEADS])
                with nc.sbuf_tensor("h_gdn", [P, KT, TOKENS], F32) as g.hT:
                    rms_norm_stage(nc, g, "norm0", LN_MIX)
                    gdn_project_stage(nc, g)
                    if stop == 1:
                        return debug_out(nc, g, {"hT": g.hT, "qkv": g.qkv, "zT": g.zT})
                    gdn_gates_stage(nc, g)
                gdn_heads_stage(nc, g)
            out_project_stage(nc, g, "gdn_out", g.d["gdn_wo"], g.zT)
        if stop == 2:
            return debug_out(nc, g, {"xT": g.xT})
        if stop != -4:
            moe(nc, g, "moe0", 0, LN_FFN)
        if stop == 3:
            return debug_out(nc, g, {"xT": g.xT})
        nsa(nc, g)
        if stop == 4:
            return debug_out(nc, g, {"xT": g.xT})
        moe(nc, g, "moe1", 1, LN_FFN + KT)
        store_stage(nc, g)


def debug_out(nc, g, what):
    for n, t in what.items():
        t_d = nc.dram_tensor("dbg_" + n, list(t.shape), F32, kind="ExternalOutput").ap()
        s = nc.semaphore("dbgs_" + n).__enter__()
        with nc.Block(no_gpsimd_drain=True) as block:
            @block.sync
            def _(sp):
                sp.dma_start(t_d, t[tuple(slice(None) for _ in t.shape)]).then_inc(s, 16)
                sp.wait_ge(s, 16)


def lay_out(i):
    a = {}
    def feature_major(x):
        return x.T.reshape(KT, P, -1).transpose(1, 0, 2)
    def tiles_of(w):
        return w.reshape(KT, P, -1, P).transpose(2, 1, 0, 3)
    a["consts"] = np.concatenate([CONSTANTS[k] for k in CONST_AT], 1)
    x = np.concatenate([i["x_prompt"].reshape(SEQ, D_MODEL), i["x_sample"].reshape(NEW, D_MODEL)])
    a["x"] = feature_major(x)
    cols = [i["ln_mix"].reshape(2 * KT, P).T, i["ln_ffn"].reshape(2 * KT, P).T, i["gdn_o_gain"][0][:, None],
            np.tile(i["nsa_q_gain"][0], 2)[:, None], np.tile(i["nsa_k_gain"][0], 2)[:, None]]
    a["gains"] = np.concatenate(cols, 1)
    w = i["gdn_w_in"][0]
    a["gdn_w"] = w[:, :4 * 1024].reshape(KT, P, 32, P).transpose(2, 1, 0, 3)
    a["gdn_w_ab"] = w[:, 4 * 1024:].reshape(KT, P, 2 * HEADS).transpose(1, 0, 2)
    a["gdn_rows"] = np.tile(np.stack([i["gdn_a_log"][0], i["gdn_dt_bias"][0]])[None], (P, 1, 1))
    a["gdn_S"] = i["state_gdn_S"][0].transpose(1, 2, 0, 3)
    a["gdn_wo"] = tiles_of(i["gdn_w_out"][0])
    a["router_w"] = np.concatenate([i["moe_w_grp"], i["moe_w_exp"]], 2).reshape(2, KT, P, -1).transpose(0, 2, 1, 3)
    a["router_b"] = np.tile(np.concatenate([i["moe_b_grp"], i["moe_b_exp"]], 1)[:, None, :], (1, P, 1))
    for x in ("w_gate", "w_up"):
        a[x] = i["moe_" + x].reshape(2, EXPERTS, KT, P, FF).transpose(0, 1, 3, 2, 4)
    a["w_down"] = i["moe_w_down"].reshape(2, EXPERTS, FF // P, P, D_MODEL).transpose(0, 1, 3, 2, 4)
    wn = i["nsa_w_in"][0]
    order = [8 * pair + 4 * half + j for pair in range(2) for j in range(GROUP) for half in range(2)]
    q_cols = (np.array(order)[:, None] * HD + np.arange(HD)).ravel()
    n_kv = NSA_HEADS * HD
    cols = np.concatenate([q_cols, np.arange(n_kv, n_kv + 12 * P)])
    a["nsa_w"] = wn[:, cols].reshape(KT, P, NSA_TILES, P).transpose(2, 1, 0, 3)
    a["nsa_w_gates"] = wn[:, n_kv + 12 * P:].reshape(KT, P, 3 * NSA_HEADS).transpose(1, 0, 2)
    a["nsa_wo"] = tiles_of(i["nsa_w_out"][0][q_cols])
    a["page_table"] = i["page_table"].reshape(1, -1).astype(np.int32)
    a["cmp_pool"] = i["cache_nsa_cmp_kv"][0].reshape(N_POOL, PAGE, 4, P).transpose(0, 3, 2, 1).reshape(N_POOL, P, -1)
    def keys_major(x):
        k = x[:, :, 0].reshape(len(x), -1, 2, P).transpose(0, 3, 2, 1).reshape(len(x), P, -1)
        v = x[:, :, 1].reshape(len(x), -1, P, KVH * HD).transpose(0, 2, 1, 3).reshape(len(x), P, -1)
        return np.concatenate([k, v], 2)
    a["slc_pool"] = keys_major(i["cache_nsa_slc_kv"][0])
    a["win"] = keys_major(i["cache_nsa_win_kv"][0]).reshape(DEC_BATCH, P, 4, 4 * P)
    a["taps"] = i["gdn_conv_w"][0].reshape(CONV, CONV_TILES, P).transpose(2, 1, 0)
    a["conv_prev"] = i["state_gdn_conv"][0].reshape(DEC_BATCH, CONV - 1, CONV_TILES, P).transpose(3, 2, 0, 1)
    return a


OUTPUTS = {"conv_out": (P, CONV_TILES, (1 + DEC_BATCH) * (CONV - 1)),
           "p_S": (HEADS, P, P), "s_S": (HEADS, P, DEC_BATCH, P),
           "kv_out": (P, 12, TOKENS), "win_out": (DEC_BATCH, P, 4, 4 * P), "y": (P, KT, TOKENS)}


def build(nc, arrays, stop=99):
    d = {}
    for name, a in arrays.items():
        d[name] = nc.dram_tensor("in_" + name, a.shape, mybir.dt.from_np(a.dtype), kind="ExternalInput").ap()
    for name, shape in OUTPUTS.items():
        d[name] = nc.dram_tensor("out_" + name, shape, F32, kind="ExternalOutput").ap()
    d["gate_scratch"] = nc.dram_tensor("gate_scratch", (NEW, 3 * NSA_HEADS), F32, kind="Internal").ap()
    decoder(nc, d, stop)
    return nc


def kernel(**inputs):
    import concourse.bacc as _bacc
    from concourse.bass_utils import run_bass_kernel_spmd

    arrays = {name: np.ascontiguousarray(a) for name, a in lay_out({n: np.asarray(a) for n, a in inputs.items()}).items()}
    nc = build(_bacc.Bacc("TRN2", target_bir_lowering=False, num_devices=1), arrays)
    r = run_bass_kernel_spmd(nc, [{"in_" + n: a for n, a in arrays.items()}], core_ids=[0]).results[0]

    def tokens_major(a):
        return a.transpose(2, 1, 0).reshape(a.shape[2], -1)
    y = tokens_major(r["out_y"])
    conv = r["out_conv_out"].transpose(2, 1, 0).reshape(1 + DEC_BATCH, CONV - 1, -1)
    kv = tokens_major(r["out_kv_out"]).reshape(TOKENS, 3, 2, KVH, HD)
    p_kv, s_kv = kv[:SEQ], kv[SEQ:].reshape(DEC_BATCH, DEC_SEQ, 3, 2, KVH, HD)
    win = r["out_win_out"].reshape(DEC_BATCH, P, 8, 2 * P)
    k_old = r["out_win_out"][:, :, 0:2, :].transpose(0, 3, 2, 1).reshape(DEC_BATCH, WINDOW, KVH, HD)
    v_old = win[:, :, 4:, :].transpose(0, 2, 1, 3).reshape(DEC_BATCH, WINDOW, KVH, HD)
    old = np.stack([k_old, v_old], 2)
    s_win = np.concatenate([old[:, DEC_SEQ:], s_kv[:, :, 2]], 1)
    out = (y[:SEQ].reshape(1, SEQ, D_MODEL), y[SEQ:].reshape(DEC_BATCH, DEC_SEQ, D_MODEL),
           r["out_p_S"][None, None], conv[None, :1], p_kv[None, None, :, 0], p_kv[None, None, :, 1],
           p_kv[None, None, :, 2], r["out_s_S"].transpose(2, 0, 1, 3)[None], conv[None, 1:],
           s_kv[None, :, :, 0], s_kv[None, :, :, 1], s_win[None])
    return tuple(np.ascontiguousarray(a) for a in out)
```

```python
from contextlib import ExitStack

import concourse.bass as bass
import numpy as np
from concourse import mybir

F32 = mybir.dt.float32
I32 = mybir.dt.int32
U32 = mybir.dt.uint32
ALU = mybir.AluOpType
ACT = mybir.ActivationFunctionType
AX_X = mybir.AxisListType.X

P = 128
D_MODEL = 1024
KT = D_MODEL // P
SEQ = 512
DEC_BATCH = 8
DEC_SEQ = 4
NEW = DEC_BATCH * DEC_SEQ
TOKENS = SEQ + NEW
HALF = TOKENS // 2
TILES = SEQ // P
PAST = 4096
PAGE = 128
N_PAGES = PAST // PAGE
N_POOL = DEC_BATCH * N_PAGES * 5 // 4
HEADS = 8
CHUNK = 64
CONV = 4
CONV_TILES = 3 * HEADS
NSA_HEADS = 16
KVH = 4
GROUP = NSA_HEADS // KVH
HD = 64
CMP = 32
SEL = 64
TOP_N = 16
WINDOW = 512
GROUPS = 4
PER_GROUP = 8
EXPERTS = 32
FF = 256
EPS = 1e-6
NEG = -1e30
SEL_BIG = 1e6

ENGINES = ("pe", "dve", "act", "pool", "sp")


class Steps:

    def __init__(self, nc, ctx, name, steps, ahead=1):
        self.sem = ctx.enter_context(nc.semaphore(name))
        self.ahead = ahead
        self.steps = steps
        self.at = 0

    def credit(self, eng):
        eng.sem_inc(self.sem, len(self.steps))

    def done(self, step):
        assert self.steps[self.at] == step, (self.steps[self.at], step)
        self.at = (self.at + 1) % len(self.steps)
        return self.sem, 1

    def past(self, step, i=0):
        return (i + self.ahead) * len(self.steps) + self.steps.index(step) + 1


def constants():
    r = np.arange(P)
    chunk = r // CHUNK
    c = {}
    c["ident"] = np.eye(P)
    c["ones"] = np.ones((P, P))
    c["head_ones"] = (r[:, None] // HD == r[None, :] // HD) * 1.0
    low = (r[:, None] <= r[None, :]) & (chunk[:, None] == chunk[None, :])
    c["tri"] = low * 1.0
    c["same"] = (chunk[:, None] == chunk[None, :]) * 1.0
    c["decay_neg"] = np.where(low, 0.0, NEG)
    c["half0"] = (chunk == 0)[:, None] * np.ones((1, P))
    c["half1"] = (chunk == 1)[:, None] * np.ones((1, P))
    for k in range(6):
        b = 1 << k
        m = (r[:, None] // (2 * b) == r[None, :] // (2 * b)) & (r[:, None] % (2 * b) < b) & (r[None, :] % (2 * b) >= b)
        c[f"level{k}"] = m * 1.0
    s = np.arange(NEW)
    own = s[:, None] // DEC_SEQ == s[None, :] // DEC_SEQ
    def rows(a):
        out = np.zeros((P, a.shape[1]))
        out[: len(a)] = a
        return out
    low4 = own & (s[:, None] <= s[None, :])
    c["tri_new"] = rows(low4 * 1.0)
    c["same_new"] = rows(own * 1.0)
    c["decay_neg_new"] = rows(np.where(low4, 0.0, NEG))
    c["batch_of"] = rows((s[:, None] // DEC_SEQ == np.arange(DEC_BATCH)[None, :]) * 1.0)
    c["first_pick"] = np.tile(float(PER_GROUP) - np.arange(PER_GROUP), (P, 1))
    c["before"] = (r[:, None] < r[None, :]) * 1.0
    c["expert"] = np.tile(np.arange(EXPERTS), (P, 1))
    c["token"] = np.arange(TILES + 1)[None, :] * P + r[:, None]
    c["causal_neg"] = np.where(r[None, :] <= r[:, None], 0.0, NEG)
    blocks = SEQ // CMP
    q = np.arange(SEQ).reshape(TILES, P).T
    seen = ((np.arange(blocks) + 1) * CMP - 1)[None, None, :] <= q[:, :, None]
    c["q_scale"] = np.full((P, 1), HD ** -0.5)
    c["cmp_seen"] = (seen * 1.0).reshape(P, TILES * blocks)
    c["cmp_neg"] = np.where(seen, 0.0, NEG).reshape(P, TILES * blocks)
    row = np.arange(KVH * GROUP * DEC_SEQ)
    t = row % DEC_SEQ
    kvh = row // (GROUP * DEC_SEQ)
    c["group_sum"] = rows(((kvh[:, None] == kvh[None, :]) & (t[:, None] == t[None, :])) * 1.0)
    key_t, key_b = np.arange(NEW) % DEC_SEQ, np.arange(NEW) // DEC_SEQ
    seen = (key_b[None, None, :] == np.arange(DEC_BATCH)[None, :, None]) & (key_t[None, None, :] <= t[:, None, None])
    c["new_neg"] = rows(np.where(seen, 0.0, NEG).reshape(len(row), -1))
    w = np.arange(WINDOW)
    c["win_neg"] = rows(np.where(w[None, :] > t[:, None], 0.0, NEG))
    n_sel = PAST // SEL + 1
    blk = np.arange(n_sel - 1)
    forced = (blk == 0) | (blk == n_sel - 2)
    c["forced"] = rows(np.tile(forced * SEL_BIG, (len(row), 1)))
    return {k: np.ascontiguousarray(v, dtype=np.float32) for k, v in c.items()}


CONSTANTS = constants()
CONST_AT = {}
_n = 0
for _k, _v in CONSTANTS.items():
    CONST_AT[_k] = (_n, _v.shape[1])
    _n += _v.shape[1]
CONST_W = _n


def halves(ap):
    return ap.rearrange("p (a b) -> p a b", a=2)


class Stage:

    def __init__(self, nc, name, clear=True):
        self.nc, self.name, self.ctx, self.clear, self.sems = nc, name, ExitStack(), clear, []

    def __enter__(self):
        return self

    def __exit__(self, failed, *_):
        if failed:
            return
        if self.clear:
            with self.block() as block:
                @block.sync
                def _(sp):
                    for sem in self.sems:
                        sp.sem_clear(sem)
        self.ctx.close()

    def sb(self, name, shape, dt=F32):
        return self.ctx.enter_context(self.nc.sbuf_tensor(f"{self.name}_{name}", shape, dt))

    def ps(self, name, shape=(P, 512)):
        return self.ctx.enter_context(self.nc.psum_tensor(f"{self.name}_{name}", list(shape), F32))

    def steps(self, name, steps):
        counted = Steps(self.nc, self.ctx, f"{self.name}_{name}", steps)
        self.sems.append(counted.sem)
        return counted

    def line(self, name, steps):
        counted = Steps(self.nc, self.ctx, f"{self.name}_{name}", steps, ahead=0)
        self.sems.append(counted.sem)
        return counted

    def sem(self, name):
        sem = self.ctx.enter_context(self.nc.semaphore(f"{self.name}_{name}"))
        self.sems.append(sem)
        return sem

    def software_dma_sem(self, name):
        return self.nc.alloc_semaphore(f"{self.name}_{name}")

    def block(self):
        return self.nc.Block(no_gpsimd_drain=True)


def load_inputs(nc, g):
    with Stage(nc, "load") as st:
        loaded = st.sem("loaded")
        with st.block() as block:
            @block.sync
            def _(sp):
                sp.dma_start(g.xT[:, :, :], g.d["x"]).then_inc(loaded, 16)
                sp.dma_start(g.consts[:, :], g.d["consts"]).then_inc(loaded, 16)
                sp.dma_start(g.gains[:, :], g.d["gains"]).then_inc(loaded, 16)
                sp.dma_start(g.page_table[:, :], g.d["page_table"]).then_inc(loaded, 16)
                sp.wait_ge(loaded, 64)


class PageSums:

    def __init__(self, nc, g, st, out, first, per):
        self.nc, self.g, self.out, self.first, self.per = nc, g, out, first, per
        self.raw = [st.sb(f"raw{s}", [P, per, 4 * PAGE]) for s in range(2)]
        self.loaded = [st.sem(f"raw_in{s}") for s in range(2)]
        self.dve_s = [st.steps(f"sums{s}", ["summed"]) for s in range(2)]

    def at(self, s, i):
        return (2 * i + s) * self.per + self.first

    def load(self, sp, s, i):
        sp.wait_ge(self.dve_s[s].sem, self.dve_s[s].past("summed", i - 1))
        _, pages = self.nc.values_load_multi_w_load_instructions(
            self.g.page_table[0:1, bass.ds(self.at(s, i), self.per)], engines=[mybir.EngineType.SP],
            min_val=0, max_val=N_POOL - 1)
        for n, page in enumerate(pages):
            sp.dma_start(self.raw[s][:, n, :], self.g.d["cmp_pool"][bass.ds(page, 1)].rearrange("g p n -> (g p) n")
                         ).then_inc(self.loaded[s], 16)

    def credit(self, dve):
        for s in range(2):
            self.dve_s[s].credit(dve)

    def sum(self, dve, s, i):
        dve.wait_ge(self.loaded[s], 16 * self.per * (i + 1))
        dve.tensor_reduce(self.out[:, bass.ds(self.at(s, i), self.per), :].rearrange("p g c -> p (g c)"),
                          self.raw[s][:, :, :].rearrange("p g (c t) -> p (g c) t", t=CMP), AX_X, ALU.add
                          ).then_inc(*self.dve_s[s].done("summed"))


PAGES_GDN = 4
PAGES_NSA = 4
PAGES_ATT = 3
PAGES_EARLY = PAGES_GDN * (CONV_TILES + HEADS)


def rms_norm_stage(nc, g, name, gain0):
    with Stage(nc, name) as st:
        sq = st.sb("sq", [P, KT, TOKENS])
        rms = st.sb("rms", [P, TOKENS])
        total = st.ps("total", (P, 2, 512))
        squares = st.sem("squares")
        summed = st.sem("summed")
        logged = st.sem("logged")
        inverted = st.sem("inverted")
        ones = g.const("ones")
        with st.block() as block:
            @block.scalar
            def _(act):
                for k in range(KT):
                    act.activation(sq[:, k, :], g.xT[:, k, :], ACT.Square).then_inc(squares, 1)
                act.wait_ge(summed, 1)
                act.activation(halves(rms[:, :]), total[:, :, 0:HALF], ACT.Ln, bias=g.eps[:, 0:1],
                               scale=1.0 / D_MODEL).then_inc(logged, 1)
                act.wait_ge(logged, 1)
                act.activation(rms[:, :], rms[:, :], ACT.Exp, scale=-0.5).then_inc(inverted, 1)

            @block.tensor
            def _(pe):
                for k in range(KT):
                    pe.wait_ge(squares, k + 1)
                    for a in range(2):
                        mm = pe.matmul(total[:, a, 0:HALF], ones, sq[:, k, a * HALF:(a + 1) * HALF],
                                       start=(k == 0), stop=(k == KT - 1))
                mm.then_inc(summed, 1)

            @block.vector
            def _(dve):
                dve.wait_ge(inverted, 1)
                for k in range(KT):
                    dve.scalar_tensor_tensor(out=g.hT[:, k, :], in0=g.xT[:, k, :],
                                             scalar=g.gains[:, gain0 + k:gain0 + k + 1], in1=rms[:, :],
                                             op0=ALU.mult, op1=ALU.mult)


def gdn_project_stage(nc, g):
    with Stage(nc, "proj") as st:
        w = [st.sb(f"w{s}", [P, KT, P]) for s in range(2)]
        xc = [st.sb(f"xc{s}", [P, CONV - 1 + SEQ]) for s in range(2)]
        xs = [st.sb(f"xs{s}", [P, DEC_BATCH, CONV - 1 + DEC_SEQ]) for s in range(2)]
        conv = [st.sb(f"conv{s}", [P, TOKENS]) for s in range(2)]
        taps = st.sb("taps", [P, CONV_TILES, CONV])
        prev = st.sb("prev", [P, CONV_TILES, DEC_BATCH, CONV - 1])
        tails = st.sb("tails", [P, CONV_TILES, (1 + DEC_BATCH) * (CONV - 1)])
        acc = [st.ps(f"acc{s}", (P, 2, 512)) for s in range(2)]
        loaded = [st.sem(f"loaded{s}") for s in range(2)]
        small = st.sem("small")
        stored = st.sem("stored")
        pe_s = [st.steps(f"pe{s}", ["product"]) for s in range(2)]
        act_s = [st.steps(f"act{s}", ["prompt out", "sample out", "silu"]) for s in range(2)]
        dve_s = [st.steps(f"dve{s}", [f"{part} tap {i}" for i in range(CONV) for part in ("prompt", "sample")])
                 for s in range(2)]
        pool_s = [st.steps(f"pool{s}", ["history", "prompt tail", "sample tail"]) for s in range(2)]
        cleared = st.sem("cleared")
        z_out = st.sem("z_out")
        rounds = CONV_TILES // 2
        z_rounds = HEADS // 2
        pages = PageSums(nc, g, st, g.first_sums, 0, PAGES_GDN)
        with st.block() as block:
            @block.sync
            def _(sp):
                sp.dma_start(taps[:, :, :], g.d["taps"]).then_inc(small, 16)
                sp.dma_start(prev[:, :, :, :], g.d["conv_prev"]).then_inc(small, 16)
                for s in range(2):
                    sp.dma_start(w[s][:, :, :], g.d["gdn_w"][s]).then_inc(loaded[s], 16)
                with sp.Fori(0, rounds + z_rounds - 1) as i:
                    for s in range(2):
                        sp.wait_ge(pe_s[s].sem, pe_s[s].past("product", i))
                        sp.dma_start(w[s][:, :, :],
                                     g.d["gdn_w"][bass.ds(2 * i + 2 + s, 1)].rearrange("t p k c -> (t p) k c")
                                     ).then_inc(loaded[s], 16)
                        pages.load(sp, s, i)
                for s in range(2):
                    pages.load(sp, s, rounds + z_rounds - 1)
                for s in range(2):
                    sp.wait_ge(pool_s[s].sem, pool_s[s].past("sample tail", rounds - 1))
                sp.dma_start(g.d["conv_out"], tails[:, :, :]).then_inc(stored, 16)
                sp.wait_ge(stored, 16)

            @block.tensor
            def _(pe):
                for s in range(2):
                    pe_s[s].credit(pe)

                def product(s, i):
                    pe.wait_ge(loaded[s], 16 * (i + 1))
                    for k in range(KT):
                        for a in range(2):
                            mm = pe.matmul(acc[s][:, a, 0:HALF], w[s][:, k, :], g.hT[:, k, a * HALF:(a + 1) * HALF],
                                           start=(k == 0), stop=(k == KT - 1))
                    mm.then_inc(*pe_s[s].done("product"))

                with pe.Fori(0, rounds) as i:
                    for s in range(2):
                        pe.wait_ge(act_s[s].sem, act_s[s].past("sample out", i - 1))
                        product(s, i)
                for i in range(z_rounds):
                    for s in range(2):
                        if i == 0:
                            pe.wait_ge(act_s[s].sem, act_s[s].past("sample out", rounds - 1))
                        else:
                            pe.wait_ge(z_out, 2 * (i - 1) + s + 1)
                        product(s, rounds + i)

            @block.scalar
            def _(act):
                for s in range(2):
                    act_s[s].credit(act)
                act.wait_ge(cleared, 2)
                with act.Fori(0, rounds) as i:
                    for s in range(2):
                        act.wait_ge(pe_s[s].sem, pe_s[s].past("product", i))
                        act.wait_ge(dve_s[s].sem, dve_s[s].past(f"sample tap {CONV - 1}", i - 1))
                        act.wait_ge(pool_s[s].sem, pool_s[s].past("sample tail", i - 1))
                        act.activation(xc[s][:, CONV - 1:CONV - 1 + HALF], acc[s][:, 0, 0:HALF],
                                       ACT.Copy).then_inc(*act_s[s].done("prompt out"))
                        act.activation(xc[s][:, CONV - 1 + HALF:], acc[s][:, 1, 0:SEQ - HALF], ACT.Copy)
                        act.activation(xs[s][:, :, CONV - 1:],
                                       acc[s][:, 1, SEQ - HALF:HALF].rearrange("p (b t) -> p b t", t=DEC_SEQ),
                                       ACT.Copy).then_inc(*act_s[s].done("sample out"))
                    for s in range(2):
                        act.wait_ge(dve_s[s].sem, dve_s[s].past(f"sample tap {CONV - 1}", i))
                        act.activation(g.qkv[:, bass.ds(2 * i + s, 1), :].rearrange("p a t -> p (a t)"),
                                       conv[s][:, :], ACT.Silu).then_inc(*act_s[s].done("silu"))
                for i in range(z_rounds):
                    for s in range(2):
                        act.wait_ge(pe_s[s].sem, pe_s[s].past("product", rounds + i))
                        act.activation(halves(g.zT[:, 2 * i + s, :]), acc[s][:, :, 0:HALF],
                                       ACT.Silu).then_inc(z_out, 1)

            @block.vector
            def _(dve):
                for s in range(2):
                    dve_s[s].credit(dve)
                    dve.memset(xc[s][:, 0:CONV - 1], 0.0).then_inc(cleared, 1)
                pages.credit(dve)
                dve.wait_ge(cleared, 2)
                dve.wait_ge(small, 32)
                with dve.Fori(0, rounds) as i:
                    for s in range(2):
                        dve.wait_ge(act_s[s].sem, act_s[s].past("sample out", i))
                        dve.wait_ge(act_s[s].sem, act_s[s].past("silu", i - 1))
                        dve.wait_ge(pool_s[s].sem, pool_s[s].past("history", i))
                        prompt = conv[s][:, 0:SEQ]
                        sample = conv[s][:, SEQ:TOKENS].rearrange("p (b t) -> p b t", t=DEC_SEQ)
                        for tap in range(CONV):
                            weight = taps[:, bass.ds(2 * i + s, 1), tap:tap + 1].rearrange("p a t -> p (a t)")
                            rows, new = xc[s][:, tap:tap + SEQ], xs[s][:, :, tap:tap + DEC_SEQ]
                            if tap == 0:
                                dve.tensor_scalar(prompt, rows, weight, None, ALU.mult
                                                  ).then_inc(*dve_s[s].done("prompt tap 0"))
                                dve.tensor_scalar(sample, new, weight, None, ALU.mult
                                                  ).then_inc(*dve_s[s].done("sample tap 0"))
                                continue
                            dve.wait_ge(dve_s[s].sem, dve_s[s].past(f"prompt tap {tap - 1}", i))
                            dve.scalar_tensor_tensor(out=prompt, in0=rows, scalar=weight, in1=prompt, op0=ALU.mult,
                                                     op1=ALU.add).then_inc(*dve_s[s].done(f"prompt tap {tap}"))
                            dve.wait_ge(dve_s[s].sem, dve_s[s].past(f"sample tap {tap - 1}", i))
                            dve.scalar_tensor_tensor(out=sample, in0=new, scalar=weight, in1=sample, op0=ALU.mult,
                                                     op1=ALU.add).then_inc(*dve_s[s].done(f"sample tap {tap}"))
                        pages.sum(dve, s, i)
                for i in range(rounds, rounds + z_rounds):
                    for s in range(2):
                        pages.sum(dve, s, i)

            @block.gpsimd
            def _(pool):
                for s in range(2):
                    pool_s[s].credit(pool)
                pool.wait_ge(small, 32)
                n = CONV - 1
                with pool.Fori(0, rounds) as i:
                    for s in range(2):
                        tile = bass.ds(2 * i + s, 1)
                        pool.wait_ge(dve_s[s].sem, dve_s[s].past(f"sample tap {CONV - 1}", i - 1))
                        pool.tensor_copy(xs[s][:, :, 0:n], prev[:, tile, :, :].rearrange("p a b t -> p (a b) t")
                                         ).then_inc(*pool_s[s].done("history"))
                        pool.wait_ge(act_s[s].sem, act_s[s].past("sample out", i))
                        pool.tensor_copy(tails[:, tile, 0:n].rearrange("p a t -> p (a t)"), xc[s][:, SEQ:SEQ + n]
                                         ).then_inc(*pool_s[s].done("prompt tail"))
                        pool.tensor_copy(
                            tails[:, tile, n:].rearrange("p a (b t) -> p (a b) t", t=n),
                            xs[s][:, :, DEC_SEQ:DEC_SEQ + n]).then_inc(*pool_s[s].done("sample tail"))


def gdn_gates_stage(nc, g):
    NT = TILES + 1
    with Stage(nc, "gates") as st:
        w = st.sb("w", [P, KT, 2 * HEADS])
        rows = st.sb("rows", [P, 2, HEADS])
        ab = st.sb("ab", [P, NT, 2 * HEADS])
        mag = st.sb("mag", [P, NT, HEADS])
        pos = st.sb("pos", [P, NT, HEADS])
        decay = st.sb("decay", [P, HEADS])
        diff = st.sb("diff", [P, NT, HEADS])
        by_batch = st.sb("by_batch", [NEW, DEC_BATCH, HEADS])
        proj, cum, whole, chunks = st.ps("proj"), st.ps("cum"), st.ps("whole"), st.ps("chunks")
        stored = st.sem("stored")
        loaded = st.sem("loaded")
        pe_s = st.line("pe", ["ab", "chunk sums", "batch sums"])
        dve_s = st.line("dve", ["clear", "copy", "copy new", "bias", "magnitude", "positive", "softplus", "g",
                                "by batch", "G", "G new", "diff", "diff new"])
        act_s = st.line("act", ["rate", "exp", "log", "beta", "eG", "tail"])
        a = ab[:, :, 0:HEADS]
        rows_of = [P] * TILES + [NEW]

        def tiles(t, n):
            return t[:, 0:NT * n].rearrange("p (t n) -> p t n", n=n)

        with st.block() as block:
            @block.sync
            def _(sp):
                sp.dma_start(w[:, :, :], g.d["gdn_w_ab"]).then_inc(loaded, 16)
                sp.dma_start(rows[:, :, :], g.d["gdn_rows"]).then_inc(loaded, 16)
                sp.dma_start(g.d["first_sums"], g.first_sums[:, :, :]).then_inc(stored, 16)
                sp.wait_ge(stored, 16)

            @block.tensor
            def _(pe):
                pe.wait_ge(loaded, 32)
                for t, n in enumerate(rows_of):
                    for k in range(KT):
                        mm = pe.matmul(tiles(proj, 2 * HEADS)[0:n, t, :], g.hT[:, k, t * P:t * P + n], w[:, k, :],
                                       start=(k == 0), stop=(k == KT - 1))
                mm.then_inc(*pe_s.done("ab"))
                pe.wait_ge(dve_s.sem, dve_s.past("g"))
                for t, n in enumerate(rows_of):
                    tri, same = ("tri", "same") if n == P else ("tri_new", "same_new")
                    pe.matmul(tiles(cum, HEADS)[0:n, t, :], g.const(tri, n)[:, 0:n], g.gate_g[0:n, t, :],
                              start=True, stop=True)
                    pe.matmul(tiles(whole, HEADS)[0:n, t, :], g.const(same, n)[:, 0:n], g.gate_g[0:n, t, :],
                              start=True, stop=True)
                for t in range(TILES):
                    for half in range(2):
                        at = (2 * t + half) * HEADS
                        mm = pe.matmul(chunks[:, at:at + HEADS], g.const(f"half{half}"), g.gate_g[:, t, :],
                                       start=True, stop=True)
                mm.then_inc(*pe_s.done("chunk sums"))
                pe.wait_ge(dve_s.sem, dve_s.past("by batch"))
                pe.matmul(chunks[:, 128:128 + DEC_BATCH * HEADS], g.const("ones", NEW),
                          by_batch[:, :, :].rearrange("s b h -> s (b h)"), start=True, stop=True
                          ).then_inc(*pe_s.done("batch sums"))

            @block.scalar
            def _(act):
                act.wait_ge(loaded, 32)
                act.activation(decay[:, :], rows[:, 0, :], ACT.Exp).then_inc(*act_s.done("rate"))
                act.wait_ge(dve_s.sem, dve_s.past("magnitude"))
                act.activation(mag[:, :, :], mag[:, :, :], ACT.Exp, scale=-1.0).then_inc(*act_s.done("exp"))
                act.wait_ge(act_s.sem, act_s.past("exp"))
                act.activation(mag[:, :, :], mag[:, :, :], ACT.Ln, bias=1.0).then_inc(*act_s.done("log"))
                act.activation(g.beta[:, :, :], ab[:, :, HEADS:], ACT.Sigmoid).then_inc(*act_s.done("beta"))
                act.wait_ge(dve_s.sem, dve_s.past("G new"))
                act.activation(g.eG[:, :, :], g.G[:, :, :], ACT.Exp).then_inc(*act_s.done("eG"))
                act.wait_ge(dve_s.sem, dve_s.past("diff new"))
                act.activation(g.tail[:, :, :], diff[:, :, :], ACT.Exp).then_inc(*act_s.done("tail"))
                act.wait_ge(pe_s.sem, pe_s.past("batch sums"))
                act.activation(g.e_chunk[:, :, :].rearrange("p c h -> p (c h)"), chunks[:, 0:2 * TILES * HEADS],
                               ACT.Exp)
                act.activation(g.e_batch[:, :, :].rearrange("p b h -> p (b h)"),
                               chunks[:, 128:128 + DEC_BATCH * HEADS], ACT.Exp)

            @block.vector
            def _(dve):
                dve.memset(ab[:, :, :], 0.0)
                dve.memset(g.G[:, TILES, :], 0.0)
                dve.memset(diff[:, TILES, :], 0.0).then_inc(*dve_s.done("clear"))
                dve.wait_ge(dve_s.sem, dve_s.past("clear"))
                dve.wait_ge(pe_s.sem, pe_s.past("ab"))
                dve.tensor_copy(ab[:, 0:TILES, :], tiles(proj, 2 * HEADS)[:, 0:TILES, :]
                                ).then_inc(*dve_s.done("copy"))
                dve.tensor_copy(ab[0:NEW, TILES, :], tiles(proj, 2 * HEADS)[0:NEW, TILES, :]
                                ).then_inc(*dve_s.done("copy new"))
                dve.wait_ge(dve_s.sem, dve_s.past("copy new"))
                dve.wait_ge(loaded, 32)
                dve.tensor_tensor(a, a, rows[:, 1:2, :].broadcast_to([P, NT, HEADS]), ALU.add
                                  ).then_inc(*dve_s.done("bias"))
                dve.wait_ge(dve_s.sem, dve_s.past("bias"))
                dve.scalar_tensor_tensor(out=mag[:, :, :], in0=a, scalar=-1.0, in1=a, op0=ALU.mult, op1=ALU.max).then_inc(*dve_s.done("magnitude"))
                dve.tensor_scalar(pos[:, :, :], a, 0.0, None, ALU.max).then_inc(*dve_s.done("positive"))
                dve.wait_ge(act_s.sem, act_s.past("log"))
                dve.wait_ge(dve_s.sem, dve_s.past("positive"))
                dve.tensor_tensor(pos[:, :, :], pos[:, :, :], mag[:, :, :], ALU.add
                                  ).then_inc(*dve_s.done("softplus"))
                dve.wait_ge(dve_s.sem, dve_s.past("softplus"))
                dve.scalar_tensor_tensor(out=g.gate_g[:, :, :], in0=pos[:, :, :], scalar=-1.0,
                                         in1=decay[:, :].unsqueeze(1).broadcast_to([P, NT, HEADS]),
                                         op0=ALU.mult, op1=ALU.mult).then_inc(*dve_s.done("g"))
                dve.wait_ge(dve_s.sem, dve_s.past("g"))
                dve.tensor_tensor(by_batch[:, :, :],
                                  g.gate_g[0:NEW, TILES, :].unsqueeze(1).broadcast_to([NEW, DEC_BATCH, HEADS]),
                                  g.const("batch_of", NEW).unsqueeze(2).broadcast_to([NEW, DEC_BATCH, HEADS]),
                                  ALU.mult).then_inc(*dve_s.done("by batch"))
                dve.wait_ge(pe_s.sem, pe_s.past("chunk sums"))
                new = slice(0, NEW)
                dve.tensor_copy(g.G[:, 0:TILES, :], tiles(cum, HEADS)[:, 0:TILES, :]).then_inc(*dve_s.done("G"))
                dve.tensor_copy(g.G[new, TILES, :], tiles(cum, HEADS)[new, TILES, :]).then_inc(*dve_s.done("G new"))
                dve.wait_ge(dve_s.sem, dve_s.past("G new"))
                dve.tensor_tensor(diff[:, 0:TILES, :], tiles(whole, HEADS)[:, 0:TILES, :], g.G[:, 0:TILES, :],
                                  ALU.subtract).then_inc(*dve_s.done("diff"))
                dve.tensor_tensor(diff[new, TILES, :], tiles(whole, HEADS)[new, TILES, :], g.G[new, TILES, :],
                                  ALU.subtract).then_inc(*dve_s.done("diff new"))


LEVELS = 6
DOUBLINGS = range(1, LEVELS)
CHUNKS = SEQ // CHUNK
LANE_PE = (["squares", "k rows", "v rows", "kk", "qk", "G wide", "beta wide", "T 0"]
           + [x for n in DOUBLINGS for x in (f"W {n}", f"TT {n}")]
           + ["u", "w", "new u w"]
           + [x for j in range(CHUNKS) for x in (f"wS {j}", f"KV {j}", f"o {j}")]
           + ["new wS qS", "new v rows", "new o", "new KV", "o squares"])
LANE_DVE = (["gates", "k beta decay staged", "k", "q", "k beta decay", "difference", "qk", "kk", "L", "TT 0"]
            + [f"T {n}" for n in DOUBLINGS]
            + [x for j in range(CHUNKS) for x in (f"v {j}", f"S {j}")]
            + ["new v", "new v by batch", "new S decayed", "new S", "new o", "o normed", "o gated"])
LANE_ACT = (["squares", "v", "log norms", "norms", "k tail", "v beta", "eG wide", "decay", "T 0"]
            + [f"W {n}" for n in DOUBLINGS]
            + ["u", "w", "new wS qS", "new v rows", "o", "o square", "o log", "o norm"])
LANE_POOL = ["clear S", "q decayed"] + [f"level {n}" for n in range(LEVELS)]


def gdn_heads_stage(nc, g):
    with Stage(nc, "heads") as st:
        class Lane:
            pass
        lanes = []
        copied = st.sem("copied")
        N = slice(0, NEW)
        for s in range(2):
            ln = Lane()
            lanes.append(ln)
            ln.s = s
            ln.sq = st.sb(f"sq{s}", [P, 2, TOKENS])
            ln.norm = st.sb(f"norm{s}", [P, 2, TOKENS])
            ln.kT = st.sb(f"kT{s}", [P, TOKENS])
            ln.qT = st.sb(f"qT{s}", [P, TOKENS])
            ln.kbe = st.sb(f"kbe{s}", [P, TILES + 1, P])
            ln.kt = st.sb(f"kt{s}", [P, TILES + 1, P])
            ln.vb = st.sb(f"vb{s}", [P, TILES + 1, P])
            ln.dec = st.sb(f"dec{s}", [P, TOKENS])
            ln.LT = st.sb(f"LT{s}", [P, TOKENS])
            ln.QK = st.sb(f"QK{s}", [P, TOKENS])
            ln.B = st.sb(f"B{s}", [P, 2, TOKENS])
            ln.T = st.sb(f"T{s}", [P, TOKENS])
            ln.TT = st.sb(f"TT{s}", [P, TOKENS])
            ln.W = st.sb(f"W{s}", [P, TOKENS])
            ln.u = st.sb(f"u{s}", [P, TILES, P])
            ln.wq = st.sb(f"wq{s}", [P, 2, TOKENS])
            ln.S = st.sb(f"S{s}", [P, P])
            ln.vn = st.sb(f"vn{s}", [P, P])
            ln.o = st.sb(f"o{s}", [P, TOKENS])
            ln.S_new = st.sb(f"S_new{s}", [P, DEC_BATCH, P])
            ln.wSqS = st.sb(f"wSqS{s}", [P, DEC_BATCH, 2, DEC_SEQ])
            ln.vT = st.sb(f"vT{s}", [P, NEW])
            ln.v_rows = st.sb(f"v_rows{s}", [NEW, P])
            ln.gates = st.sb(f"gates{s}", [P, 5, TILES + 1])
            ln.v_batch = ln.B[N, :, :].rearrange("s a t -> s (a t)")[:, 0:DEC_BATCH * P].rearrange(
                "s (b v) -> s b v", b=DEC_BATCH)
            ln.bank = [st.ps(f"bank{s}{n}") for n in range(4)]
            ln.pe = st.steps(f"pe{s}", LANE_PE)
            ln.dve = st.steps(f"dve{s}", LANE_DVE)
            ln.act = st.steps(f"act{s}", LANE_ACT)
            ln.pool = st.steps(f"pool{s}", LANE_POOL)
            ln.sp = st.steps(f"sp{s}", ["states stored"])
            ln.loaded = st.sem(f"loaded{s}")
            ln.stored = st.sem(f"stored{s}")
        rounds = HEADS // 2
        NT = slice(SEQ, TOKENS)
        G_, BETA, CUM, BETA_DECAY, TAIL = range(5)

        def tile(t):
            return slice(t * P, (t + 1) * P)

        def tiled(ap):
            return ap.rearrange("p (t c) -> p t c", c=P)

        def wide(mask):
            return g.const(mask).unsqueeze(1).broadcast_to([P, TILES, P])

        def new_const(name):
            return g.const(name, NEW)[:, 0:NEW]

        def head_of(t, ln, i):
            return t[:, bass.ds(2 * i + ln.s, 1), :].rearrange("p a t -> p (a t)")

        def alternate(rule, i):
            for _ in zip(*(rule(ln, i) for ln in lanes)):
                pass

        with st.block() as block:
            @block.sync
            def _(sp):
                sp.dma_start(g.d["win_out"].rearrange("b p a n -> (b p) (a n)"),
                             g.d["win"].rearrange("b p a n -> (b p) (a n)")).then_inc(copied, 16)
                for ln in lanes:
                    ln.sp.credit(sp)
                with sp.Fori(0, rounds) as i:
                    for ln in lanes:
                        h = bass.ds(2 * i + ln.s, 1)
                        sp.dma_start(ln.S_new[:, :, :], g.d["gdn_S"][h].rearrange("h k b v -> (h k) b v")
                                     ).then_inc(ln.loaded, 16)
                    for ln in lanes:
                        h = bass.ds(2 * i + ln.s, 1)
                        sp.wait_ge(ln.dve.sem, ln.dve.past(f"S {CHUNKS - 1}", i))
                        sp.dma_start(g.d["p_S"][h].rearrange("h k v -> (h k) v"), ln.S[:, :]).then_inc(ln.stored, 16)
                    for ln in lanes:
                        h = bass.ds(2 * i + ln.s, 1)
                        sp.wait_ge(ln.dve.sem, ln.dve.past("new S", i))
                        sp.dma_start(g.d["s_S"][h].rearrange("h k b v -> (h k) b v"), ln.S_new[:, :, :]
                                     ).then_inc(ln.stored, 16)
                    for ln in lanes:
                        sp.wait_ge(ln.stored, 32 * (i + 1))
                        sp.sem_inc(*ln.sp.done("states stored"))
                sp.wait_ge(copied, 16)

            @block.tensor
            def _(pe):
                def rule(ln, i):
                    b0, b1, b2, b3 = ln.bank

                    def each(out, lhsT, rhs):
                        for t in range(TILES):
                            mm = pe.matmul(out[:, tile(t)], lhsT(t), rhs(t), start=True, stop=True)
                        return mm

                    def new(out, lhsT, rhs):
                        return pe.matmul(out, lhsT, rhs, start=True, stop=True)
                    ones, ident = g.const("ones"), g.const("ident")
                    pe.wait_ge(ln.act.sem, ln.act.past("squares", i))
                    pe.wait_ge(ln.dve.sem, ln.dve.past("new S", i - 1))
                    pe.wait_ge(ln.act.sem, ln.act.past("o norm", i - 1))
                    new(b0[:, :], ones, ln.sq[:, 0, 0:SEQ])
                    new(b1[:, :], ones, ln.sq[:, 1, 0:SEQ])
                    new(b2[:, 0:NEW], ones, ln.sq[:, 0, NT])
                    new(b2[:, NEW:2 * NEW], ones, ln.sq[:, 1, NT]).then_inc(*ln.pe.done("squares"))
                    yield
                    pe.wait_ge(ln.dve.sem, ln.dve.past("k", i))
                    for t in range(TILES):
                        pe.transpose(b3[:, tile(t)], ln.kT[:, tile(t)], ident)
                    pe.transpose(b2[N, 192:320], ln.QK[:, NT], ident)
                    pe.transpose(b2[N, 64:192], ln.kT[:, NT], ident).then_inc(*ln.pe.done("k rows"))
                    yield
                    for t in range(TILES):
                        mm = pe.transpose(b0[:, tile(t)], ln.QK[:, tile(t)], ident)
                    mm.then_inc(*ln.pe.done("v rows"))
                    yield
                    each(b1, lambda t: ln.kT[:, tile(t)], lambda t: ln.kT[:, tile(t)]
                         ).then_inc(*ln.pe.done("kk"))
                    yield
                    pe.wait_ge(ln.act.sem, ln.act.past("k tail", i))
                    each(b3, lambda t: ln.kT[:, tile(t)], lambda t: ln.qT[:, tile(t)]
                         ).then_inc(*ln.pe.done("qk"))
                    yield
                    pe.wait_ge(ln.act.sem, ln.act.past("v beta", i))
                    each(b0, lambda t: ln.gates[:, G_, t:t + 1].broadcast_to([P, P]), lambda t: g.const("tri"))
                    new(b2[N, 320:352], ln.kT[:, NT], ln.kT[:, NT])
                    new(b2[N, 352:384], ln.kT[:, NT], ln.qT[:, NT])
                    new(b2[:, 384:416], ln.gates[N, G_, TILES:TILES + 1].broadcast_to([NEW, P]),
                        new_const("tri_new")).then_inc(*ln.pe.done("G wide"))
                    yield
                    pe.wait_ge(ln.act.sem, ln.act.past("eG wide", i))
                    each(b0, lambda t: ln.gates[:, BETA, t:t + 1].broadcast_to([P, P]), lambda t: ident)
                    new(b2[N, 416:448], ln.gates[N, BETA, TILES:TILES + 1].broadcast_to([NEW, NEW]),
                        new_const("ident")).then_inc(*ln.pe.done("beta wide"))
                    yield
                    pe.wait_ge(ln.dve.sem, ln.dve.past("TT 0", i))
                    for t in range(TILES):
                        pe.transpose(b1[:, tile(t)], ln.TT[:, tile(t)], ident)
                    pe.transpose(b2[N, 0:32], ln.TT[N, NT], new_const("ident")).then_inc(*ln.pe.done("T 0"))
                    yield
                    for n in DOUBLINGS:
                        pe.wait_ge(ln.pool.sem, ln.pool.past(f"level {n}", i))
                        if n == 1:
                            pe.wait_ge(ln.act.sem, ln.act.past("T 0", i))
                        else:
                            pe.wait_ge(ln.dve.sem, ln.dve.past(f"T {n - 1}", i))
                        mm = each(b1, lambda t: ln.B[:, n % 2, tile(t)], lambda t: ln.T[:, tile(t)])
                        if n == 1:
                            mm = new(b2[N, 32:64], ln.B[N, 1, NT], ln.T[N, NT])
                        mm.then_inc(*ln.pe.done(f"W {n}"))
                        yield
                        pe.wait_ge(ln.act.sem, ln.act.past(f"W {n}", i))
                        if n < LEVELS - 1:
                            each(b3, lambda t: ln.TT[:, tile(t)], lambda t: ln.W[:, tile(t)])
                        mm = each(b0, lambda t: ln.W[:, tile(t)], lambda t: ln.TT[:, tile(t)])
                        if n == 1:
                            mm = new(b2[N, 64:96], ln.W[N, NT], ln.TT[N, NT])
                        mm.then_inc(*ln.pe.done(f"TT {n}"))
                        yield
                    pe.wait_ge(ln.dve.sem, ln.dve.past(f"T {LEVELS - 1}", i))
                    each(b1, lambda t: ln.TT[:, tile(t)], lambda t: ln.vb[:, t, :]).then_inc(*ln.pe.done("u"))
                    each(b3, lambda t: ln.kbe[:, t, :], lambda t: ln.TT[:, tile(t)]).then_inc(*ln.pe.done("w"))
                    new(b2[:, 96:128], ln.vb[N, TILES, :], ln.TT[N, NT])
                    new(b2[:, 128:160], ln.kbe[N, TILES, :], ln.TT[N, NT]).then_inc(*ln.pe.done("new u w"))
                    yield
                    pe.wait_ge(ln.pool.sem, ln.pool.past("q decayed", i))
                    pe.wait_ge(ln.act.sem, ln.act.past("w", i))
                    for j in range(CHUNKS):
                        t, R, C = j // 2, slice(CHUNK * (j % 2), CHUNK * (j % 2 + 1)), slice(j * CHUNK, (j + 1) * CHUNK)
                        if j:
                            pe.wait_ge(ln.dve.sem, ln.dve.past(f"S {j - 1}", i))
                        new(b1[R, 0:P], ln.wq[:, 0, C], ln.S[:, :]).then_inc(*ln.pe.done(f"wS {j}"))
                        pe.matmul(b0[:, C], ln.S[:, :], ln.wq[:, 1, C], start=True, stop=False)
                        yield
                        pe.wait_ge(ln.dve.sem, ln.dve.past(f"v {j}", i))
                        new(b3[:, 0:P], ln.kt[R, t, :], ln.vn[R, :]).then_inc(*ln.pe.done(f"KV {j}"))
                        pe.matmul(b0[:, C], ln.vn[R, :], ln.QK[R, C], start=False, stop=True
                                  ).then_inc(*ln.pe.done(f"o {j}"))
                        yield
                    pe.wait_ge(ln.loaded, 16 * (i + 1))
                    for b in range(DEC_BATCH):
                        at = 160 + 2 * DEC_SEQ * b
                        mm = new(b2[:, at:at + 2 * DEC_SEQ].rearrange("p (w t) -> p w t", w=2), ln.S_new[:, b, :],
                                 ln.wq[:, :, SEQ + DEC_SEQ * b:SEQ + DEC_SEQ * (b + 1)])
                    mm.then_inc(*ln.pe.done("new wS qS"))
                    yield
                    pe.wait_ge(ln.dve.sem, ln.dve.past("new v", i))
                    pe.transpose(b2[N, 224:352], ln.vT[:, :], ident).then_inc(*ln.pe.done("new v rows"))
                    yield
                    pe.wait_ge(ln.act.sem, ln.act.past("new v rows", i))
                    new(b2[:, 352:384], ln.v_rows[:, :], ln.QK[N, NT]).then_inc(*ln.pe.done("new o"))
                    pe.wait_ge(ln.dve.sem, ln.dve.past("new v by batch", i))
                    for a, bank in enumerate((b1, b3)):
                        mm = new(bank[:, :], ln.kt[N, TILES, :],
                                 ln.v_batch[:, 4 * a:4 * a + 4, :].rearrange("s b v -> s (b v)"))
                    mm.then_inc(*ln.pe.done("new KV"))
                    yield
                    pe.wait_ge(ln.act.sem, ln.act.past("o square", i))
                    new(b0[:, :], ones, ln.sq[:, 1, 0:SEQ])
                    new(b2[:, 384:416], ones, ln.sq[:, 1, NT]).then_inc(*ln.pe.done("o squares"))
                    yield

                for ln in lanes:
                    ln.pe.credit(pe)
                with pe.Fori(0, rounds) as i:
                    alternate(rule, i)

            @block.scalar
            def _(act):
                def rule(ln, i):
                    b0, b1, b2, b3 = ln.bank
                    q, k, v = (g.qkv[:, bass.ds(2 * i + ln.s + HEADS * n, 1), :].rearrange("p a t -> p (a t)")
                               for n in range(3))
                    act.wait_ge(ln.pe.sem, ln.pe.past("o squares", i - 1))
                    act.wait_ge(ln.pool.sem, ln.pool.past("q decayed", i - 1))
                    act.activation(ln.sq[:, 0, :], q, ACT.Square)
                    act.activation(ln.sq[:, 1, :], k, ACT.Square).then_inc(*ln.act.done("squares"))
                    act.activation(ln.QK[:, :], v, ACT.Copy).then_inc(*ln.act.done("v"))
                    yield
                    act.wait_ge(ln.pe.sem, ln.pe.past("squares", i))
                    act.wait_ge(ln.dve.sem, ln.dve.past("o normed", i - 1))
                    for n, bank in enumerate((b0, b1)):
                        act.activation(ln.norm[:, n, 0:SEQ], bank[:, :], ACT.Ln, bias=g.eps[:, 0:1])
                    act.activation(ln.norm[:, :, NT], b2[:, 0:2 * NEW].rearrange("p (n t) -> p n t", n=2), ACT.Ln,
                                   bias=g.eps[:, 0:1]).then_inc(*ln.act.done("log norms"))
                    act.wait_ge(ln.act.sem, ln.act.past("log norms", i))
                    act.activation(ln.norm[:, :, :], ln.norm[:, :, :], ACT.Exp, scale=-0.5
                                   ).then_inc(*ln.act.done("norms"))
                    yield
                    act.wait_ge(ln.dve.sem, ln.dve.past("k beta decay", i))
                    for t in range(TILES):
                        act.activation(ln.kt[:, t, :], b3[:, tile(t)], ACT.Copy, scale=ln.gates[:, TAIL, t:t + 1])
                    act.activation(ln.kt[N, TILES, :], b2[N, 64:192], ACT.Copy,
                                   scale=ln.gates[N, TAIL, TILES:TILES + 1]).then_inc(*ln.act.done("k tail"))
                    act.wait_ge(ln.pe.sem, ln.pe.past("v rows", i))
                    for t in range(TILES):
                        act.activation(ln.vb[:, t, :], b0[:, tile(t)], ACT.Copy, scale=ln.gates[:, BETA, t:t + 1])
                    act.activation(ln.vb[N, TILES, :], b2[N, 192:320], ACT.Copy,
                                   scale=ln.gates[N, BETA, TILES:TILES + 1]).then_inc(*ln.act.done("v beta"))
                    yield
                    act.wait_ge(ln.dve.sem, ln.dve.past("difference", i))
                    act.activation(ln.sq[:, 0, 0:SEQ], b0[:, :], ACT.Exp)
                    act.activation(ln.sq[:, 0, NT], b2[:, 384:416], ACT.Exp).then_inc(*ln.act.done("eG wide"))
                    act.activation(ln.dec[:, 0:SEQ], ln.dec[:, 0:SEQ], ACT.Exp)
                    act.activation(ln.dec[N, NT], ln.dec[N, NT], ACT.Exp).then_inc(*ln.act.done("decay"))
                    yield
                    act.wait_ge(ln.pe.sem, ln.pe.past("T 0", i))
                    act.activation(ln.T[:, 0:SEQ], b1[:, :], ACT.Copy)
                    act.activation(ln.T[N, NT], b2[N, 0:32], ACT.Copy).then_inc(*ln.act.done("T 0"))
                    yield
                    for n in DOUBLINGS:
                        act.wait_ge(ln.pe.sem, ln.pe.past(f"W {n}", i))
                        if n == 1:
                            act.activation(ln.W[N, NT], b2[N, 32:64], ACT.Copy)
                        act.activation(ln.W[:, 0:SEQ], b1[:, :], ACT.Copy).then_inc(*ln.act.done(f"W {n}"))
                        yield
                    act.wait_ge(ln.pe.sem, ln.pe.past("u", i))
                    act.activation(ln.u[:, :, :].rearrange("p t v -> p (t v)"), b1[:, :], ACT.Copy
                                   ).then_inc(*ln.act.done("u"))
                    act.wait_ge(ln.pe.sem, ln.pe.past("new u w", i))
                    act.activation(ln.wq[:, 0, 0:SEQ], b3[:, :], ACT.Copy)
                    act.activation(ln.wq[:, 0, NT], b2[:, 128:160], ACT.Copy).then_inc(*ln.act.done("w"))
                    yield
                    act.wait_ge(ln.pe.sem, ln.pe.past("new wS qS", i))
                    act.activation(ln.wSqS[:, :, :, :].rearrange("p b w t -> p (b w t)"), b2[:, 160:224], ACT.Copy
                                   ).then_inc(*ln.act.done("new wS qS"))
                    yield
                    act.wait_ge(ln.pe.sem, ln.pe.past("new v rows", i))
                    act.activation(ln.v_rows[:, :], b2[N, 224:352], ACT.Copy).then_inc(*ln.act.done("new v rows"))
                    yield
                    act.wait_ge(ln.dve.sem, ln.dve.past("o gated", i - 1))
                    act.activation(ln.o[:, 0:SEQ], b0[:, :], ACT.Copy).then_inc(*ln.act.done("o"))
                    act.wait_ge(ln.act.sem, ln.act.past("o", i))
                    act.wait_ge(ln.dve.sem, ln.dve.past("new o", i))
                    act.activation(ln.sq[:, 1, :], ln.o[:, :], ACT.Square).then_inc(*ln.act.done("o square"))
                    yield
                    act.wait_ge(ln.pe.sem, ln.pe.past("o squares", i))
                    act.activation(ln.norm[:, 0, 0:SEQ], b0[:, :], ACT.Ln, scale=1.0 / P, bias=g.eps[:, 0:1])
                    act.activation(ln.norm[:, 0, NT], b2[:, 384:416], ACT.Ln, scale=1.0 / P, bias=g.eps[:, 0:1]
                                   ).then_inc(*ln.act.done("o log"))
                    act.wait_ge(ln.act.sem, ln.act.past("o log", i))
                    act.activation(ln.norm[:, 0, :], ln.norm[:, 0, :], ACT.Exp, scale=-0.5
                                   ).then_inc(*ln.act.done("o norm"))
                    yield

                for ln in lanes:
                    ln.act.credit(act)
                with act.Fori(0, rounds) as i:
                    alternate(rule, i)

            @block.vector
            def _(dve):
                def rule(ln, i):
                    b0, b1, b2, b3 = ln.bank
                    h = bass.ds(2 * i + ln.s, 1)
                    q, k = (g.qkv[:, bass.ds(2 * i + ln.s + HEADS * n, 1), :].rearrange("p a t -> p (a t)")
                            for n in range(2))
                    dve.wait_ge(ln.pe.sem, ln.pe.past("beta wide", i - 1))
                    dve.wait_ge(ln.act.sem, ln.act.past("v beta", i - 1))
                    for n, gate in ((G_, g.gate_g), (BETA, g.beta), (CUM, g.G), (TAIL, g.tail)):
                        dve.tensor_copy(ln.gates[:, n, :], gate[:, :, h].rearrange("p t a -> p (t a)"))
                    dve.tensor_copy(ln.gates[:, BETA_DECAY, :], g.eG[:, :, h].rearrange("p t a -> p (t a)")
                                    ).then_inc(*ln.dve.done("gates"))
                    dve.wait_ge(ln.dve.sem, ln.dve.past("gates", i))
                    dve.tensor_tensor(ln.gates[:, BETA_DECAY, :], ln.gates[:, BETA_DECAY, :], ln.gates[:, BETA, :],
                                      ALU.mult).then_inc(*ln.dve.done("k beta decay staged"))
                    yield
                    dve.wait_ge(ln.act.sem, ln.act.past("norms", i))
                    dve.tensor_tensor(ln.kT[:, :], k, ln.norm[:, 1, :], ALU.mult).then_inc(*ln.dve.done("k"))
                    dve.scalar_tensor_tensor(out=ln.qT[:, :], in0=q, scalar=float(P) ** -0.5, in1=ln.norm[:, 0, :],
                                             op0=ALU.mult, op1=ALU.mult).then_inc(*ln.dve.done("q"))
                    yield
                    dve.wait_ge(ln.pe.sem, ln.pe.past("k rows", i))
                    dve.wait_ge(ln.dve.sem, ln.dve.past("k beta decay staged", i))
                    for t in range(TILES):
                        dve.tensor_scalar(ln.kbe[:, t, :], b3[:, tile(t)], ln.gates[:, BETA_DECAY, t:t + 1], None,
                                          ALU.mult)
                    dve.tensor_scalar(ln.kbe[N, TILES, :], b2[N, 64:192], ln.gates[N, BETA_DECAY, TILES:TILES + 1],
                                      None, ALU.mult).then_inc(*ln.dve.done("k beta decay"))
                    yield
                    dve.wait_ge(ln.pe.sem, ln.pe.past("G wide", i))
                    for t in range(TILES):
                        dve.scalar_tensor_tensor(out=ln.dec[:, tile(t)], in0=b0[:, tile(t)],
                                                 scalar=ln.gates[:, CUM, t:t + 1], in1=g.const("decay_neg"),
                                                 op0=ALU.subtract, op1=ALU.add)
                    dve.scalar_tensor_tensor(out=ln.dec[N, NT], in0=b2[N, 384:416],
                                             scalar=ln.gates[N, CUM, TILES:TILES + 1],
                                             in1=new_const("decay_neg_new"), op0=ALU.subtract, op1=ALU.add
                                             ).then_inc(*ln.dve.done("difference"))
                    yield
                    dve.wait_ge(ln.act.sem, ln.act.past("decay", i))
                    dve.wait_ge(ln.pe.sem, ln.pe.past("beta wide", i))
                    dve.tensor_tensor(ln.QK[:, 0:SEQ], b3[:, :], ln.dec[:, 0:SEQ], ALU.mult)
                    dve.tensor_tensor(ln.QK[N, NT], b2[N, 352:384], ln.dec[N, NT], ALU.mult
                                      ).then_inc(*ln.dve.done("qk"))
                    dve.tensor_tensor(ln.LT[:, 0:SEQ], b1[:, :], ln.dec[:, 0:SEQ], ALU.mult)
                    dve.tensor_tensor(ln.LT[N, NT], b2[N, 320:352], ln.dec[N, NT], ALU.mult
                                      ).then_inc(*ln.dve.done("kk"))
                    dve.wait_ge(ln.dve.sem, ln.dve.past("kk", i))
                    dve.tensor_tensor(ln.LT[:, 0:SEQ], ln.LT[:, 0:SEQ], b0[:, :], ALU.mult)
                    dve.tensor_tensor(ln.LT[N, NT], ln.LT[N, NT], b2[N, 416:448], ALU.mult
                                      ).then_inc(*ln.dve.done("L"))
                    yield
                    dve.wait_ge(ln.pool.sem, ln.pool.past("level 0", i))
                    dve.scalar_tensor_tensor(out=tiled(ln.TT[:, 0:SEQ]), in0=tiled(ln.B[:, 0, 0:SEQ]), scalar=-1.0,
                                             in1=wide("ident"), op0=ALU.mult, op1=ALU.add)
                    dve.scalar_tensor_tensor(out=ln.TT[N, NT], in0=ln.B[N, 0, NT], scalar=-1.0,
                                             in1=new_const("ident"), op0=ALU.mult, op1=ALU.add
                                             ).then_inc(*ln.dve.done("TT 0"))
                    yield
                    for n in DOUBLINGS:
                        dve.wait_ge(ln.pe.sem, ln.pe.past(f"TT {n}", i))
                        if n == 1:
                            dve.tensor_tensor(ln.TT[N, NT], ln.TT[N, NT], b2[N, 64:96], ALU.subtract)
                        if n < LEVELS - 1:
                            dve.tensor_tensor(ln.T[:, 0:SEQ], ln.T[:, 0:SEQ], b3[:, :], ALU.subtract)
                        dve.tensor_tensor(ln.TT[:, 0:SEQ], ln.TT[:, 0:SEQ], b0[:, :], ALU.subtract
                                          ).then_inc(*ln.dve.done(f"T {n}"))
                        yield
                    dve.wait_ge(ln.act.sem, ln.act.past("u", i))
                    dve.wait_ge(ln.pool.sem, ln.pool.past("clear S", i))
                    for j in range(CHUNKS):
                        t, R = j // 2, slice(CHUNK * (j % 2), CHUNK * (j % 2 + 1))
                        dve.wait_ge(ln.pe.sem, ln.pe.past(f"wS {j}", i))
                        dve.tensor_tensor(ln.vn[R, :], ln.u[R, t, :], b1[R, 0:P], ALU.subtract
                                          ).then_inc(*ln.dve.done(f"v {j}"))
                        yield
                        dve.wait_ge(ln.pe.sem, ln.pe.past(f"KV {j}", i))
                        if j:
                            dve.wait_ge(ln.dve.sem, ln.dve.past(f"S {j - 1}", i))
                        dve.scalar_tensor_tensor(out=ln.S[:, :], in0=ln.S[:, :],
                                                 scalar=g.e_chunk[:, j:j + 1, h].rearrange("p a b -> p (a b)"),
                                                 in1=b3[:, 0:P], op0=ALU.mult, op1=ALU.add
                                                 ).then_inc(*ln.dve.done(f"S {j}"))
                        yield
                    dve.wait_ge(ln.act.sem, ln.act.past("new wS qS", i))
                    dve.tensor_tensor(ln.vT[:, :].rearrange("p (b t) -> p b t", t=DEC_SEQ),
                                      b2[:, 96:128].rearrange("p (b t) -> p b t", t=DEC_SEQ),
                                      ln.wSqS[:, :, 0, :], ALU.subtract).then_inc(*ln.dve.done("new v"))
                    yield
                    dve.wait_ge(ln.act.sem, ln.act.past("new v rows", i))
                    dve.tensor_tensor(ln.v_batch[:, :, :],
                                      ln.v_rows[:, :].unsqueeze(1).broadcast_to([NEW, DEC_BATCH, P]),
                                      g.const("batch_of", NEW).unsqueeze(2).broadcast_to([NEW, DEC_BATCH, P]),
                                      ALU.mult).then_inc(*ln.dve.done("new v by batch"))
                    dve.tensor_tensor(ln.S_new[:, :, :], ln.S_new[:, :, :],
                                      g.e_batch[:, :, h].broadcast_to([P, DEC_BATCH, P]), ALU.mult
                                      ).then_inc(*ln.dve.done("new S decayed"))
                    yield
                    dve.wait_ge(ln.pe.sem, ln.pe.past("new KV", i))
                    dve.wait_ge(ln.dve.sem, ln.dve.past("new S decayed", i))
                    for a, bank in enumerate((b1, b3)):
                        part = ln.S_new[:, 4 * a:4 * a + 4, :].rearrange("p b v -> p (b v)")
                        ins = dve.tensor_tensor(part, part, bank[:, :], ALU.add)
                    ins.then_inc(*ln.dve.done("new S"))
                    dve.wait_ge(ln.dve.sem, ln.dve.past("o gated", i - 1))
                    dve.tensor_tensor(ln.o[:, NT].rearrange("p (b t) -> p b t", t=DEC_SEQ),
                                      b2[:, 352:384].rearrange("p (b t) -> p b t", t=DEC_SEQ),
                                      ln.wSqS[:, :, 1, :], ALU.add).then_inc(*ln.dve.done("new o"))
                    yield
                    dve.wait_ge(ln.act.sem, ln.act.past("o norm", i))
                    dve.scalar_tensor_tensor(out=ln.o[:, :], in0=ln.o[:, :], scalar=g.gains[:, O_GAIN:O_GAIN + 1],
                                             in1=ln.norm[:, 0, :], op0=ALU.mult, op1=ALU.mult
                                             ).then_inc(*ln.dve.done("o normed"))
                    dve.wait_ge(ln.dve.sem, ln.dve.past("o normed", i))
                    z = head_of(g.zT, ln, i)
                    dve.tensor_tensor(z, z, ln.o[:, :], ALU.mult).then_inc(*ln.dve.done("o gated"))
                    yield

                for ln in lanes:
                    ln.dve.credit(dve)
                with dve.Fori(0, rounds) as i:
                    alternate(rule, i)

            @block.gpsimd
            def _(pool):
                def rule(ln, i):
                    pool.wait_ge(ln.sp.sem, ln.sp.past("states stored", i - 1))
                    pool.tensor_tensor(ln.S[:, :], g.const("ident"), g.const("ident"), ALU.subtract).then_inc(*ln.pool.done("clear S"))
                    pool.wait_ge(ln.act.sem, ln.act.past("eG wide", i))
                    pool.wait_ge(ln.dve.sem, ln.dve.past("q", i))
                    pool.wait_ge(ln.pe.sem, ln.pe.past("new wS qS", i - 1))
                    pool.tensor_tensor(ln.wq[:, 1, :], ln.qT[:, :], ln.sq[:, 0, :], ALU.mult
                                       ).then_inc(*ln.pool.done("q decayed"))
                    yield
                    pool.wait_ge(ln.dve.sem, ln.dve.past("L", i))
                    for n in range(LEVELS):
                        if n == 2:
                            pool.wait_ge(ln.dve.sem, ln.dve.past("TT 0", i))
                        if n > 2:
                            pool.wait_ge(ln.pe.sem, ln.pe.past(f"W {n - 2}", i))
                        if n < 2:
                            pool.tensor_tensor(ln.B[N, n, NT], ln.LT[N, NT], new_const(f"level{n}"), ALU.mult)
                        pool.tensor_tensor(tiled(ln.B[:, n % 2, 0:SEQ]), tiled(ln.LT[:, 0:SEQ]), wide(f"level{n}"),
                                           ALU.mult).then_inc(*ln.pool.done(f"level {n}"))
                        yield

                for ln in lanes:
                    ln.pool.credit(pool)
                with pool.Fori(0, rounds) as i:
                    alternate(rule, i)


def out_project_stage(nc, g, name, w_d, src):
    with Stage(nc, name) as st:
        w = [st.sb(f"w{s}", [P, KT, P]) for s in range(2)]
        acc = [st.ps(f"acc{s}", (P, 2, 512)) for s in range(2)]
        loaded = [st.sem(f"loaded{s}") for s in range(2)]
        multiplied, added = st.sem("multiplied"), st.sem("added")
        with st.block() as block:
            @block.sync
            def _(sp):
                for m in range(KT):
                    if m >= 2:
                        sp.wait_ge(multiplied, m - 1)
                    sp.dma_start(w[m % 2][:, :, :], w_d[m]).then_inc(loaded[m % 2], 16)

            @block.tensor
            def _(pe):
                for m in range(KT):
                    pe.wait_ge(loaded[m % 2], 16 * (m // 2 + 1))
                    if m >= 2:
                        pe.wait_ge(added, m - 1)
                    for k in range(KT):
                        for a in range(2):
                            mm = pe.matmul(acc[m % 2][:, a, 0:HALF], w[m % 2][:, k, :],
                                           src[:, k, a * HALF:(a + 1) * HALF], start=(k == 0), stop=(k == KT - 1))
                    mm.then_inc(multiplied, 1)

            @block.vector
            def _(dve):
                for m in range(KT):
                    dve.wait_ge(multiplied, m + 1)
                    dve.tensor_tensor(halves(g.xT[:, m, :]), acc[m % 2][:, :, 0:HALF], halves(g.xT[:, m, :]),
                                      ALU.add).then_inc(added, 1)


SLOTS = P
PASSES = -(-TOKENS // SLOTS)
COLUMNS = PASSES * EXPERTS
SRC, DST, WEIGHT, WORDS = 0, 1, 2, 4
NOWHERE = 1 << 20


def router_stage(nc, g, name, layer):
    NT = TILES + 1
    n_log = GROUPS + EXPERTS
    with Stage(nc, name) as st:
        w = st.sb("w", [P, KT, n_log])
        bias = st.sb("bias", [P, n_log])
        logits = st.sb("logits", [P, NT, n_log])

        def col(x):
            return st.sb(x, [P, NT, 1])
        grp_max, grp_sum, grp_pick, m1, m2, p1, p2, e2, den = (
            col(x) for x in ("grp_max", "grp_sum", "grp_pick", "m1", "m2", "p1", "p2", "e2", "den"))
        weight = [col("w1"), col("w2")]
        place, over, address = col("place"), col("over"), col("address")
        e_grp = st.sb("e_grp", [P, NT, GROUPS])
        grp = st.sb("grp", [P, NT, GROUPS])
        inside, part, rest = (st.sb(x, [P, NT, PER_GROUP]) for x in ("inside", "part", "rest"))
        pick = [st.sb(x, [P, NT, PER_GROUP]) for x in ("first", "second")]
        onehot = [st.sb(f"onehot{j}", [P, NT, EXPERTS]) for j in range(2)]
        picked = st.sb("picked", [P, NT, EXPERTS])
        earlier = st.sb("earlier", [P, NT, EXPERTS])
        at_pick = st.sb("at_pick", [P, NT, EXPERTS])
        fullest, n_pass = st.sb("fullest", [P, 1]), st.sb("n_pass", [P, 1])
        slot_of = [st.sb(f"slot_of{j}", [P, NT], U32) for j in range(2)]
        entry = [st.sb(f"entry{j}", [P, NT, WORDS], U32) for j in range(2)]
        empty = st.sb("empty", [P, COLUMNS + 2, WORDS], U32)
        rows = [st.sb(f"rows{s}", [P, D_MODEL]) for s in range(2)]
        proj, counts = st.ps("proj"), st.ps("counts")
        turned = [st.ps(f"turned{s}", (P, 2, 512)) for s in range(2)]
        loaded, emptied, cleared = st.sem("loaded"), st.sem("emptied"), st.sem("cleared")
        stored = [st.sem(f"stored{s}") for s in range(2)]
        scattered, table_in = st.software_dma_sem("scattered"), st.sem("table_in")
        pe_done, rows_turned, rows_out, dve_step, act_done = (
            st.sem(x) for x in ("pe_done", "rows_turned", "rows_out", "dve_step", "act_done"))
        rows_of = [P] * TILES + [NEW]
        pr = proj[:, 0:NT * n_log].rearrange("p (t n) -> p t n", n=n_log)
        cn = counts[:, 0:(NT + 1) * EXPERTS].rearrange("p (t n) -> p t n", n=EXPERTS)
        at = {}

        with st.block() as block:
            @block.vector
            def _(dve):
                taken = [0]

                def step(ins):
                    ins.then_inc(dve_step, 1)
                    taken[0] += 1
                    dve.wait_ge(dve_step, taken[0])

                def wide(t, n):
                    return t[:, :, :].broadcast_to([P, NT, n])

                def first_of(out, top_at, like, top_value, n):
                    step(dve.tensor_tensor(out, like, wide(top_value, n), ALU.is_equal))
                    order = g.const("first_pick")[:, 0:n].unsqueeze(1).broadcast_to([P, NT, n])
                    step(dve.tensor_tensor(out, out, order, ALU.mult))
                    step(dve.tensor_reduce(top_at[:, :, :], out, AX_X, ALU.max))
                    step(dve.tensor_tensor(out, out, wide(top_at, n), ALU.is_equal))

                step(dve.memset(empty[:, :, :], NOWHERE))
                dve.memset(empty[:, :, WEIGHT:WORDS], 0).then_inc(cleared, 1)
                for j in range(2):
                    dve.memset(entry[j][:, :, :], 0)
                step(dve.memset(logits[:, :, :], 0.0))
                dve.wait_ge(loaded, 32)
                dve.wait_ge(pe_done, 1)
                b = bias[:, :].unsqueeze(1)
                step(dve.tensor_tensor(logits[:, 0:TILES, :], pr[:, 0:TILES, :], b.broadcast_to([P, TILES, n_log]),
                                       ALU.add))
                step(dve.tensor_tensor(logits[0:NEW, TILES:NT, :], pr[0:NEW, TILES:NT, :],
                                       bias[0:NEW, :].unsqueeze(1), ALU.add))
                lg = logits[:, :, 0:GROUPS]
                step(dve.tensor_reduce(grp_max[:, :, :], lg, AX_X, ALU.max))
                step(dve.tensor_tensor(e_grp[:, :, :], lg, wide(grp_max, GROUPS), ALU.subtract))
                at["group logits"] = taken[0]
                first_of(grp[:, :, :], grp_pick, lg, grp_max, GROUPS)
                for k in range(GROUPS):
                    le = logits[:, :, GROUPS + k * PER_GROUP:GROUPS + (k + 1) * PER_GROUP]
                    own = grp[:, :, k:k + 1].broadcast_to([P, NT, PER_GROUP])
                    if k == 0:
                        step(dve.tensor_tensor(inside[:, :, :], le, own, ALU.mult))
                    else:
                        step(dve.tensor_tensor(part[:, :, :], le, own, ALU.mult))
                        step(dve.tensor_tensor(inside[:, :, :], inside[:, :, :], part[:, :, :], ALU.add))
                step(dve.tensor_reduce(m1[:, :, :], inside[:, :, :], AX_X, ALU.max))
                first_of(pick[0][:, :, :], p1, inside[:, :, :], m1, PER_GROUP)
                step(dve.scalar_tensor_tensor(out=rest[:, :, :], in0=pick[0][:, :, :], scalar=NEG,
                                              in1=inside[:, :, :], op0=ALU.mult, op1=ALU.add))
                step(dve.tensor_reduce(m2[:, :, :], rest[:, :, :], AX_X, ALU.max))
                step(dve.tensor_tensor(e2[:, :, :], m2[:, :, :], m1[:, :, :], ALU.subtract))
                at["pair logits"] = taken[0]
                first_of(pick[1][:, :, :], p2, rest[:, :, :], m2, PER_GROUP)
                for j in range(2):
                    for k in range(GROUPS):
                        ins = dve.tensor_tensor(onehot[j][:, :, k * PER_GROUP:(k + 1) * PER_GROUP],
                                                pick[j][:, :, :], grp[:, :, k:k + 1].broadcast_to([P, NT, PER_GROUP]),
                                                ALU.mult)
                step(ins)
                step(dve.tensor_tensor(picked[:, :, :], onehot[0][:, :, :], onehot[1][:, :, :], ALU.add))
                at["picked"] = taken[0]
                dve.wait_ge(act_done, 2)
                step(dve.tensor_reduce(grp_sum[:, :, :], e_grp[:, :, :], AX_X, ALU.add))
                step(dve.scalar_tensor_tensor(out=den[:, :, :], in0=e2[:, :, :], scalar=1.0, in1=grp_sum[:, :, :],
                                              op0=ALU.add, op1=ALU.mult))
                step(dve.reciprocal(weight[0][:, :, :], den[:, :, :]))
                step(dve.tensor_tensor(weight[1][:, :, :], weight[0][:, :, :], e2[:, :, :], ALU.mult))
                dve.wait_ge(pe_done, 2)
                step(dve.memset(earlier[:, :, :], 0.0))
                dve.tensor_copy(earlier[:, 0:TILES, :], cn[:, 0:TILES, :])
                dve.tensor_copy(earlier[0:NEW, TILES, :], cn[0:NEW, TILES, :])
                step(dve.tensor_reduce(fullest[:, :], cn[:, NT, :], AX_X, ALU.max))
                step(dve.tensor_scalar(n_pass[:, :], fullest[:, :], float(SLOTS), 1.0, ALU.is_gt, ALU.add))
                for m in range(2, PASSES):
                    step(dve.scalar_tensor_tensor(out=n_pass[:, :], in0=fullest[:, :], scalar=float(m * SLOTS),
                                                  in1=n_pass[:, :], op0=ALU.is_gt, op1=ALU.add))
                step(dve.tensor_copy(g.passes[:, :], n_pass[0:1, :]))
                for j in range(2):
                    step(dve.tensor_tensor(at_pick[:, :, :], earlier[:, :, :], onehot[j][:, :, :], ALU.mult))
                    step(dve.tensor_reduce(place[:, :, :], at_pick[:, :, :], AX_X, ALU.add))
                    step(dve.tensor_tensor(at_pick[:, :, :], onehot[j][:, :, :],
                                           g.const("expert").unsqueeze(1).broadcast_to([P, NT, EXPERTS]), ALU.mult))
                    step(dve.tensor_reduce(address[:, :, :], at_pick[:, :, :], AX_X, ALU.add))
                    step(dve.scalar_tensor_tensor(out=address[:, :, :], in0=place[:, :, :], scalar=float(COLUMNS + 2),
                                                  in1=address[:, :, :], op0=ALU.mult, op1=ALU.add))
                    for m in range(1, PASSES):
                        step(dve.tensor_scalar(over[:, :, :], place[:, :, :], float(m * SLOTS),
                                               float(EXPERTS - SLOTS * (COLUMNS + 2)), ALU.is_ge, ALU.mult))
                        step(dve.tensor_tensor(address[:, :, :], address[:, :, :], over[:, :, :], ALU.add))
                    dve.tensor_copy(slot_of[j][:, :], address[:, :, 0])
                    dve.tensor_copy(entry[j][:, :, SRC], g.const("token"))
                    dve.tensor_scalar(entry[j][:, :, DST], g.const("token"), float(j * TOKENS), None, ALU.add)
                    step(dve.tensor_copy(entry[j][:, :, WEIGHT:WEIGHT + 1].bitcast(F32), weight[j][:, :, :]))
                    at[f"entry {j}"] = taken[0]

            @block.sync
            def _(sp):
                sp.dma_start(w[:, :, :], g.d["router_w"][layer]).then_inc(loaded, 16)
                sp.dma_start(bias[:, :], g.d["router_b"][layer]).then_inc(loaded, 16)
                sp.wait_ge(cleared, 1)
                sp.dma_start(g.d["table"], empty[:, :, :]).then_inc(emptied, 16)
                for t, n in enumerate(rows_of):
                    sp.wait_ge(rows_out, t + 1)
                    sp.dma_start(g.d["h_rows"][t * P:t * P + n, :], rows[t % 2][0:n, :]).then_inc(stored[t % 2], 16)
                sp.wait_ge(scattered, 16 * 2 * NT)
                sp.dma_start(g.table[:, :, :], g.d["table"]).then_inc(table_in, 16)
                sp.wait_ge(table_in, 16)
                for s in range(2):
                    sp.wait_ge(stored[s], 16 * ((NT + 1 - s) // 2))

            @block.gpsimd
            def _(pool):
                pool.wait_ge(emptied, 16)
                flat = g.d["table"].rearrange("p c w -> (p c) w")
                for j in range(2):
                    pool.wait_ge(dve_step, at[f"entry {j}"])
                    for t, n in enumerate(rows_of):
                        pool.indirect_dma_start(
                            out=flat, out_offset=bass.IndirectOffsetOnAxis(ap=slot_of[j][0:n, t:t + 1], axis=0),
                            in_=entry[j][0:n, t, :], in_offset=None).then_inc(scattered, 16)

            @block.scalar
            def _(act):
                def rows_copied(t):
                    act.wait_ge(rows_turned, t + 1)
                    if t >= 2:
                        act.wait_ge(stored[t % 2], 16 * (t // 2))
                    n = rows_of[t]
                    act.activation(rows[t % 2][0:n, :].rearrange("p (a c) -> p a c", a=2), turned[t % 2][0:n, :, :],
                                   ACT.Copy).then_inc(rows_out, 1)
                act.wait_ge(dve_step, at["group logits"])
                act.activation(e_grp[:, :, :], e_grp[:, :, :], ACT.Exp).then_inc(act_done, 1)
                rows_copied(0)
                rows_copied(1)
                act.wait_ge(dve_step, at["pair logits"])
                act.activation(e2[:, :, :], e2[:, :, :], ACT.Exp).then_inc(act_done, 1)
                for t in range(2, NT):
                    rows_copied(t)

            @block.tensor
            def _(pe):
                pe.wait_ge(loaded, 32)
                for t, n in enumerate(rows_of):
                    for k in range(KT):
                        mm = pe.matmul(pr[0:n, t, :], g.hT[:, k, t * P:t * P + n], w[:, k, :],
                                       start=(k == 0), stop=(k == KT - 1))
                mm.then_inc(pe_done, 1)

                def turn(t):
                    n = rows_of[t]
                    if t >= 2:
                        pe.wait_ge(rows_out, t - 1)
                    for k in range(KT):
                        mm = pe.transpose(turned[t % 2][0:n, k // 4, (k % 4) * P:(k % 4 + 1) * P],
                                          g.hT[:, k, t * P:t * P + n], g.const("ident"))
                    mm.then_inc(rows_turned, 1)
                for t in range(NT):
                    turn(t)
                pe.wait_ge(dve_step, at["picked"])
                for t in range(NT + 1):
                    n = rows_of[t] if t < NT else P
                    for u in range(min(t, TILES)):
                        pe.matmul(cn[0:n, t, :], g.const("ones")[:, 0:n], picked[:, u, :],
                                  start=(u == 0), stop=False)
                    if t < NT:
                        mm = pe.matmul(cn[0:n, t, :], g.const("before", n)[:, 0:n], picked[0:n, t, :],
                                       start=(t == 0), stop=True)
                    else:
                        mm = pe.matmul(cn[:, t, :], g.const("ones", NEW), picked[0:NEW, TILES, :],
                                       start=False, stop=True)
                mm.then_inc(pe_done, 1)


MOE_PE = ["rows turned"] + ["gate up 0", "gate up 1", "h turned 0", "h turned 1", "down"]
MOE_ACT = ["x low"] + ["silu 0", "silu 1", "hT 0", "hT 1", "y low"]
MOE_DVE = ["x high"] + ["h 0", "h 1", "y high"]


def experts_stage(nc, g, name, layer):
    with Stage(nc, name) as st:
        class Lane:
            pass
        lanes = []
        for s in range(2):
            ln = Lane()
            lanes.append(ln)
            ln.s = s
            ln.gu = st.sb(f"gu{s}", [P, KT, 2 * FF])
            ln.down = st.sb(f"down{s}", [P, FF // P, D_MODEL])
            ln.x = st.sb(f"x{s}", [P, D_MODEL])
            ln.xT = st.sb(f"xT{s}", [P, KT, P])
            ln.gate = st.sb(f"gate{s}", [P, FF])
            ln.h = st.sb(f"h{s}", [P, FF])
            ln.hT = st.sb(f"hT{s}", [P, FF])
            ln.y = st.sb(f"y{s}", [P, D_MODEL])
            ln.src = st.sb(f"src{s}", [P, WORDS], U32)
            ln.dst = st.sb(f"dst{s}", [P, WORDS], U32)
            ln.gu_in, ln.down_in = st.sem(f"gu_in{s}"), st.sem(f"down_in{s}")
            ln.x_in, ln.y_out = st.software_dma_sem(f"x_in{s}"), st.software_dma_sem(f"y_out{s}")
            ln.pe, ln.act = st.steps(f"pe{s}", MOE_PE), st.steps(f"act{s}", MOE_ACT)
            ln.dve = st.steps(f"dve{s}", MOE_DVE)
            ln.source, ln.dest = st.steps(f"source{s}", ["read"]), st.steps(f"dest{s}", ["read"])
        x_bank, gu_bank, y_bank = ([st.ps(f"{x}{n}") for n in range(2)] for x in ("bank_x", "bank_gu", "bank_y"))
        h_bank = [st.ps(f"bank_h{n}") for n in range(2)]
        zeroed = st.sem("zeroed")
        rounds = EXPERTS // 2

        def over_experts(eng, body):
            passes = eng.value_load(g.passes[0:1, 0:1], min_val=1, max_val=PASSES)
            with eng.Fori(0, passes) as p:
                with eng.Fori(0, rounds) as i:
                    body(p * rounds + i, i)
            return passes

        def before(ln, r):
            return lanes[1 - ln.s], (r if ln.s else r - 1)

        with st.block() as block:
            @block.sync
            def _(sp):
                def body(r, i):
                    for ln in lanes:
                        expert = bass.ds(2 * i + ln.s, 1)
                        sp.wait_ge(ln.pe.sem, ln.pe.past("gate up 1", r - 1))
                        sp.dma_start(ln.gu[:, :, :], g.d["w_gate_up"][layer][expert].rearrange("e p k f -> (e p) k f")
                                     ).then_inc(ln.gu_in, 16)
                        sp.wait_ge(ln.pe.sem, ln.pe.past("down", r - 1))
                        sp.dma_start(ln.down[:, :, :], g.d["w_down"][layer][expert].rearrange("e p k f -> (e p) k f")
                                     ).then_inc(ln.down_in, 16)
                over_experts(sp, body)

            @block.gpsimd
            def _(pool):
                def gather(ln, column):
                    pool.tensor_copy(ln.src[:, :], g.table[:, bass.ds(column, 1), :].rearrange("p a w -> p (a w)")
                                     ).then_inc(*ln.source.done("read"))

                def scatter(ln):
                    pool.nop(nofuse=True)
                    pool.indirect_dma_start(
                        out=g.d["y_rows"], out_offset=bass.IndirectOffsetOnAxis(ap=ln.dst[:, DST:DST + 1], axis=0),
                        in_=ln.y[:, :], in_offset=None, bounds_check=2 * TOKENS - 1, oob_is_err=False
                    ).then_inc(ln.y_out, 16)

                def fetch(ln, r):
                    pool.wait_ge(ln.source.sem, ln.source.past("read", r))
                    pool.nop(nofuse=True)
                    pool.indirect_dma_start(
                        out=ln.x[:, :], out_offset=None, in_=g.d["h_rows"],
                        in_offset=bass.IndirectOffsetOnAxis(ap=ln.src[:, SRC:SRC + 1], axis=0),
                        bounds_check=TOKENS - 1, oob_is_err=False).then_inc(ln.x_in, 16)

                for ln in lanes:
                    ln.source.credit(pool)
                pool.wait_ge(zeroed, 4)
                for ln in lanes:
                    pool.tensor_copy(ln.dst[:, :], g.table[:, COLUMNS, :]).then_inc(*ln.dest.done("read"))
                for ln in lanes:
                    pool.wait_ge(ln.dest.sem, 1)
                    scatter(ln)
                for ln in lanes:
                    gather(ln, ln.s)
                for ln in lanes:
                    fetch(ln, 0)

                def body(r, i):
                    for ln in lanes:
                        pool.wait_ge(ln.y_out, 16 * (r + 1))
                        pool.tensor_copy(ln.dst[:, :], g.table[:, bass.ds(2 * r + ln.s, 1), :].rearrange(
                            "p a w -> p (a w)")).then_inc(*ln.dest.done("read"))
                    for ln in lanes:
                        pool.wait_ge(ln.x_in, 16 * (r + 1))
                        pool.wait_ge(ln.pe.sem, ln.pe.past("rows turned", r))
                        gather(ln, 2 * r + 2 + ln.s)
                    for ln in lanes:
                        fetch(ln, r + 1)
                    for ln in lanes:
                        pool.wait_ge(ln.dest.sem, ln.dest.past("read", r))
                        pool.wait_ge(ln.act.sem, ln.act.past("y low", r))
                        pool.wait_ge(ln.dve.sem, ln.dve.past("y high", r))
                        scatter(ln)
                passes = over_experts(pool, body)
                for ln in lanes:
                    pool.wait_ge(ln.x_in, 16 * (passes * rounds + 1))
                    pool.wait_ge(ln.y_out, 16 * (passes * rounds + 1))

            @block.tensor
            def _(pe):
                for ln in lanes:
                    ln.pe.credit(pe)
                ident = g.const("ident")

                def body(r, i):
                    for ln in lanes:
                        other, ro = before(ln, r)
                        pe.wait_ge(ln.x_in, 16 * (r + 1))
                        pe.wait_ge(other.act.sem, other.act.past("x low", ro))
                        pe.wait_ge(other.dve.sem, other.dve.past("x high", ro))
                        for k in range(KT):
                            mm = pe.transpose(x_bank[k // 4][:, (k % 4) * P:(k % 4 + 1) * P],
                                              ln.x[:, k * P:(k + 1) * P], ident)
                        mm.then_inc(*ln.pe.done("rows turned"))
                    for ln in lanes:
                        other, ro = before(ln, r)
                        pe.wait_ge(ln.gu_in, 16 * (r + 1))
                        pe.wait_ge(ln.act.sem, ln.act.past("x low", r))
                        pe.wait_ge(ln.dve.sem, ln.dve.past("x high", r))
                        for m in range(2):
                            pe.wait_ge(other.dve.sem, other.dve.past(f"h {m}", ro))
                            for k in range(KT):
                                mm = pe.matmul(gu_bank[m][:, 0:FF], ln.xT[:, k, :], ln.gu[:, k, m * FF:(m + 1) * FF],
                                               start=(k == 0), stop=(k == KT - 1))
                            mm.then_inc(*ln.pe.done(f"gate up {m}"))
                        pe.wait_ge(ln.down_in, 16 * (r + 1))
                        for m in range(2):
                            pe.wait_ge(ln.dve.sem, ln.dve.past(f"h {m}", r))
                            pe.wait_ge(other.act.sem, other.act.past(f"hT {m}", ro))
                            pe.transpose(h_bank[m][:, 0:P], ln.h[:, m * P:(m + 1) * P], ident
                                         ).then_inc(*ln.pe.done(f"h turned {m}"))
                        for m in range(2):
                            pe.wait_ge(ln.act.sem, ln.act.past(f"hT {m}", r))
                            if m == 0:
                                pe.wait_ge(other.act.sem, other.act.past("y low", ro))
                                pe.wait_ge(other.dve.sem, other.dve.past("y high", ro))
                            for a in range(2):
                                mm = pe.matmul(y_bank[a][:, :], ln.hT[:, m * P:(m + 1) * P],
                                               ln.down[:, m, a * 512:(a + 1) * 512], start=(m == 0), stop=(m == 1))
                        mm.then_inc(*ln.pe.done("down"))
                over_experts(pe, body)

            @block.scalar
            def _(act):
                for ln in lanes:
                    ln.act.credit(act)

                def body(r, i):
                    for ln in lanes:
                        act.wait_ge(ln.pe.sem, ln.pe.past("rows turned", r))
                        act.activation(ln.xT[:, 0:KT // 2, :].rearrange("p k c -> p (k c)"), x_bank[0][:, :],
                                       ACT.Copy).then_inc(*ln.act.done("x low"))
                    for ln in lanes:
                        for m in range(2):
                            act.wait_ge(ln.pe.sem, ln.pe.past(f"gate up {m}", r))
                            act.wait_ge(ln.dve.sem, ln.dve.past(f"h {m}", r - 1))
                            act.activation(ln.gate[:, m * P:(m + 1) * P], gu_bank[m][:, 0:P], ACT.Silu
                                           ).then_inc(*ln.act.done(f"silu {m}"))
                        for m in range(2):
                            act.wait_ge(ln.pe.sem, ln.pe.past(f"h turned {m}", r))
                            act.activation(ln.hT[:, m * P:(m + 1) * P], h_bank[m][:, 0:P], ACT.Copy
                                           ).then_inc(*ln.act.done(f"hT {m}"))
                        act.wait_ge(ln.pe.sem, ln.pe.past("down", r))
                        act.wait_ge(ln.y_out, 16 * (r + 1))
                        act.activation(ln.y[:, 0:512], y_bank[0][:, :], ACT.Copy).then_inc(*ln.act.done("y low"))
                over_experts(act, body)

            @block.vector
            def _(dve):
                for ln in lanes:
                    ln.dve.credit(dve)
                    dve.memset(ln.x[:, :], 0.0).then_inc(zeroed, 1)
                    dve.memset(ln.y[:, :], 0.0).then_inc(zeroed, 1)

                def body(r, i):
                    for ln in lanes:
                        dve.wait_ge(ln.pe.sem, ln.pe.past("rows turned", r))
                        dve.tensor_copy(ln.xT[:, KT // 2:, :].rearrange("p k c -> p (k c)"), x_bank[1][:, :]
                                        ).then_inc(*ln.dve.done("x high"))
                    for ln in lanes:
                        weight = g.table[:, bass.ds(2 * r + ln.s, 1), WEIGHT:WEIGHT + 1].rearrange("p a w -> p (a w)")
                        for m in range(2):
                            dve.wait_ge(ln.act.sem, ln.act.past(f"silu {m}", r))
                            dve.wait_ge(ln.pe.sem, ln.pe.past(f"gate up {m}", r))
                            dve.scalar_tensor_tensor(out=ln.h[:, m * P:(m + 1) * P], in0=gu_bank[m][:, P:2 * P],
                                                     scalar=weight.bitcast(F32), in1=ln.gate[:, m * P:(m + 1) * P],
                                                     op0=ALU.mult, op1=ALU.mult).then_inc(*ln.dve.done(f"h {m}"))
                        dve.wait_ge(ln.pe.sem, ln.pe.past("down", r))
                        dve.wait_ge(ln.y_out, 16 * (r + 1))
                        dve.tensor_copy(ln.y[:, 512:], y_bank[1][:, :]).then_inc(*ln.dve.done("y high"))
                over_experts(dve, body)


def gather_results_stage(nc, g, name):
    NT = TILES + 1
    rows_of = [P] * TILES + [NEW]
    with Stage(nc, name) as st:
        y = [[st.sb(f"y{s}{j}", [P, D_MODEL]) for j in range(2)] for s in range(2)]
        turned = [st.ps(f"turned{s}", (P, 2, 512)) for s in range(2)]
        loaded = [st.sem(f"loaded{s}") for s in range(2)]
        summed, turned_s, added = st.sem("summed"), st.sem("turned_s"), st.sem("added")
        with st.block() as block:
            @block.sync
            def _(sp):
                for t, n in enumerate(rows_of):
                    if t >= 2:
                        sp.wait_ge(turned_s, t - 1)
                    for j in range(2):
                        at = j * TOKENS + t * P
                        sp.dma_start(y[t % 2][j][0:n, :], g.d["y_rows"][at:at + n, :]).then_inc(loaded[t % 2], 16)

            @block.tensor
            def _(pe):
                for t, n in enumerate(rows_of):
                    pe.wait_ge(summed, t + 1)
                    if t >= 2:
                        pe.wait_ge(added, t - 1)
                    for k in range(KT):
                        mm = pe.transpose(turned[t % 2][:, k // 4, (k % 4) * n:(k % 4 + 1) * n],
                                          y[t % 2][0][0:n, k * P:(k + 1) * P], g.const("ident", n)[:, 0:n])
                    mm.then_inc(turned_s, 1)

            @block.vector
            def _(dve):
                def add(t):
                    n = rows_of[t]
                    dve.wait_ge(turned_s, t + 1)
                    x = g.xT[:, :, t * P:t * P + n].rearrange("p (a k) c -> p a k c", a=2)
                    dve.tensor_tensor(x, turned[t % 2][:, :, 0:4 * n].rearrange("p a (k c) -> p a k c", k=4), x,
                                      ALU.add).then_inc(added, 1)
                for t, n in enumerate(rows_of):
                    dve.wait_ge(loaded[t % 2], 32 * (t // 2 + 1))
                    dve.tensor_tensor(y[t % 2][0][0:n, :], y[t % 2][0][0:n, :], y[t % 2][1][0:n, :], ALU.add
                                      ).then_inc(summed, 1)
                    if t:
                        add(t - 1)
                add(NT - 1)


def moe(nc, g, name, layer, gain0):
    with ExitStack() as ctx:
        g.table = ctx.enter_context(nc.sbuf_tensor(name + "_table", [P, COLUMNS + 2, WORDS], U32))
        g.passes = ctx.enter_context(nc.sbuf_tensor(name + "_passes", [1, 1], I32))
        with nc.sbuf_tensor(name + "_h", [P, KT, TOKENS], F32) as g.hT:
            rms_norm_stage(nc, g, name + "_norm", gain0)
            router_stage(nc, g, name + "_router", layer)
        experts_stage(nc, g, name + "_experts", layer)
        gather_results_stage(nc, g, name + "_results")


Q_TILES = NSA_HEADS // 2
CMP_K, CMP_V, SLC_K, SLC_V, WIN_K, WIN_V = (Q_TILES + 2 * n for n in range(6))
NSA_TILES = Q_TILES + 12
ROWS = NSA_HEADS * DEC_SEQ
BLOCKS = PAST // CMP
P_BLOCKS = SEQ // CMP


def nsa_project_stage(nc, g):
    with Stage(nc, "nproj") as st:
        w = [st.sb(f"w{s}", [P, KT, P]) for s in range(2)]
        wg = st.sb("wg", [P, KT, 3 * NSA_HEADS])
        new_gates = st.sb("new_gates", [NEW, 3 * NSA_HEADS])
        acc = [st.ps(f"acc{s}", (P, 2, 512)) for s in range(2)]
        gate_acc = st.ps("gate_acc")
        loaded = [st.sem(f"loaded{s}") for s in range(2)]
        gates_loaded, gates_done, new_gates_done = st.sem("gates_loaded"), st.sem("gates_done"), st.sem("new_gates_done")
        spread, sums_in = st.sem("spread"), st.sem("sums_in")
        pe_s = [st.steps(f"pe{s}", ["product"]) for s in range(2)]
        act_s = [st.steps(f"act{s}", ["copied"]) for s in range(2)]
        rounds = NSA_TILES // 2
        NG = 3 * NSA_HEADS
        pages = PageSums(nc, g, st, g.past_c, PAGES_EARLY, PAGES_NSA)
        with st.block() as block:
            @block.sync
            def _(sp):
                sp.dma_start(wg[:, :, :], g.d["nsa_w_gates"]).then_inc(gates_loaded, 16)
                sp.dma_start(g.past_c[:, 0:PAGES_EARLY, :], g.d["first_sums"]).then_inc(sums_in, 16)
                for s in range(2):
                    sp.dma_start(w[s][:, :, :], g.d["nsa_w"][s]).then_inc(loaded[s], 16)
                with sp.Fori(0, rounds - 1) as i:
                    for s in range(2):
                        sp.wait_ge(pe_s[s].sem, pe_s[s].past("product", i))
                        sp.dma_start(w[s][:, :, :],
                                     g.d["nsa_w"][bass.ds(2 * i + 2 + s, 1)].rearrange("t p k c -> (t p) k c")
                                     ).then_inc(loaded[s], 16)
                        pages.load(sp, s, i)
                for s in range(2):
                    pages.load(sp, s, rounds - 1)
                sp.wait_ge(new_gates_done, 1)
                sp.dma_start(g.d["gate_scratch"], new_gates[:, :]).then_inc(spread, 16)
                sp.wait_ge(spread, 16)
                for t in range(DEC_SEQ):
                    src = g.d["gate_scratch"].rearrange("(b t) (h r) -> t h b r", t=DEC_SEQ, r=3)
                    sp.dma_start(g.row_gates[t:ROWS:DEC_SEQ, :, :], src[t]).then_inc(spread, 16)
                sp.wait_ge(spread, 16 * (1 + DEC_SEQ))
                sp.wait_ge(sums_in, 16)

            @block.tensor
            def _(pe):
                for s in range(2):
                    pe_s[s].credit(pe)
                pe.wait_ge(gates_loaded, 16)
                for t in range(TILES + 1):
                    n = P if t < TILES else NEW
                    for k in range(KT):
                        mm = pe.matmul(gate_acc[0:n, t * NG:(t + 1) * NG], g.hT[:, k, t * P:t * P + n], wg[:, k, :],
                                       start=(k == 0), stop=(k == KT - 1))
                mm.then_inc(gates_done, 1)
                with pe.Fori(0, rounds) as i:
                    for s in range(2):
                        pe.wait_ge(loaded[s], 16 * (i + 1))
                        pe.wait_ge(act_s[s].sem, act_s[s].past("copied", i - 1))
                        for k in range(KT):
                            for a in range(2):
                                mm = pe.matmul(acc[s][:, a, 0:HALF], w[s][:, k, :],
                                               g.hT[:, k, a * HALF:(a + 1) * HALF], start=(k == 0), stop=(k == KT - 1))
                        mm.then_inc(*pe_s[s].done("product"))

            @block.vector
            def _(dve):
                pages.credit(dve)
                with dve.Fori(0, rounds) as i:
                    for s in range(2):
                        pages.sum(dve, s, i)

            @block.scalar
            def _(act):
                for s in range(2):
                    act_s[s].credit(act)
                act.wait_ge(gates_done, 1)
                act.activation(new_gates[:, :], gate_acc[0:NEW, TILES * NG:(TILES + 1) * NG], ACT.Sigmoid
                               ).then_inc(new_gates_done, 1)
                act.activation(g.gates[:, :, :, :].rearrange("p t h r -> p (t h r)"), gate_acc[:, 0:TILES * NG],
                               ACT.Sigmoid)
                with act.Fori(0, rounds) as i:
                    for s in range(2):
                        act.wait_ge(pe_s[s].sem, pe_s[s].past("product", i))
                        act.activation(halves(g.proj[:, bass.ds(2 * i + s, 1), :].rearrange("p a t -> p (a t)")),
                                       acc[s][:, :, 0:HALF], ACT.Copy).then_inc(*act_s[s].done("copied"))


def nsa_norm_stage(nc, g):
    normed = list(range(Q_TILES)) + [SLC_K, SLC_K + 1, WIN_K, WIN_K + 1]
    n_norm = len(normed) + 1
    with Stage(nc, "nnorm") as st:
        sq = [st.sb(f"sq{s}", [P, TOKENS]) for s in range(2)]
        root = [st.sb(f"root{s}", [P, TOKENS]) for s in range(2)]
        means = st.sb("means", [P, 4, P_BLOCKS])
        total = [st.ps(f"total{s}", (P, 2, 512)) for s in range(2)]
        turn = [st.ps(f"turn{s}") for s in range(2)]
        squared, summed, rooted = st.sem("squared"), st.sem("summed"), st.sem("rooted")
        logged, normalised = st.sem("logged"), st.sem("normalised")
        turned, turn_out = st.sem("turned"), st.sem("turn_out")
        averaged, cleared = st.sem("averaged"), st.sem("cleared")
        stored = st.sem("stored")
        ident = g.const("ident")
        turns = []
        for n, V in enumerate((SLC_V, WIN_V)):
            for pair in range(2):
                for t in range(TILES):
                    turns.append((g.proj[:, V + pair, t * P:(t + 1) * P], g.v_rows[:, n, t, pair * P:(pair + 1) * P]))
                turns.append((g.proj[:, V + pair, SEQ:TOKENS], g.v_new[:, n, pair * P:(pair + 1) * P]))
        for pair in range(2):
            turns.append((means[:, 2 + pair, :], g.vc[:, pair * P:(pair + 1) * P]))
        with st.block() as block:
            @block.sync
            def _(sp):
                sp.wait_ge(normalised, n_norm)
                sp.dma_start(g.d["kv_out"], g.proj[:, Q_TILES:, :]).then_inc(stored, 16)
                sp.wait_ge(stored, 16)

            @block.scalar
            def _(act):
                def rest(n):
                    w = TOKENS if n < len(normed) else 2 * P_BLOCKS
                    act.wait_ge(summed, n + 1)
                    out, tot = root[n % 2][:, 0:w], total[n % 2]
                    if n >= 2:
                        act.wait_ge(normalised, n - 1)
                    src = tot[:, :, 0:HALF] if w == TOKENS else tot[:, 0, 0:w]
                    act.activation(halves(out) if w == TOKENS else out, src, ACT.Ln, scale=1.0 / HD,
                                   bias=g.eps[:, 0:1]).then_inc(logged, 1)
                    act.wait_ge(logged, n + 1)
                    act.activation(out, out, ACT.Exp, scale=-0.5).then_inc(rooted, 1)

                for n in range(n_norm):
                    if n >= 2:
                        act.wait_ge(summed, n - 1)
                    if n < len(normed):
                        act.activation(sq[n % 2][:, :], g.proj[:, normed[n], :], ACT.Square).then_inc(squared, 1)
                    else:
                        act.wait_ge(averaged, 2)
                        act.activation(sq[n % 2][:, 0:2 * P_BLOCKS], means[:, 0:2, :].rearrange("p a c -> p (a c)"),
                                       ACT.Square).then_inc(squared, 1)
                    if n:
                        rest(n - 1)
                rest(n_norm - 1)

            @block.tensor
            def _(pe):
                for n in range(n_norm):
                    pe.wait_ge(squared, n + 1)
                    if n >= 2:
                        pe.wait_ge(logged, n - 1)
                    if n < len(normed):
                        for a in range(2):
                            mm = pe.matmul(total[n % 2][:, a, 0:HALF], g.const("head_ones"),
                                           sq[n % 2][:, a * HALF:(a + 1) * HALF], start=True, stop=True)
                    else:
                        mm = pe.matmul(total[n % 2][:, 0, 0:2 * P_BLOCKS], g.const("head_ones"),
                                       sq[n % 2][:, 0:2 * P_BLOCKS], start=True, stop=True)
                    mm.then_inc(summed, 1)
                pe.wait_ge(averaged, 2)
                for n, (src, dst) in enumerate(turns):
                    if n >= 2:
                        pe.wait_ge(turn_out, n - 1)
                    pe.transpose(turn[n % 2][0:dst.shape[0], 0:P], src, ident).then_inc(turned, 1)

            @block.vector
            def _(dve):
                dve.tensor_reduce(means[:, :, :], g.proj[:, CMP_K:CMP_K + 4, 0:SEQ].rearrange(
                    "p a (c t) -> p a c t", t=CMP), AX_X, ALU.add).then_inc(averaged, 1)
                dve.wait_ge(averaged, 1)
                dve.tensor_scalar(means[:, :, :], means[:, :, :], 1.0 / CMP, None, ALU.mult).then_inc(averaged, 1)
                dve.memset(g.qb[:, :, :, :], 0.0).then_inc(cleared, 1)
                for n in range(n_norm):
                    dve.wait_ge(rooted, n + 1)
                    if n < len(normed):
                        x = g.proj[:, normed[n], :]
                        gain = Q_GAIN if normed[n] < Q_TILES else K_GAIN
                        dve.scalar_tensor_tensor(out=x, in0=x, scalar=g.gains[:, gain:gain + 1],
                                                 in1=root[n % 2][:, :], op0=ALU.mult, op1=ALU.mult
                                                 ).then_inc(normalised, 1)
                    else:
                        dve.wait_ge(averaged, 2)
                        dve.scalar_tensor_tensor(out=g.kc[:, :, :].rearrange("p a c -> p (a c)"),
                                                 in0=means[:, 0:2, :].rearrange("p a c -> p (a c)"),
                                                 scalar=g.gains[:, K_GAIN:K_GAIN + 1],
                                                 in1=root[n % 2][:, 0:2 * P_BLOCKS],
                                                 op0=ALU.mult, op1=ALU.mult).then_inc(normalised, 1)
                dve.wait_ge(normalised, Q_TILES)
                dve.wait_ge(cleared, 1)
                for pair in range(2):
                    for half in range(2):
                        R = slice(HD * half, HD * (half + 1))
                        for j in range(GROUP):
                            at = 16 * half + DEC_SEQ * j
                            dve.tensor_scalar(
                                g.qb[R, pair, :, at:at + DEC_SEQ],
                                g.proj[R, pair * GROUP + j, SEQ:TOKENS].rearrange("p (b t) -> p b t", t=DEC_SEQ),
                                HD ** -0.5, None, ALU.mult)
                dve.wait_ge(normalised, len(normed))
                for n, K in enumerate((SLC_K, WIN_K)):
                    dve.tensor_copy(g.k_new[:, n, :, :], g.proj[:, K:K + 2, SEQ:TOKENS])
                for n, (src, dst) in enumerate(turns):
                    dve.wait_ge(turned, n + 1)
                    dve.tensor_copy(dst, turn[n % 2][0:dst.shape[0], 0:P]).then_inc(turn_out, 1)


UNIT_PE = ["scores", "turn slc", "turn win", "out"]
UNIT_DVE = ["mask", "mask cmp", "max", "max cmp", "seen", "cmp sum", "floor", "inverse", "gate", "scale", "cmp turned"]
UNIT_ACT = ["exp", "slc turned", "win turned", "out"]


def prompt_attention_stage(nc, g):
    assert SEQ // SEL <= TOP_N and SEQ <= WINDOW
    with Stage(nc, "patt") as st:
        class Lane:
            pass
        lanes = []
        for s in range(2):
            ln = Lane()
            lanes.append(ln)
            ln.s, ln.R = s, slice(HD * s, HD * (s + 1))
            ln.p = st.sb(f"p{s}", [P, 2, SEQ])
            ln.pT = st.sb(f"pT{s}", [P, 2, SEQ])
            ln.sc = st.sb(f"sc{s}", [P, P_BLOCKS])
            ln.pcT = st.sb(f"pcT{s}", [P_BLOCKS, P])
            ln.neg_max = st.sb(f"neg_max{s}", [P, 3])
            ln.sums = st.sb(f"sums{s}", [P, 3])
            ln.scores = st.ps(f"scores{s}", (P, 2, 512))
            ln.turn = st.ps(f"turn{s}")
            ln.out = st.ps(f"out{s}")
            def unit_steps(engine, names, s=s):
                return st.steps(f"{engine}{s}", [f"{n} {t}" for t in range(TILES) for n in names])
            ln.pe, ln.dve, ln.act = (unit_steps("pe", UNIT_PE), unit_steps("dve", UNIT_DVE),
                                     unit_steps("act", UNIT_ACT))
        q = st.sb("q", [P, SEQ])
        q_staged = st.steps("q_staged", ["q"])
        taken = PAGES_EARLY + PAGES_NSA * NSA_TILES
        pages = PageSums(nc, g, st, g.past_c, taken, PAGES_ATT)
        assert taken + 2 * PAGES_ATT * 2 * GROUP == DEC_BATCH * N_PAGES
        ident = g.const("ident")

        def alternate(rule, i, pair):
            for _ in zip(*(rule(ln, i, pair) for ln in lanes)):
                pass

        def before(steps, name, t, i):
            return steps.past(f"{name} {t - 1}", i) if t else steps.past(f"{name} {TILES - 1}", i - 1)

        with st.block() as block:
            @block.sync
            def _(sp):
                with sp.Fori(0, 2 * GROUP) as i:
                    for s in range(2):
                        pages.load(sp, s, i)

            @block.gpsimd
            def _(pool):
                q_staged.credit(pool)
                for pair in range(2):
                    with pool.Fori(pair * GROUP, (pair + 1) * GROUP) as i:
                        for ln in lanes:
                            pool.wait_ge(ln.pe.sem, ln.pe.past(f"scores {TILES - 1}", i - 1))
                        pool.tensor_tensor(q[:, :], g.proj[:, bass.ds(i, 1), 0:SEQ].rearrange("p a t -> p (a t)"),
                                           g.const("q_scale").broadcast_to([P, SEQ]), ALU.mult).then_inc(*q_staged.done("q"))

            @block.tensor
            def _(pe):
                def rule(ln, i, pair):
                    kvh = 2 * pair + ln.s
                    V = slice(kvh * HD, (kvh + 1) * HD)
                    for t in range(TILES):
                        n = (t + 1) * P
                        q_t = q[ln.R, t * P:(t + 1) * P]
                        if t == 0:
                            pe.wait_ge(q_staged.sem, q_staged.past("q", i))
                        pe.wait_ge(ln.act.sem, before(ln.act, "out", t, i))
                        for a, K in enumerate((SLC_K, WIN_K)):
                            pe.matmul(ln.scores[:, a, 0:n], q_t, g.proj[ln.R, K + pair, 0:n], start=True, stop=True)
                        pe.matmul(ln.out[:, 128:128 + P_BLOCKS], q_t, g.kc[ln.R, pair, :], start=True, stop=True
                                  ).then_inc(*ln.pe.done(f"scores {t}"))
                        yield
                        pe.wait_ge(ln.dve.sem, ln.dve.past(f"scale {t}", i))
                        for a, name in enumerate(("slc", "win")):
                            if a:
                                pe.wait_ge(ln.act.sem, ln.act.past(f"slc turned {t}", i))
                            for b in range(t + 1):
                                mm = pe.transpose(ln.turn[:, b * P:(b + 1) * P], ln.p[:, a, b * P:(b + 1) * P], ident)
                            if a == 0:
                                mm = pe.transpose(ln.out[0:P_BLOCKS, 256:384], ln.sc[:, :], ident)
                            mm.then_inc(*ln.pe.done(f"turn {name} {t}"))
                            yield
                        pe.wait_ge(ln.act.sem, ln.act.past(f"win turned {t}", i))
                        pe.wait_ge(ln.dve.sem, ln.dve.past(f"cmp turned {t}", i))
                        out = ln.out[ln.R, 0:P]
                        pe.matmul(out, g.vc[:, V], ln.pcT[:, :], start=True, stop=False)
                        for a in range(2):
                            for b in range(t + 1):
                                mm = pe.matmul(out, g.v_rows[:, a, b, V], ln.pT[:, a, b * P:(b + 1) * P],
                                               start=False, stop=(a == 1 and b == t))
                        mm.then_inc(*ln.pe.done(f"out {t}"))
                        yield

                for ln in lanes:
                    ln.pe.credit(pe)
                for pair in range(2):
                    with pe.Fori(pair * GROUP, (pair + 1) * GROUP) as i:
                        alternate(rule, i, pair)

            @block.vector
            def _(dve):
                def rule(ln, i, pair):
                    for t in range(TILES):
                        n = (t + 1) * P
                        blocks = slice(t * P_BLOCKS, (t + 1) * P_BLOCKS)
                        d = ln.dve

                        def after(name):
                            dve.wait_ge(d.sem, d.past(f"{name} {t}", i))
                        dve.wait_ge(ln.pe.sem, ln.pe.past(f"scores {t}", i))
                        own = ln.scores[:, :, t * P:n]
                        dve.tensor_tensor(own, own, g.const("causal_neg").unsqueeze(1).broadcast_to([P, 2, P]),
                                          ALU.add).then_inc(*d.done(f"mask {t}"))
                        dve.tensor_tensor(ln.sc[:, :], ln.out[:, 128:128 + P_BLOCKS], g.const("cmp_neg")[:, blocks],
                                          ALU.add).then_inc(*d.done(f"mask cmp {t}"))
                        after("mask")
                        dve.tensor_reduce(ln.neg_max[:, 1:3], ln.scores[:, :, 0:n], AX_X, ALU.max, negate=True
                                          ).then_inc(*d.done(f"max {t}"))
                        after("mask cmp")
                        dve.tensor_reduce(ln.neg_max[:, 0:1], ln.sc[:, :], AX_X, ALU.max, negate=True
                                          ).then_inc(*d.done(f"max cmp {t}"))
                        yield
                        dve.wait_ge(ln.act.sem, ln.act.past(f"exp {t}", i))
                        dve.tensor_tensor(ln.sc[:, :], ln.sc[:, :], g.const("cmp_seen")[:, blocks], ALU.mult
                                          ).then_inc(*d.done(f"seen {t}"))
                        after("seen")
                        dve.tensor_reduce(ln.sums[:, 0:1], ln.sc[:, :], AX_X, ALU.add).then_inc(*d.done(f"cmp sum {t}"))
                        after("cmp sum")
                        dve.tensor_scalar(ln.sums[:, :], ln.sums[:, :], 1e-30, None, ALU.max
                                          ).then_inc(*d.done(f"floor {t}"))
                        after("floor")
                        dve.reciprocal(ln.sums[:, :], ln.sums[:, :]).then_inc(*d.done(f"inverse {t}"))
                        after("inverse")
                        head = bass.ds(i + GROUP * (pair + ln.s), 1)
                        dve.tensor_tensor(ln.sums[:, :], ln.sums[:, :],
                                          g.gates[:, t, head, :].rearrange("p a r -> p (a r)"), ALU.mult
                                          ).then_inc(*d.done(f"gate {t}"))
                        after("gate")
                        for a in range(2):
                            dve.tensor_scalar(ln.p[:, a, 0:n], ln.p[:, a, 0:n], ln.sums[:, a + 1:a + 2], None, ALU.mult)
                        dve.tensor_scalar(ln.sc[:, :], ln.sc[:, :], ln.sums[:, 0:1], None, ALU.mult
                                          ).then_inc(*d.done(f"scale {t}"))
                        yield
                        dve.wait_ge(ln.pe.sem, ln.pe.past(f"turn slc {t}", i))
                        dve.tensor_copy(ln.pcT[:, :], ln.out[0:P_BLOCKS, 256:384]
                                        ).then_inc(*d.done(f"cmp turned {t}"))
                        if t == 2:
                            pages.sum(dve, ln.s, i)
                        yield

                for ln in lanes:
                    ln.dve.credit(dve)
                pages.credit(dve)
                for pair in range(2):
                    with dve.Fori(pair * GROUP, (pair + 1) * GROUP) as i:
                        alternate(rule, i, pair)

            @block.scalar
            def _(act):
                def rule(ln, i, pair):
                    for t in range(TILES):
                        n = (t + 1) * P
                        a_ = ln.act
                        act.wait_ge(ln.dve.sem, ln.dve.past(f"max cmp {t}", i))
                        act.wait_ge(ln.pe.sem, before(ln.pe, "turn win", t, i))
                        for a in range(2):
                            act.activation(ln.p[:, a, 0:n], ln.scores[:, a, 0:n], ACT.Exp,
                                           bias=ln.neg_max[:, a + 1:a + 2], accum_out=ln.sums[:, a + 1:a + 2])
                        act.activation(ln.sc[:, :], ln.sc[:, :], ACT.Exp, bias=ln.neg_max[:, 0:1]
                                       ).then_inc(*a_.done(f"exp {t}"))
                        yield
                        for a, name in enumerate(("slc", "win")):
                            act.wait_ge(ln.pe.sem, ln.pe.past(f"turn {name} {t}", i))
                            act.activation(ln.pT[:, a, 0:n], ln.turn[:, 0:n], ACT.Copy
                                           ).then_inc(*a_.done(f"{name} turned {t}"))
                            yield
                        act.wait_ge(ln.pe.sem, ln.pe.past(f"out {t}", i))
                        act.activation(g.attT[ln.R, bass.ds(i, 1), t * P:n].rearrange("p a t -> p (a t)"),
                                       ln.out[ln.R, 0:P], ACT.Copy).then_inc(*a_.done(f"out {t}"))
                        yield

                for ln in lanes:
                    ln.act.credit(act)
                for pair in range(2):
                    with act.Fori(pair * GROUP, (pair + 1) * GROUP) as i:
                        alternate(rule, i, pair)


def compress_norm_stage(nc, g):
    with Stage(nc, "cnorm") as st:
        sq = st.sb("sq", [P, 4, 512])
        root = st.sb("root", [P, 4, 512])
        v = st.sb("v", [P, 2, DEC_BATCH * BLOCKS])
        total = st.ps("total", (P, 4, 512))
        turn = [st.ps(f"turn{s}") for s in range(2)]
        squared, summed, logged, rooted = st.sem("squared"), st.sem("summed"), st.sem("logged"), st.sem("rooted")
        averaged, turned, turn_out = st.sem("averaged"), st.sem("turned"), st.sem("turn_out")
        src = g.past_c[:, :, :].rearrange("p g (a c) -> p g a c", a=4)
        per = 64 * 8
        with st.block() as block:
            @block.vector
            def _(dve):
                for pair in range(2):
                    dve.tensor_scalar(src[:, :, pair, :], src[:, :, pair, :], 1.0 / CMP, None, ALU.mult)
                    ins = dve.tensor_scalar(v[:, pair, :].rearrange("p (g c) -> p g c", c=4), src[:, :, 2 + pair, :],
                                            1.0 / CMP, None, ALU.mult)
                ins.then_inc(averaged, 1)
                for n in range(4):
                    dve.wait_ge(rooted, n + 1)
                    dve.wait_ge(averaged, 1)
                    part = src[:, 64 * n:64 * (n + 1), 0:2, :]
                    for pair in range(2):
                        dve.scalar_tensor_tensor(
                            out=part[:, :, pair, :], in0=part[:, :, pair, :], scalar=g.gains[:, K_GAIN:K_GAIN + 1],
                            in1=root[:, n, :].rearrange("p (g a c) -> p g a c", a=2, c=4)[:, :, pair, :],
                            op0=ALU.mult, op1=ALU.mult)
                for b in range(DEC_BATCH):
                    for pair in range(2):
                        n = 2 * b + pair
                        dve.wait_ge(turned, n + 1)
                        dve.tensor_copy(g.vc_past[:, b, pair * P:(pair + 1) * P], turn[n % 2][:, 0:P]
                                        ).then_inc(turn_out, 1)

            @block.scalar
            def _(act):
                act.wait_ge(averaged, 1)
                for n in range(4):
                    act.activation(sq[:, n, :].rearrange("p (g a c) -> p g (a c)", a=2, c=4),
                                   src[:, 64 * n:64 * (n + 1), 0:2, :].rearrange("p g a c -> p g (a c)"), ACT.Square
                                   ).then_inc(squared, 1)
                for n in range(4):
                    act.wait_ge(summed, n + 1)
                    act.activation(root[:, n, :], total[:, n, :], ACT.Ln, scale=1.0 / HD, bias=g.eps[:, 0:1]
                                   ).then_inc(logged, 1)
                    act.wait_ge(logged, n + 1)
                    act.activation(root[:, n, :], root[:, n, :], ACT.Exp, scale=-0.5).then_inc(rooted, 1)

            @block.tensor
            def _(pe):
                for n in range(4):
                    pe.wait_ge(squared, n + 1)
                    pe.matmul(total[:, n, :], g.const("head_ones"), sq[:, n, :], start=True, stop=True
                              ).then_inc(summed, 1)
                pe.wait_ge(averaged, 1)
                for b in range(DEC_BATCH):
                    for pair in range(2):
                        n = 2 * b + pair
                        if n >= 2:
                            pe.wait_ge(turn_out, n - 1)
                        pe.transpose(turn[n % 2][:, 0:P],
                                     v[:, pair, b * BLOCKS:(b + 1) * BLOCKS], g.const("ident")
                                     ).then_inc(turned, 1)


CHUNKS_KV = 8
PAGES_C = N_PAGES // CHUNKS_KV
KEYS_C = PAGES_C * PAGE
SLC_END = PAST + NEW
WIN_END = SLC_END + WINDOW
KEYS = WIN_END + NEW
SMP_GROUPS = 4
PAGES_G = N_PAGES // SMP_GROUPS


def sample_attention_stage(nc, g):
    n_sel = PAST // SEL + 1
    assert TOP_N == 16
    with Stage(nc, "satt") as st:
        kv = st.sb("kv", [P, CHUNKS_KV, PAGES_C, 4 * P])
        win = st.sb("win", [P, 4, 4 * P])
        qb = st.sb("qb", [P, 2, NEW])
        kc = st.sb("kc", [P, 2, BLOCKS])
        vc = st.sb("vc", [P, KVH * HD])
        s_all = st.sb("s_all", [ROWS, KEYS])
        pc = st.sb("pc", [ROWS, BLOCKS])
        pT = st.sb("pT", [P, N_PAGES + 7, ROWS])
        table = st.sb("table", [1, DEC_BATCH * N_PAGES], I32)
        score = [st.sb(f"score{n}", [ROWS, n_sel]) for n in range(3)]
        best = [st.sb(f"best{n}", [ROWS, 8]) for n in range(2)]
        unselected = st.sb("unselected", [ROWS, n_sel])
        neg_max = st.sb("neg_max", [ROWS, 3])
        sums = st.sb("sums", [ROWS, 3])
        out = st.sb("out", [ROWS, KVH * HD])
        ps = [st.ps(f"scores{n}") for n in range(2)]
        ps_cmp, ps_new = st.ps("cmp"), st.ps("new")
        ps_turn = [st.ps(f"turn{n}") for n in range(2)]
        ps_out, ps_end = st.ps("out_acc"), st.ps("end")
        kv_in = [st.sem(f"kv_in{c}") for c in range(CHUNKS_KV)]
        win_in, table_in, cleared = st.sem("win_in"), st.sem("table_in"), st.sem("cleared")
        groups = range(SMP_GROUPS + 1)
        pe_s = st.steps("pe", ["cmp scores", "scores 0", "scores 1", "importance"]
                        + [f"scores {c}" for c in range(2, CHUNKS_KV)] + ["new scores", "win scores"]
                        + [f"{x} {n}" for n in groups for x in ("turn", "out")] + ["end"])
        dve_s = st.steps("dve", ["cmp max", "cmp floor", "cmp inverse", "cmp p", "imp", "score", "top a", "out a",
                                 "top b", "out b", "unselected"]
                         + [f"masked {c}" for c in range(CHUNKS_KV)]
                         + ["new masked", "win masked", "slc max", "win max", "floor", "inverse", "gate",
                            "cmp scaled", "slc scaled", "win scaled"] + ["placed"])
        act_s = st.steps("act", ["cmp exp", "slc exp", "win exp"] + [f"turned {n}" for n in groups] + ["out"])
        pool_s = st.steps("pool", ["staged"])
        NEW_SLC, NEW_WIN = N_PAGES + 5, N_PAGES + 6
        CMP_AT = N_PAGES + 4
        ident = g.const("ident")

        with st.block() as block:
            @block.sync
            def _(sp):
                sp.dma_start(table[:, :], g.d["page_table"]).then_inc(table_in, 16)
                sp.wait_ge(table_in, 16)
                with sp.Fori(0, DEC_BATCH) as i:
                    for c in range(CHUNKS_KV):
                        sp.wait_ge(pe_s.sem, pe_s.past(f"out {c * PAGES_C // PAGES_G}", i - 1))
                        for n in range(PAGES_C):
                            page = sp.value_load(table[0:1, bass.ds(i * N_PAGES + c * PAGES_C + n, 1)], min_val=0,
                                                 max_val=N_POOL - 1)
                            sp.dma_start(kv[:, c, n, :], g.d["slc_pool"][bass.ds(page, 1)].rearrange("g p n -> (g p) n")
                                         ).then_inc(kv_in[c], 16)
                    sp.wait_ge(pe_s.sem, pe_s.past(f"out {SMP_GROUPS}", i - 1))
                    sp.dma_start(win[:, :, :], g.d["win"][bass.ds(i, 1)].rearrange("b p a n -> (b p) a n")
                                 ).then_inc(win_in, 16)

            @block.gpsimd
            def _(pool):
                pool_s.credit(pool)
                with pool.Fori(0, DEC_BATCH) as i:
                    pool.wait_ge(pe_s.sem, pe_s.past(f"out {SMP_GROUPS}", i - 1))
                    pool.tensor_copy(qb[:, :, :], g.qb[:, :, bass.ds(i, 1), :].rearrange("p a b n -> p a (b n)"))
                    pages = g.past_c[:, bass.ds(i * N_PAGES, N_PAGES), :]
                    for pair in range(2):
                        pool.tensor_copy(kc[:, pair, :].rearrange("p (g c) -> p g c", c=PAGE // CMP),
                                         pages[:, :, 4 * pair:4 * pair + 4])
                    pool.tensor_copy(vc[:, :], g.vc_past[:, bass.ds(i, 1), :].rearrange("p a n -> p (a n)")
                                     ).then_inc(*pool_s.done("staged"))

            @block.tensor
            def _(pe):
                def by_pair(out_, rhs):
                    for pair in range(2):
                        mm = pe.matmul(out_[NEW * pair:NEW * (pair + 1), :], qb[:, pair, :], rhs(pair),
                                       start=True, stop=True)
                    return mm

                def chunk_scores(c, i):
                    pe.wait_ge(kv_in[c], 16 * PAGES_C * (i + 1))
                    if c >= 2:
                        pe.wait_ge(dve_s.sem, dve_s.past(f"masked {c - 2}", i))
                    by_pair(ps[c % 2][0:ROWS, :], lambda pair: kv[:, c, :, pair * P:(pair + 1) * P]
                            ).then_inc(*pe_s.done(f"scores {c}"))

                pe_s.credit(pe)
                with pe.Fori(0, DEC_BATCH) as i:
                    pe.wait_ge(pool_s.sem, pool_s.past("staged", i))
                    by_pair(ps_cmp[0:ROWS, 0:BLOCKS], lambda pair: kc[:, pair, :]).then_inc(*pe_s.done("cmp scores"))
                    pe.wait_ge(dve_s.sem, dve_s.past("win masked", i - 1))
                    chunk_scores(0, i)
                    chunk_scores(1, i)
                    pe.wait_ge(dve_s.sem, dve_s.past("cmp p", i))
                    pe.nop(nofuse=True)
                    pe.matmul(ps_cmp[0:ROWS, BLOCKS:2 * BLOCKS], g.const("group_sum", ROWS)[:, 0:ROWS], pc[:, :],
                              start=True, stop=True).then_inc(*pe_s.done("importance"))
                    for c in range(2, CHUNKS_KV):
                        chunk_scores(c, i)
                    by_pair(ps_new[0:ROWS, 0:NEW], lambda pair: g.k_new[:, 0, pair, :])
                    by_pair(ps_new[0:ROWS, NEW:2 * NEW], lambda pair: g.k_new[:, 1, pair, :]
                            ).then_inc(*pe_s.done("new scores"))
                    pe.wait_ge(win_in, 16 * (i + 1))
                    pe.wait_ge(dve_s.sem, dve_s.past(f"masked {CHUNKS_KV - 2}", i))
                    by_pair(ps[0][0:ROWS, :], lambda pair: win[:, pair, :]).then_inc(*pe_s.done("win scores"))
                    small = g.const("ident", ROWS)[:, 0:ROWS]
                    for n in groups:
                        pe.wait_ge(dve_s.sem, dve_s.past("win scaled" if n == SMP_GROUPS else "slc scaled", i))
                        if n >= 2:
                            pe.wait_ge(act_s.sem, act_s.past(f"turned {n - 2}", i))
                        pe.nop(nofuse=True)
                        turn = ps_turn[n % 2]

                        def turned(slot, keys, src):
                            return pe.transpose(turn[0:keys, slot * ROWS:(slot + 1) * ROWS], src, small)
                        if n < SMP_GROUPS:
                            for m in range(PAGES_G):
                                at = (n * PAGES_G + m) * PAGE
                                mm = turned(m, P, s_all[:, at:at + PAGE])
                        else:
                            for m in range(WINDOW // P):
                                at = SLC_END + m * P
                                turned(m, P, s_all[:, at:at + P])
                            turned(4, P, pc[:, :])
                            turned(5, NEW, s_all[:, PAST:SLC_END])
                            mm = turned(6, NEW, s_all[:, WIN_END:KEYS])
                        mm.then_inc(*pe_s.done(f"turn {n}"))
                        pe.wait_ge(act_s.sem, act_s.past(f"turned {n}", i))
                        acc = ps_out[0:ROWS, 0:KVH * HD]
                        if n < SMP_GROUPS:
                            for m in range(PAGES_G):
                                page = n * PAGES_G + m
                                mm = pe.matmul(acc, pT[:, page, :], kv[:, page // PAGES_C, page % PAGES_C, 2 * P:4 * P],
                                               start=(page == 0), stop=False)
                        else:
                            for m in range(WINDOW // P):
                                pe.matmul(acc, pT[:, N_PAGES + m, :],
                                          win[:, 2 + m // 2, (m % 2) * 256:(m % 2 + 1) * 256], start=False, stop=False)
                            pe.matmul(acc, pT[:, CMP_AT, :], vc[:, :], start=False, stop=False)
                            pe.matmul(acc, pT[0:NEW, NEW_SLC, :], g.v_new[:, 0, :], start=False, stop=False)
                            mm = pe.matmul(acc, pT[0:NEW, NEW_WIN, :], g.v_new[:, 1, :], start=False, stop=True)
                        mm.then_inc(*pe_s.done(f"out {n}"))
                    pe.wait_ge(act_s.sem, act_s.past("out", i))
                    pe.nop(nofuse=True)
                    for pair in range(2):
                        mm = pe.transpose(ps_end[:, pair * ROWS:(pair + 1) * ROWS], out[:, pair * P:(pair + 1) * P], small)
                    mm.then_inc(*pe_s.done("end"))

            @block.scalar
            def _(act):
                act_s.credit(act)
                with act.Fori(0, DEC_BATCH) as i:
                    act.wait_ge(dve_s.sem, dve_s.past("cmp max", i))
                    act.wait_ge(pe_s.sem, pe_s.past(f"turn {SMP_GROUPS}", i - 1))
                    act.activation(pc[:, :], ps_cmp[0:ROWS, 0:BLOCKS], ACT.Exp, bias=neg_max[:, 0:1],
                                   accum_out=sums[:, 0:1]).then_inc(*act_s.done("cmp exp"))
                    act.wait_ge(dve_s.sem, dve_s.past("slc max", i))
                    x = s_all[:, 0:SLC_END]
                    act.activation(x, x, ACT.Exp, bias=neg_max[:, 1:2], accum_out=sums[:, 1:2]
                                   ).then_inc(*act_s.done("slc exp"))
                    act.wait_ge(dve_s.sem, dve_s.past("win max", i))
                    x = s_all[:, SLC_END:KEYS]
                    act.activation(x, x, ACT.Exp, bias=neg_max[:, 2:3], accum_out=sums[:, 2:3]
                                   ).then_inc(*act_s.done("win exp"))
                    for n in groups:
                        act.wait_ge(pe_s.sem, pe_s.past(f"turn {n}", i))
                        at = n * PAGES_G
                        if n < SMP_GROUPS:
                            act.activation(pT[:, at:at + PAGES_G, :].rearrange("p g r -> p (g r)"), ps_turn[n % 2][:, :],
                                           ACT.Copy).then_inc(*act_s.done(f"turned {n}"))
                        else:
                            act.activation(pT[:, at:at + 5, :].rearrange("p g r -> p (g r)"),
                                           ps_turn[n % 2][:, 0:5 * ROWS], ACT.Copy)
                            act.activation(pT[0:NEW, at + 5:at + 7, :].rearrange("p g r -> p (g r)"),
                                           ps_turn[n % 2][0:NEW, 5 * ROWS:7 * ROWS], ACT.Copy
                                           ).then_inc(*act_s.done(f"turned {n}"))
                    act.wait_ge(pe_s.sem, pe_s.past(f"out {SMP_GROUPS}", i))
                    act.activation(out[:, :], ps_out[0:ROWS, 0:KVH * HD], ACT.Copy).then_inc(*act_s.done("out"))

            @block.vector
            def _(dve):
                def own(name, i):
                    dve.wait_ge(dve_s.sem, dve_s.past(name, i))
                rows = g.const("group_sum", ROWS)
                dve_s.credit(dve)
                dve.memset(score[0][:, n_sel - 1:n_sel], SEL_BIG).then_inc(cleared, 1)
                dve.wait_ge(cleared, 1)
                with dve.Fori(0, DEC_BATCH) as i:
                    dve.wait_ge(pe_s.sem, pe_s.past("cmp scores", i))
                    dve.tensor_reduce(neg_max[:, 0:1], ps_cmp[0:ROWS, 0:BLOCKS], AX_X, ALU.max, negate=True
                                      ).then_inc(*dve_s.done("cmp max"))
                    dve.wait_ge(act_s.sem, act_s.past("cmp exp", i))
                    dve.tensor_scalar(sums[:, 0:1], sums[:, 0:1], 1e-30, None, ALU.max
                                      ).then_inc(*dve_s.done("cmp floor"))
                    own("cmp floor", i)
                    dve.reciprocal(sums[:, 0:1], sums[:, 0:1]).then_inc(*dve_s.done("cmp inverse"))
                    own("cmp inverse", i)
                    dve.tensor_scalar(pc[:, :], pc[:, :], sums[:, 0:1], None, ALU.mult
                                      ).then_inc(*dve_s.done("cmp p"))
                    dve.wait_ge(pe_s.sem, pe_s.past("importance", i))
                    past = slice(0, n_sel - 1)
                    dve.tensor_reduce(score[1][:, past], ps_cmp[0:ROWS, BLOCKS:2 * BLOCKS].rearrange(
                        "r (s c) -> r s c", c=SEL // CMP), AX_X, ALU.add).then_inc(*dve_s.done("imp"))
                    own("imp", i)
                    dve.tensor_tensor(score[0][:, past], score[1][:, past], g.const("forced", ROWS), ALU.max
                                      ).then_inc(*dve_s.done("score"))
                    for n, name in enumerate(("a", "b")):
                        own("score" if n == 0 else "out a", i)
                        dve.nop(nofuse=True)
                        dve.max(best[n][:, :], score[n][:, :]).then_inc(*dve_s.done(f"top {name}"))
                        own(f"top {name}", i)
                        dve.nop(nofuse=True)
                        dve.match_replace(score[n + 1][:, :], best[n][:, :], score[n][:, :], NEG
                                          ).then_inc(*dve_s.done(f"out {name}"))
                    own("out b", i)
                    dve.tensor_scalar(unselected[:, :], score[2][:, :], NEG / 10, NEG, ALU.is_gt, ALU.mult
                                      ).then_inc(*dve_s.done("unselected"))
                    own("unselected", i)
                    per = KEYS_C // SEL
                    for c in range(CHUNKS_KV):
                        dve.wait_ge(pe_s.sem, pe_s.past(f"scores {c}", i))
                        dve.tensor_tensor(
                            s_all[:, c * KEYS_C:(c + 1) * KEYS_C].rearrange("r (s k) -> r s k", k=SEL),
                            ps[c % 2][0:ROWS, :].rearrange("r (s k) -> r s k", k=SEL),
                            unselected[:, c * per:(c + 1) * per].unsqueeze(2).broadcast_to([ROWS, per, SEL]), ALU.add
                        ).then_inc(*dve_s.done(f"masked {c}"))
                    dve.wait_ge(pe_s.sem, pe_s.past("new scores", i))
                    new_neg = g.const("new_neg", ROWS).rearrange("r (b k) -> r b k", b=DEC_BATCH)
                    new_neg = new_neg[:, bass.ds(i, 1), :].rearrange("r b k -> r (b k)")
                    dve.tensor_tensor(s_all[:, PAST:SLC_END], ps_new[0:ROWS, 0:NEW], new_neg, ALU.add)
                    dve.tensor_tensor(s_all[:, WIN_END:KEYS], ps_new[0:ROWS, NEW:2 * NEW], new_neg, ALU.add
                                      ).then_inc(*dve_s.done("new masked"))
                    dve.wait_ge(pe_s.sem, pe_s.past("win scores", i))
                    dve.tensor_tensor(s_all[:, SLC_END:WIN_END], ps[0][0:ROWS, :], g.const("win_neg", ROWS), ALU.add
                                      ).then_inc(*dve_s.done("win masked"))
                    own("new masked", i)
                    dve.tensor_reduce(neg_max[:, 1:2], s_all[:, 0:SLC_END], AX_X, ALU.max, negate=True
                                      ).then_inc(*dve_s.done("slc max"))
                    own("win masked", i)
                    dve.tensor_reduce(neg_max[:, 2:3], s_all[:, SLC_END:KEYS], AX_X, ALU.max, negate=True
                                      ).then_inc(*dve_s.done("win max"))
                    dve.wait_ge(act_s.sem, act_s.past("win exp", i))
                    dve.tensor_scalar(sums[:, 1:3], sums[:, 1:3], 1e-30, None, ALU.max).then_inc(*dve_s.done("floor"))
                    own("floor", i)
                    dve.reciprocal(sums[:, 1:3], sums[:, 1:3]).then_inc(*dve_s.done("inverse"))
                    gate = g.row_gates[:, bass.ds(i, 1), :].rearrange("r b n -> r (b n)")
                    own("inverse", i)
                    dve.tensor_tensor(sums[:, 1:3], sums[:, 1:3], gate[:, 1:3], ALU.mult
                                      ).then_inc(*dve_s.done("gate"))
                    dve.tensor_scalar(pc[:, :], pc[:, :], gate[:, 0:1], None, ALU.mult
                                      ).then_inc(*dve_s.done("cmp scaled"))
                    own("gate", i)
                    dve.tensor_scalar(s_all[:, 0:SLC_END], s_all[:, 0:SLC_END], sums[:, 1:2], None, ALU.mult
                                      ).then_inc(*dve_s.done("slc scaled"))
                    dve.tensor_scalar(s_all[:, SLC_END:KEYS], s_all[:, SLC_END:KEYS], sums[:, 2:3], None, ALU.mult
                                      ).then_inc(*dve_s.done("win scaled"))
                    dve.wait_ge(pe_s.sem, pe_s.past("end", i))
                    for pair in range(2):
                        for half in range(2):
                            R = slice(HD * half, HD * (half + 1))
                            at = pair * ROWS + 16 * (2 * pair + half)
                            ins = dve.tensor_copy(
                                g.attT[R, pair * GROUP:(pair + 1) * GROUP, bass.ds(i * DEC_SEQ + SEQ, DEC_SEQ)],
                                ps_end[R, at:at + 16].rearrange("p (j t) -> p j t", t=DEC_SEQ))
                    ins.then_inc(*dve_s.done("placed"))


def nsa(nc, g):
    with ExitStack() as ctx:
        def sb(stack, name, shape):
            return stack.enter_context(nc.sbuf_tensor("nsa_" + name, shape, F32))
        g.attT = sb(ctx, "attT", [P, KT, TOKENS])
        with ExitStack() as smp:
            g.past_c = sb(smp, "past_c", [P, DEC_BATCH * N_PAGES, 4 * PAGE // CMP])
            g.vc_past = sb(smp, "vc_past", [P, DEC_BATCH, KVH * HD])
            g.row_gates = sb(smp, "row_gates", [ROWS, DEC_BATCH, 3])
            g.qb = sb(smp, "qb", [P, 2, DEC_BATCH, NEW])
            g.k_new = sb(smp, "k_new", [P, 2, 2, NEW])
            g.v_new = sb(smp, "v_new", [NEW, 2, KVH * HD])
            with ExitStack() as prompt:
                g.proj = sb(prompt, "proj", [P, NSA_TILES, TOKENS])
                g.gates = sb(prompt, "gates", [P, TILES, NSA_HEADS, 3])
                g.v_rows = sb(prompt, "v_rows", [P, 2, TILES, KVH * HD])
                g.kc = sb(prompt, "kc", [P, 2, P_BLOCKS])
                g.vc = sb(prompt, "vc", [P_BLOCKS, KVH * HD])
                with nc.sbuf_tensor("nsa_h", [P, KT, TOKENS], F32) as g.hT:
                    rms_norm_stage(nc, g, "norm1", LN_MIX + KT)
                    nsa_project_stage(nc, g)
                nsa_norm_stage(nc, g)
                prompt_attention_stage(nc, g)
            compress_norm_stage(nc, g)
            sample_attention_stage(nc, g)
        out_project_stage(nc, g, "nsa_out", g.d["nsa_wo"], g.attT)


def store_stage(nc, g):
    with Stage(nc, "store") as st:
        stored = st.sem("stored")
        with st.block() as block:
            @block.sync
            def _(sp):
                sp.dma_start(g.d["y"], g.xT[:, :, :]).then_inc(stored, 16)
                sp.wait_ge(stored, 16)


class Globals:

    def const(self, name, rows=P):
        at, n = CONST_AT[name]
        return self.consts[0:rows, at:at + n]


LN_MIX, LN_FFN, O_GAIN, Q_GAIN, K_GAIN, GAINS = 0, 16, 32, 33, 34, 35


def decoder(nc, d, stop=99):
    g = Globals()
    g.d = d
    with ExitStack() as ctx:
        def sb(name, shape, dt=F32):
            return ctx.enter_context(nc.sbuf_tensor(name, shape, dt))

        g.consts = sb("consts", [P, CONST_W])
        g.gains = sb("gains_sb", [P, GAINS])
        g.eps = sb("eps", [P, 1])
        g.xT = sb("xT", [P, KT, TOKENS])
        g.page_table = sb("page_table_sb", [1, DEC_BATCH * N_PAGES], I32)
        eps_set = ctx.enter_context(nc.semaphore("eps_set"))
        with nc.Block(no_gpsimd_drain=True) as block:
            @block.vector
            def _(dve):
                dve.memset(g.eps[:, :], EPS).then_inc(eps_set, 1)
                dve.wait_ge(eps_set, 1)
        load_inputs(nc, g)
        with ExitStack() as gdn:
            g.zT = gdn.enter_context(nc.sbuf_tensor("zT", [P, HEADS, TOKENS], F32))
            with ExitStack() as mixer:
                g.qkv = mixer.enter_context(nc.sbuf_tensor("qkv", [P, CONV_TILES, TOKENS], F32))
                def gate(name, shape):
                    return mixer.enter_context(nc.sbuf_tensor("gate_" + name, shape, F32))
                g.gate_g, g.beta, g.G, g.eG, g.tail = (
                    gate(n, [P, TILES + 1, HEADS]) for n in ("g", "beta", "G", "eG", "tail"))
                g.e_chunk = gate("e_chunk", [P, 2 * TILES, HEADS])
                g.e_batch = gate("e_batch", [P, DEC_BATCH, HEADS])
                with (nc.sbuf_tensor("h_gdn", [P, KT, TOKENS], F32) as g.hT,
                      nc.sbuf_tensor("first_sums", [P, PAGES_EARLY, 4 * PAGE // CMP], F32) as g.first_sums):
                    rms_norm_stage(nc, g, "norm0", LN_MIX)
                    gdn_project_stage(nc, g)
                    if stop == 1:
                        return debug_out(nc, g, {"hT": g.hT, "qkv": g.qkv, "zT": g.zT})
                    gdn_gates_stage(nc, g)
                gdn_heads_stage(nc, g)
            out_project_stage(nc, g, "gdn_out", g.d["gdn_wo"], g.zT)
        if stop == 2:
            return debug_out(nc, g, {"xT": g.xT})
        if stop != -4:
            moe(nc, g, "moe0", 0, LN_FFN)
        if stop == 3:
            return debug_out(nc, g, {"xT": g.xT})
        nsa(nc, g)
        if stop == 4:
            return debug_out(nc, g, {"xT": g.xT})
        moe(nc, g, "moe1", 1, LN_FFN + KT)
        store_stage(nc, g)


def debug_out(nc, g, what):
    for n, t in what.items():
        t_d = nc.dram_tensor("dbg_" + n, list(t.shape), F32, kind="ExternalOutput").ap()
        s = nc.semaphore("dbgs_" + n).__enter__()
        with nc.Block(no_gpsimd_drain=True) as block:
            @block.sync
            def _(sp):
                sp.dma_start(t_d, t[tuple(slice(None) for _ in t.shape)]).then_inc(s, 16)
                sp.wait_ge(s, 16)


def lay_out(i):
    a = {}
    def feature_major(x):
        return x.T.reshape(KT, P, -1).transpose(1, 0, 2)
    def tiles_of(w):
        return w.reshape(KT, P, -1, P).transpose(2, 1, 0, 3)
    a["consts"] = np.concatenate([CONSTANTS[k] for k in CONST_AT], 1)
    x = np.concatenate([i["x_prompt"].reshape(SEQ, D_MODEL), i["x_sample"].reshape(NEW, D_MODEL)])
    a["x"] = feature_major(x)
    cols = [i["ln_mix"].reshape(2 * KT, P).T, i["ln_ffn"].reshape(2 * KT, P).T, i["gdn_o_gain"][0][:, None],
            np.tile(i["nsa_q_gain"][0], 2)[:, None], np.tile(i["nsa_k_gain"][0], 2)[:, None]]
    a["gains"] = np.concatenate(cols, 1)
    w = i["gdn_w_in"][0]
    a["gdn_w"] = w[:, :4 * 1024].reshape(KT, P, 32, P).transpose(2, 1, 0, 3)
    a["gdn_w_ab"] = w[:, 4 * 1024:].reshape(KT, P, 2 * HEADS).transpose(1, 0, 2)
    a["gdn_rows"] = np.tile(np.stack([i["gdn_a_log"][0], i["gdn_dt_bias"][0]])[None], (P, 1, 1))
    a["gdn_S"] = i["state_gdn_S"][0].transpose(1, 2, 0, 3)
    a["gdn_wo"] = tiles_of(i["gdn_w_out"][0])
    a["router_w"] = np.concatenate([i["moe_w_grp"], i["moe_w_exp"]], 2).reshape(2, KT, P, -1).transpose(0, 2, 1, 3)
    a["router_b"] = np.tile(np.concatenate([i["moe_b_grp"], i["moe_b_exp"]], 1)[:, None, :], (1, P, 1))
    gu = np.stack([i["moe_w_gate"], i["moe_w_up"]], 3).reshape(2, EXPERTS, KT, P, 2, 2, P)
    a["w_gate_up"] = gu.transpose(0, 1, 3, 2, 5, 4, 6).reshape(2, EXPERTS, P, KT, 2 * FF)
    a["w_down"] = i["moe_w_down"].reshape(2, EXPERTS, FF // P, P, D_MODEL).transpose(0, 1, 3, 2, 4)
    wn = i["nsa_w_in"][0]
    order = [8 * pair + 4 * half + j for pair in range(2) for j in range(GROUP) for half in range(2)]
    q_cols = (np.array(order)[:, None] * HD + np.arange(HD)).ravel()
    n_kv = NSA_HEADS * HD
    cols = np.concatenate([q_cols, np.arange(n_kv, n_kv + 12 * P)])
    a["nsa_w"] = wn[:, cols].reshape(KT, P, NSA_TILES, P).transpose(2, 1, 0, 3)
    a["nsa_w_gates"] = wn[:, n_kv + 12 * P:].reshape(KT, P, 3 * NSA_HEADS).transpose(1, 0, 2)
    a["nsa_wo"] = tiles_of(i["nsa_w_out"][0][q_cols])
    a["page_table"] = i["page_table"].reshape(1, -1).astype(np.int32)
    a["cmp_pool"] = i["cache_nsa_cmp_kv"][0].reshape(N_POOL, PAGE, 4, P).transpose(0, 3, 2, 1).reshape(N_POOL, P, -1)
    def keys_major(x):
        k = x[:, :, 0].reshape(len(x), -1, 2, P).transpose(0, 3, 2, 1).reshape(len(x), P, -1)
        v = x[:, :, 1].reshape(len(x), -1, P, KVH * HD).transpose(0, 2, 1, 3).reshape(len(x), P, -1)
        return np.concatenate([k, v], 2)
    a["slc_pool"] = keys_major(i["cache_nsa_slc_kv"][0])
    a["win"] = keys_major(i["cache_nsa_win_kv"][0]).reshape(DEC_BATCH, P, 4, 4 * P)
    a["taps"] = i["gdn_conv_w"][0].reshape(CONV, CONV_TILES, P).transpose(2, 1, 0)
    a["conv_prev"] = i["state_gdn_conv"][0].reshape(DEC_BATCH, CONV - 1, CONV_TILES, P).transpose(3, 2, 0, 1)
    return a


OUTPUTS = {"conv_out": (P, CONV_TILES, (1 + DEC_BATCH) * (CONV - 1)),
           "p_S": (HEADS, P, P), "s_S": (HEADS, P, DEC_BATCH, P),
           "kv_out": (P, 12, TOKENS), "win_out": (DEC_BATCH, P, 4, 4 * P), "y": (P, KT, TOKENS)}


def build(nc, arrays, stop=99):
    d = {}
    for name, a in arrays.items():
        d[name] = nc.dram_tensor("in_" + name, a.shape, mybir.dt.from_np(a.dtype), kind="ExternalInput").ap()
    for name, shape in OUTPUTS.items():
        d[name] = nc.dram_tensor("out_" + name, shape, F32, kind="ExternalOutput").ap()
    d["h_rows"] = nc.dram_tensor("h_rows", (TOKENS, D_MODEL), F32, kind="Internal").ap()
    d["y_rows"] = nc.dram_tensor("y_rows", (2 * TOKENS, D_MODEL), F32, kind="Internal").ap()
    d["table"] = nc.dram_tensor("table", (P, COLUMNS + 2, WORDS), U32, kind="Internal").ap()
    d["first_sums"] = nc.dram_tensor("first_sums_d", (P, PAGES_EARLY, 4 * PAGE // CMP), F32, kind="Internal").ap()
    d["gate_scratch"] = nc.dram_tensor("gate_scratch", (NEW, 3 * NSA_HEADS), F32, kind="Internal").ap()
    decoder(nc, d, stop)
    return nc


def kernel(**inputs):
    import concourse.bacc as _bacc
    from concourse.bass_utils import run_bass_kernel_spmd

    arrays = {name: np.ascontiguousarray(a) for name, a in lay_out({n: np.asarray(a) for n, a in inputs.items()}).items()}
    nc = build(_bacc.Bacc("TRN2", target_bir_lowering=False, num_devices=1), arrays)
    r = run_bass_kernel_spmd(nc, [{"in_" + n: a for n, a in arrays.items()}], core_ids=[0]).results[0]

    def tokens_major(a):
        return a.transpose(2, 1, 0).reshape(a.shape[2], -1)
    y = tokens_major(r["out_y"])
    conv = r["out_conv_out"].transpose(2, 1, 0).reshape(1 + DEC_BATCH, CONV - 1, -1)
    kv = tokens_major(r["out_kv_out"]).reshape(TOKENS, 3, 2, KVH, HD)
    p_kv, s_kv = kv[:SEQ], kv[SEQ:].reshape(DEC_BATCH, DEC_SEQ, 3, 2, KVH, HD)
    win = r["out_win_out"].reshape(DEC_BATCH, P, 8, 2 * P)
    k_old = r["out_win_out"][:, :, 0:2, :].transpose(0, 3, 2, 1).reshape(DEC_BATCH, WINDOW, KVH, HD)
    v_old = win[:, :, 4:, :].transpose(0, 2, 1, 3).reshape(DEC_BATCH, WINDOW, KVH, HD)
    old = np.stack([k_old, v_old], 2)
    s_win = np.concatenate([old[:, DEC_SEQ:], s_kv[:, :, 2]], 1)
    out = (y[:SEQ].reshape(1, SEQ, D_MODEL), y[SEQ:].reshape(DEC_BATCH, DEC_SEQ, D_MODEL),
           r["out_p_S"][None, None], conv[None, :1], p_kv[None, None, :, 0], p_kv[None, None, :, 1],
           p_kv[None, None, :, 2], r["out_s_S"].transpose(2, 0, 1, 3)[None], conv[None, 1:],
           s_kv[None, :, :, 0], s_kv[None, :, :, 1], s_win[None])
    return tuple(np.ascontiguousarray(a) for a in out)
```

```python
from contextlib import ExitStack

import concourse.bass as bass
import numpy as np
from concourse import mybir

F32 = mybir.dt.float32
I32 = mybir.dt.int32
U32 = mybir.dt.uint32
ALU = mybir.AluOpType
ACT = mybir.ActivationFunctionType
AX_X = mybir.AxisListType.X

P = 128
D_MODEL = 1024
KT = D_MODEL // P
SEQ = 512
DEC_BATCH = 8
DEC_SEQ = 4
NEW = DEC_BATCH * DEC_SEQ
TOKENS = SEQ + NEW
HALF = TOKENS // 2
TILES = SEQ // P
PAST = 4096
PAGE = 128
N_PAGES = PAST // PAGE
N_POOL = DEC_BATCH * N_PAGES * 5 // 4
HEADS = 8
CHUNK = 64
CONV = 4
CONV_TILES = 3 * HEADS
NSA_HEADS = 16
KVH = 4
GROUP = NSA_HEADS // KVH
HD = 64
CMP = 32
SEL = 64
TOP_N = 16
WINDOW = 512
GROUPS = 4
PER_GROUP = 8
EXPERTS = 32
FF = 256
SLOTS = P // 2
PASSES = -(-TOKENS // SLOTS)
PAIRS = EXPERTS // 2
COLUMNS = PASSES * PAIRS
MOE_LANES = 2
TABLE_COLUMNS = COLUMNS + MOE_LANES
EPS = 1e-6
NEG = -1e30
SEL_BIG = 1e6

EXP_LN_SET = "natural_log_exp_and_others"
SILU_SET = "silu_and_others"


class Steps:

    def __init__(self, nc, ctx, name, steps, ahead=1):
        self.sem = ctx.enter_context(nc.semaphore(name))
        self.ahead = ahead
        self.steps = steps
        self.at = 0

    def credit(self, eng):
        eng.sem_inc(self.sem, len(self.steps))

    def done(self, step):
        assert self.steps[self.at] == step, (self.steps[self.at], step)
        self.at = (self.at + 1) % len(self.steps)
        return self.sem, 1

    def past(self, step, i=0):
        return (i + self.ahead) * len(self.steps) + self.steps.index(step) + 1


def constants():
    r = np.arange(P)
    chunk = r // CHUNK
    c = {}
    c["ident"] = np.eye(P)
    c["ones"] = np.ones((P, P))
    c["head_ones"] = (r[:, None] // HD == r[None, :] // HD) * 1.0
    low = (r[:, None] <= r[None, :]) & (chunk[:, None] == chunk[None, :])
    c["tri"] = low * 1.0
    c["same"] = (chunk[:, None] == chunk[None, :]) * 1.0
    c["decay_neg"] = np.where(low, 0.0, NEG)
    c["half0"] = (chunk == 0)[:, None] * np.ones((1, P))
    c["half1"] = (chunk == 1)[:, None] * np.ones((1, P))
    for k in range(6):
        b = 1 << k
        m = (r[:, None] // (2 * b) == r[None, :] // (2 * b)) & (r[:, None] % (2 * b) < b) & (r[None, :] % (2 * b) >= b)
        c[f"level{k}"] = m * 1.0
    s = np.arange(NEW)
    own = s[:, None] // DEC_SEQ == s[None, :] // DEC_SEQ
    def rows(a):
        out = np.zeros((P, a.shape[1]))
        out[: len(a)] = a
        return out
    low4 = own & (s[:, None] <= s[None, :])
    c["tri_new"] = rows(low4 * 1.0)
    c["same_new"] = rows(own * 1.0)
    c["decay_neg_new"] = rows(np.where(low4, 0.0, NEG))
    c["batch_of"] = rows((s[:, None] // DEC_SEQ == np.arange(DEC_BATCH)[None, :]) * 1.0)
    c["first_pick"] = np.tile(float(PER_GROUP) - np.arange(PER_GROUP), (P, 1))
    c["before"] = (r[:, None] < r[None, :]) * 1.0
    e = np.arange(EXPERTS)
    c["first_slot"] = np.tile(e % 2 * SLOTS * TABLE_COLUMNS + e // 2, (P, 1))
    c["token"] = np.arange(TILES + 1)[None, :] * P + r[:, None]
    c["causal_neg"] = np.where(r[None, :] <= r[:, None], 0.0, NEG)
    blocks = SEQ // CMP
    q = np.arange(SEQ).reshape(TILES, P).T
    seen = ((np.arange(blocks) + 1) * CMP - 1)[None, None, :] <= q[:, :, None]
    c["q_scale"] = np.full((P, 1), HD ** -0.5)
    c["cmp_seen"] = (seen * 1.0).reshape(P, TILES * blocks)
    c["cmp_neg"] = np.where(seen, 0.0, NEG).reshape(P, TILES * blocks)
    row = np.arange(KVH * GROUP * DEC_SEQ)
    t = row % DEC_SEQ
    kvh = row // (GROUP * DEC_SEQ)
    c["group_sum"] = rows(((kvh[:, None] == kvh[None, :]) & (t[:, None] == t[None, :])) * 1.0)
    key_t, key_b = np.arange(NEW) % DEC_SEQ, np.arange(NEW) // DEC_SEQ
    seen = (key_b[None, None, :] == np.arange(DEC_BATCH)[None, :, None]) & (key_t[None, None, :] <= t[:, None, None])
    c["new_neg"] = rows(np.where(seen, 0.0, NEG).reshape(len(row), -1))
    w = np.arange(WINDOW)
    c["win_neg"] = rows(np.where(w[None, :] > t[:, None], 0.0, NEG))
    n_sel = PAST // SEL + 1
    blk = np.arange(n_sel - 1)
    forced = (blk == 0) | (blk == n_sel - 2)
    c["forced"] = rows(np.tile(forced * SEL_BIG, (len(row), 1)))
    return {k: np.ascontiguousarray(v, dtype=np.float32) for k, v in c.items()}


CONSTANTS = constants()
CONST_AT = {}
_n = 0
for _k, _v in CONSTANTS.items():
    CONST_AT[_k] = (_n, _v.shape[1])
    _n += _v.shape[1]
CONST_W = _n


def halves(ap):
    return ap.rearrange("p (a b) -> p a b", a=2)


class Stage:

    def __init__(self, nc, name, clear=True):
        self.nc, self.name, self.ctx, self.clear, self.sems = nc, name, ExitStack(), clear, []

    def __enter__(self):
        return self

    def __exit__(self, failed, *_):
        if failed:
            return
        if self.clear:
            with self.block() as block:
                @block.sync
                def _(sp):
                    for sem in self.sems:
                        sp.sem_clear(sem)
        self.ctx.close()

    def sb(self, name, shape, dt=F32):
        return self.ctx.enter_context(self.nc.sbuf_tensor(f"{self.name}_{name}", shape, dt))

    def ps(self, name, shape=(P, 512)):
        return self.ctx.enter_context(self.nc.psum_tensor(f"{self.name}_{name}", list(shape), F32))

    def steps(self, name, steps):
        counted = Steps(self.nc, self.ctx, f"{self.name}_{name}", steps)
        self.sems.append(counted.sem)
        return counted

    def line(self, name, steps):
        counted = Steps(self.nc, self.ctx, f"{self.name}_{name}", steps, ahead=0)
        self.sems.append(counted.sem)
        return counted

    def sem(self, name):
        sem = self.ctx.enter_context(self.nc.semaphore(f"{self.name}_{name}"))
        self.sems.append(sem)
        return sem

    def software_dma_sem(self, name):
        return self.nc.alloc_semaphore(f"{self.name}_{name}")

    def block(self):
        return self.nc.Block(no_gpsimd_drain=True)


def load_inputs(nc, g):
    with Stage(nc, "load") as st:
        loaded = st.sem("loaded")
        with st.block() as block:
            @block.sync
            def _(sp):
                sp.dma_start(g.xT[:, :, :], g.d["x"]).then_inc(loaded, 16)
                sp.dma_start(g.consts[:, :], g.d["consts"]).then_inc(loaded, 16)
                sp.dma_start(g.gains[:, :], g.d["gains"]).then_inc(loaded, 16)
                sp.dma_start(g.page_table[:, :], g.d["page_table"]).then_inc(loaded, 16)
                sp.wait_ge(loaded, 64)


class PageSums:

    def __init__(self, nc, g, st, out, first, per):
        self.nc, self.g, self.out, self.first, self.per = nc, g, out, first, per
        self.raw = [st.sb(f"raw{s}", [P, per, 4 * PAGE]) for s in range(2)]
        self.loaded = [st.sem(f"raw_in{s}") for s in range(2)]
        self.dve_s = [st.steps(f"sums{s}", ["summed"]) for s in range(2)]

    def at(self, s, i):
        return (2 * i + s) * self.per + self.first

    def load(self, sp, s, i):
        sp.wait_ge(self.dve_s[s].sem, self.dve_s[s].past("summed", i - 1))
        _, pages = self.nc.values_load_multi_w_load_instructions(
            self.g.page_table[0:1, bass.ds(self.at(s, i), self.per)], engines=[mybir.EngineType.SP],
            min_val=0, max_val=N_POOL - 1)
        for n, page in enumerate(pages):
            sp.dma_start(self.raw[s][:, n, :], self.g.d["cmp_pool"][bass.ds(page, 1)].rearrange("g p n -> (g p) n")
                         ).then_inc(self.loaded[s], 16)

    def credit(self, dve):
        for s in range(2):
            self.dve_s[s].credit(dve)

    def sum(self, dve, s, i):
        dve.wait_ge(self.loaded[s], 16 * self.per * (i + 1))
        dve.tensor_reduce(self.out[:, bass.ds(self.at(s, i), self.per), :].rearrange("p g c -> p (g c)"),
                          self.raw[s][:, :, :].rearrange("p g (c t) -> p (g c) t", t=CMP), AX_X, ALU.add
                          ).then_inc(*self.dve_s[s].done("summed"))


PAGES_GDN = 4
PAGES_NSA = 4
PAGES_ATT = 3
PAGES_EARLY = PAGES_GDN * (CONV_TILES + HEADS)


def rms_norm_stage(nc, g, name, gain0, prefetch=None):
    with Stage(nc, name) as st:
        sq = st.sb("sq", [P, KT, TOKENS])
        rms = st.sb("rms", [P, TOKENS])
        total = st.ps("total", (P, 2, 512))
        squares = st.sem("squares")
        summed = st.sem("summed")
        logged = st.sem("logged")
        inverted = st.sem("inverted")
        ones = g.const("ones")
        with st.block() as block:
            @block.sync
            def _(sp):
                if prefetch:
                    prefetch(sp)

            @block.scalar
            def _(act):
                for k in range(KT):
                    act.activation(sq[:, k, :], g.xT[:, k, :], ACT.Square).then_inc(squares, 1)
                act.wait_ge(summed, 1)
                act.activation(halves(rms[:, :]), total[:, :, 0:HALF], ACT.Ln, bias=g.eps[:, 0:1],
                               scale=1.0 / D_MODEL).then_inc(logged, 1)
                act.wait_ge(logged, 1)
                act.activation(rms[:, :], rms[:, :], ACT.Exp, scale=-0.5).then_inc(inverted, 1)

            @block.tensor
            def _(pe):
                for k in range(KT):
                    pe.wait_ge(squares, k + 1)
                    for a in range(2):
                        mm = pe.matmul(total[:, a, 0:HALF], ones, sq[:, k, a * HALF:(a + 1) * HALF],
                                       start=(k == 0), stop=(k == KT - 1))
                mm.then_inc(summed, 1)

            @block.vector
            def _(dve):
                dve.wait_ge(inverted, 1)
                for k in range(KT):
                    dve.scalar_tensor_tensor(out=g.hT[:, k, :], in0=g.xT[:, k, :],
                                             scalar=g.gains[:, gain0 + k:gain0 + k + 1], in1=rms[:, :],
                                             op0=ALU.mult, op1=ALU.mult)


def gdn_project_stage(nc, g):
    with Stage(nc, "proj") as st:
        w = [st.sb(f"w{s}", [P, KT, P]) for s in range(2)]
        xc = [st.sb(f"xc{s}", [P, CONV - 1 + SEQ]) for s in range(2)]
        xs = [st.sb(f"xs{s}", [P, DEC_BATCH, CONV - 1 + DEC_SEQ]) for s in range(2)]
        conv = [st.sb(f"conv{s}", [P, TOKENS]) for s in range(2)]
        taps = st.sb("taps", [P, CONV_TILES, CONV])
        prev = st.sb("prev", [P, CONV_TILES, DEC_BATCH, CONV - 1])
        tails = st.sb("tails", [P, CONV_TILES, (1 + DEC_BATCH) * (CONV - 1)])
        acc = [st.ps(f"acc{s}", (P, 2, 512)) for s in range(2)]
        loaded = [st.sem(f"loaded{s}") for s in range(2)]
        small = st.sem("small")
        stored = st.sem("stored")
        pe_s = [st.steps(f"pe{s}", ["product"]) for s in range(2)]
        act_s = [st.steps(f"act{s}", ["prompt out", "sample out", "silu"]) for s in range(2)]
        dve_s = [st.steps(f"dve{s}", [f"{part} tap {i}" for i in range(CONV) for part in ("prompt", "sample")])
                 for s in range(2)]
        pool_s = [st.steps(f"pool{s}", ["history", "prompt tail", "sample tail"]) for s in range(2)]
        cleared = st.sem("cleared")
        z_out = st.sem("z_out")
        rounds = CONV_TILES // 2
        z_rounds = HEADS // 2
        pages = PageSums(nc, g, st, g.first_sums, 0, PAGES_GDN)
        with st.block() as block:
            @block.sync
            def _(sp):
                sp.dma_start(taps[:, :, :], g.d["taps"]).then_inc(small, 16)
                sp.dma_start(prev[:, :, :, :], g.d["conv_prev"]).then_inc(small, 16)
                for s in range(2):
                    sp.dma_start(w[s][:, :, :], g.d["gdn_w"][s]).then_inc(loaded[s], 16)
                with sp.Fori(0, rounds + z_rounds - 1) as i:
                    for s in range(2):
                        sp.wait_ge(pe_s[s].sem, pe_s[s].past("product", i))
                        sp.dma_start(w[s][:, :, :],
                                     g.d["gdn_w"][bass.ds(2 * i + 2 + s, 1)].rearrange("t p k c -> (t p) k c")
                                     ).then_inc(loaded[s], 16)
                        pages.load(sp, s, i)
                for s in range(2):
                    pages.load(sp, s, rounds + z_rounds - 1)
                for s in range(2):
                    sp.wait_ge(pool_s[s].sem, pool_s[s].past("sample tail", rounds - 1))
                sp.dma_start(g.d["conv_out"], tails[:, :, :]).then_inc(stored, 16)
                sp.wait_ge(stored, 16)

            @block.tensor
            def _(pe):
                for s in range(2):
                    pe_s[s].credit(pe)

                def product(s, i):
                    pe.wait_ge(loaded[s], 16 * (i + 1))
                    for k in range(KT):
                        for a in range(2):
                            mm = pe.matmul(acc[s][:, a, 0:HALF], w[s][:, k, :], g.hT[:, k, a * HALF:(a + 1) * HALF],
                                           start=(k == 0), stop=(k == KT - 1))
                    mm.then_inc(*pe_s[s].done("product"))

                with pe.Fori(0, rounds) as i:
                    for s in range(2):
                        pe.wait_ge(act_s[s].sem, act_s[s].past("sample out", i - 1))
                        product(s, i)
                for i in range(z_rounds):
                    for s in range(2):
                        if i == 0:
                            pe.wait_ge(act_s[s].sem, act_s[s].past("sample out", rounds - 1))
                        else:
                            pe.wait_ge(z_out, 2 * (i - 1) + s + 1)
                        product(s, rounds + i)

            @block.scalar
            def _(act):
                act.preload_act_table_set(SILU_SET)
                for s in range(2):
                    act_s[s].credit(act)
                act.wait_ge(cleared, 2)
                with act.Fori(0, rounds) as i:
                    for s in range(2):
                        act.wait_ge(pe_s[s].sem, pe_s[s].past("product", i))
                        act.wait_ge(dve_s[s].sem, dve_s[s].past(f"sample tap {CONV - 1}", i - 1))
                        act.wait_ge(pool_s[s].sem, pool_s[s].past("sample tail", i - 1))
                        act.activation(xc[s][:, CONV - 1:CONV - 1 + HALF], acc[s][:, 0, 0:HALF],
                                       ACT.Copy).then_inc(*act_s[s].done("prompt out"))
                        act.activation(xc[s][:, CONV - 1 + HALF:], acc[s][:, 1, 0:SEQ - HALF], ACT.Copy)
                        act.activation(xs[s][:, :, CONV - 1:],
                                       acc[s][:, 1, SEQ - HALF:HALF].rearrange("p (b t) -> p b t", t=DEC_SEQ),
                                       ACT.Copy).then_inc(*act_s[s].done("sample out"))
                    for s in range(2):
                        act.wait_ge(dve_s[s].sem, dve_s[s].past(f"sample tap {CONV - 1}", i))
                        act.activation(g.qkv[:, bass.ds(2 * i + s, 1), :].rearrange("p a t -> p (a t)"),
                                       conv[s][:, :], ACT.Silu).then_inc(*act_s[s].done("silu"))
                for i in range(z_rounds):
                    for s in range(2):
                        act.wait_ge(pe_s[s].sem, pe_s[s].past("product", rounds + i))
                        act.activation(halves(g.zT[:, 2 * i + s, :]), acc[s][:, :, 0:HALF],
                                       ACT.Silu).then_inc(z_out, 1)

            @block.vector
            def _(dve):
                for s in range(2):
                    dve_s[s].credit(dve)
                    dve.memset(xc[s][:, 0:CONV - 1], 0.0).then_inc(cleared, 1)
                pages.credit(dve)
                dve.wait_ge(cleared, 2)
                dve.wait_ge(small, 32)
                with dve.Fori(0, rounds) as i:
                    for s in range(2):
                        dve.wait_ge(act_s[s].sem, act_s[s].past("sample out", i))
                        dve.wait_ge(act_s[s].sem, act_s[s].past("silu", i - 1))
                        dve.wait_ge(pool_s[s].sem, pool_s[s].past("history", i))
                        prompt = conv[s][:, 0:SEQ]
                        sample = conv[s][:, SEQ:TOKENS].rearrange("p (b t) -> p b t", t=DEC_SEQ)
                        for tap in range(CONV):
                            weight = taps[:, bass.ds(2 * i + s, 1), tap:tap + 1].rearrange("p a t -> p (a t)")
                            rows, new = xc[s][:, tap:tap + SEQ], xs[s][:, :, tap:tap + DEC_SEQ]
                            if tap == 0:
                                dve.tensor_scalar(prompt, rows, weight, None, ALU.mult
                                                  ).then_inc(*dve_s[s].done("prompt tap 0"))
                                dve.tensor_scalar(sample, new, weight, None, ALU.mult
                                                  ).then_inc(*dve_s[s].done("sample tap 0"))
                                continue
                            dve.wait_ge(dve_s[s].sem, dve_s[s].past(f"prompt tap {tap - 1}", i))
                            dve.scalar_tensor_tensor(out=prompt, in0=rows, scalar=weight, in1=prompt, op0=ALU.mult,
                                                     op1=ALU.add).then_inc(*dve_s[s].done(f"prompt tap {tap}"))
                            dve.wait_ge(dve_s[s].sem, dve_s[s].past(f"sample tap {tap - 1}", i))
                            dve.scalar_tensor_tensor(out=sample, in0=new, scalar=weight, in1=sample, op0=ALU.mult,
                                                     op1=ALU.add).then_inc(*dve_s[s].done(f"sample tap {tap}"))
                        pages.sum(dve, s, i)
                for i in range(rounds, rounds + z_rounds):
                    for s in range(2):
                        pages.sum(dve, s, i)

            @block.gpsimd
            def _(pool):
                for s in range(2):
                    pool_s[s].credit(pool)
                pool.wait_ge(small, 32)
                n = CONV - 1
                with pool.Fori(0, rounds) as i:
                    for s in range(2):
                        tile = bass.ds(2 * i + s, 1)
                        pool.wait_ge(dve_s[s].sem, dve_s[s].past(f"sample tap {CONV - 1}", i - 1))
                        pool.tensor_copy(xs[s][:, :, 0:n], prev[:, tile, :, :].rearrange("p a b t -> p (a b) t")
                                         ).then_inc(*pool_s[s].done("history"))
                        pool.wait_ge(act_s[s].sem, act_s[s].past("sample out", i))
                        pool.tensor_copy(tails[:, tile, 0:n].rearrange("p a t -> p (a t)"), xc[s][:, SEQ:SEQ + n]
                                         ).then_inc(*pool_s[s].done("prompt tail"))
                        pool.tensor_copy(
                            tails[:, tile, n:].rearrange("p a (b t) -> p (a b) t", t=n),
                            xs[s][:, :, DEC_SEQ:DEC_SEQ + n]).then_inc(*pool_s[s].done("sample tail"))


def gdn_gates_stage(nc, g):
    NT = TILES + 1
    with Stage(nc, "gates") as st:
        w = st.sb("w", [P, KT, 2 * HEADS])
        rows = st.sb("rows", [P, 2, HEADS])
        ab = st.sb("ab", [P, NT, 2 * HEADS])
        mag = st.sb("mag", [P, NT, HEADS])
        pos = st.sb("pos", [P, NT, HEADS])
        decay = st.sb("decay", [P, HEADS])
        diff = st.sb("diff", [P, NT, HEADS])
        by_batch = st.sb("by_batch", [NEW, DEC_BATCH, HEADS])
        proj, cum, whole, chunks = st.ps("proj"), st.ps("cum"), st.ps("whole"), st.ps("chunks")
        stored = st.sem("stored")
        loaded = st.sem("loaded")
        pe_s = st.line("pe", ["ab", "chunk sums", "batch sums"])
        dve_s = st.line("dve", ["clear", "copy", "copy new", "bias", "magnitude", "positive", "softplus", "g",
                                "by batch", "G", "G new", "diff", "diff new"])
        act_s = st.line("act", ["rate", "exp", "log", "beta", "eG", "tail"])
        a = ab[:, :, 0:HEADS]
        rows_of = [P] * TILES + [NEW]

        def tiles(t, n):
            return t[:, 0:NT * n].rearrange("p (t n) -> p t n", n=n)

        with st.block() as block:
            @block.sync
            def _(sp):
                sp.dma_start(w[:, :, :], g.d["gdn_w_ab"]).then_inc(loaded, 16)
                sp.dma_start(rows[:, :, :], g.d["gdn_rows"]).then_inc(loaded, 16)
                sp.dma_start(g.d["first_sums"], g.first_sums[:, :, :]).then_inc(stored, 16)
                sp.wait_ge(stored, 16)

            @block.tensor
            def _(pe):
                pe.wait_ge(loaded, 32)
                for t, n in enumerate(rows_of):
                    for k in range(KT):
                        mm = pe.matmul(tiles(proj, 2 * HEADS)[0:n, t, :], g.hT[:, k, t * P:t * P + n], w[:, k, :],
                                       start=(k == 0), stop=(k == KT - 1))
                mm.then_inc(*pe_s.done("ab"))
                pe.wait_ge(dve_s.sem, dve_s.past("g"))
                for t, n in enumerate(rows_of):
                    tri, same = ("tri", "same") if n == P else ("tri_new", "same_new")
                    pe.matmul(tiles(cum, HEADS)[0:n, t, :], g.const(tri, n)[:, 0:n], g.gate_g[0:n, t, :],
                              start=True, stop=True)
                    pe.matmul(tiles(whole, HEADS)[0:n, t, :], g.const(same, n)[:, 0:n], g.gate_g[0:n, t, :],
                              start=True, stop=True)
                for t in range(TILES):
                    for half in range(2):
                        at = (2 * t + half) * HEADS
                        mm = pe.matmul(chunks[:, at:at + HEADS], g.const(f"half{half}"), g.gate_g[:, t, :],
                                       start=True, stop=True)
                mm.then_inc(*pe_s.done("chunk sums"))
                pe.wait_ge(dve_s.sem, dve_s.past("by batch"))
                pe.matmul(chunks[:, 128:128 + DEC_BATCH * HEADS], g.const("ones", NEW),
                          by_batch[:, :, :].rearrange("s b h -> s (b h)"), start=True, stop=True
                          ).then_inc(*pe_s.done("batch sums"))

            @block.scalar
            def _(act):
                act.wait_ge(loaded, 32)
                act.activation(decay[:, :], rows[:, 0, :], ACT.Exp).then_inc(*act_s.done("rate"))
                act.wait_ge(dve_s.sem, dve_s.past("magnitude"))
                act.activation(mag[:, :, :], mag[:, :, :], ACT.Exp, scale=-1.0).then_inc(*act_s.done("exp"))
                act.wait_ge(act_s.sem, act_s.past("exp"))
                act.activation(mag[:, :, :], mag[:, :, :], ACT.Ln, bias=1.0).then_inc(*act_s.done("log"))
                act.activation(g.beta[:, :, :], ab[:, :, HEADS:], ACT.Sigmoid).then_inc(*act_s.done("beta"))
                act.wait_ge(dve_s.sem, dve_s.past("G new"))
                act.activation(g.eG[:, :, :], g.G[:, :, :], ACT.Exp).then_inc(*act_s.done("eG"))
                act.wait_ge(dve_s.sem, dve_s.past("diff new"))
                act.activation(g.tail[:, :, :], diff[:, :, :], ACT.Exp).then_inc(*act_s.done("tail"))
                act.wait_ge(pe_s.sem, pe_s.past("batch sums"))
                act.activation(g.e_chunk[:, :, :].rearrange("p c h -> p (c h)"), chunks[:, 0:2 * TILES * HEADS],
                               ACT.Exp)
                act.activation(g.e_batch[:, :, :].rearrange("p b h -> p (b h)"),
                               chunks[:, 128:128 + DEC_BATCH * HEADS], ACT.Exp)

            @block.vector
            def _(dve):
                dve.memset(ab[:, :, :], 0.0)
                dve.memset(g.G[:, TILES, :], 0.0)
                dve.memset(diff[:, TILES, :], 0.0).then_inc(*dve_s.done("clear"))
                dve.wait_ge(dve_s.sem, dve_s.past("clear"))
                dve.wait_ge(pe_s.sem, pe_s.past("ab"))
                dve.tensor_copy(ab[:, 0:TILES, :], tiles(proj, 2 * HEADS)[:, 0:TILES, :]
                                ).then_inc(*dve_s.done("copy"))
                dve.tensor_copy(ab[0:NEW, TILES, :], tiles(proj, 2 * HEADS)[0:NEW, TILES, :]
                                ).then_inc(*dve_s.done("copy new"))
                dve.wait_ge(dve_s.sem, dve_s.past("copy new"))
                dve.wait_ge(loaded, 32)
                dve.tensor_tensor(a, a, rows[:, 1:2, :].broadcast_to([P, NT, HEADS]), ALU.add
                                  ).then_inc(*dve_s.done("bias"))
                dve.wait_ge(dve_s.sem, dve_s.past("bias"))
                dve.scalar_tensor_tensor(out=mag[:, :, :], in0=a, scalar=-1.0, in1=a, op0=ALU.mult, op1=ALU.max).then_inc(*dve_s.done("magnitude"))
                dve.tensor_scalar(pos[:, :, :], a, 0.0, None, ALU.max).then_inc(*dve_s.done("positive"))
                dve.wait_ge(act_s.sem, act_s.past("log"))
                dve.wait_ge(dve_s.sem, dve_s.past("positive"))
                dve.tensor_tensor(pos[:, :, :], pos[:, :, :], mag[:, :, :], ALU.add
                                  ).then_inc(*dve_s.done("softplus"))
                dve.wait_ge(dve_s.sem, dve_s.past("softplus"))
                dve.scalar_tensor_tensor(out=g.gate_g[:, :, :], in0=pos[:, :, :], scalar=-1.0,
                                         in1=decay[:, :].unsqueeze(1).broadcast_to([P, NT, HEADS]),
                                         op0=ALU.mult, op1=ALU.mult).then_inc(*dve_s.done("g"))
                dve.wait_ge(dve_s.sem, dve_s.past("g"))
                dve.tensor_tensor(by_batch[:, :, :],
                                  g.gate_g[0:NEW, TILES, :].unsqueeze(1).broadcast_to([NEW, DEC_BATCH, HEADS]),
                                  g.const("batch_of", NEW).unsqueeze(2).broadcast_to([NEW, DEC_BATCH, HEADS]),
                                  ALU.mult).then_inc(*dve_s.done("by batch"))
                dve.wait_ge(pe_s.sem, pe_s.past("chunk sums"))
                new = slice(0, NEW)
                dve.tensor_copy(g.G[:, 0:TILES, :], tiles(cum, HEADS)[:, 0:TILES, :]).then_inc(*dve_s.done("G"))
                dve.tensor_copy(g.G[new, TILES, :], tiles(cum, HEADS)[new, TILES, :]).then_inc(*dve_s.done("G new"))
                dve.wait_ge(dve_s.sem, dve_s.past("G new"))
                dve.tensor_tensor(diff[:, 0:TILES, :], tiles(whole, HEADS)[:, 0:TILES, :], g.G[:, 0:TILES, :],
                                  ALU.subtract).then_inc(*dve_s.done("diff"))
                dve.tensor_tensor(diff[new, TILES, :], tiles(whole, HEADS)[new, TILES, :], g.G[new, TILES, :],
                                  ALU.subtract).then_inc(*dve_s.done("diff new"))


LEVELS = 6
DOUBLINGS = range(1, LEVELS)
CHUNKS = SEQ // CHUNK
LANE_PE = (["squares", "k rows", "v rows", "kk", "qk", "G wide", "beta wide", "T 0"]
           + [x for n in DOUBLINGS for x in (f"W {n}", f"TT {n}")]
           + ["u", "w", "new u w"]
           + [x for j in range(CHUNKS) for x in (f"wS {j}", f"KV {j}", f"o {j}")]
           + ["new wS qS", "new v rows", "new o", "new KV", "o squares"])
LANE_DVE = (["gates", "k beta decay staged", "k", "q", "k beta decay", "difference", "qk", "kk", "L", "TT 0"]
            + [f"T {n}" for n in DOUBLINGS]
            + [x for j in range(CHUNKS) for x in (f"v {j}", f"S {j}")]
            + ["new v", "new v by batch", "new S decayed", "new S", "new o", "o normed", "o gated"])
LANE_ACT = (["squares", "v", "log norms", "norms", "k tail", "v beta", "eG wide", "decay", "T 0"]
            + [f"W {n}" for n in DOUBLINGS]
            + ["u", "w", "new wS qS", "new v rows", "o", "o square", "o log", "o norm"])
LANE_POOL = ["clear S", "q decayed"] + [f"level {n}" for n in range(LEVELS)]


def gdn_heads_stage(nc, g):
    with Stage(nc, "heads") as st:
        class Lane:
            pass
        lanes = []
        copied = st.sem("copied")
        N = slice(0, NEW)
        for s in range(2):
            ln = Lane()
            lanes.append(ln)
            ln.s = s
            ln.sq = st.sb(f"sq{s}", [P, 2, TOKENS])
            ln.norm = st.sb(f"norm{s}", [P, 2, TOKENS])
            ln.kT = st.sb(f"kT{s}", [P, TOKENS])
            ln.qT = st.sb(f"qT{s}", [P, TOKENS])
            ln.kbe = st.sb(f"kbe{s}", [P, TILES + 1, P])
            ln.kt = st.sb(f"kt{s}", [P, TILES + 1, P])
            ln.vb = st.sb(f"vb{s}", [P, TILES + 1, P])
            ln.dec = st.sb(f"dec{s}", [P, TOKENS])
            ln.LT = st.sb(f"LT{s}", [P, TOKENS])
            ln.QK = st.sb(f"QK{s}", [P, TOKENS])
            ln.B = st.sb(f"B{s}", [P, 2, TOKENS])
            ln.T = st.sb(f"T{s}", [P, TOKENS])
            ln.TT = st.sb(f"TT{s}", [P, TOKENS])
            ln.W = st.sb(f"W{s}", [P, TOKENS])
            ln.u = st.sb(f"u{s}", [P, TILES, P])
            ln.wq = st.sb(f"wq{s}", [P, 2, TOKENS])
            ln.S = st.sb(f"S{s}", [P, P])
            ln.vn = st.sb(f"vn{s}", [P, P])
            ln.o = st.sb(f"o{s}", [P, TOKENS])
            ln.S_new = st.sb(f"S_new{s}", [P, DEC_BATCH, P])
            ln.wSqS = st.sb(f"wSqS{s}", [P, DEC_BATCH, 2, DEC_SEQ])
            ln.vT = st.sb(f"vT{s}", [P, NEW])
            ln.v_rows = st.sb(f"v_rows{s}", [NEW, P])
            ln.gates = st.sb(f"gates{s}", [P, 5, TILES + 1])
            ln.v_batch = ln.B[N, :, :].rearrange("s a t -> s (a t)")[:, 0:DEC_BATCH * P].rearrange(
                "s (b v) -> s b v", b=DEC_BATCH)
            ln.bank = [st.ps(f"bank{s}{n}") for n in range(4)]
            ln.pe = st.steps(f"pe{s}", LANE_PE)
            ln.dve = st.steps(f"dve{s}", LANE_DVE)
            ln.act = st.steps(f"act{s}", LANE_ACT)
            ln.pool = st.steps(f"pool{s}", LANE_POOL)
            ln.sp = st.steps(f"sp{s}", ["states stored"])
            ln.loaded = st.sem(f"loaded{s}")
            ln.stored = st.sem(f"stored{s}")
        rounds = HEADS // 2
        NT = slice(SEQ, TOKENS)
        G_, BETA, CUM, BETA_DECAY, TAIL = range(5)

        def tile(t):
            return slice(t * P, (t + 1) * P)

        def tiled(ap):
            return ap.rearrange("p (t c) -> p t c", c=P)

        def wide(mask):
            return g.const(mask).unsqueeze(1).broadcast_to([P, TILES, P])

        def new_const(name):
            return g.const(name, NEW)[:, 0:NEW]

        def head_of(t, ln, i):
            return t[:, bass.ds(2 * i + ln.s, 1), :].rearrange("p a t -> p (a t)")

        def alternate(rule, i):
            for _ in zip(*(rule(ln, i) for ln in lanes)):
                pass

        with st.block() as block:
            @block.sync
            def _(sp):
                sp.dma_start(g.d["win_out"].rearrange("b p a n -> (b p) (a n)"),
                             g.d["win"].rearrange("b p a n -> (b p) (a n)")).then_inc(copied, 16)
                for ln in lanes:
                    ln.sp.credit(sp)
                with sp.Fori(0, rounds) as i:
                    for ln in lanes:
                        h = bass.ds(2 * i + ln.s, 1)
                        sp.dma_start(ln.S_new[:, :, :], g.d["gdn_S"][h].rearrange("h k b v -> (h k) b v")
                                     ).then_inc(ln.loaded, 16)
                    for ln in lanes:
                        h = bass.ds(2 * i + ln.s, 1)
                        sp.wait_ge(ln.dve.sem, ln.dve.past(f"S {CHUNKS - 1}", i))
                        sp.dma_start(g.d["p_S"][h].rearrange("h k v -> (h k) v"), ln.S[:, :]).then_inc(ln.stored, 16)
                    for ln in lanes:
                        h = bass.ds(2 * i + ln.s, 1)
                        sp.wait_ge(ln.dve.sem, ln.dve.past("new S", i))
                        sp.dma_start(g.d["s_S"][h].rearrange("h k b v -> (h k) b v"), ln.S_new[:, :, :]
                                     ).then_inc(ln.stored, 16)
                    for ln in lanes:
                        sp.wait_ge(ln.stored, 32 * (i + 1))
                        sp.sem_inc(*ln.sp.done("states stored"))
                sp.wait_ge(copied, 16)

            @block.tensor
            def _(pe):
                def rule(ln, i):
                    b0, b1, b2, b3 = ln.bank

                    def each(out, lhsT, rhs):
                        for t in range(TILES):
                            mm = pe.matmul(out[:, tile(t)], lhsT(t), rhs(t), start=True, stop=True)
                        return mm

                    def new(out, lhsT, rhs):
                        return pe.matmul(out, lhsT, rhs, start=True, stop=True)
                    ones, ident = g.const("ones"), g.const("ident")
                    pe.wait_ge(ln.act.sem, ln.act.past("squares", i))
                    pe.wait_ge(ln.dve.sem, ln.dve.past("new S", i - 1))
                    pe.wait_ge(ln.act.sem, ln.act.past("o norm", i - 1))
                    new(b0[:, :], ones, ln.sq[:, 0, 0:SEQ])
                    new(b1[:, :], ones, ln.sq[:, 1, 0:SEQ])
                    new(b2[:, 0:NEW], ones, ln.sq[:, 0, NT])
                    new(b2[:, NEW:2 * NEW], ones, ln.sq[:, 1, NT]).then_inc(*ln.pe.done("squares"))
                    yield
                    pe.wait_ge(ln.dve.sem, ln.dve.past("k", i))
                    for t in range(TILES):
                        pe.transpose(b3[:, tile(t)], ln.kT[:, tile(t)], ident)
                    pe.transpose(b2[N, 192:320], ln.QK[:, NT], ident)
                    pe.transpose(b2[N, 64:192], ln.kT[:, NT], ident).then_inc(*ln.pe.done("k rows"))
                    yield
                    for t in range(TILES):
                        mm = pe.transpose(b0[:, tile(t)], ln.QK[:, tile(t)], ident)
                    mm.then_inc(*ln.pe.done("v rows"))
                    yield
                    each(b1, lambda t: ln.kT[:, tile(t)], lambda t: ln.kT[:, tile(t)]
                         ).then_inc(*ln.pe.done("kk"))
                    yield
                    pe.wait_ge(ln.act.sem, ln.act.past("k tail", i))
                    each(b3, lambda t: ln.kT[:, tile(t)], lambda t: ln.qT[:, tile(t)]
                         ).then_inc(*ln.pe.done("qk"))
                    yield
                    pe.wait_ge(ln.act.sem, ln.act.past("v beta", i))
                    each(b0, lambda t: ln.gates[:, G_, t:t + 1].broadcast_to([P, P]), lambda t: g.const("tri"))
                    new(b2[N, 320:352], ln.kT[:, NT], ln.kT[:, NT])
                    new(b2[N, 352:384], ln.kT[:, NT], ln.qT[:, NT])
                    new(b2[:, 384:416], ln.gates[N, G_, TILES:TILES + 1].broadcast_to([NEW, P]),
                        new_const("tri_new")).then_inc(*ln.pe.done("G wide"))
                    yield
                    pe.wait_ge(ln.act.sem, ln.act.past("eG wide", i))
                    each(b0, lambda t: ln.gates[:, BETA, t:t + 1].broadcast_to([P, P]), lambda t: ident)
                    new(b2[N, 416:448], ln.gates[N, BETA, TILES:TILES + 1].broadcast_to([NEW, NEW]),
                        new_const("ident")).then_inc(*ln.pe.done("beta wide"))
                    yield
                    pe.wait_ge(ln.dve.sem, ln.dve.past("TT 0", i))
                    for t in range(TILES):
                        pe.transpose(b1[:, tile(t)], ln.TT[:, tile(t)], ident)
                    pe.transpose(b2[N, 0:32], ln.TT[N, NT], new_const("ident")).then_inc(*ln.pe.done("T 0"))
                    yield
                    for n in DOUBLINGS:
                        pe.wait_ge(ln.pool.sem, ln.pool.past(f"level {n}", i))
                        if n == 1:
                            pe.wait_ge(ln.act.sem, ln.act.past("T 0", i))
                        else:
                            pe.wait_ge(ln.dve.sem, ln.dve.past(f"T {n - 1}", i))
                        mm = each(b1, lambda t: ln.B[:, n % 2, tile(t)], lambda t: ln.T[:, tile(t)])
                        if n == 1:
                            mm = new(b2[N, 32:64], ln.B[N, 1, NT], ln.T[N, NT])
                        mm.then_inc(*ln.pe.done(f"W {n}"))
                        yield
                        pe.wait_ge(ln.act.sem, ln.act.past(f"W {n}", i))
                        if n < LEVELS - 1:
                            each(b3, lambda t: ln.TT[:, tile(t)], lambda t: ln.W[:, tile(t)])
                        mm = each(b0, lambda t: ln.W[:, tile(t)], lambda t: ln.TT[:, tile(t)])
                        if n == 1:
                            mm = new(b2[N, 64:96], ln.W[N, NT], ln.TT[N, NT])
                        mm.then_inc(*ln.pe.done(f"TT {n}"))
                        yield
                    pe.wait_ge(ln.dve.sem, ln.dve.past(f"T {LEVELS - 1}", i))
                    each(b1, lambda t: ln.TT[:, tile(t)], lambda t: ln.vb[:, t, :]).then_inc(*ln.pe.done("u"))
                    each(b3, lambda t: ln.kbe[:, t, :], lambda t: ln.TT[:, tile(t)]).then_inc(*ln.pe.done("w"))
                    new(b2[:, 96:128], ln.vb[N, TILES, :], ln.TT[N, NT])
                    new(b2[:, 128:160], ln.kbe[N, TILES, :], ln.TT[N, NT]).then_inc(*ln.pe.done("new u w"))
                    yield
                    pe.wait_ge(ln.pool.sem, ln.pool.past("q decayed", i))
                    pe.wait_ge(ln.act.sem, ln.act.past("w", i))
                    for j in range(CHUNKS):
                        t, R, C = j // 2, slice(CHUNK * (j % 2), CHUNK * (j % 2 + 1)), slice(j * CHUNK, (j + 1) * CHUNK)
                        if j:
                            pe.wait_ge(ln.dve.sem, ln.dve.past(f"S {j - 1}", i))
                        new(b1[R, 0:P], ln.wq[:, 0, C], ln.S[:, :]).then_inc(*ln.pe.done(f"wS {j}"))
                        pe.matmul(b0[:, C], ln.S[:, :], ln.wq[:, 1, C], start=True, stop=False)
                        yield
                        pe.wait_ge(ln.dve.sem, ln.dve.past(f"v {j}", i))
                        new(b3[:, 0:P], ln.kt[R, t, :], ln.vn[R, :]).then_inc(*ln.pe.done(f"KV {j}"))
                        pe.matmul(b0[:, C], ln.vn[R, :], ln.QK[R, C], start=False, stop=True
                                  ).then_inc(*ln.pe.done(f"o {j}"))
                        yield
                    pe.wait_ge(ln.loaded, 16 * (i + 1))
                    for b in range(DEC_BATCH):
                        at = 160 + 2 * DEC_SEQ * b
                        mm = new(b2[:, at:at + 2 * DEC_SEQ].rearrange("p (w t) -> p w t", w=2), ln.S_new[:, b, :],
                                 ln.wq[:, :, SEQ + DEC_SEQ * b:SEQ + DEC_SEQ * (b + 1)])
                    mm.then_inc(*ln.pe.done("new wS qS"))
                    yield
                    pe.wait_ge(ln.dve.sem, ln.dve.past("new v", i))
                    pe.transpose(b2[N, 224:352], ln.vT[:, :], ident).then_inc(*ln.pe.done("new v rows"))
                    yield
                    pe.wait_ge(ln.act.sem, ln.act.past("new v rows", i))
                    new(b2[:, 352:384], ln.v_rows[:, :], ln.QK[N, NT]).then_inc(*ln.pe.done("new o"))
                    pe.wait_ge(ln.dve.sem, ln.dve.past("new v by batch", i))
                    for a, bank in enumerate((b1, b3)):
                        mm = new(bank[:, :], ln.kt[N, TILES, :],
                                 ln.v_batch[:, 4 * a:4 * a + 4, :].rearrange("s b v -> s (b v)"))
                    mm.then_inc(*ln.pe.done("new KV"))
                    yield
                    pe.wait_ge(ln.act.sem, ln.act.past("o square", i))
                    new(b0[:, :], ones, ln.sq[:, 1, 0:SEQ])
                    new(b2[:, 384:416], ones, ln.sq[:, 1, NT]).then_inc(*ln.pe.done("o squares"))
                    yield

                for ln in lanes:
                    ln.pe.credit(pe)
                with pe.Fori(0, rounds) as i:
                    alternate(rule, i)

            @block.scalar
            def _(act):
                def rule(ln, i):
                    b0, b1, b2, b3 = ln.bank
                    q, k, v = (g.qkv[:, bass.ds(2 * i + ln.s + HEADS * n, 1), :].rearrange("p a t -> p (a t)")
                               for n in range(3))
                    act.wait_ge(ln.pe.sem, ln.pe.past("o squares", i - 1))
                    act.wait_ge(ln.pool.sem, ln.pool.past("q decayed", i - 1))
                    act.activation(ln.sq[:, 0, :], q, ACT.Square)
                    act.activation(ln.sq[:, 1, :], k, ACT.Square).then_inc(*ln.act.done("squares"))
                    act.activation(ln.QK[:, :], v, ACT.Copy).then_inc(*ln.act.done("v"))
                    yield
                    act.wait_ge(ln.pe.sem, ln.pe.past("squares", i))
                    act.wait_ge(ln.dve.sem, ln.dve.past("o normed", i - 1))
                    for n, bank in enumerate((b0, b1)):
                        act.activation(ln.norm[:, n, 0:SEQ], bank[:, :], ACT.Ln, bias=g.eps[:, 0:1])
                    act.activation(ln.norm[:, :, NT], b2[:, 0:2 * NEW].rearrange("p (n t) -> p n t", n=2), ACT.Ln,
                                   bias=g.eps[:, 0:1]).then_inc(*ln.act.done("log norms"))
                    yield
                    act.wait_ge(ln.act.sem, ln.act.past("log norms", i))
                    act.activation(ln.norm[:, :, :], ln.norm[:, :, :], ACT.Exp, scale=-0.5
                                   ).then_inc(*ln.act.done("norms"))
                    yield
                    act.wait_ge(ln.dve.sem, ln.dve.past("k beta decay", i))
                    for t in range(TILES):
                        act.activation(ln.kt[:, t, :], b3[:, tile(t)], ACT.Copy, scale=ln.gates[:, TAIL, t:t + 1])
                    act.activation(ln.kt[N, TILES, :], b2[N, 64:192], ACT.Copy,
                                   scale=ln.gates[N, TAIL, TILES:TILES + 1]).then_inc(*ln.act.done("k tail"))
                    act.wait_ge(ln.pe.sem, ln.pe.past("v rows", i))
                    for t in range(TILES):
                        act.activation(ln.vb[:, t, :], b0[:, tile(t)], ACT.Copy, scale=ln.gates[:, BETA, t:t + 1])
                    act.activation(ln.vb[N, TILES, :], b2[N, 192:320], ACT.Copy,
                                   scale=ln.gates[N, BETA, TILES:TILES + 1]).then_inc(*ln.act.done("v beta"))
                    yield
                    act.wait_ge(ln.dve.sem, ln.dve.past("difference", i))
                    act.activation(ln.sq[:, 0, 0:SEQ], b0[:, :], ACT.Exp)
                    act.activation(ln.sq[:, 0, NT], b2[:, 384:416], ACT.Exp).then_inc(*ln.act.done("eG wide"))
                    act.activation(ln.dec[:, 0:SEQ], ln.dec[:, 0:SEQ], ACT.Exp)
                    act.activation(ln.dec[N, NT], ln.dec[N, NT], ACT.Exp).then_inc(*ln.act.done("decay"))
                    yield
                    act.wait_ge(ln.pe.sem, ln.pe.past("T 0", i))
                    act.activation(ln.T[:, 0:SEQ], b1[:, :], ACT.Copy)
                    act.activation(ln.T[N, NT], b2[N, 0:32], ACT.Copy).then_inc(*ln.act.done("T 0"))
                    yield
                    for n in DOUBLINGS:
                        act.wait_ge(ln.pe.sem, ln.pe.past(f"W {n}", i))
                        if n == 1:
                            act.activation(ln.W[N, NT], b2[N, 32:64], ACT.Copy)
                        act.activation(ln.W[:, 0:SEQ], b1[:, :], ACT.Copy).then_inc(*ln.act.done(f"W {n}"))
                        yield
                    act.wait_ge(ln.pe.sem, ln.pe.past("u", i))
                    act.activation(ln.u[:, :, :].rearrange("p t v -> p (t v)"), b1[:, :], ACT.Copy
                                   ).then_inc(*ln.act.done("u"))
                    act.wait_ge(ln.pe.sem, ln.pe.past("new u w", i))
                    act.activation(ln.wq[:, 0, 0:SEQ], b3[:, :], ACT.Copy)
                    act.activation(ln.wq[:, 0, NT], b2[:, 128:160], ACT.Copy).then_inc(*ln.act.done("w"))
                    yield
                    act.wait_ge(ln.pe.sem, ln.pe.past("new wS qS", i))
                    act.activation(ln.wSqS[:, :, :, :].rearrange("p b w t -> p (b w t)"), b2[:, 160:224], ACT.Copy
                                   ).then_inc(*ln.act.done("new wS qS"))
                    yield
                    act.wait_ge(ln.pe.sem, ln.pe.past("new v rows", i))
                    act.activation(ln.v_rows[:, :], b2[N, 224:352], ACT.Copy).then_inc(*ln.act.done("new v rows"))
                    yield
                    act.wait_ge(ln.dve.sem, ln.dve.past("o gated", i - 1))
                    act.activation(ln.o[:, 0:SEQ], b0[:, :], ACT.Copy).then_inc(*ln.act.done("o"))
                    act.wait_ge(ln.act.sem, ln.act.past("o", i))
                    act.wait_ge(ln.dve.sem, ln.dve.past("new o", i))
                    act.activation(ln.sq[:, 1, :], ln.o[:, :], ACT.Square).then_inc(*ln.act.done("o square"))
                    yield
                    act.wait_ge(ln.pe.sem, ln.pe.past("o squares", i))
                    act.activation(ln.norm[:, 0, 0:SEQ], b0[:, :], ACT.Ln, scale=1.0 / P, bias=g.eps[:, 0:1])
                    act.activation(ln.norm[:, 0, NT], b2[:, 384:416], ACT.Ln, scale=1.0 / P, bias=g.eps[:, 0:1]
                                   ).then_inc(*ln.act.done("o log"))
                    yield
                    act.wait_ge(ln.act.sem, ln.act.past("o log", i))
                    act.activation(ln.norm[:, 0, :], ln.norm[:, 0, :], ACT.Exp, scale=-0.5
                                   ).then_inc(*ln.act.done("o norm"))
                    yield

                for ln in lanes:
                    ln.act.credit(act)
                with act.Fori(0, rounds) as i:
                    alternate(rule, i)

            @block.vector
            def _(dve):
                def rule(ln, i):
                    b0, b1, b2, b3 = ln.bank
                    h = bass.ds(2 * i + ln.s, 1)
                    q, k = (g.qkv[:, bass.ds(2 * i + ln.s + HEADS * n, 1), :].rearrange("p a t -> p (a t)")
                            for n in range(2))
                    dve.wait_ge(ln.pe.sem, ln.pe.past("beta wide", i - 1))
                    dve.wait_ge(ln.act.sem, ln.act.past("v beta", i - 1))
                    for n, gate in ((G_, g.gate_g), (BETA, g.beta), (CUM, g.G), (TAIL, g.tail)):
                        dve.tensor_copy(ln.gates[:, n, :], gate[:, :, h].rearrange("p t a -> p (t a)"))
                    dve.tensor_copy(ln.gates[:, BETA_DECAY, :], g.eG[:, :, h].rearrange("p t a -> p (t a)")
                                    ).then_inc(*ln.dve.done("gates"))
                    dve.wait_ge(ln.dve.sem, ln.dve.past("gates", i))
                    dve.tensor_tensor(ln.gates[:, BETA_DECAY, :], ln.gates[:, BETA_DECAY, :], ln.gates[:, BETA, :],
                                      ALU.mult).then_inc(*ln.dve.done("k beta decay staged"))
                    yield
                    dve.wait_ge(ln.act.sem, ln.act.past("norms", i))
                    dve.tensor_tensor(ln.kT[:, :], k, ln.norm[:, 1, :], ALU.mult).then_inc(*ln.dve.done("k"))
                    dve.scalar_tensor_tensor(out=ln.qT[:, :], in0=q, scalar=float(P) ** -0.5, in1=ln.norm[:, 0, :],
                                             op0=ALU.mult, op1=ALU.mult).then_inc(*ln.dve.done("q"))
                    yield
                    dve.wait_ge(ln.pe.sem, ln.pe.past("k rows", i))
                    dve.wait_ge(ln.dve.sem, ln.dve.past("k beta decay staged", i))
                    for t in range(TILES):
                        dve.tensor_scalar(ln.kbe[:, t, :], b3[:, tile(t)], ln.gates[:, BETA_DECAY, t:t + 1], None,
                                          ALU.mult)
                    dve.tensor_scalar(ln.kbe[N, TILES, :], b2[N, 64:192], ln.gates[N, BETA_DECAY, TILES:TILES + 1],
                                      None, ALU.mult).then_inc(*ln.dve.done("k beta decay"))
                    yield
                    dve.wait_ge(ln.pe.sem, ln.pe.past("G wide", i))
                    for t in range(TILES):
                        dve.scalar_tensor_tensor(out=ln.dec[:, tile(t)], in0=b0[:, tile(t)],
                                                 scalar=ln.gates[:, CUM, t:t + 1], in1=g.const("decay_neg"),
                                                 op0=ALU.subtract, op1=ALU.add)
                    dve.scalar_tensor_tensor(out=ln.dec[N, NT], in0=b2[N, 384:416],
                                             scalar=ln.gates[N, CUM, TILES:TILES + 1],
                                             in1=new_const("decay_neg_new"), op0=ALU.subtract, op1=ALU.add
                                             ).then_inc(*ln.dve.done("difference"))
                    yield
                    dve.wait_ge(ln.act.sem, ln.act.past("decay", i))
                    dve.wait_ge(ln.pe.sem, ln.pe.past("beta wide", i))
                    dve.tensor_tensor(ln.QK[:, 0:SEQ], b3[:, :], ln.dec[:, 0:SEQ], ALU.mult)
                    dve.tensor_tensor(ln.QK[N, NT], b2[N, 352:384], ln.dec[N, NT], ALU.mult
                                      ).then_inc(*ln.dve.done("qk"))
                    dve.tensor_tensor(ln.LT[:, 0:SEQ], b1[:, :], ln.dec[:, 0:SEQ], ALU.mult)
                    dve.tensor_tensor(ln.LT[N, NT], b2[N, 320:352], ln.dec[N, NT], ALU.mult
                                      ).then_inc(*ln.dve.done("kk"))
                    dve.wait_ge(ln.dve.sem, ln.dve.past("kk", i))
                    dve.tensor_tensor(ln.LT[:, 0:SEQ], ln.LT[:, 0:SEQ], b0[:, :], ALU.mult)
                    dve.tensor_tensor(ln.LT[N, NT], ln.LT[N, NT], b2[N, 416:448], ALU.mult
                                      ).then_inc(*ln.dve.done("L"))
                    yield
                    dve.wait_ge(ln.pool.sem, ln.pool.past("level 0", i))
                    dve.scalar_tensor_tensor(out=tiled(ln.TT[:, 0:SEQ]), in0=tiled(ln.B[:, 0, 0:SEQ]), scalar=-1.0,
                                             in1=wide("ident"), op0=ALU.mult, op1=ALU.add)
                    dve.scalar_tensor_tensor(out=ln.TT[N, NT], in0=ln.B[N, 0, NT], scalar=-1.0,
                                             in1=new_const("ident"), op0=ALU.mult, op1=ALU.add
                                             ).then_inc(*ln.dve.done("TT 0"))
                    yield
                    for n in DOUBLINGS:
                        dve.wait_ge(ln.pe.sem, ln.pe.past(f"TT {n}", i))
                        if n == 1:
                            dve.tensor_tensor(ln.TT[N, NT], ln.TT[N, NT], b2[N, 64:96], ALU.subtract)
                        if n < LEVELS - 1:
                            dve.tensor_tensor(ln.T[:, 0:SEQ], ln.T[:, 0:SEQ], b3[:, :], ALU.subtract)
                        dve.tensor_tensor(ln.TT[:, 0:SEQ], ln.TT[:, 0:SEQ], b0[:, :], ALU.subtract
                                          ).then_inc(*ln.dve.done(f"T {n}"))
                        yield
                    dve.wait_ge(ln.act.sem, ln.act.past("u", i))
                    dve.wait_ge(ln.pool.sem, ln.pool.past("clear S", i))
                    for j in range(CHUNKS):
                        t, R = j // 2, slice(CHUNK * (j % 2), CHUNK * (j % 2 + 1))
                        dve.wait_ge(ln.pe.sem, ln.pe.past(f"wS {j}", i))
                        dve.tensor_tensor(ln.vn[R, :], ln.u[R, t, :], b1[R, 0:P], ALU.subtract
                                          ).then_inc(*ln.dve.done(f"v {j}"))
                        yield
                        dve.wait_ge(ln.pe.sem, ln.pe.past(f"KV {j}", i))
                        if j:
                            dve.wait_ge(ln.dve.sem, ln.dve.past(f"S {j - 1}", i))
                        dve.scalar_tensor_tensor(out=ln.S[:, :], in0=ln.S[:, :],
                                                 scalar=g.e_chunk[:, j:j + 1, h].rearrange("p a b -> p (a b)"),
                                                 in1=b3[:, 0:P], op0=ALU.mult, op1=ALU.add
                                                 ).then_inc(*ln.dve.done(f"S {j}"))
                        yield
                    dve.wait_ge(ln.act.sem, ln.act.past("new wS qS", i))
                    dve.tensor_tensor(ln.vT[:, :].rearrange("p (b t) -> p b t", t=DEC_SEQ),
                                      b2[:, 96:128].rearrange("p (b t) -> p b t", t=DEC_SEQ),
                                      ln.wSqS[:, :, 0, :], ALU.subtract).then_inc(*ln.dve.done("new v"))
                    yield
                    dve.wait_ge(ln.act.sem, ln.act.past("new v rows", i))
                    dve.tensor_tensor(ln.v_batch[:, :, :],
                                      ln.v_rows[:, :].unsqueeze(1).broadcast_to([NEW, DEC_BATCH, P]),
                                      g.const("batch_of", NEW).unsqueeze(2).broadcast_to([NEW, DEC_BATCH, P]),
                                      ALU.mult).then_inc(*ln.dve.done("new v by batch"))
                    dve.tensor_tensor(ln.S_new[:, :, :], ln.S_new[:, :, :],
                                      g.e_batch[:, :, h].broadcast_to([P, DEC_BATCH, P]), ALU.mult
                                      ).then_inc(*ln.dve.done("new S decayed"))
                    yield
                    dve.wait_ge(ln.pe.sem, ln.pe.past("new KV", i))
                    dve.wait_ge(ln.dve.sem, ln.dve.past("new S decayed", i))
                    for a, bank in enumerate((b1, b3)):
                        part = ln.S_new[:, 4 * a:4 * a + 4, :].rearrange("p b v -> p (b v)")
                        ins = dve.tensor_tensor(part, part, bank[:, :], ALU.add)
                    ins.then_inc(*ln.dve.done("new S"))
                    dve.wait_ge(ln.dve.sem, ln.dve.past("o gated", i - 1))
                    dve.tensor_tensor(ln.o[:, NT].rearrange("p (b t) -> p b t", t=DEC_SEQ),
                                      b2[:, 352:384].rearrange("p (b t) -> p b t", t=DEC_SEQ),
                                      ln.wSqS[:, :, 1, :], ALU.add).then_inc(*ln.dve.done("new o"))
                    yield
                    dve.wait_ge(ln.act.sem, ln.act.past("o norm", i))
                    dve.scalar_tensor_tensor(out=ln.o[:, :], in0=ln.o[:, :], scalar=g.gains[:, O_GAIN:O_GAIN + 1],
                                             in1=ln.norm[:, 0, :], op0=ALU.mult, op1=ALU.mult
                                             ).then_inc(*ln.dve.done("o normed"))
                    dve.wait_ge(ln.dve.sem, ln.dve.past("o normed", i))
                    z = head_of(g.zT, ln, i)
                    dve.tensor_tensor(z, z, ln.o[:, :], ALU.mult).then_inc(*ln.dve.done("o gated"))
                    yield

                for ln in lanes:
                    ln.dve.credit(dve)
                with dve.Fori(0, rounds) as i:
                    alternate(rule, i)

            @block.gpsimd
            def _(pool):
                def rule(ln, i):
                    pool.wait_ge(ln.sp.sem, ln.sp.past("states stored", i - 1))
                    pool.tensor_tensor(ln.S[:, :], g.const("ident"), g.const("ident"), ALU.subtract).then_inc(*ln.pool.done("clear S"))
                    pool.wait_ge(ln.act.sem, ln.act.past("eG wide", i))
                    pool.wait_ge(ln.dve.sem, ln.dve.past("q", i))
                    pool.wait_ge(ln.pe.sem, ln.pe.past("new wS qS", i - 1))
                    pool.tensor_tensor(ln.wq[:, 1, :], ln.qT[:, :], ln.sq[:, 0, :], ALU.mult
                                       ).then_inc(*ln.pool.done("q decayed"))
                    yield
                    pool.wait_ge(ln.dve.sem, ln.dve.past("L", i))
                    for n in range(LEVELS):
                        if n == 2:
                            pool.wait_ge(ln.dve.sem, ln.dve.past("TT 0", i))
                        if n > 2:
                            pool.wait_ge(ln.pe.sem, ln.pe.past(f"W {n - 2}", i))
                        if n < 2:
                            pool.tensor_tensor(ln.B[N, n, NT], ln.LT[N, NT], new_const(f"level{n}"), ALU.mult)
                        pool.tensor_tensor(tiled(ln.B[:, n % 2, 0:SEQ]), tiled(ln.LT[:, 0:SEQ]), wide(f"level{n}"),
                                           ALU.mult).then_inc(*ln.pool.done(f"level {n}"))
                        yield

                for ln in lanes:
                    ln.pool.credit(pool)
                with pool.Fori(0, rounds) as i:
                    alternate(rule, i)


def out_project_stage(nc, g, name, w_d, src):
    with Stage(nc, name) as st:
        w = [st.sb(f"w{s}", [P, KT, P]) for s in range(2)]
        acc = [st.ps(f"acc{s}", (P, 2, 512)) for s in range(2)]
        loaded = [st.sem(f"loaded{s}") for s in range(2)]
        multiplied, added = st.sem("multiplied"), st.sem("added")
        with st.block() as block:
            @block.sync
            def _(sp):
                for m in range(KT):
                    if m >= 2:
                        sp.wait_ge(multiplied, m - 1)
                    sp.dma_start(w[m % 2][:, :, :], w_d[m]).then_inc(loaded[m % 2], 16)

            @block.tensor
            def _(pe):
                for m in range(KT):
                    pe.wait_ge(loaded[m % 2], 16 * (m // 2 + 1))
                    if m >= 2:
                        pe.wait_ge(added, m - 1)
                    for k in range(KT):
                        for a in range(2):
                            mm = pe.matmul(acc[m % 2][:, a, 0:HALF], w[m % 2][:, k, :],
                                           src[:, k, a * HALF:(a + 1) * HALF], start=(k == 0), stop=(k == KT - 1))
                    mm.then_inc(multiplied, 1)

            @block.vector
            def _(dve):
                for m in range(KT):
                    dve.wait_ge(multiplied, m + 1)
                    dve.tensor_tensor(halves(g.xT[:, m, :]), acc[m % 2][:, :, 0:HALF], halves(g.xT[:, m, :]),
                                      ALU.add).then_inc(added, 1)


SRC, DST, WEIGHT, WORDS = 0, 1, 2, 4
SLOT_BITS = SLOTS.bit_length() - 1
assert SLOTS == 1 << SLOT_BITS
NOWHERE = 1 << 20


def router_stage(nc, g, name, w, bias, loaded):
    NT = TILES + 1
    n_log = GROUPS + EXPERTS
    with Stage(nc, name) as st:
        logits = st.sb("logits", [P, NT, n_log])

        def col(x):
            return st.sb(x, [P, NT, 1])
        grp_max, grp_sum, grp_pick, m1, m2, p1, p2, e2, den = (
            col(x) for x in ("grp_max", "grp_sum", "grp_pick", "m1", "m2", "p1", "p2", "e2", "den"))
        weight = [col("w1"), col("w2")]
        place, over, address = col("place"), col("over"), col("address")
        e_grp = st.sb("e_grp", [P, NT, GROUPS])
        grp = st.sb("grp", [P, NT, GROUPS])
        inside, part, rest = (st.sb(x, [P, NT, PER_GROUP]) for x in ("inside", "part", "rest"))
        pick = [st.sb(x, [P, NT, PER_GROUP]) for x in ("first", "second")]
        onehot = [st.sb(f"onehot{j}", [P, NT, EXPERTS]) for j in range(2)]
        picked = st.sb("picked", [P, NT, EXPERTS])
        earlier = st.sb("earlier", [P, NT, EXPERTS])
        at_pick = st.sb("at_pick", [P, NT, EXPERTS])
        fullest, n_pass = st.sb("fullest", [P, 1]), st.sb("n_pass", [P, 1], I32)
        whole = st.sb("whole", [P, NT], I32)
        slot_of = [st.sb(f"slot_of{j}", [P, NT], U32) for j in range(2)]
        entry = [st.sb(f"entry{j}", [P, NT, WORDS], U32) for j in range(2)]
        empty = st.sb("empty", [P, TABLE_COLUMNS, WORDS], U32)
        rows = [st.sb(f"rows{s}", [P, D_MODEL]) for s in range(2)]
        proj, counts = st.ps("proj"), st.ps("counts")
        turned = [st.ps(f"turned{s}", (P, 2, 512)) for s in range(2)]
        emptied, cleared = st.sem("emptied"), st.sem("cleared")
        stored = [st.sem(f"stored{s}") for s in range(2)]
        scattered, table_in = st.software_dma_sem("scattered"), st.sem("table_in")
        pe_done, rows_turned, rows_out, dve_step, act_done = (
            st.sem(x) for x in ("pe_done", "rows_turned", "rows_out", "dve_step", "act_done"))
        rows_of = [P] * TILES + [NEW]
        pr = proj[:, 0:NT * n_log].rearrange("p (t n) -> p t n", n=n_log)
        cn = counts[:, 0:(NT + 1) * EXPERTS].rearrange("p (t n) -> p t n", n=EXPERTS)
        at = {}

        with st.block() as block:
            @block.vector
            def _(dve):
                taken = [0]

                def step(ins):
                    ins.then_inc(dve_step, 1)
                    taken[0] += 1
                    dve.wait_ge(dve_step, taken[0])

                def wide(t, n):
                    return t[:, :, :].broadcast_to([P, NT, n])

                def first_of(out, top_at, like, top_value, n):
                    step(dve.tensor_tensor(out, like, wide(top_value, n), ALU.is_equal))
                    order = g.const("first_pick")[:, 0:n].unsqueeze(1).broadcast_to([P, NT, n])
                    step(dve.tensor_tensor(out, out, order, ALU.mult))
                    step(dve.tensor_reduce(top_at[:, :, :], out, AX_X, ALU.max))
                    step(dve.tensor_tensor(out, out, wide(top_at, n), ALU.is_equal))

                step(dve.memset(empty[:, :, :], NOWHERE))
                dve.memset(empty[:, :, WEIGHT:WORDS], 0).then_inc(cleared, 1)
                for j in range(2):
                    dve.memset(entry[j][:, :, :], 0)
                step(dve.memset(logits[:, :, :], 0.0))
                dve.wait_ge(loaded, 32)
                dve.wait_ge(pe_done, 1)
                b = bias[:, :].unsqueeze(1)
                step(dve.tensor_tensor(logits[:, 0:TILES, :], pr[:, 0:TILES, :], b.broadcast_to([P, TILES, n_log]),
                                       ALU.add))
                step(dve.tensor_tensor(logits[0:NEW, TILES:NT, :], pr[0:NEW, TILES:NT, :],
                                       bias[0:NEW, :].unsqueeze(1), ALU.add))
                lg = logits[:, :, 0:GROUPS]
                step(dve.tensor_reduce(grp_max[:, :, :], lg, AX_X, ALU.max))
                step(dve.tensor_tensor(e_grp[:, :, :], lg, wide(grp_max, GROUPS), ALU.subtract))
                at["group logits"] = taken[0]
                first_of(grp[:, :, :], grp_pick, lg, grp_max, GROUPS)
                for k in range(GROUPS):
                    le = logits[:, :, GROUPS + k * PER_GROUP:GROUPS + (k + 1) * PER_GROUP]
                    own = grp[:, :, k:k + 1].broadcast_to([P, NT, PER_GROUP])
                    if k == 0:
                        step(dve.tensor_tensor(inside[:, :, :], le, own, ALU.mult))
                    else:
                        step(dve.tensor_tensor(part[:, :, :], le, own, ALU.mult))
                        step(dve.tensor_tensor(inside[:, :, :], inside[:, :, :], part[:, :, :], ALU.add))
                step(dve.tensor_reduce(m1[:, :, :], inside[:, :, :], AX_X, ALU.max))
                first_of(pick[0][:, :, :], p1, inside[:, :, :], m1, PER_GROUP)
                step(dve.scalar_tensor_tensor(out=rest[:, :, :], in0=pick[0][:, :, :], scalar=NEG,
                                              in1=inside[:, :, :], op0=ALU.mult, op1=ALU.add))
                step(dve.tensor_reduce(m2[:, :, :], rest[:, :, :], AX_X, ALU.max))
                step(dve.tensor_tensor(e2[:, :, :], m2[:, :, :], m1[:, :, :], ALU.subtract))
                at["pair logits"] = taken[0]
                first_of(pick[1][:, :, :], p2, rest[:, :, :], m2, PER_GROUP)
                for j in range(2):
                    for k in range(GROUPS):
                        ins = dve.tensor_tensor(onehot[j][:, :, k * PER_GROUP:(k + 1) * PER_GROUP],
                                                pick[j][:, :, :], grp[:, :, k:k + 1].broadcast_to([P, NT, PER_GROUP]),
                                                ALU.mult)
                step(ins)
                step(dve.tensor_tensor(picked[:, :, :], onehot[0][:, :, :], onehot[1][:, :, :], ALU.add))
                at["picked"] = taken[0]
                dve.wait_ge(act_done, 2)
                step(dve.tensor_reduce(grp_sum[:, :, :], e_grp[:, :, :], AX_X, ALU.add))
                step(dve.scalar_tensor_tensor(out=den[:, :, :], in0=e2[:, :, :], scalar=1.0, in1=grp_sum[:, :, :],
                                              op0=ALU.add, op1=ALU.mult))
                step(dve.reciprocal(weight[0][:, :, :], den[:, :, :]))
                step(dve.tensor_tensor(weight[1][:, :, :], weight[0][:, :, :], e2[:, :, :], ALU.mult))
                dve.wait_ge(pe_done, 2)
                step(dve.memset(earlier[:, :, :], 0.0))
                dve.tensor_copy(earlier[:, 0:TILES, :], cn[:, 0:TILES, :])
                dve.tensor_copy(earlier[0:NEW, TILES, :], cn[0:NEW, TILES, :])
                step(dve.tensor_reduce(fullest[:, :], cn[:, NT, :], AX_X, ALU.max))
                step(dve.tensor_scalar(fullest[:, :], fullest[:, :], float(SLOTS - 1), None, ALU.add))
                step(dve.tensor_copy(n_pass[:, :], fullest[:, :]))
                step(dve.tensor_scalar(n_pass[:, :], n_pass[:, :], SLOT_BITS, None, ALU.logical_shift_right))
                step(dve.tensor_copy(g.passes[:, :], n_pass[0:1, :]))
                for j in range(2):
                    step(dve.tensor_tensor(at_pick[:, :, :], earlier[:, :, :], onehot[j][:, :, :], ALU.mult))
                    step(dve.tensor_reduce(place[:, :, :], at_pick[:, :, :], AX_X, ALU.add))
                    step(dve.tensor_tensor(at_pick[:, :, :], onehot[j][:, :, :],
                                           g.const("first_slot").unsqueeze(1).broadcast_to([P, NT, EXPERTS]),
                                           ALU.mult))
                    step(dve.tensor_reduce(address[:, :, :], at_pick[:, :, :], AX_X, ALU.add))
                    step(dve.scalar_tensor_tensor(out=address[:, :, :], in0=place[:, :, :],
                                                  scalar=float(TABLE_COLUMNS), in1=address[:, :, :],
                                                  op0=ALU.mult, op1=ALU.add))
                    step(dve.tensor_copy(whole[:, :], place[:, :, 0]))
                    step(dve.tensor_scalar(whole[:, :], whole[:, :], SLOT_BITS, None, ALU.logical_shift_right))
                    step(dve.tensor_copy(over[:, :, 0], whole[:, :]))
                    step(dve.scalar_tensor_tensor(out=address[:, :, :], in0=over[:, :, :],
                                                  scalar=float(PAIRS - SLOTS * TABLE_COLUMNS),
                                                  in1=address[:, :, :], op0=ALU.mult, op1=ALU.add))
                    dve.tensor_copy(slot_of[j][:, :], address[:, :, 0])
                    dve.tensor_copy(entry[j][:, :, SRC], g.const("token"))
                    dve.tensor_scalar(entry[j][:, :, DST], g.const("token"), float(j * TOKENS), None, ALU.add)
                    step(dve.tensor_copy(entry[j][:, :, WEIGHT:WEIGHT + 1].bitcast(F32), weight[j][:, :, :]))
                    at[f"entry {j}"] = taken[0]

            @block.sync
            def _(sp):
                sp.wait_ge(cleared, 1)
                sp.dma_start(g.d["table"], empty[:, :, :]).then_inc(emptied, 16)
                for t, n in enumerate(rows_of):
                    sp.wait_ge(rows_out, t + 1)
                    sp.dma_start(g.d["h_rows"][t * P:t * P + n, :], rows[t % 2][0:n, :]).then_inc(stored[t % 2], 16)
                sp.wait_ge(scattered, 16 * 2 * NT)
                sp.dma_start(g.table[:, :, :], g.d["table"]).then_inc(table_in, 16)
                sp.wait_ge(table_in, 16)
                for s in range(2):
                    sp.wait_ge(stored[s], 16 * ((NT + 1 - s) // 2))

            @block.gpsimd
            def _(pool):
                pool.wait_ge(emptied, 16)
                flat = g.d["table"].rearrange("p c w -> (p c) w")
                for j in range(2):
                    pool.wait_ge(dve_step, at[f"entry {j}"])
                    for t, n in enumerate(rows_of):
                        pool.indirect_dma_start(
                            out=flat, out_offset=bass.IndirectOffsetOnAxis(ap=slot_of[j][0:n, t:t + 1], axis=0),
                            in_=entry[j][0:n, t, :], in_offset=None).then_inc(scattered, 16)

            @block.scalar
            def _(act):
                def rows_copied(t):
                    act.wait_ge(rows_turned, t + 1)
                    if t >= 2:
                        act.wait_ge(stored[t % 2], 16 * (t // 2))
                    n = rows_of[t]
                    act.activation(rows[t % 2][0:n, :].rearrange("p (a c) -> p a c", a=2), turned[t % 2][0:n, :, :],
                                   ACT.Copy).then_inc(rows_out, 1)
                act.wait_ge(dve_step, at["group logits"])
                act.activation(e_grp[:, :, :], e_grp[:, :, :], ACT.Exp).then_inc(act_done, 1)
                rows_copied(0)
                rows_copied(1)
                act.wait_ge(dve_step, at["pair logits"])
                act.activation(e2[:, :, :], e2[:, :, :], ACT.Exp).then_inc(act_done, 1)
                for t in range(2, NT):
                    rows_copied(t)

            @block.tensor
            def _(pe):
                pe.wait_ge(loaded, 32)
                for t, n in enumerate(rows_of):
                    for k in range(KT):
                        mm = pe.matmul(pr[0:n, t, :], g.hT[:, k, t * P:t * P + n], w[:, k, :],
                                       start=(k == 0), stop=(k == KT - 1))
                mm.then_inc(pe_done, 1)

                def turn(t):
                    n = rows_of[t]
                    if t >= 2:
                        pe.wait_ge(rows_out, t - 1)
                    for k in range(KT):
                        mm = pe.transpose(turned[t % 2][0:n, k // 4, (k % 4) * P:(k % 4 + 1) * P],
                                          g.hT[:, k, t * P:t * P + n], g.const("ident"))
                    mm.then_inc(rows_turned, 1)
                for t in range(NT):
                    turn(t)
                pe.wait_ge(dve_step, at["picked"])
                for t in range(NT + 1):
                    n = rows_of[t] if t < NT else P
                    for u in range(min(t, TILES)):
                        pe.matmul(cn[0:n, t, :], g.const("ones")[:, 0:n], picked[:, u, :],
                                  start=(u == 0), stop=False)
                    if t < NT:
                        mm = pe.matmul(cn[0:n, t, :], g.const("before", n)[:, 0:n], picked[0:n, t, :],
                                       start=(t == 0), stop=True)
                    else:
                        mm = pe.matmul(cn[:, t, :], g.const("ones", NEW), picked[0:NEW, TILES, :],
                                       start=False, stop=True)
                mm.then_inc(pe_done, 1)


HALVES = [slice(0, SLOTS), slice(SLOTS, P)]
MOE_PE = ["rows turned"] + ["gate up 0", "gate up 1", "h turned 0", "h turned 1", "down"]
MOE_ACT = ["x low"] + ["silu 0", "silu 1", "hT 0", "hT 1", "y low"]
MOE_DVE = ["x high"] + ["h 0", "h 1", "y high"]


class ExpertWeights:

    def __init__(self, g, st, s, layer):
        self.g, self.s, self.layer = g, s, layer
        self.gu = st.sb(f"gu{s}", [P, KT, 2 * FF])
        self.down = st.sb(f"down{s}", [P, FF // P, D_MODEL])
        self.gu_in, self.down_in = st.sem(f"gu_in{s}"), st.sem(f"down_in{s}")

    def load_gate_up(self, sp, round_):
        expert = bass.ds(2 * MOE_LANES * round_ + self.s, 1)
        sp.dma_start(self.gu[:, :, :], self.g.d["w_gate_up"][self.layer][expert].rearrange("e p k f -> (e p) k f")
                     ).then_inc(self.gu_in, 16)

    def load_down(self, sp, round_):
        expert = bass.ds(2 * MOE_LANES * round_ + self.s, 1)
        sp.dma_start(self.down[:, :, :], self.g.d["w_down"][self.layer][expert].rearrange("e p k f -> (e p) k f")
                     ).then_inc(self.down_in, 16)


def experts_stage(nc, g, name, weights):
    with Stage(nc, name) as st:
        class Lane:
            pass
        lanes = []
        for s in range(MOE_LANES):
            ln = Lane()
            lanes.append(ln)
            ln.s = s
            ln.w = weights[2 * s:2 * s + 2]
            ln.x = st.sb(f"x{s}", [P, D_MODEL])
            ln.xT = st.sb(f"xT{s}", [P, KT, P])
            ln.gate = st.sb(f"gate{s}", [P, FF])
            ln.h = st.sb(f"h{s}", [P, FF])
            ln.hT = st.sb(f"hT{s}", [P, FF])
            ln.y = st.sb(f"y{s}", [P, D_MODEL])
            ln.src = st.sb(f"src{s}", [P, WORDS], U32)
            ln.dst = st.sb(f"dst{s}", [P, WORDS], U32)
            ln.x_in, ln.y_out = st.software_dma_sem(f"x_in{s}"), st.software_dma_sem(f"y_out{s}")
            ln.pe, ln.act = st.steps(f"pe{s}", MOE_PE), st.steps(f"act{s}", MOE_ACT)
            ln.dve = st.steps(f"dve{s}", MOE_DVE)
            ln.source, ln.dest = st.steps(f"source{s}", ["read"]), st.steps(f"dest{s}", ["read"])
        x_bank, gu_bank, y_bank = ([st.ps(f"{x}{n}") for n in range(2)] for x in ("bank_x", "bank_gu", "bank_y"))
        h_bank = [st.ps(f"bank_h{n}") for n in range(2)]
        zeroed = st.sem("zeroed")
        rounds = PAIRS // MOE_LANES

        def over_experts(eng, body):
            passes = eng.value_load(g.passes[0:1, 0:1], min_val=1, max_val=PASSES)
            with eng.Fori(0, passes) as p:
                with eng.Fori(0, rounds) as i:
                    body(p * rounds + i, i)
            return passes

        def before(ln, r):
            return lanes[ln.s - 1], (r if ln.s else r - 1)

        def after(ln, r):
            last = ln.s == MOE_LANES - 1
            return lanes[0 if last else ln.s + 1], (r + 1 if last else r)

        with st.block() as block:
            @block.sync
            def _(sp):
                def load(ln, last_round, i):
                    sp.wait_ge(ln.pe.sem, ln.pe.past("gate up 1", last_round))
                    for w in ln.w:
                        w.load_gate_up(sp, i)
                    sp.wait_ge(ln.pe.sem, ln.pe.past("down", last_round))
                    for w in ln.w:
                        w.load_down(sp, i)

                with sp.Fori(0, rounds - 1) as i:
                    for ln in lanes:
                        load(ln, i, i + 1)
                passes = sp.value_load(g.passes[0:1, 0:1], min_val=1, max_val=PASSES)
                count = st.ctx.enter_context(sp.register(f"{name}_passes"))
                sp.reg_load(count, g.passes[0:1, 0:1])
                with sp.If_ne(count, 1):
                    with sp.Fori(1, passes) as p:
                        with sp.Fori(0, rounds) as i:
                            for ln in lanes:
                                load(ln, p * rounds + i - 1, i)

            @block.gpsimd
            def _(pool):
                def gather(ln, column):
                    pool.tensor_copy(ln.src[:, :], g.table[:, bass.ds(column, 1), :].rearrange("p a w -> p (a w)")
                                     ).then_inc(*ln.source.done("read"))

                def scatter(ln):
                    pool.nop(nofuse=True)
                    pool.indirect_dma_start(
                        out=g.d["y_rows"], out_offset=bass.IndirectOffsetOnAxis(ap=ln.dst[:, DST:DST + 1], axis=0),
                        in_=ln.y[:, :], in_offset=None, bounds_check=2 * TOKENS - 1, oob_is_err=False
                    ).then_inc(ln.y_out, 16)

                def fetch(ln, r):
                    pool.wait_ge(ln.source.sem, ln.source.past("read", r))
                    pool.nop(nofuse=True)
                    pool.indirect_dma_start(
                        out=ln.x[:, :], out_offset=None, in_=g.d["h_rows"],
                        in_offset=bass.IndirectOffsetOnAxis(ap=ln.src[:, SRC:SRC + 1], axis=0),
                        bounds_check=TOKENS - 1, oob_is_err=False).then_inc(ln.x_in, 16)

                for ln in lanes:
                    ln.source.credit(pool)
                for ln in lanes:
                    gather(ln, ln.s)
                for ln in lanes:
                    pool.wait_ge(zeroed, ln.s + 1)
                    fetch(ln, 0)
                for ln in lanes:
                    pool.tensor_copy(ln.dst[:, :], g.table[:, COLUMNS, :]).then_inc(*ln.dest.done("read"))
                pool.wait_ge(zeroed, 2 * MOE_LANES)
                for ln in lanes:
                    pool.wait_ge(ln.dest.sem, 1)
                    scatter(ln)

                def body(r, i):
                    for ln in lanes:
                        pool.wait_ge(ln.y_out, 16 * (r + 1))
                        pool.tensor_copy(ln.dst[:, :], g.table[:, bass.ds(MOE_LANES * r + ln.s, 1), :].rearrange(
                            "p a w -> p (a w)")).then_inc(*ln.dest.done("read"))
                        pool.wait_ge(ln.x_in, 16 * (r + 1))
                        pool.wait_ge(ln.pe.sem, ln.pe.past("rows turned", r))
                        gather(ln, MOE_LANES * (r + 1) + ln.s)
                        fetch(ln, r + 1)
                        pool.wait_ge(ln.dest.sem, ln.dest.past("read", r))
                        pool.wait_ge(ln.act.sem, ln.act.past("y low", r))
                        pool.wait_ge(ln.dve.sem, ln.dve.past("y high", r))
                        scatter(ln)
                passes = over_experts(pool, body)
                for ln in lanes:
                    pool.wait_ge(ln.x_in, 16 * (passes * rounds + 1))
                    pool.wait_ge(ln.y_out, 16 * (passes * rounds + 1))

            @block.tensor
            def _(pe):
                for ln in lanes:
                    ln.pe.credit(pe)
                ident = g.const("ident")

                def turn(ln, r):
                    other, ro = before(ln, r)
                    pe.wait_ge(ln.x_in, 16 * (r + 1))
                    pe.wait_ge(other.act.sem, other.act.past("x low", ro))
                    pe.wait_ge(other.dve.sem, other.dve.past("x high", ro))
                    for k in range(KT):
                        mm = pe.transpose(x_bank[k // 4][:, (k % 4) * P:(k % 4 + 1) * P],
                                          ln.x[:, k * P:(k + 1) * P], ident)
                    mm.then_inc(*ln.pe.done("rows turned"))

                turn(lanes[0], 0)

                def body(r, i):
                    for ln in lanes:
                        other, ro = before(ln, r)
                        for w in ln.w:
                            pe.wait_ge(w.gu_in, 16 * (r + 1))
                        pe.wait_ge(ln.act.sem, ln.act.past("x low", r))
                        pe.wait_ge(ln.dve.sem, ln.dve.past("x high", r))
                        for m in range(2):
                            pe.wait_ge(other.dve.sem, other.dve.past(f"h {m}", ro))
                            for k in range(KT):
                                for w, H in zip(ln.w, HALVES):
                                    mm = pe.matmul(gu_bank[m][H, 0:FF], ln.xT[:, k, H], w.gu[:, k, m * FF:(m + 1) * FF],
                                                   start=(k == 0), stop=(k == KT - 1))
                            mm.then_inc(*ln.pe.done(f"gate up {m}"))
                        turn(*after(ln, r))
                        for w in ln.w:
                            pe.wait_ge(w.down_in, 16 * (r + 1))
                        for m in range(2):
                            pe.wait_ge(ln.dve.sem, ln.dve.past(f"h {m}", r))
                            pe.wait_ge(other.act.sem, other.act.past(f"hT {m}", ro))
                            pe.transpose(h_bank[m][:, 0:P], ln.h[:, m * P:(m + 1) * P], ident
                                         ).then_inc(*ln.pe.done(f"h turned {m}"))
                        for m in range(2):
                            pe.wait_ge(ln.act.sem, ln.act.past(f"hT {m}", r))
                            if m == 0:
                                pe.wait_ge(other.act.sem, other.act.past("y low", ro))
                                pe.wait_ge(other.dve.sem, other.dve.past("y high", ro))
                            for a in range(2):
                                for n, (w, H) in enumerate(zip(ln.w, HALVES)):
                                    at = m * P + n * SLOTS
                                    mm = pe.matmul(y_bank[a][H, :], ln.hT[:, at:at + SLOTS],
                                                   w.down[:, m, a * 512:(a + 1) * 512], start=(m == 0), stop=(m == 1))
                        mm.then_inc(*ln.pe.done("down"))
                over_experts(pe, body)

            @block.scalar
            def _(act):
                act.preload_act_table_set(SILU_SET)
                for ln in lanes:
                    ln.act.credit(act)

                def copy_x(ln, r):
                    act.wait_ge(ln.pe.sem, ln.pe.past("rows turned", r))
                    act.activation(ln.xT[:, 0:KT // 2, :].rearrange("p k c -> p (k c)"), x_bank[0][:, :],
                                   ACT.Copy).then_inc(*ln.act.done("x low"))

                copy_x(lanes[0], 0)

                def body(r, i):
                    for ln in lanes:
                        for m in range(2):
                            act.wait_ge(ln.pe.sem, ln.pe.past(f"gate up {m}", r))
                            act.wait_ge(ln.dve.sem, ln.dve.past(f"h {m}", r - 1))
                            act.activation(ln.gate[:, m * P:(m + 1) * P], gu_bank[m][:, 0:P], ACT.Silu
                                           ).then_inc(*ln.act.done(f"silu {m}"))
                        copy_x(*after(ln, r))
                        for m in range(2):
                            act.wait_ge(ln.pe.sem, ln.pe.past(f"h turned {m}", r))
                            act.activation(ln.hT[:, m * P:(m + 1) * P], h_bank[m][:, 0:P], ACT.Copy
                                           ).then_inc(*ln.act.done(f"hT {m}"))
                        act.wait_ge(ln.pe.sem, ln.pe.past("down", r))
                        act.wait_ge(ln.y_out, 16 * (r + 1))
                        act.activation(ln.y[:, 0:512], y_bank[0][:, :], ACT.Copy).then_inc(*ln.act.done("y low"))
                over_experts(act, body)

            @block.vector
            def _(dve):
                for ln in lanes:
                    ln.dve.credit(dve)
                    dve.memset(ln.x[:, :], 0.0).then_inc(zeroed, 1)
                for ln in lanes:
                    dve.memset(ln.y[:, :], 0.0).then_inc(zeroed, 1)

                def copy_x(ln, r):
                    dve.wait_ge(ln.pe.sem, ln.pe.past("rows turned", r))
                    dve.tensor_copy(ln.xT[:, KT // 2:, :].rearrange("p k c -> p (k c)"), x_bank[1][:, :]
                                    ).then_inc(*ln.dve.done("x high"))

                copy_x(lanes[0], 0)

                def body(r, i):
                    for ln in lanes:
                        weight = g.table[:, bass.ds(MOE_LANES * r + ln.s, 1), WEIGHT:WEIGHT + 1].rearrange("p a w -> p (a w)")
                        for m in range(2):
                            dve.wait_ge(ln.act.sem, ln.act.past(f"silu {m}", r))
                            dve.wait_ge(ln.pe.sem, ln.pe.past(f"gate up {m}", r))
                            dve.scalar_tensor_tensor(out=ln.h[:, m * P:(m + 1) * P], in0=gu_bank[m][:, P:2 * P],
                                                     scalar=weight.bitcast(F32), in1=ln.gate[:, m * P:(m + 1) * P],
                                                     op0=ALU.mult, op1=ALU.mult).then_inc(*ln.dve.done(f"h {m}"))
                        copy_x(*after(ln, r))
                        dve.wait_ge(ln.pe.sem, ln.pe.past("down", r))
                        dve.wait_ge(ln.y_out, 16 * (r + 1))
                        dve.tensor_copy(ln.y[:, 512:], y_bank[1][:, :]).then_inc(*ln.dve.done("y high"))
                over_experts(dve, body)


def gather_results_stage(nc, g, name):
    NT = TILES + 1
    rows_of = [P] * TILES + [NEW]
    with Stage(nc, name) as st:
        y = [[st.sb(f"y{s}{j}", [P, D_MODEL]) for j in range(2)] for s in range(2)]
        turned = [st.ps(f"turned{s}", (P, 2, 512)) for s in range(2)]
        loaded = [st.sem(f"loaded{s}") for s in range(2)]
        summed, turned_s, added = st.sem("summed"), st.sem("turned_s"), st.sem("added")
        with st.block() as block:
            @block.sync
            def _(sp):
                for t, n in enumerate(rows_of):
                    if t >= 2:
                        sp.wait_ge(turned_s, t - 1)
                    for j in range(2):
                        at = j * TOKENS + t * P
                        sp.dma_start(y[t % 2][j][0:n, :], g.d["y_rows"][at:at + n, :]).then_inc(loaded[t % 2], 16)

            @block.tensor
            def _(pe):
                for t, n in enumerate(rows_of):
                    pe.wait_ge(summed, t + 1)
                    if t >= 2:
                        pe.wait_ge(added, t - 1)
                    for k in range(KT):
                        mm = pe.transpose(turned[t % 2][:, k // 4, (k % 4) * n:(k % 4 + 1) * n],
                                          y[t % 2][0][0:n, k * P:(k + 1) * P], g.const("ident", n)[:, 0:n])
                    mm.then_inc(turned_s, 1)

            @block.vector
            def _(dve):
                def add(t):
                    n = rows_of[t]
                    dve.wait_ge(turned_s, t + 1)
                    x = g.xT[:, :, t * P:t * P + n].rearrange("p (a k) c -> p a k c", a=2)
                    dve.tensor_tensor(x, turned[t % 2][:, :, 0:4 * n].rearrange("p a (k c) -> p a k c", k=4), x,
                                      ALU.add).then_inc(added, 1)
                for t, n in enumerate(rows_of):
                    dve.wait_ge(loaded[t % 2], 32 * (t // 2 + 1))
                    dve.tensor_tensor(y[t % 2][0][0:n, :], y[t % 2][0][0:n, :], y[t % 2][1][0:n, :], ALU.add
                                      ).then_inc(summed, 1)
                    if t:
                        add(t - 1)
                add(NT - 1)


def moe(nc, g, name, layer, gain0):
    with ExitStack() as ctx:
        g.table = ctx.enter_context(nc.sbuf_tensor(name + "_table", [P, TABLE_COLUMNS, WORDS], U32))
        g.passes = ctx.enter_context(nc.sbuf_tensor(name + "_passes", [1, 1], I32))
        with Stage(nc, name + "_weights") as st:
            weights = [ExpertWeights(g, st, s, layer) for s in range(2 * MOE_LANES)]
            router_w = st.sb("router_w", [P, KT, GROUPS + EXPERTS])
            router_b = st.sb("router_b", [P, GROUPS + EXPERTS])
            router_in = st.sem("router_in")

            def prefetch(sp):
                sp.dma_start(router_w[:, :, :], g.d["router_w"][layer]).then_inc(router_in, 16)
                sp.dma_start(router_b[:, :], g.d["router_b"][layer]).then_inc(router_in, 16)
                for w in weights:
                    w.load_gate_up(sp, 0)
                    w.load_down(sp, 0)
            with nc.sbuf_tensor(name + "_h", [P, KT, TOKENS], F32) as g.hT:
                rms_norm_stage(nc, g, name + "_norm", gain0, prefetch)
                router_stage(nc, g, name + "_router", router_w, router_b, router_in)
            experts_stage(nc, g, name + "_experts", weights)
        gather_results_stage(nc, g, name + "_results")


Q_TILES = NSA_HEADS // 2
CMP_K, CMP_V, SLC_K, SLC_V, WIN_K, WIN_V = (Q_TILES + 2 * n for n in range(6))
NSA_TILES = Q_TILES + 12
ROWS = NSA_HEADS * DEC_SEQ
BLOCKS = PAST // CMP
P_BLOCKS = SEQ // CMP


def nsa_project_stage(nc, g):
    with Stage(nc, "nproj") as st:
        w = [st.sb(f"w{s}", [P, KT, P]) for s in range(2)]
        wg = st.sb("wg", [P, KT, 3 * NSA_HEADS])
        new_gates = st.sb("new_gates", [NEW, 3 * NSA_HEADS])
        acc = [st.ps(f"acc{s}", (P, 2, 512)) for s in range(2)]
        gate_acc = st.ps("gate_acc")
        loaded = [st.sem(f"loaded{s}") for s in range(2)]
        gates_loaded, gates_done, new_gates_done = st.sem("gates_loaded"), st.sem("gates_done"), st.sem("new_gates_done")
        spread, sums_in = st.sem("spread"), st.sem("sums_in")
        pe_s = [st.steps(f"pe{s}", ["product"]) for s in range(2)]
        act_s = [st.steps(f"act{s}", ["copied"]) for s in range(2)]
        rounds = NSA_TILES // 2
        NG = 3 * NSA_HEADS
        pages = PageSums(nc, g, st, g.past_c, PAGES_EARLY, PAGES_NSA)
        with st.block() as block:
            @block.sync
            def _(sp):
                sp.dma_start(wg[:, :, :], g.d["nsa_w_gates"]).then_inc(gates_loaded, 16)
                sp.dma_start(g.past_c[:, 0:PAGES_EARLY, :], g.d["first_sums"]).then_inc(sums_in, 16)
                for s in range(2):
                    sp.dma_start(w[s][:, :, :], g.d["nsa_w"][s]).then_inc(loaded[s], 16)
                with sp.Fori(0, rounds - 1) as i:
                    for s in range(2):
                        sp.wait_ge(pe_s[s].sem, pe_s[s].past("product", i))
                        sp.dma_start(w[s][:, :, :],
                                     g.d["nsa_w"][bass.ds(2 * i + 2 + s, 1)].rearrange("t p k c -> (t p) k c")
                                     ).then_inc(loaded[s], 16)
                        pages.load(sp, s, i)
                for s in range(2):
                    pages.load(sp, s, rounds - 1)
                sp.wait_ge(new_gates_done, 1)
                sp.dma_start(g.d["gate_scratch"], new_gates[:, :]).then_inc(spread, 16)
                sp.wait_ge(spread, 16)
                for t in range(DEC_SEQ):
                    src = g.d["gate_scratch"].rearrange("(b t) (h r) -> t h b r", t=DEC_SEQ, r=3)
                    sp.dma_start(g.row_gates[t:ROWS:DEC_SEQ, :, :], src[t]).then_inc(spread, 16)
                sp.wait_ge(spread, 16 * (1 + DEC_SEQ))
                sp.wait_ge(sums_in, 16)

            @block.tensor
            def _(pe):
                for s in range(2):
                    pe_s[s].credit(pe)
                pe.wait_ge(gates_loaded, 16)
                for t in range(TILES + 1):
                    n = P if t < TILES else NEW
                    for k in range(KT):
                        mm = pe.matmul(gate_acc[0:n, t * NG:(t + 1) * NG], g.hT[:, k, t * P:t * P + n], wg[:, k, :],
                                       start=(k == 0), stop=(k == KT - 1))
                mm.then_inc(gates_done, 1)
                with pe.Fori(0, rounds) as i:
                    for s in range(2):
                        pe.wait_ge(loaded[s], 16 * (i + 1))
                        pe.wait_ge(act_s[s].sem, act_s[s].past("copied", i - 1))
                        for k in range(KT):
                            for a in range(2):
                                mm = pe.matmul(acc[s][:, a, 0:HALF], w[s][:, k, :],
                                               g.hT[:, k, a * HALF:(a + 1) * HALF], start=(k == 0), stop=(k == KT - 1))
                        mm.then_inc(*pe_s[s].done("product"))

            @block.vector
            def _(dve):
                pages.credit(dve)
                with dve.Fori(0, rounds) as i:
                    for s in range(2):
                        pages.sum(dve, s, i)

            @block.scalar
            def _(act):
                for s in range(2):
                    act_s[s].credit(act)
                act.wait_ge(gates_done, 1)
                act.activation(new_gates[:, :], gate_acc[0:NEW, TILES * NG:(TILES + 1) * NG], ACT.Sigmoid
                               ).then_inc(new_gates_done, 1)
                act.activation(g.gates[:, :, :, :].rearrange("p t h r -> p (t h r)"), gate_acc[:, 0:TILES * NG],
                               ACT.Sigmoid)
                with act.Fori(0, rounds) as i:
                    for s in range(2):
                        act.wait_ge(pe_s[s].sem, pe_s[s].past("product", i))
                        act.activation(halves(g.proj[:, bass.ds(2 * i + s, 1), :].rearrange("p a t -> p (a t)")),
                                       acc[s][:, :, 0:HALF], ACT.Copy).then_inc(*act_s[s].done("copied"))


def nsa_norm_stage(nc, g):
    normed = list(range(Q_TILES)) + [SLC_K, SLC_K + 1, WIN_K, WIN_K + 1]
    n_norm = len(normed) + 1
    with Stage(nc, "nnorm") as st:
        sq = [st.sb(f"sq{s}", [P, TOKENS]) for s in range(2)]
        root = [st.sb(f"root{s}", [P, TOKENS]) for s in range(2)]
        means = st.sb("means", [P, 4, P_BLOCKS])
        total = [st.ps(f"total{s}", (P, 2, 512)) for s in range(2)]
        turn = [st.ps(f"turn{s}") for s in range(2)]
        squared, summed, rooted = st.sem("squared"), st.sem("summed"), st.sem("rooted")
        logged, normalised = st.sem("logged"), st.sem("normalised")
        turned, turn_out = st.sem("turned"), st.sem("turn_out")
        averaged, cleared = st.sem("averaged"), st.sem("cleared")
        stored = st.sem("stored")
        ident = g.const("ident")
        turns = []
        for n, V in enumerate((SLC_V, WIN_V)):
            for pair in range(2):
                for t in range(TILES):
                    turns.append((g.proj[:, V + pair, t * P:(t + 1) * P], g.v_rows[:, n, t, pair * P:(pair + 1) * P]))
                turns.append((g.proj[:, V + pair, SEQ:TOKENS], g.v_new[:, n, pair * P:(pair + 1) * P]))
        for pair in range(2):
            turns.append((means[:, 2 + pair, :], g.vc[:, pair * P:(pair + 1) * P]))
        with st.block() as block:
            @block.sync
            def _(sp):
                sp.wait_ge(normalised, n_norm)
                sp.dma_start(g.d["kv_out"], g.proj[:, Q_TILES:, :]).then_inc(stored, 16)
                sp.wait_ge(stored, 16)

            @block.scalar
            def _(act):
                act.preload_act_table_set(EXP_LN_SET)
                def rest(n):
                    w = TOKENS if n < len(normed) else 2 * P_BLOCKS
                    act.wait_ge(summed, n + 1)
                    out, tot = root[n % 2][:, 0:w], total[n % 2]
                    if n >= 2:
                        act.wait_ge(normalised, n - 1)
                    src = tot[:, :, 0:HALF] if w == TOKENS else tot[:, 0, 0:w]
                    act.activation(halves(out) if w == TOKENS else out, src, ACT.Ln, scale=1.0 / HD,
                                   bias=g.eps[:, 0:1]).then_inc(logged, 1)
                    act.wait_ge(logged, n + 1)
                    act.activation(out, out, ACT.Exp, scale=-0.5).then_inc(rooted, 1)

                for n in range(n_norm):
                    if n >= 2:
                        act.wait_ge(summed, n - 1)
                    if n < len(normed):
                        act.activation(sq[n % 2][:, :], g.proj[:, normed[n], :], ACT.Square).then_inc(squared, 1)
                    else:
                        act.wait_ge(averaged, 2)
                        act.activation(sq[n % 2][:, 0:2 * P_BLOCKS], means[:, 0:2, :].rearrange("p a c -> p (a c)"),
                                       ACT.Square).then_inc(squared, 1)
                    if n:
                        rest(n - 1)
                rest(n_norm - 1)

            @block.tensor
            def _(pe):
                for n in range(n_norm):
                    pe.wait_ge(squared, n + 1)
                    if n >= 2:
                        pe.wait_ge(logged, n - 1)
                    if n < len(normed):
                        for a in range(2):
                            mm = pe.matmul(total[n % 2][:, a, 0:HALF], g.const("head_ones"),
                                           sq[n % 2][:, a * HALF:(a + 1) * HALF], start=True, stop=True)
                    else:
                        mm = pe.matmul(total[n % 2][:, 0, 0:2 * P_BLOCKS], g.const("head_ones"),
                                       sq[n % 2][:, 0:2 * P_BLOCKS], start=True, stop=True)
                    mm.then_inc(summed, 1)
                pe.wait_ge(averaged, 2)
                for n, (src, dst) in enumerate(turns):
                    if n >= 2:
                        pe.wait_ge(turn_out, n - 1)
                    pe.transpose(turn[n % 2][0:dst.shape[0], 0:P], src, ident).then_inc(turned, 1)

            @block.vector
            def _(dve):
                dve.tensor_reduce(means[:, :, :], g.proj[:, CMP_K:CMP_K + 4, 0:SEQ].rearrange(
                    "p a (c t) -> p a c t", t=CMP), AX_X, ALU.add).then_inc(averaged, 1)
                dve.wait_ge(averaged, 1)
                dve.tensor_scalar(means[:, :, :], means[:, :, :], 1.0 / CMP, None, ALU.mult).then_inc(averaged, 1)
                dve.memset(g.qb[:, :, :, :], 0.0).then_inc(cleared, 1)
                for n in range(n_norm):
                    dve.wait_ge(rooted, n + 1)
                    if n < len(normed):
                        x = g.proj[:, normed[n], :]
                        gain = Q_GAIN if normed[n] < Q_TILES else K_GAIN
                        dve.scalar_tensor_tensor(out=x, in0=x, scalar=g.gains[:, gain:gain + 1],
                                                 in1=root[n % 2][:, :], op0=ALU.mult, op1=ALU.mult
                                                 ).then_inc(normalised, 1)
                    else:
                        dve.wait_ge(averaged, 2)
                        dve.scalar_tensor_tensor(out=g.kc[:, :, :].rearrange("p a c -> p (a c)"),
                                                 in0=means[:, 0:2, :].rearrange("p a c -> p (a c)"),
                                                 scalar=g.gains[:, K_GAIN:K_GAIN + 1],
                                                 in1=root[n % 2][:, 0:2 * P_BLOCKS],
                                                 op0=ALU.mult, op1=ALU.mult).then_inc(normalised, 1)
                dve.wait_ge(normalised, Q_TILES)
                dve.wait_ge(cleared, 1)
                for pair in range(2):
                    for half in range(2):
                        R = slice(HD * half, HD * (half + 1))
                        for j in range(GROUP):
                            at = 16 * half + DEC_SEQ * j
                            dve.tensor_scalar(
                                g.qb[R, pair, :, at:at + DEC_SEQ],
                                g.proj[R, pair * GROUP + j, SEQ:TOKENS].rearrange("p (b t) -> p b t", t=DEC_SEQ),
                                HD ** -0.5, None, ALU.mult)
                dve.wait_ge(normalised, len(normed))
                for n, K in enumerate((SLC_K, WIN_K)):
                    dve.tensor_copy(g.k_new[:, n, :, :], g.proj[:, K:K + 2, SEQ:TOKENS])
                for n, (src, dst) in enumerate(turns):
                    dve.wait_ge(turned, n + 1)
                    dve.tensor_copy(dst, turn[n % 2][0:dst.shape[0], 0:P]).then_inc(turn_out, 1)


UNIT_DVE = ["mask cmp", "mask", "max cmp", "max", "seen", "cmp sum", "floor", "inverse", "gate", "scale",
            "cmp turned", "win turned"]
ATT_PE = ["scores 0"] + [x for t in range(TILES)
                         for x in (f"turn {t}", f"scores {t + 1}", f"out {t}") if x != f"scores {TILES}"]
ATT_DVE = [f"{n} {t}" for t in range(TILES) for n in UNIT_DVE]
ATT_ACT = ["exp cmp 0", "exp 0"] + [
    x for t in range(TILES) for x in (f"slc turned {t}", f"exp cmp {t + 1}", f"exp {t + 1}", f"out {t}")
    if not x.endswith(f" {TILES}")]


def prompt_attention_stage(nc, g):
    assert SEQ // SEL <= TOP_N and SEQ <= WINDOW
    with Stage(nc, "patt") as st:
        class Lane:
            pass
        lanes = []
        for s in range(2):
            ln = Lane()
            lanes.append(ln)
            ln.s, ln.R = s, slice(HD * s, HD * (s + 1))
            ln.p = st.sb(f"p{s}", [P, 2, SEQ])
            ln.pT = st.sb(f"pT{s}", [P, 2, SEQ])
            ln.sc = st.sb(f"sc{s}", [P, P_BLOCKS])
            ln.pcT = st.sb(f"pcT{s}", [P_BLOCKS, P])
            ln.neg_max = st.sb(f"neg_max{s}", [P, 3])
            ln.sums = st.sb(f"sums{s}", [P, 3])
            ln.scores = st.ps(f"scores{s}", (P, 2, 512))
            ln.cmp = st.ps(f"cmp{s}")
            ln.out = st.ps(f"out{s}")
            ln.pe, ln.dve, ln.act = (st.steps(f"pe{s}", ATT_PE), st.steps(f"dve{s}", ATT_DVE),
                                     st.steps(f"act{s}", ATT_ACT))
        q = st.sb("q", [P, SEQ])
        q_staged = st.steps("q_staged", ["q"])
        taken = PAGES_EARLY + PAGES_NSA * NSA_TILES
        pages = PageSums(nc, g, st, g.past_c, taken, PAGES_ATT)
        assert taken + 2 * PAGES_ATT * 2 * GROUP == DEC_BATCH * N_PAGES
        ident = g.const("ident")

        def alternate(rule, i, pair):
            for _ in zip(*(rule(ln, i, pair) for ln in lanes)):
                pass

        def before(steps, name, t, i):
            return steps.past(f"{name} {t - 1}", i) if t else steps.past(f"{name} {TILES - 1}", i - 1)

        with st.block() as block:
            @block.sync
            def _(sp):
                with sp.Fori(0, 2 * GROUP) as i:
                    for s in range(2):
                        pages.load(sp, s, i)

            @block.gpsimd
            def _(pool):
                q_staged.credit(pool)
                for pair in range(2):
                    with pool.Fori(pair * GROUP, (pair + 1) * GROUP) as i:
                        for ln in lanes:
                            pool.wait_ge(ln.pe.sem, ln.pe.past(f"scores {TILES - 1}", i - 1))
                        pool.tensor_tensor(q[:, :], g.proj[:, bass.ds(i, 1), 0:SEQ].rearrange("p a t -> p (a t)"),
                                           g.const("q_scale").broadcast_to([P, SEQ]), ALU.mult).then_inc(*q_staged.done("q"))

            @block.tensor
            def _(pe):
                def rule(ln, i, pair):
                    kvh = 2 * pair + ln.s
                    V = slice(kvh * HD, (kvh + 1) * HD)

                    def scores(t):
                        n = (t + 1) * P
                        q_t = q[ln.R, t * P:(t + 1) * P]
                        if t == 0:
                            pe.wait_ge(q_staged.sem, q_staged.past("q", i))
                        pe.wait_ge(ln.act.sem, before(ln.act, "slc turned", t, i))
                        pe.wait_ge(ln.dve.sem, before(ln.dve, "win turned", t, i))
                        pe.matmul(ln.cmp[:, 0:P_BLOCKS], q_t, g.kc[ln.R, pair, :], start=True, stop=True)
                        for a, K in enumerate((SLC_K, WIN_K)):
                            mm = pe.matmul(ln.scores[:, a, 0:n], q_t, g.proj[ln.R, K + pair, 0:n],
                                           start=True, stop=True)
                        mm.then_inc(*ln.pe.done(f"scores {t}"))

                    scores(0)
                    yield
                    for t in range(TILES):
                        pe.wait_ge(ln.dve.sem, ln.dve.past(f"scale {t}", i))
                        pe.transpose(ln.cmp[0:P_BLOCKS, 128:256], ln.sc[:, :], ident)
                        for a in range(2):
                            for b in range(t + 1):
                                mm = pe.transpose(ln.scores[:, a, b * P:(b + 1) * P], ln.p[:, a, b * P:(b + 1) * P],
                                                  ident)
                        mm.then_inc(*ln.pe.done(f"turn {t}"))
                        yield
                        if t + 1 < TILES:
                            scores(t + 1)
                            yield
                        pe.wait_ge(ln.act.sem, ln.act.past(f"slc turned {t}", i))
                        pe.wait_ge(ln.dve.sem, ln.dve.past(f"win turned {t}", i))
                        pe.wait_ge(ln.act.sem, before(ln.act, "out", t, i))
                        out = ln.out[ln.R, 0:P]
                        pe.matmul(out, g.vc[:, V], ln.pcT[:, :], start=True, stop=False)
                        for a in range(2):
                            for b in range(t + 1):
                                mm = pe.matmul(out, g.v_rows[:, a, b, V], ln.pT[:, a, b * P:(b + 1) * P],
                                               start=False, stop=(a == 1 and b == t))
                        mm.then_inc(*ln.pe.done(f"out {t}"))
                        yield

                for ln in lanes:
                    ln.pe.credit(pe)
                for pair in range(2):
                    with pe.Fori(pair * GROUP, (pair + 1) * GROUP) as i:
                        alternate(rule, i, pair)

            @block.vector
            def _(dve):
                def rule(ln, i, pair):
                    for t in range(TILES):
                        n = (t + 1) * P
                        blocks = slice(t * P_BLOCKS, (t + 1) * P_BLOCKS)
                        d = ln.dve

                        def after(name):
                            dve.wait_ge(d.sem, d.past(f"{name} {t}", i))
                        dve.wait_ge(ln.pe.sem, ln.pe.past(f"scores {t}", i))
                        own = ln.scores[:, :, t * P:n]
                        dve.tensor_tensor(ln.sc[:, :], ln.cmp[:, 0:P_BLOCKS], g.const("cmp_neg")[:, blocks],
                                          ALU.add).then_inc(*d.done(f"mask cmp {t}"))
                        dve.tensor_tensor(own, own, g.const("causal_neg").unsqueeze(1).broadcast_to([P, 2, P]),
                                          ALU.add).then_inc(*d.done(f"mask {t}"))
                        after("mask cmp")
                        dve.tensor_reduce(ln.neg_max[:, 0:1], ln.sc[:, :], AX_X, ALU.max, negate=True
                                          ).then_inc(*d.done(f"max cmp {t}"))
                        after("mask")
                        dve.tensor_reduce(ln.neg_max[:, 1:3], ln.scores[:, :, 0:n], AX_X, ALU.max, negate=True
                                          ).then_inc(*d.done(f"max {t}"))
                        yield
                        dve.wait_ge(ln.act.sem, ln.act.past(f"exp cmp {t}", i))
                        dve.tensor_tensor(ln.sc[:, :], ln.sc[:, :], g.const("cmp_seen")[:, blocks], ALU.mult
                                          ).then_inc(*d.done(f"seen {t}"))
                        after("seen")
                        dve.tensor_reduce(ln.sums[:, 0:1], ln.sc[:, :], AX_X, ALU.add).then_inc(*d.done(f"cmp sum {t}"))
                        yield
                        after("cmp sum")
                        dve.wait_ge(ln.act.sem, ln.act.past(f"exp {t}", i))
                        dve.tensor_scalar(ln.sums[:, :], ln.sums[:, :], 1e-30, None, ALU.max
                                          ).then_inc(*d.done(f"floor {t}"))
                        after("floor")
                        dve.reciprocal(ln.sums[:, :], ln.sums[:, :]).then_inc(*d.done(f"inverse {t}"))
                        after("inverse")
                        head = bass.ds(i + GROUP * (pair + ln.s), 1)
                        dve.tensor_tensor(ln.sums[:, :], ln.sums[:, :],
                                          g.gates[:, t, head, :].rearrange("p a r -> p (a r)"), ALU.mult
                                          ).then_inc(*d.done(f"gate {t}"))
                        after("gate")
                        for a in range(2):
                            dve.tensor_scalar(ln.p[:, a, 0:n], ln.p[:, a, 0:n], ln.sums[:, a + 1:a + 2], None, ALU.mult)
                        dve.tensor_scalar(ln.sc[:, :], ln.sc[:, :], ln.sums[:, 0:1], None, ALU.mult
                                          ).then_inc(*d.done(f"scale {t}"))
                        yield
                        dve.wait_ge(ln.pe.sem, ln.pe.past(f"turn {t}", i))
                        dve.wait_ge(ln.pe.sem, before(ln.pe, "out", t, i))
                        dve.tensor_copy(ln.pcT[:, :], ln.cmp[0:P_BLOCKS, 128:256]
                                        ).then_inc(*d.done(f"cmp turned {t}"))
                        dve.tensor_copy(ln.pT[:, 1, 0:n], ln.scores[:, 1, 0:n]).then_inc(*d.done(f"win turned {t}"))
                        if t == 2:
                            pages.sum(dve, ln.s, i)
                        yield

                for ln in lanes:
                    ln.dve.credit(dve)
                pages.credit(dve)
                for pair in range(2):
                    with dve.Fori(pair * GROUP, (pair + 1) * GROUP) as i:
                        alternate(rule, i, pair)

            @block.scalar
            def _(act):
                def rule(ln, i, pair):
                    def exps(t):
                        n = (t + 1) * P
                        act.wait_ge(ln.dve.sem, ln.dve.past(f"max cmp {t}", i))
                        act.activation(ln.sc[:, :], ln.sc[:, :], ACT.Exp, bias=ln.neg_max[:, 0:1]
                                       ).then_inc(*ln.act.done(f"exp cmp {t}"))
                        act.wait_ge(ln.dve.sem, ln.dve.past(f"max {t}", i))
                        act.wait_ge(ln.pe.sem, before(ln.pe, "turn", t, i))
                        for a in range(2):
                            ins = act.activation(ln.p[:, a, 0:n], ln.scores[:, a, 0:n], ACT.Exp,
                                                 bias=ln.neg_max[:, a + 1:a + 2],
                                                 accum_out=ln.sums[:, a + 1:a + 2])
                        ins.then_inc(*ln.act.done(f"exp {t}"))

                    exps(0)
                    yield
                    for t in range(TILES):
                        n = (t + 1) * P
                        act.wait_ge(ln.pe.sem, ln.pe.past(f"turn {t}", i))
                        act.activation(ln.pT[:, 0, 0:n], ln.scores[:, 0, 0:n], ACT.Copy
                                       ).then_inc(*ln.act.done(f"slc turned {t}"))
                        yield
                        if t + 1 < TILES:
                            exps(t + 1)
                            yield
                        act.wait_ge(ln.pe.sem, ln.pe.past(f"out {t}", i))
                        act.activation(g.attT[ln.R, bass.ds(i, 1), t * P:n].rearrange("p a t -> p (a t)"),
                                       ln.out[ln.R, 0:P], ACT.Copy).then_inc(*ln.act.done(f"out {t}"))
                        yield

                for ln in lanes:
                    ln.act.credit(act)
                for pair in range(2):
                    with act.Fori(pair * GROUP, (pair + 1) * GROUP) as i:
                        alternate(rule, i, pair)


def compress_norm_stage(nc, g):
    with Stage(nc, "cnorm") as st:
        sq = st.sb("sq", [P, 4, 512])
        root = st.sb("root", [P, 4, 512])
        v = st.sb("v", [P, 2, DEC_BATCH * BLOCKS])
        total = st.ps("total", (P, 4, 512))
        turn = [st.ps(f"turn{s}") for s in range(2)]
        squared, summed, logged, rooted = st.sem("squared"), st.sem("summed"), st.sem("logged"), st.sem("rooted")
        averaged, turned, turn_out = st.sem("averaged"), st.sem("turned"), st.sem("turn_out")
        src = g.past_c[:, :, :].rearrange("p g (a c) -> p g a c", a=4)
        per = 64 * 8
        with st.block() as block:
            @block.vector
            def _(dve):
                for pair in range(2):
                    dve.tensor_scalar(src[:, :, pair, :], src[:, :, pair, :], 1.0 / CMP, None, ALU.mult)
                    ins = dve.tensor_scalar(v[:, pair, :].rearrange("p (g c) -> p g c", c=4), src[:, :, 2 + pair, :],
                                            1.0 / CMP, None, ALU.mult)
                ins.then_inc(averaged, 1)
                for n in range(4):
                    dve.wait_ge(rooted, n + 1)
                    dve.wait_ge(averaged, 1)
                    part = src[:, 64 * n:64 * (n + 1), 0:2, :]
                    for pair in range(2):
                        dve.scalar_tensor_tensor(
                            out=part[:, :, pair, :], in0=part[:, :, pair, :], scalar=g.gains[:, K_GAIN:K_GAIN + 1],
                            in1=root[:, n, :].rearrange("p (g a c) -> p g a c", a=2, c=4)[:, :, pair, :],
                            op0=ALU.mult, op1=ALU.mult)
                for b in range(DEC_BATCH):
                    for pair in range(2):
                        n = 2 * b + pair
                        dve.wait_ge(turned, n + 1)
                        dve.tensor_copy(g.vc_past[:, b, pair * P:(pair + 1) * P], turn[n % 2][:, 0:P]
                                        ).then_inc(turn_out, 1)

            @block.scalar
            def _(act):
                act.preload_act_table_set(EXP_LN_SET)
                act.wait_ge(averaged, 1)
                for n in range(4):
                    act.activation(sq[:, n, :].rearrange("p (g a c) -> p g (a c)", a=2, c=4),
                                   src[:, 64 * n:64 * (n + 1), 0:2, :].rearrange("p g a c -> p g (a c)"), ACT.Square
                                   ).then_inc(squared, 1)
                for n in range(4):
                    act.wait_ge(summed, n + 1)
                    act.activation(root[:, n, :], total[:, n, :], ACT.Ln, scale=1.0 / HD, bias=g.eps[:, 0:1]
                                   ).then_inc(logged, 1)
                    act.wait_ge(logged, n + 1)
                    act.activation(root[:, n, :], root[:, n, :], ACT.Exp, scale=-0.5).then_inc(rooted, 1)

            @block.tensor
            def _(pe):
                for n in range(4):
                    pe.wait_ge(squared, n + 1)
                    pe.matmul(total[:, n, :], g.const("head_ones"), sq[:, n, :], start=True, stop=True
                              ).then_inc(summed, 1)
                pe.wait_ge(averaged, 1)
                for b in range(DEC_BATCH):
                    for pair in range(2):
                        n = 2 * b + pair
                        if n >= 2:
                            pe.wait_ge(turn_out, n - 1)
                        pe.transpose(turn[n % 2][:, 0:P],
                                     v[:, pair, b * BLOCKS:(b + 1) * BLOCKS], g.const("ident")
                                     ).then_inc(turned, 1)


CHUNKS_KV = 8
PAGES_C = N_PAGES // CHUNKS_KV
KEYS_C = PAGES_C * PAGE
SLC_END = PAST + NEW
WIN_END = SLC_END + WINDOW
KEYS = WIN_END + NEW
SMP_GROUPS = 4
PAGES_G = N_PAGES // SMP_GROUPS
REST = 0
SMP_OUT = (["turn 0"] + [x for n in range(SMP_GROUPS) for x in (f"turn {n + 1}", f"out {n}")]
           + [f"out {SMP_GROUPS}"])


def sample_attention_stage(nc, g):
    n_sel = PAST // SEL + 1
    assert TOP_N == 16
    with Stage(nc, "satt") as st:
        keys = st.sb("keys", [P, N_PAGES, 2 * PAGE])
        values = st.sb("values", [P, N_PAGES, KVH * HD])
        win_k = st.sb("win_k", [P, 2, WINDOW])
        win_v = st.sb("win_v", [P, WINDOW // P, KVH * HD])
        qb = st.sb("qb", [P, 2, NEW])
        kc = st.sb("kc", [P, 2, BLOCKS])
        s_all = [st.sb(f"s_all{s}", [ROWS, KEYS]) for s in range(2)]
        pc = [st.sb(f"pc{s}", [ROWS, BLOCKS]) for s in range(2)]
        pT = st.sb("pT", [P, N_PAGES + 7, ROWS])
        score = [st.sb(f"score{n}", [ROWS, n_sel]) for n in range(3)]
        best = [st.sb(f"best{n}", [ROWS, 8]) for n in range(2)]
        unselected = st.sb("unselected", [ROWS, n_sel])
        neg_max = st.sb("neg_max", [ROWS, 3])
        sums = st.sb("sums", [ROWS, 3])
        out = st.sb("out", [ROWS, KVH * HD])
        ps = [st.ps(f"scores{n}") for n in range(2)]
        ps_cmp, ps_new = st.ps("cmp"), st.ps("new")
        ps_turn = [st.ps(f"turn{n}") for n in range(2)]
        ps_out, ps_end = st.ps("out_acc"), st.ps("end")
        k_in = [st.sem(f"k_in{c}") for c in range(CHUNKS_KV)]
        v_in = [st.sem(f"v_in{n}") for n in range(SMP_GROUPS)]
        win_k_in, win_v_in, cleared = st.sem("win_k_in"), st.sem("win_v_in"), st.sem("cleared")
        chunks = range(CHUNKS_KV)
        pe_select = st.steps("pe_select", ["cmp scores", "importance"])
        pe_score = st.steps("pe_score", [f"scores {c}" for c in chunks] + ["new scores", "win scores"])
        pe_sum = st.steps("pe_sum", SMP_OUT)
        pe_end = st.steps("pe_end", ["end"])
        dve_select = st.steps("dve_select", ["cmp max", "cmp floor", "cmp inverse", "cmp p", "imp", "score", "top a",
                                             "out a", "top b", "out b", "unselected"])
        dve_score = st.steps("dve_score", [f"masked {c}" for c in chunks]
                             + ["new masked", "win masked", "slc max", "win max"])
        dve_soften = st.steps("dve_soften", ["floor", "inverse", "gate", "cmp scaled", "slc scaled", "win scaled"])
        dve_end = st.steps("dve_end", ["placed"])
        act_select, act_soften = st.steps("act_select", ["cmp exp"]), st.steps("act_soften", ["slc exp", "win exp"])
        pool_select = st.steps("pool_select", ["staged"])
        dve_sum = st.steps("dve_sum", [f"turned {n}" for n in range(SMP_GROUPS + 1)] + ["out"])
        NEW_SLC, NEW_WIN = N_PAGES + 5, N_PAGES + 6
        CMP_AT = N_PAGES + 4
        ident = g.const("ident")

        def pages_of(eng, i, first, count):
            _, pages = nc.values_load_multi_w_load_instructions(
                g.page_table[0:1, bass.ds(i * N_PAGES + first, count)], engines=[eng], min_val=0, max_val=N_POOL - 1)
            return enumerate(pages, first)

        def page_part(page, part):
            return g.d["slc_pool"][bass.ds(page, 1)].rearrange("g p n -> (g p) n")[:, part * 256:(part + 1) * 256]

        def window_of(i):
            return g.d["win"][bass.ds(i, 1)].rearrange("b p a n -> (b p) a n")

        def over_batches(eng, body):
            with eng.Fori(0, DEC_BATCH // 2 - 1) as j:
                for s in range(2):
                    body(2 * j + s, s, True, True)
            body(DEC_BATCH - 2, 0, True, False)
            body(DEC_BATCH - 1, 1, False, False)

        with st.block() as block:
            @block.sync
            def _(sp):
                with sp.Fori(0, DEC_BATCH) as i:
                    for c in chunks:
                        sp.wait_ge(pe_score.sem, pe_score.past(f"scores {c}", i - 1))
                        for n, page in pages_of(mybir.EngineType.SP, i, c * PAGES_C, PAGES_C):
                            sp.dma_start(keys[:, n, :], page_part(page, 0)).then_inc(k_in[c], 16)
                    sp.wait_ge(pe_score.sem, pe_score.past("win scores", i - 1))
                    sp.dma_start(win_k[:, :, :], window_of(i)[:, 0:2, :]).then_inc(win_k_in, 16)

            @block.gpsimd
            def _(pool):
                def stage(i):
                    pool.wait_ge(pe_score.sem, pe_score.past("win scores", i - 1))
                    pool.tensor_copy(qb[:, :, :], g.qb[:, :, bass.ds(i, 1), :].rearrange("p a b n -> p a (b n)"))
                    pages = g.past_c[:, bass.ds(i * N_PAGES, N_PAGES), :]
                    for pair in range(2):
                        ins = pool.tensor_copy(kc[:, pair, :].rearrange("p (g c) -> p g c", c=PAGE // CMP),
                                               pages[:, :, 4 * pair:4 * pair + 4])
                    ins.then_inc(*pool_select.done("staged"))

                def body(i, s, more, yet_more):
                    if yet_more:
                        stage(i + 2)

                pool_select.credit(pool)
                for i in range(2):
                    stage(i)
                over_batches(pool, body)

            @block.tensor
            def _(pe):
                small = g.const("ident", ROWS)[:, 0:ROWS]

                def by_pair(out_, rhs):
                    for pair in range(2):
                        mm = pe.matmul(out_[NEW * pair:NEW * (pair + 1), :], qb[:, pair, :], rhs(pair),
                                       start=True, stop=True)
                    return mm

                def select_scores(i):
                    pe.wait_ge(pool_select.sem, pool_select.past("staged", i))
                    pe.wait_ge(dve_select.sem, dve_select.past("imp", i - 1))
                    by_pair(ps_cmp[0:ROWS, 0:BLOCKS], lambda pair: kc[:, pair, :]
                            ).then_inc(*pe_select.done("cmp scores"))

                def select_importance(i, s):
                    pe.wait_ge(dve_select.sem, dve_select.past("cmp p", i))
                    pe.nop(nofuse=True)
                    pe.matmul(ps_cmp[0:ROWS, BLOCKS:2 * BLOCKS], g.const("group_sum", ROWS)[:, 0:ROWS], pc[s][:, :],
                              start=True, stop=True).then_inc(*pe_select.done("importance"))

                def score_all(i):
                    for c in chunks:
                        pe.wait_ge(k_in[c], 16 * PAGES_C * (i + 1))
                        pe.wait_ge(dve_score.sem, dve_score.past(f"masked {c - 2}", i) if c >= 2 else
                                   dve_score.past("win masked", i - 1))
                        by_pair(ps[c % 2][0:ROWS, :],
                                lambda pair: keys[:, c * PAGES_C:(c + 1) * PAGES_C, pair * P:(pair + 1) * P]
                                ).then_inc(*pe_score.done(f"scores {c}"))
                    by_pair(ps_new[0:ROWS, 0:NEW], lambda pair: g.k_new[:, 0, pair, :])
                    by_pair(ps_new[0:ROWS, NEW:2 * NEW], lambda pair: g.k_new[:, 1, pair, :]
                            ).then_inc(*pe_score.done("new scores"))
                    pe.wait_ge(win_k_in, 16 * (i + 1))
                    pe.wait_ge(dve_score.sem, dve_score.past(f"masked {CHUNKS_KV - 2}", i))
                    by_pair(ps[0][0:ROWS, :], lambda pair: win_k[:, pair, :]).then_inc(*pe_score.done("win scores"))

                def turn(n, i, s):
                    bank = ps_turn[n % 2]
                    if n < 2:
                        pe.wait_ge(dve_soften.sem, dve_soften.past("win scaled", i))
                    else:
                        pe.wait_ge(dve_sum.sem, dve_sum.past(f"turned {n - 2}", i))
                    pe.nop(nofuse=True)

                    def turned(slot, n_keys, src):
                        return pe.transpose(bank[0:n_keys, slot * ROWS:(slot + 1) * ROWS], src, small)
                    if n == REST:
                        for m in range(WINDOW // P):
                            at = SLC_END + m * P
                            turned(m, P, s_all[s][:, at:at + P])
                        turned(4, P, pc[s][:, :])
                        turned(5, NEW, s_all[s][:, PAST:SLC_END])
                        mm = turned(6, NEW, s_all[s][:, WIN_END:KEYS])
                    else:
                        for m in range(PAGES_G):
                            at = ((n - 1) * PAGES_G + m) * PAGE
                            mm = turned(m, P, s_all[s][:, at:at + PAGE])
                    mm.then_inc(*pe_sum.done(f"turn {n}"))

                def multiply(n, i):
                    acc = ps_out[0:ROWS, 0:KVH * HD]
                    pe.wait_ge(dve_sum.sem, dve_sum.past(f"turned {n}", i))
                    if n == REST:
                        pe.wait_ge(dve_sum.sem, dve_sum.past("out", i - 1))
                        pe.wait_ge(win_v_in, 16 * (i + 1))
                        for m in range(WINDOW // P):
                            pe.matmul(acc, pT[:, N_PAGES + m, :], win_v[:, m, :], start=(m == 0), stop=False)
                        pe.matmul(acc, pT[:, CMP_AT, :], g.vc_past[:, bass.ds(i, 1), :].rearrange("p a n -> p (a n)"),
                                  start=False, stop=False)
                        pe.matmul(acc, pT[0:NEW, NEW_SLC, :], g.v_new[:, 0, :], start=False, stop=False)
                        mm = pe.matmul(acc, pT[0:NEW, NEW_WIN, :], g.v_new[:, 1, :], start=False, stop=False)
                    else:
                        pe.wait_ge(v_in[n - 1], 16 * PAGES_G * (i + 1))
                        for m in range(PAGES_G):
                            page = (n - 1) * PAGES_G + m
                            mm = pe.matmul(acc, pT[:, page, :], values[:, page, :], start=False,
                                           stop=(page == N_PAGES - 1))
                    mm.then_inc(*pe_sum.done(f"out {n}"))

                def end(i):
                    pe.wait_ge(dve_sum.sem, dve_sum.past("out", i))
                    pe.wait_ge(dve_end.sem, dve_end.past("placed", i - 1))
                    pe.nop(nofuse=True)
                    for pair in range(2):
                        mm = pe.transpose(ps_end[:, pair * ROWS:(pair + 1) * ROWS], out[:, pair * P:(pair + 1) * P],
                                          small)
                    mm.then_inc(*pe_end.done("end"))

                def body(i, s, more, yet_more):
                    if more:
                        score_all(i + 1)
                    turn(0, i, s)
                    if yet_more:
                        select_scores(i + 2)
                    for n in range(SMP_GROUPS):
                        turn(n + 1, i, s)
                        if n == SMP_GROUPS - 1 and yet_more:
                            select_importance(i + 2, s)
                        multiply(n, i)
                    multiply(SMP_GROUPS, i)
                    end(i)

                for steps in (pe_select, pe_score, pe_sum, pe_end):
                    steps.credit(pe)
                for i in range(2):
                    select_scores(i)
                    select_importance(i, i)
                    if i == 0:
                        score_all(0)
                over_batches(pe, body)

            @block.scalar
            def _(act):
                def load_values(i):
                    act.wait_ge(pe_sum.sem, pe_sum.past("out 0", i - 1))
                    act.dma_start(win_v[:, :, :].rearrange("p (a m) n -> p a (m n)", a=2), window_of(i)[:, 2:4, :]
                                  ).then_inc(win_v_in, 16)
                    for n in range(SMP_GROUPS):
                        act.wait_ge(pe_sum.sem, pe_sum.past(f"out {n + 1}", i - 1))
                        for m, page in pages_of(mybir.EngineType.Activation, i, n * PAGES_G, PAGES_G):
                            act.dma_start(values[:, m, :], page_part(page, 1)).then_inc(v_in[n], 16)

                def select(i, s, first=False):
                    act.wait_ge(dve_select.sem, dve_select.past("cmp max", i))
                    if not first:
                        act.wait_ge(pe_sum.sem, pe_sum.past("turn 0", i - 2))
                    act.activation(pc[s][:, :], ps_cmp[0:ROWS, 0:BLOCKS], ACT.Exp, bias=neg_max[:, 0:1],
                                   accum_out=sums[:, 0:1]).then_inc(*act_select.done("cmp exp"))

                def soften(i, s):
                    for a, (name, x) in enumerate((("slc", s_all[s][:, 0:SLC_END]), ("win", s_all[s][:, SLC_END:KEYS]))):
                        act.wait_ge(dve_score.sem, dve_score.past(f"{name} max", i))
                        act.activation(x, x, ACT.Exp, bias=neg_max[:, a + 1:a + 2], accum_out=sums[:, a + 1:a + 2]
                                       ).then_inc(*act_soften.done(f"{name} exp"))

                def body(i, s, more, yet_more):
                    if more:
                        soften(i + 1, 1 - s)
                    if yet_more:
                        select(i + 2, s)
                    if more:
                        load_values(i + 1)

                for steps in (act_select, act_soften):
                    steps.credit(act)
                select(0, 0, first=True)
                load_values(0)
                select(1, 1)
                soften(0, 0)
                over_batches(act, body)

            @block.vector
            def _(dve):
                def own_select(name, i):
                    dve.wait_ge(dve_select.sem, dve_select.past(name, i))

                def select_weights(i, s):
                    dve.wait_ge(pe_select.sem, pe_select.past("cmp scores", i))
                    dve.tensor_reduce(neg_max[:, 0:1], ps_cmp[0:ROWS, 0:BLOCKS], AX_X, ALU.max, negate=True
                                      ).then_inc(*dve_select.done("cmp max"))
                    dve.wait_ge(act_select.sem, act_select.past("cmp exp", i))
                    dve.tensor_scalar(sums[:, 0:1], sums[:, 0:1], 1e-30, None, ALU.max
                                      ).then_inc(*dve_select.done("cmp floor"))
                    own_select("cmp floor", i)
                    dve.reciprocal(sums[:, 0:1], sums[:, 0:1]).then_inc(*dve_select.done("cmp inverse"))
                    own_select("cmp inverse", i)
                    dve.tensor_scalar(pc[s][:, :], pc[s][:, :], sums[:, 0:1], None, ALU.mult
                                      ).then_inc(*dve_select.done("cmp p"))

                def select_blocks(i):
                    dve.wait_ge(pe_select.sem, pe_select.past("importance", i))
                    past = slice(0, n_sel - 1)
                    dve.tensor_reduce(score[1][:, past], ps_cmp[0:ROWS, BLOCKS:2 * BLOCKS].rearrange(
                        "r (s c) -> r s c", c=SEL // CMP), AX_X, ALU.add).then_inc(*dve_select.done("imp"))
                    own_select("imp", i)
                    dve.tensor_tensor(score[0][:, past], score[1][:, past], g.const("forced", ROWS), ALU.max
                                      ).then_inc(*dve_select.done("score"))
                    for n, name in enumerate(("a", "b")):
                        own_select("score" if n == 0 else "out a", i)
                        dve.nop(nofuse=True)
                        dve.max(best[n][:, :], score[n][:, :]).then_inc(*dve_select.done(f"top {name}"))
                        own_select(f"top {name}", i)
                        dve.nop(nofuse=True)
                        dve.match_replace(score[n + 1][:, :], best[n][:, :], score[n][:, :], NEG
                                          ).then_inc(*dve_select.done(f"out {name}"))
                    own_select("out b", i)
                    dve.tensor_scalar(unselected[:, :], score[2][:, :], NEG / 10, NEG, ALU.is_gt, ALU.mult
                                      ).then_inc(*dve_select.done("unselected"))

                def mask_all(i, s, first=False):
                    x = s_all[s]
                    dve.wait_ge(dve_select.sem, dve_select.past("unselected", i))
                    if not first:
                        dve.wait_ge(pe_sum.sem, pe_sum.past(f"turn {SMP_GROUPS}", i - 2))
                    per = KEYS_C // SEL
                    for c in chunks:
                        dve.wait_ge(pe_score.sem, pe_score.past(f"scores {c}", i))
                        dve.tensor_tensor(
                            x[:, c * KEYS_C:(c + 1) * KEYS_C].rearrange("r (s k) -> r s k", k=SEL),
                            ps[c % 2][0:ROWS, :].rearrange("r (s k) -> r s k", k=SEL),
                            unselected[:, c * per:(c + 1) * per].unsqueeze(2).broadcast_to([ROWS, per, SEL]), ALU.add
                        ).then_inc(*dve_score.done(f"masked {c}"))
                    dve.wait_ge(pe_score.sem, pe_score.past("new scores", i))
                    new_neg = g.const("new_neg", ROWS).rearrange("r (b k) -> r b k", b=DEC_BATCH)
                    new_neg = new_neg[:, bass.ds(i, 1), :].rearrange("r b k -> r (b k)")
                    dve.tensor_tensor(x[:, PAST:SLC_END], ps_new[0:ROWS, 0:NEW], new_neg, ALU.add)
                    dve.tensor_tensor(x[:, WIN_END:KEYS], ps_new[0:ROWS, NEW:2 * NEW], new_neg, ALU.add
                                      ).then_inc(*dve_score.done("new masked"))
                    dve.wait_ge(pe_score.sem, pe_score.past("win scores", i))
                    dve.tensor_tensor(x[:, SLC_END:WIN_END], ps[0][0:ROWS, :], g.const("win_neg", ROWS), ALU.add
                                      ).then_inc(*dve_score.done("win masked"))

                def maxima(i, s):
                    x = s_all[s]
                    dve.wait_ge(dve_score.sem, dve_score.past("new masked", i))
                    dve.tensor_reduce(neg_max[:, 1:2], x[:, 0:SLC_END], AX_X, ALU.max, negate=True
                                      ).then_inc(*dve_score.done("slc max"))
                    dve.wait_ge(dve_score.sem, dve_score.past("win masked", i))
                    dve.tensor_reduce(neg_max[:, 2:3], x[:, SLC_END:KEYS], AX_X, ALU.max, negate=True
                                      ).then_inc(*dve_score.done("win max"))

                def soften(i, s):
                    x = s_all[s]

                    def own(name):
                        dve.wait_ge(dve_soften.sem, dve_soften.past(name, i))
                    dve.wait_ge(act_soften.sem, act_soften.past("win exp", i))
                    dve.tensor_scalar(sums[:, 1:3], sums[:, 1:3], 1e-30, None, ALU.max
                                      ).then_inc(*dve_soften.done("floor"))
                    own("floor")
                    dve.reciprocal(sums[:, 1:3], sums[:, 1:3]).then_inc(*dve_soften.done("inverse"))
                    gate = g.row_gates[:, bass.ds(i, 1), :].rearrange("r b n -> r (b n)")
                    own("inverse")
                    dve.tensor_tensor(sums[:, 1:3], sums[:, 1:3], gate[:, 1:3], ALU.mult
                                      ).then_inc(*dve_soften.done("gate"))
                    dve.tensor_scalar(pc[s][:, :], pc[s][:, :], gate[:, 0:1], None, ALU.mult
                                      ).then_inc(*dve_soften.done("cmp scaled"))
                    own("gate")
                    dve.tensor_scalar(x[:, 0:SLC_END], x[:, 0:SLC_END], sums[:, 1:2], None, ALU.mult
                                      ).then_inc(*dve_soften.done("slc scaled"))
                    dve.tensor_scalar(x[:, SLC_END:KEYS], x[:, SLC_END:KEYS], sums[:, 2:3], None, ALU.mult
                                      ).then_inc(*dve_soften.done("win scaled"))

                def place(i):
                    dve.wait_ge(pe_end.sem, pe_end.past("end", i))
                    for pair in range(2):
                        for half in range(2):
                            R = slice(HD * half, HD * (half + 1))
                            at = pair * ROWS + 16 * (2 * pair + half)
                            ins = dve.tensor_copy(
                                g.attT[R, pair * GROUP:(pair + 1) * GROUP, bass.ds(i * DEC_SEQ + SEQ, DEC_SEQ)],
                                ps_end[R, at:at + 16].rearrange("p (j t) -> p j t", t=DEC_SEQ))
                    ins.then_inc(*dve_end.done("placed"))

                def turned(n, i):
                    dve.wait_ge(pe_sum.sem, pe_sum.past(f"turn {n}", i))
                    bank = ps_turn[n % 2]
                    if n == REST:
                        at = N_PAGES
                        dve.tensor_copy(pT[:, at:at + 5, :].rearrange("p g r -> p (g r)"), bank[:, 0:5 * ROWS])
                        ins = dve.tensor_copy(pT[0:NEW, at + 5:at + 7, :].rearrange("p g r -> p (g r)"),
                                              bank[0:NEW, 5 * ROWS:7 * ROWS])
                    else:
                        at = (n - 1) * PAGES_G
                        ins = dve.tensor_copy(pT[:, at:at + PAGES_G, :].rearrange("p g r -> p (g r)"), bank[:, :])
                    ins.then_inc(*dve_sum.done(f"turned {n}"))

                def body(i, s, more, yet_more):
                    if more:
                        mask_all(i + 1, 1 - s)
                    turned(0, i)
                    turned(1, i)
                    if more:
                        maxima(i + 1, 1 - s)
                    turned(2, i)
                    turned(3, i)
                    if yet_more:
                        select_weights(i + 2, s)
                    turned(4, i)
                    if yet_more:
                        select_blocks(i + 2)
                    if more:
                        soften(i + 1, 1 - s)
                    dve.wait_ge(pe_sum.sem, pe_sum.past(f"out {SMP_GROUPS}", i))
                    dve.wait_ge(pe_end.sem, pe_end.past("end", i - 1))
                    dve.tensor_copy(out[:, :], ps_out[0:ROWS, 0:KVH * HD]).then_inc(*dve_sum.done("out"))
                    place(i)

                for steps in (dve_select, dve_score, dve_soften, dve_sum, dve_end):
                    steps.credit(dve)
                dve.memset(score[0][:, n_sel - 1:n_sel], SEL_BIG).then_inc(cleared, 1)
                dve.wait_ge(cleared, 1)
                select_weights(0, 0)
                select_blocks(0)
                mask_all(0, 0, first=True)
                maxima(0, 0)
                select_weights(1, 1)
                select_blocks(1)
                soften(0, 0)
                over_batches(dve, body)


def nsa(nc, g):
    with ExitStack() as ctx:
        def sb(stack, name, shape):
            return stack.enter_context(nc.sbuf_tensor("nsa_" + name, shape, F32))
        g.attT = sb(ctx, "attT", [P, KT, TOKENS])
        with ExitStack() as smp:
            g.past_c = sb(smp, "past_c", [P, DEC_BATCH * N_PAGES, 4 * PAGE // CMP])
            g.vc_past = sb(smp, "vc_past", [P, DEC_BATCH, KVH * HD])
            g.row_gates = sb(smp, "row_gates", [ROWS, DEC_BATCH, 3])
            g.qb = sb(smp, "qb", [P, 2, DEC_BATCH, NEW])
            g.k_new = sb(smp, "k_new", [P, 2, 2, NEW])
            g.v_new = sb(smp, "v_new", [NEW, 2, KVH * HD])
            with ExitStack() as prompt:
                g.proj = sb(prompt, "proj", [P, NSA_TILES, TOKENS])
                g.gates = sb(prompt, "gates", [P, TILES, NSA_HEADS, 3])
                g.v_rows = sb(prompt, "v_rows", [P, 2, TILES, KVH * HD])
                g.kc = sb(prompt, "kc", [P, 2, P_BLOCKS])
                g.vc = sb(prompt, "vc", [P_BLOCKS, KVH * HD])
                with nc.sbuf_tensor("nsa_h", [P, KT, TOKENS], F32) as g.hT:
                    rms_norm_stage(nc, g, "norm1", LN_MIX + KT)
                    nsa_project_stage(nc, g)
                nsa_norm_stage(nc, g)
                prompt_attention_stage(nc, g)
            compress_norm_stage(nc, g)
            sample_attention_stage(nc, g)
        out_project_stage(nc, g, "nsa_out", g.d["nsa_wo"], g.attT)


def store_stage(nc, g):
    with Stage(nc, "store") as st:
        stored = st.sem("stored")
        with st.block() as block:
            @block.sync
            def _(sp):
                sp.dma_start(g.d["y"], g.xT[:, :, :]).then_inc(stored, 16)
                sp.wait_ge(stored, 16)


class Globals:

    def const(self, name, rows=P):
        at, n = CONST_AT[name]
        return self.consts[0:rows, at:at + n]


LN_MIX, LN_FFN, O_GAIN, Q_GAIN, K_GAIN, GAINS = 0, 16, 32, 33, 34, 35


def decoder(nc, d, stop=99):
    g = Globals()
    g.d = d
    with ExitStack() as ctx:
        def sb(name, shape, dt=F32):
            return ctx.enter_context(nc.sbuf_tensor(name, shape, dt))

        g.consts = sb("consts", [P, CONST_W])
        g.gains = sb("gains_sb", [P, GAINS])
        g.eps = sb("eps", [P, 1])
        g.xT = sb("xT", [P, KT, TOKENS])
        g.page_table = sb("page_table_sb", [1, DEC_BATCH * N_PAGES], I32)
        eps_set = ctx.enter_context(nc.semaphore("eps_set"))
        with nc.Block(no_gpsimd_drain=True) as block:
            @block.vector
            def _(dve):
                dve.memset(g.eps[:, :], EPS).then_inc(eps_set, 1)
                dve.wait_ge(eps_set, 1)
        load_inputs(nc, g)
        with ExitStack() as gdn:
            g.zT = gdn.enter_context(nc.sbuf_tensor("zT", [P, HEADS, TOKENS], F32))
            with ExitStack() as mixer:
                g.qkv = mixer.enter_context(nc.sbuf_tensor("qkv", [P, CONV_TILES, TOKENS], F32))
                def gate(name, shape):
                    return mixer.enter_context(nc.sbuf_tensor("gate_" + name, shape, F32))
                g.gate_g, g.beta, g.G, g.eG, g.tail = (
                    gate(n, [P, TILES + 1, HEADS]) for n in ("g", "beta", "G", "eG", "tail"))
                g.e_chunk = gate("e_chunk", [P, 2 * TILES, HEADS])
                g.e_batch = gate("e_batch", [P, DEC_BATCH, HEADS])
                with (nc.sbuf_tensor("h_gdn", [P, KT, TOKENS], F32) as g.hT,
                      nc.sbuf_tensor("first_sums", [P, PAGES_EARLY, 4 * PAGE // CMP], F32) as g.first_sums):
                    rms_norm_stage(nc, g, "norm0", LN_MIX)
                    gdn_project_stage(nc, g)
                    if stop == 1:
                        return debug_out(nc, g, {"hT": g.hT, "qkv": g.qkv, "zT": g.zT})
                    gdn_gates_stage(nc, g)
                gdn_heads_stage(nc, g)
            out_project_stage(nc, g, "gdn_out", g.d["gdn_wo"], g.zT)
        if stop == 2:
            return debug_out(nc, g, {"xT": g.xT})
        if stop != -4:
            moe(nc, g, "moe0", 0, LN_FFN)
        if stop == 3:
            return debug_out(nc, g, {"xT": g.xT})
        nsa(nc, g)
        if stop == 4:
            return debug_out(nc, g, {"xT": g.xT})
        moe(nc, g, "moe1", 1, LN_FFN + KT)
        store_stage(nc, g)


def debug_out(nc, g, what):
    for n, t in what.items():
        t_d = nc.dram_tensor("dbg_" + n, list(t.shape), F32, kind="ExternalOutput").ap()
        s = nc.semaphore("dbgs_" + n).__enter__()
        with nc.Block(no_gpsimd_drain=True) as block:
            @block.sync
            def _(sp):
                sp.dma_start(t_d, t[tuple(slice(None) for _ in t.shape)]).then_inc(s, 16)
                sp.wait_ge(s, 16)


def lay_out(i):
    a = {}
    def feature_major(x):
        return x.T.reshape(KT, P, -1).transpose(1, 0, 2)
    def tiles_of(w):
        return w.reshape(KT, P, -1, P).transpose(2, 1, 0, 3)
    a["consts"] = np.concatenate([CONSTANTS[k] for k in CONST_AT], 1)
    x = np.concatenate([i["x_prompt"].reshape(SEQ, D_MODEL), i["x_sample"].reshape(NEW, D_MODEL)])
    a["x"] = feature_major(x)
    cols = [i["ln_mix"].reshape(2 * KT, P).T, i["ln_ffn"].reshape(2 * KT, P).T, i["gdn_o_gain"][0][:, None],
            np.tile(i["nsa_q_gain"][0], 2)[:, None], np.tile(i["nsa_k_gain"][0], 2)[:, None]]
    a["gains"] = np.concatenate(cols, 1)
    w = i["gdn_w_in"][0]
    a["gdn_w"] = w[:, :4 * 1024].reshape(KT, P, 32, P).transpose(2, 1, 0, 3)
    a["gdn_w_ab"] = w[:, 4 * 1024:].reshape(KT, P, 2 * HEADS).transpose(1, 0, 2)
    a["gdn_rows"] = np.tile(np.stack([i["gdn_a_log"][0], i["gdn_dt_bias"][0]])[None], (P, 1, 1))
    a["gdn_S"] = i["state_gdn_S"][0].transpose(1, 2, 0, 3)
    a["gdn_wo"] = tiles_of(i["gdn_w_out"][0])
    a["router_w"] = np.concatenate([i["moe_w_grp"], i["moe_w_exp"]], 2).reshape(2, KT, P, -1).transpose(0, 2, 1, 3)
    a["router_b"] = np.tile(np.concatenate([i["moe_b_grp"], i["moe_b_exp"]], 1)[:, None, :], (1, P, 1))
    gu = np.stack([i["moe_w_gate"], i["moe_w_up"]], 3).reshape(2, EXPERTS, KT, P, 2, 2, P)
    a["w_gate_up"] = gu.transpose(0, 1, 3, 2, 5, 4, 6).reshape(2, EXPERTS, P, KT, 2 * FF)
    a["w_down"] = i["moe_w_down"].reshape(2, EXPERTS, FF // P, P, D_MODEL).transpose(0, 1, 3, 2, 4)
    wn = i["nsa_w_in"][0]
    order = [8 * pair + 4 * half + j for pair in range(2) for j in range(GROUP) for half in range(2)]
    q_cols = (np.array(order)[:, None] * HD + np.arange(HD)).ravel()
    n_kv = NSA_HEADS * HD
    cols = np.concatenate([q_cols, np.arange(n_kv, n_kv + 12 * P)])
    a["nsa_w"] = wn[:, cols].reshape(KT, P, NSA_TILES, P).transpose(2, 1, 0, 3)
    a["nsa_w_gates"] = wn[:, n_kv + 12 * P:].reshape(KT, P, 3 * NSA_HEADS).transpose(1, 0, 2)
    a["nsa_wo"] = tiles_of(i["nsa_w_out"][0][q_cols])
    a["page_table"] = i["page_table"].reshape(1, -1).astype(np.int32)
    a["cmp_pool"] = i["cache_nsa_cmp_kv"][0].reshape(N_POOL, PAGE, 4, P).transpose(0, 3, 2, 1).reshape(N_POOL, P, -1)
    def keys_major(x):
        k = x[:, :, 0].reshape(len(x), -1, 2, P).transpose(0, 3, 2, 1).reshape(len(x), P, -1)
        v = x[:, :, 1].reshape(len(x), -1, P, KVH * HD).transpose(0, 2, 1, 3).reshape(len(x), P, -1)
        return np.concatenate([k, v], 2)
    a["slc_pool"] = keys_major(i["cache_nsa_slc_kv"][0])
    a["win"] = keys_major(i["cache_nsa_win_kv"][0]).reshape(DEC_BATCH, P, 4, 4 * P)
    a["taps"] = i["gdn_conv_w"][0].reshape(CONV, CONV_TILES, P).transpose(2, 1, 0)
    a["conv_prev"] = i["state_gdn_conv"][0].reshape(DEC_BATCH, CONV - 1, CONV_TILES, P).transpose(3, 2, 0, 1)
    return a


OUTPUTS = {"conv_out": (P, CONV_TILES, (1 + DEC_BATCH) * (CONV - 1)),
           "p_S": (HEADS, P, P), "s_S": (HEADS, P, DEC_BATCH, P),
           "kv_out": (P, 12, TOKENS), "win_out": (DEC_BATCH, P, 4, 4 * P), "y": (P, KT, TOKENS)}


def build(nc, arrays, stop=99):
    d = {}
    for name, a in arrays.items():
        d[name] = nc.dram_tensor("in_" + name, a.shape, mybir.dt.from_np(a.dtype), kind="ExternalInput").ap()
    for name, shape in OUTPUTS.items():
        d[name] = nc.dram_tensor("out_" + name, shape, F32, kind="ExternalOutput").ap()
    d["h_rows"] = nc.dram_tensor("h_rows", (TOKENS, D_MODEL), F32, kind="Internal").ap()
    d["y_rows"] = nc.dram_tensor("y_rows", (2 * TOKENS, D_MODEL), F32, kind="Internal").ap()
    d["table"] = nc.dram_tensor("table", (P, TABLE_COLUMNS, WORDS), U32, kind="Internal").ap()
    d["first_sums"] = nc.dram_tensor("first_sums_d", (P, PAGES_EARLY, 4 * PAGE // CMP), F32, kind="Internal").ap()
    d["gate_scratch"] = nc.dram_tensor("gate_scratch", (NEW, 3 * NSA_HEADS), F32, kind="Internal").ap()
    decoder(nc, d, stop)
    return nc


def kernel(**inputs):
    import concourse.bacc as _bacc
    from concourse.bass_utils import run_bass_kernel_spmd

    arrays = {name: np.ascontiguousarray(a) for name, a in lay_out({n: np.asarray(a) for n, a in inputs.items()}).items()}
    nc = build(_bacc.Bacc("TRN2", target_bir_lowering=False, num_devices=1), arrays)
    r = run_bass_kernel_spmd(nc, [{"in_" + n: a for n, a in arrays.items()}], core_ids=[0]).results[0]

    def tokens_major(a):
        return a.transpose(2, 1, 0).reshape(a.shape[2], -1)
    y = tokens_major(r["out_y"])
    conv = r["out_conv_out"].transpose(2, 1, 0).reshape(1 + DEC_BATCH, CONV - 1, -1)
    kv = tokens_major(r["out_kv_out"]).reshape(TOKENS, 3, 2, KVH, HD)
    p_kv, s_kv = kv[:SEQ], kv[SEQ:].reshape(DEC_BATCH, DEC_SEQ, 3, 2, KVH, HD)
    win = r["out_win_out"].reshape(DEC_BATCH, P, 8, 2 * P)
    k_old = r["out_win_out"][:, :, 0:2, :].transpose(0, 3, 2, 1).reshape(DEC_BATCH, WINDOW, KVH, HD)
    v_old = win[:, :, 4:, :].transpose(0, 2, 1, 3).reshape(DEC_BATCH, WINDOW, KVH, HD)
    old = np.stack([k_old, v_old], 2)
    s_win = np.concatenate([old[:, DEC_SEQ:], s_kv[:, :, 2]], 1)
    out = (y[:SEQ].reshape(1, SEQ, D_MODEL), y[SEQ:].reshape(DEC_BATCH, DEC_SEQ, D_MODEL),
           r["out_p_S"][None, None], conv[None, :1], p_kv[None, None, :, 0], p_kv[None, None, :, 1],
           p_kv[None, None, :, 2], r["out_s_S"].transpose(2, 0, 1, 3)[None], conv[None, 1:],
           s_kv[None, :, :, 0], s_kv[None, :, :, 1], s_win[None])
    return tuple(np.ascontiguousarray(a) for a in out)
```
